# Optimizing a Trainium2 kernel written in Bass

```python
import math
import jax
import jax.numpy as jnp
from jax import lax
import numpy as np
import jax, jax.numpy as jnp

D_MODEL = 1024
BATCH = 1
SEQ = 1024
DEPTH = 2

CTX_LEN = 256
GRID_W = 64
HEAD_DIM = 64
ROPE_BASE = 10000.0
EPS = 1e-6
NEG_INF = -1e30
ATTN_SCALE = HEAD_DIM ** -0.5
Q_BLOCK = 128
N_EVEN = (DEPTH + 1) // 2
N_ODD = DEPTH // 2

A_HEADS = 8
A_KV_HEADS = 2
A_GROUP = A_HEADS // A_KV_HEADS
WINDOW = 128
A_WIDTH = A_HEADS * HEAD_DIM
B_HEADS = 4
B_VDIM = 2 * HEAD_DIM
B_WIDTH = B_HEADS * B_VDIM
EVEN_SPLITS = (A_WIDTH, A_KV_HEADS * HEAD_DIM, A_KV_HEADS * HEAD_DIM, A_WIDTH,
               B_HEADS * 2 * HEAD_DIM, B_HEADS * 2 * HEAD_DIM, B_WIDTH, B_WIDTH)
EVEN_IN = sum(EVEN_SPLITS)

G_HEADS = 4
G_DK = (D_MODEL // 2) // G_HEADS
G_DV = D_MODEL // G_HEADS
G_RANK = 16
G_TAU = 16.0
G_CHUNK = 64
ODD_SPLITS = (G_HEADS * G_DK, G_HEADS * G_DK, G_HEADS * G_DV, G_HEADS * G_DV, G_RANK, G_RANK)
ODD_IN = sum(ODD_SPLITS)


def rms_norm(x, g):
    xf = x.astype(jnp.float32)
    y = xf * lax.rsqrt(jnp.mean(xf * xf, axis=-1, keepdims=True) + EPS)
    return (y * g.astype(jnp.float32)).astype(x.dtype)

def split_cols(p, sizes):
    out, start = [], 0
    for s in sizes:
        out.append(p[..., start:start + s])
        start += s
    return out

def adaln_params(cond, w, b):
    m = jax.nn.silu(cond) @ w + b
    return jnp.split(m, 3, axis=-1)

def grid_positions(n_rows):
    rows = jnp.repeat(jnp.arange(n_rows, dtype=jnp.int32), GRID_W)
    cols = jnp.tile(jnp.arange(GRID_W, dtype=jnp.int32), n_rows)
    return rows, cols

def rope_1d(x, pos):
    m = x.shape[-1] // 2
    inv = ROPE_BASE ** (-jnp.arange(m, dtype=jnp.float32) / m)
    ang = pos.astype(jnp.float32)[:, None] * inv[None, :]
    cos = jnp.cos(ang)[:, None, :]
    sin = jnp.sin(ang)[:, None, :]
    x1 = x[..., :m].astype(jnp.float32)
    x2 = x[..., m:].astype(jnp.float32)
    return jnp.concatenate([x1 * cos - x2 * sin, x2 * cos + x1 * sin], axis=-1)

def rope_axial(x, rows, cols):
    h = x.shape[-1] // 2
    return jnp.concatenate([rope_1d(x[..., :h], rows), rope_1d(x[..., h:], cols)], axis=-1).astype(x.dtype)

def sink_attention(qg, k, v, sink, valid):
    s = jnp.einsum('bqhgd,bkhd->bhgqk', qg, k).astype(jnp.float32) * ATTN_SCALE
    if valid is not None:
        s = jnp.where(valid, s, NEG_INF)
    sink_col = jnp.broadcast_to(sink.astype(jnp.float32).reshape(1, A_KV_HEADS, A_GROUP, 1, 1),
                                s.shape[:-1] + (1,))
    p = jax.nn.softmax(jnp.concatenate([s, sink_col], axis=-1), axis=-1)[..., :-1]
    return jnp.einsum('bhgqk,bkhd->bqhgd', p, v.astype(jnp.float32))

def window_sink_attention(q, k, v, kc, vc, sink):
    Bn, T = q.shape[:2]
    nb = T // Q_BLOCK
    band = Q_BLOCK + 2 * WINDOW
    qg = q.reshape(Bn, T, A_KV_HEADS, A_GROUP, HEAD_DIM)
    pad = ((0, 0), (WINDOW, WINDOW), (0, 0), (0, 0))
    kp = jnp.pad(k, pad)
    vp = jnp.pad(v, pad)
    ctx_valid = jnp.ones((Q_BLOCK, kc.shape[1]), dtype=bool)

    def block(i):
        start = i * Q_BLOCK
        qb = lax.dynamic_slice_in_dim(qg, start, Q_BLOCK, axis=1)
        kb = lax.dynamic_slice_in_dim(kp, start, band, axis=1)
        vb = lax.dynamic_slice_in_dim(vp, start, band, axis=1)
        qpos = start + jnp.arange(Q_BLOCK)
        kpos = start - WINDOW + jnp.arange(band)
        valid = ((kpos[None, :] >= 0) & (kpos[None, :] < T)
                 & (jnp.abs(qpos[:, None] - kpos[None, :]) <= WINDOW))
        valid = jnp.concatenate([valid, ctx_valid], axis=1)
        return sink_attention(qb, jnp.concatenate([kb, kc], axis=1),
                              jnp.concatenate([vb, vc], axis=1), sink, valid)

    out = lax.map(block, jnp.arange(nb))
    return jnp.moveaxis(out, 0, 1).reshape(Bn, T, A_KV_HEADS, A_GROUP, HEAD_DIM)

def diff_attention(q1, q2, k1, k2, v, lam):
    s1 = jnp.einsum('bqhd,bkhd->bhqk', q1, k1).astype(jnp.float32) * ATTN_SCALE
    s2 = jnp.einsum('bqhd,bkhd->bhqk', q2, k2).astype(jnp.float32) * ATTN_SCALE
    w = jax.nn.softmax(s1, axis=-1) - lam * jax.nn.softmax(s2, axis=-1)
    return jnp.einsum('bhqk,bkhe->bqhe', w, v.astype(jnp.float32))

def blocked_diff_attention(q1, q2, k1, k2, v, lam):
    Bn, T = q1.shape[:2]
    nb = T // Q_BLOCK

    def block(i):
        start = i * Q_BLOCK
        return diff_attention(lax.dynamic_slice_in_dim(q1, start, Q_BLOCK, axis=1),
                              lax.dynamic_slice_in_dim(q2, start, Q_BLOCK, axis=1),
                              k1, k2, v, lam)

    out = lax.map(block, jnp.arange(nb))
    return jnp.moveaxis(out, 0, 1).reshape(Bn, T, B_HEADS, B_VDIM)

def even_mixer(hx, hc, rows, cols, w_in, a_qn, a_kn, a_sink, b_qn, b_kn,
               lq1, lk1, lq2, lk2, b_subln, lambda_init, need_ctx):
    dt = hx.dtype

    def project(h):
        Bn, T = h.shape[:2]
        qa, ka, va, ga, qb, kb, vb, gb = split_cols(h @ w_in, EVEN_SPLITS)
        qa = rms_norm(qa.reshape(Bn, T, A_HEADS, HEAD_DIM), a_qn)
        ka = rms_norm(ka.reshape(Bn, T, A_KV_HEADS, HEAD_DIM), a_kn)
        va = va.reshape(Bn, T, A_KV_HEADS, HEAD_DIM)
        qb = rms_norm(qb.reshape(Bn, T, 2 * B_HEADS, HEAD_DIM), b_qn)
        kb = rms_norm(kb.reshape(Bn, T, 2 * B_HEADS, HEAD_DIM), b_kn)
        vb = vb.reshape(Bn, T, B_HEADS, B_VDIM)
        return qa, ka, va, ga, qb, kb, vb, gb

    def split_pair(t):
        Bn, T = t.shape[:2]
        t = t.reshape(Bn, T, B_HEADS, 2, HEAD_DIM)
        return t[..., 0, :], t[..., 1, :]

    def merge(oa, ga, ob, gb):
        Bn, T = oa.shape[:2]
        ob = rms_norm(ob, b_subln) * (1.0 - lambda_init)
        oa = oa.reshape(Bn, T, A_WIDTH).astype(dt) * jax.nn.silu(ga)
        ob = ob.reshape(Bn, T, B_WIDTH).astype(dt) * jax.nn.silu(gb)
        return jnp.concatenate([oa, ob], axis=-1)

    qa_x, ka_x, va_x, ga_x, qb_x, kb_x, vb_x, gb_x = project(hx)
    qa_c, ka_c, va_c, ga_c, qb_c, kb_c, vb_c, gb_c = project(hc)
    qa_x = rope_axial(qa_x, rows, cols)
    ka_x = rope_axial(ka_x, rows, cols)
    qb_x = rope_axial(qb_x, rows, cols)
    kb_x = rope_axial(kb_x, rows, cols)

    lam = (jnp.exp(jnp.sum(lq1.astype(jnp.float32) * lk1.astype(jnp.float32)))
           - jnp.exp(jnp.sum(lq2.astype(jnp.float32) * lk2.astype(jnp.float32))) + lambda_init)

    q1x, q2x = split_pair(qb_x)
    k1x, k2x = split_pair(kb_x)
    k1c, k2c = split_pair(kb_c)

    oa_x = window_sink_attention(qa_x, ka_x, va_x, ka_c, va_c, a_sink)
    ob_x = blocked_diff_attention(q1x, q2x,
                                  jnp.concatenate([k1x, k1c], axis=1),
                                  jnp.concatenate([k2x, k2c], axis=1),
                                  jnp.concatenate([vb_x, vb_c], axis=1), lam)
    ox = merge(oa_x, ga_x, ob_x, gb_x)
    if not need_ctx:
        return ox, None
    Bn, L = hc.shape[:2]
    oa_c = sink_attention(qa_c.reshape(Bn, L, A_KV_HEADS, A_GROUP, HEAD_DIM), ka_c, va_c, a_sink, None)
    q1c, q2c = split_pair(qb_c)
    ob_c = diff_attention(q1c, q2c, k1c, k2c, vb_c, lam)
    oc = merge(oa_c, ga_c, ob_c, gb_c)
    return ox, oc

def gla_chunked(q, k, v, log_a, s0, with_output):
    Bn, H, T, dk = q.shape
    dv = v.shape[-1]
    n = T // G_CHUNK
    f32 = jnp.float32

    def ch(t):
        return t.astype(f32).reshape(Bn, H, n, G_CHUNK, t.shape[-1])

    q, k, v, la = ch(q), ch(k), ch(v), ch(log_a)
    b = jnp.cumsum(la, axis=3)
    b_last = b[:, :, :, -1:, :]
    d_state = jnp.einsum('bhncd,bhnce->bhnde', k * jnp.exp(b_last - b), v)
    decay = jnp.exp(b_last[:, :, :, 0, :])

    def step(S, inp):
        dec, ds = inp
        return dec[..., None] * S + ds, S

    s_fin, s_prev = lax.scan(step, s0.astype(f32),
                             (jnp.moveaxis(decay, 2, 0), jnp.moveaxis(d_state, 2, 0)))
    if not with_output:
        return None, s_fin
    s_prev = jnp.moveaxis(s_prev, 0, 2)
    qd = q * jnp.exp(b)
    kd = k * jnp.exp(-b)
    tri = jnp.tril(jnp.ones((G_CHUNK, G_CHUNK), dtype=bool))
    att = jnp.where(tri, jnp.einsum('bhncd,bhnsd->bhncs', qd, kd), 0.0)
    o = (jnp.einsum('bhncs,bhnse->bhnce', att, v)
         + jnp.einsum('bhncd,bhnde->bhnce', qd, s_prev))
    return o.reshape(Bn, H, T, dv), s_fin

def gla_mixer(hx, hc, w_in, wa_f, ba_f, wa_b, ba_b, out_norm, need_ctx):
    dt = hx.dtype

    def project(h):
        Bn, T = h.shape[:2]
        q, k, v, g, rf, rb = split_cols(h @ w_in, ODD_SPLITS)

        def heads(t, d):
            return t.reshape(Bn, T, G_HEADS, d).transpose(0, 2, 1, 3)

        la_f = jax.nn.log_sigmoid((rf @ wa_f + ba_f).astype(jnp.float32)) / G_TAU
        la_b = jax.nn.log_sigmoid((rb @ wa_b + ba_b).astype(jnp.float32)) / G_TAU
        return (heads(q, G_DK) * (G_DK ** -0.5), heads(k, G_DK), heads(v, G_DV), g,
                heads(la_f, G_DK), heads(la_b, G_DK))

    def flip(t):
        return jnp.flip(t, axis=2)

    def finish(o, g):
        Bn, H, T, dv = o.shape
        o = rms_norm(o.transpose(0, 2, 1, 3), out_norm).reshape(Bn, T, H * dv)
        return o.astype(dt) * jax.nn.silu(g)

    qx, kx, vx, gx, lfx, lbx = project(hx)
    qc, kc, vc, gc, lfc, lbc = project(hc)
    Bn = hx.shape[0]
    s0 = jnp.zeros((Bn, G_HEADS, G_DK, G_DV), jnp.float32)
    oc_f, sc_f = gla_chunked(qc, kc, vc, lfc, s0, need_ctx)
    oc_b, sc_b = gla_chunked(flip(qc), flip(kc), flip(vc), flip(lbc), s0, need_ctx)
    ox_f, _ = gla_chunked(qx, kx, vx, lfx, sc_f, True)
    ox_b, _ = gla_chunked(flip(qx), flip(kx), flip(vx), flip(lbx), sc_b, True)
    ox = finish(ox_f + flip(ox_b), gx)
    if not need_ctx:
        return ox, None
    oc = finish(oc_f + flip(oc_b), gc)
    return ox, oc

def first_inputs(seed: int = 0) -> dict:
    key = jax.random.key(seed)
    ks = jax.random.split(key, 32)
    f32 = jnp.float32

    def nrm(k, shape, scale):
        return jax.random.normal(k, shape, f32) * scale

    def gain(k, shape):
        return 1.0 + 0.1 * jax.random.normal(k, shape, f32)

    D = D_MODEL
    return {
        'x': nrm(ks[0], (BATCH, SEQ, D), 1.0),
        'c': nrm(ks[1], (BATCH, D), 1.0),
        'ctx': nrm(ks[2], (BATCH, CTX_LEN, D), 1.0),
        'c_ctx': nrm(ks[3], (D,), 1.0),
        'adaln_w': nrm(ks[4], (DEPTH, D, 3 * D), 0.5 * D ** -0.5),
        'adaln_b': nrm(ks[5], (DEPTH, 3 * D), 0.02),
        'norm_g': gain(ks[6], (DEPTH, D)),
        'w_out': nrm(ks[7], (DEPTH, D, D), D ** -0.5),
        'ab_w_in': nrm(ks[8], (N_EVEN, D, EVEN_IN), D ** -0.5),
        'a_q_norm': gain(ks[9], (N_EVEN, HEAD_DIM)),
        'a_k_norm': gain(ks[10], (N_EVEN, HEAD_DIM)),
        'a_sink': nrm(ks[11], (N_EVEN, A_HEADS), 0.5),
        'b_q_norm': gain(ks[12], (N_EVEN, HEAD_DIM)),
        'b_k_norm': gain(ks[13], (N_EVEN, HEAD_DIM)),
        'b_lambda_q1': nrm(ks[14], (N_EVEN, HEAD_DIM), 0.1),
        'b_lambda_k1': nrm(ks[15], (N_EVEN, HEAD_DIM), 0.1),
        'b_lambda_q2': nrm(ks[16], (N_EVEN, HEAD_DIM), 0.1),
        'b_lambda_k2': nrm(ks[17], (N_EVEN, HEAD_DIM), 0.1),
        'b_subln': gain(ks[18], (N_EVEN, B_VDIM)),
        'gla_w_in': nrm(ks[19], (N_ODD, D, ODD_IN), D ** -0.5),
        'gla_wa_f': nrm(ks[20], (N_ODD, G_RANK, G_HEADS * G_DK), G_RANK ** -0.5),
        'gla_ba_f': nrm(ks[21], (N_ODD, G_HEADS * G_DK), 0.1),
        'gla_wa_b': nrm(ks[22], (N_ODD, G_RANK, G_HEADS * G_DK), G_RANK ** -0.5),
        'gla_ba_b': nrm(ks[23], (N_ODD, G_HEADS * G_DK), 0.1),
        'gla_out_norm': gain(ks[24], (N_ODD, G_DV)),
    }

def first_block(x, c, ctx, c_ctx, adaln_w, adaln_b, norm_g, w_out, ab_w_in, a_q_norm, a_k_norm,
              a_sink, b_q_norm, b_k_norm, b_lambda_q1, b_lambda_k1, b_lambda_q2, b_lambda_k2,
              b_subln, gla_w_in, gla_wa_f, gla_ba_f, gla_wa_b, gla_ba_b, gla_out_norm):
    ROWS = x.shape[1] // GRID_W
    rows, cols = grid_positions(ROWS)
    for layer in range(DEPTH):
        need_ctx = layer < DEPTH - 1
        shx, scx, gtx = adaln_params(c, adaln_w[layer], adaln_b[layer])
        shc, scc, gtc = adaln_params(c_ctx, adaln_w[layer], adaln_b[layer])
        hx = rms_norm(x, norm_g[layer]) * (1.0 + scx[:, None, :]) + shx[:, None, :]
        hc = rms_norm(ctx, norm_g[layer]) * (1.0 + scc) + shc
        j = layer // 2
        if layer % 2 == 0:
            lambda_init = 0.8 - 0.6 * math.exp(-0.3 * layer)
            ox, oc = even_mixer(hx, hc, rows, cols, ab_w_in[j], a_q_norm[j], a_k_norm[j], a_sink[j],
                                b_q_norm[j], b_k_norm[j], b_lambda_q1[j], b_lambda_k1[j],
                                b_lambda_q2[j], b_lambda_k2[j], b_subln[j], lambda_init, need_ctx)
        else:
            ox, oc = gla_mixer(hx, hc, gla_w_in[j], gla_wa_f[j], gla_ba_f[j], gla_wa_b[j], gla_ba_b[j],
                               gla_out_norm[j], need_ctx)
        x = x + gtx[:, None, :] * (ox @ w_out[layer])
        if need_ctx:
            ctx = ctx + gtc * (oc @ w_out[layer])
    return x


DEPTH_2 = 1

CHUNK = 64
N_META = 16

D_MIX = D_MODEL
LRU_WIDTH = D_MIX // 4
LRU_HEADS = LRU_WIDTH // HEAD_DIM
CONV_A = 4
LRU_C = 8.0
FOX_WIDTH = D_MIX // 2
FOX_HEADS = FOX_WIDTH // HEAD_DIM
RWKV_WIDTH = D_MIX - LRU_WIDTH - FOX_WIDTH
RWKV_HEADS = RWKV_WIDTH // HEAD_DIM
W_RANK = 64
A_RANK = 64
G_RANK_2 = 128
V_RANK = 32
GN_EPS = 64e-5
A_COLS = 2 * LRU_WIDTH
B_COLS = 3 * FOX_WIDTH + FOX_HEADS
C_COLS = 3 * RWKV_WIDTH + W_RANK + A_RANK + G_RANK_2
D_IN = A_COLS + B_COLS + C_COLS
C_SPLITS = (RWKV_WIDTH, 2 * RWKV_WIDTH, 3 * RWKV_WIDTH, 3 * RWKV_WIDTH + W_RANK, 3 * RWKV_WIDTH + W_RANK + A_RANK)
D_FF = 2816
CONV_F = 3


def rms_norm_2(x, g):
    xf = x.astype(jnp.float32)
    y = xf * lax.rsqrt(jnp.mean(xf * xf, axis=-1, keepdims=True) + EPS)
    return (y * g.astype(jnp.float32)).astype(x.dtype)

def causal_dwconv(x, w):
    k = w.shape[0]
    return lax.conv_general_dilated(
        x, w[:, None, :].astype(x.dtype), window_strides=(1,), padding=[(k - 1, 0)],
        dimension_numbers=('NWC', 'WIO', 'NWC'), feature_group_count=x.shape[-1])

def token_shift(p):
    return jnp.pad(p, ((0, 0), (1, 0), (0, 0)))[:, :-1]

def rg_lru_group(xa, ya, conv_w, conv_b, ga_w, ga_b, gx_w, gx_b, lam):
    bsz, t, _ = xa.shape
    u = causal_dwconv(xa, conv_w) + conv_b
    uh = u.reshape(bsz, t, LRU_HEADS, HEAD_DIM)
    r = jax.nn.sigmoid(jnp.einsum('bthi,hij->bthj', uh, ga_w).reshape(bsz, t, LRU_WIDTH) + ga_b)
    i = jax.nn.sigmoid(jnp.einsum('bthi,hij->bthj', uh, gx_w).reshape(bsz, t, LRU_WIDTH) + gx_b)
    log_a = -LRU_C * r.astype(jnp.float32) * jax.nn.softplus(-lam.astype(jnp.float32))
    a = jnp.exp(log_a)
    b = jnp.sqrt(-jnp.expm1(2.0 * log_a)) * (i * u).astype(jnp.float32)

    def combine(left, right):
        a1, b1 = left
        a2, b2 = right
        return a1 * a2, a2 * b1 + b2

    _, h = lax.associative_scan(combine, (a, b), axis=1)
    return h.astype(xa.dtype) * jax.nn.gelu(ya, approximate=True)

def forgetting_attention_group(q, k, v, f_logit, f_bias):
    bsz, t, _ = q.shape
    n_blk = -(-t // Q_BLOCK)
    tp = n_blk * Q_BLOCK

    def heads(z):
        z = jnp.pad(z, ((0, 0), (0, tp - t), (0, 0)))
        return z.reshape(bsz, tp, FOX_HEADS, HEAD_DIM).transpose(0, 2, 1, 3)

    qh = heads(q) * (HEAD_DIM ** -0.5)
    kh = heads(k)
    vh = heads(v)
    log_f = jax.nn.log_sigmoid((f_logit + f_bias).astype(jnp.float32))
    log_f = jnp.pad(log_f, ((0, 0), (0, tp - t), (0, 0)))
    c = jnp.cumsum(log_f, axis=1).transpose(0, 2, 1)
    kpos = jnp.arange(tp)

    def block(i):
        start = i * Q_BLOCK
        qb = lax.dynamic_slice_in_dim(qh, start, Q_BLOCK, axis=2)
        cb = lax.dynamic_slice_in_dim(c, start, Q_BLOCK, axis=2)
        qpos = start + jnp.arange(Q_BLOCK)
        s = jnp.einsum('bhqd,bhkd->bhqk', qb, kh).astype(jnp.float32) + (cb[..., :, None] - c[..., None, :])
        s = jnp.where(kpos[None, :] <= qpos[:, None], s, -jnp.inf)
        p = jax.nn.softmax(s, axis=-1)
        return jnp.einsum('bhqk,bhkd->bhqd', p.astype(vh.dtype), vh)

    o = lax.map(block, jnp.arange(n_blk))
    o = o.transpose(1, 0, 3, 2, 4).reshape(bsz, tp, FOX_WIDTH)
    return o[:, :t]

def rwkv7_group(pc, mu, w0, w_up, a0, a_up, g_up, k_k, k_a, r_k, ln_w, ln_b, v_first, v_mix):
    f32 = jnp.float32
    bsz, t, _ = pc.shape
    pc = pc + (token_shift(pc) - pc) * mu
    r, k, v, wd, ad, gd = jnp.split(pc, C_SPLITS, axis=-1)
    v_own = v
    if v_mix is not None:
        v0, v_down, v_up = v_mix
        v = v + (v_first - v) * jax.nn.sigmoid(v0 + (v @ v_down) @ v_up)
    w_log = -jax.nn.softplus(-(w0 + jnp.tanh(wd) @ w_up).astype(f32)) - 0.5
    decay = jnp.exp(-jnp.exp(w_log))
    a = jax.nn.sigmoid(a0 + ad @ a_up)
    g = jax.nn.sigmoid(gd) @ g_up

    def heads(z):
        return z.astype(f32).reshape(bsz, t, RWKV_HEADS, HEAD_DIM)

    kk = heads(k * k_k)
    kk = kk / jnp.maximum(jnp.sqrt(jnp.sum(kk * kk, axis=-1, keepdims=True)), 1e-12)
    k = k * (1.0 + (a - 1.0) * k_a)
    rh, kh, vh, ah, wh = heads(r), heads(k), heads(v), heads(a), heads(decay)
    xs = tuple(z.transpose(1, 0, 2, 3) for z in (rh, wh, kh, vh, kk, ah))

    def step(S, inp):
        r_t, w_t, k_t, v_t, kk_t, a_t = inp
        s_kk = jnp.einsum('bhij,bhj->bhi', S, kk_t)
        S = S * w_t[:, :, None, :] - s_kk[..., None] * (kk_t * a_t)[:, :, None, :] + v_t[..., None] * k_t[:, :, None, :]
        return S, jnp.einsum('bhij,bhj->bhi', S, r_t)

    s0 = jnp.zeros((bsz, RWKV_HEADS, HEAD_DIM, HEAD_DIM), f32)
    _, o = lax.scan(step, s0, xs)
    o = o.transpose(1, 0, 2, 3)
    mean = jnp.mean(o, axis=-1, keepdims=True)
    var = jnp.mean(jnp.square(o - mean), axis=-1, keepdims=True)
    o = ((o - mean) * lax.rsqrt(var + GN_EPS)).reshape(bsz, t, RWKV_WIDTH) * ln_w + ln_b
    bonus = (jnp.sum(rh * kh * r_k, axis=-1, keepdims=True) * vh).reshape(bsz, t, RWKV_WIDTH)
    out = ((o + bonus) * g.astype(f32)).astype(pc.dtype)
    return out, v_own

def second_inputs(seed: int = 0) -> dict:
    key = jax.random.key(seed)
    ks = iter(jax.random.split(key, 40))
    f32 = jnp.float32

    def nrm(shape, scale):
        return scale * jax.random.normal(next(ks), shape, f32)

    def unif(shape, lo, hi):
        return jax.random.uniform(next(ks), shape, f32, lo, hi)

    L = DEPTH_2
    Lv = DEPTH_2 - 1
    x = nrm((BATCH, SEQ, D_MODEL), 1.0)
    meta_tokens = nrm((N_META, D_MODEL), 1.0)
    norm_mix_pre = 1.0 + nrm((L, D_MODEL), 0.05)
    norm_mix_post = 1.0 + nrm((L, D_MODEL), 0.05)
    norm_ffn_pre = 1.0 + nrm((L, D_MODEL), 0.05)
    norm_ffn_post = 1.0 + nrm((L, D_MODEL), 0.05)
    w_in = nrm((L, D_MODEL, D_IN), D_MODEL ** -0.5)
    w_out = nrm((L, D_MIX, D_MODEL), D_MIX ** -0.5)
    lru_conv_w = nrm((L, CONV_A, LRU_WIDTH), CONV_A ** -0.5)
    lru_conv_b = nrm((L, LRU_WIDTH), 0.02)
    lru_gate_a_w = nrm((L, LRU_HEADS, HEAD_DIM, HEAD_DIM), HEAD_DIM ** -0.5)
    lru_gate_a_b = nrm((L, LRU_WIDTH), 0.02)
    lru_gate_x_w = nrm((L, LRU_HEADS, HEAD_DIM, HEAD_DIM), HEAD_DIM ** -0.5)
    lru_gate_x_b = nrm((L, LRU_WIDTH), 0.02)
    a_init = unif((L, LRU_WIDTH), 0.9, 0.999) ** (1.0 / LRU_C)
    lru_lambda = jnp.log(a_init) - jnp.log1p(-a_init)
    fox_f_bias = unif((L, FOX_HEADS), 1.0, 4.0)
    rwkv_mu = unif((L, C_COLS), 0.0, 1.0)
    rwkv_w0 = unif((L, RWKV_WIDTH), -6.0, -1.0)
    rwkv_w_up = nrm((L, W_RANK, RWKV_WIDTH), 0.1 * W_RANK ** -0.5)
    rwkv_a0 = nrm((L, RWKV_WIDTH), 0.1)
    rwkv_a_up = nrm((L, A_RANK, RWKV_WIDTH), 0.5 * A_RANK ** -0.5)
    rwkv_g_up = nrm((L, G_RANK_2, RWKV_WIDTH), G_RANK_2 ** -0.5)
    rwkv_v0 = 1.0 + nrm((Lv, RWKV_WIDTH), 0.1)
    rwkv_v_down = nrm((Lv, RWKV_WIDTH, V_RANK), RWKV_WIDTH ** -0.5)
    rwkv_v_up = nrm((Lv, V_RANK, RWKV_WIDTH), 0.5 * V_RANK ** -0.5)
    rwkv_k_k = 0.85 + nrm((L, RWKV_WIDTH), 0.05)
    rwkv_k_a = 1.0 + nrm((L, RWKV_WIDTH), 0.05)
    rwkv_r_k = nrm((L, RWKV_HEADS, HEAD_DIM), 0.1)
    rwkv_ln_w = 1.0 + nrm((L, RWKV_WIDTH), 0.05)
    rwkv_ln_b = nrm((L, RWKV_WIDTH), 0.02)
    ffn_up = nrm((L, D_MODEL, 2 * D_FF), D_MODEL ** -0.5)
    ffn_conv = nrm((L, CONV_F, 2 * D_FF), CONV_F ** -0.5)
    ffn_down = nrm((L, D_FF, D_MODEL), D_FF ** -0.5)
    return {
        'x': x, 'meta_tokens': meta_tokens,
        'norm_mix_pre': norm_mix_pre, 'norm_mix_post': norm_mix_post,
        'norm_ffn_pre': norm_ffn_pre, 'norm_ffn_post': norm_ffn_post,
        'w_in': w_in, 'w_out': w_out,
        'lru_conv_w': lru_conv_w, 'lru_conv_b': lru_conv_b,
        'lru_gate_a_w': lru_gate_a_w, 'lru_gate_a_b': lru_gate_a_b,
        'lru_gate_x_w': lru_gate_x_w, 'lru_gate_x_b': lru_gate_x_b,
        'lru_lambda': lru_lambda, 'fox_f_bias': fox_f_bias,
        'rwkv_mu': rwkv_mu, 'rwkv_w0': rwkv_w0, 'rwkv_w_up': rwkv_w_up,
        'rwkv_a0': rwkv_a0, 'rwkv_a_up': rwkv_a_up, 'rwkv_g_up': rwkv_g_up,
        'rwkv_v0': rwkv_v0, 'rwkv_v_down': rwkv_v_down, 'rwkv_v_up': rwkv_v_up,
        'rwkv_k_k': rwkv_k_k, 'rwkv_k_a': rwkv_k_a, 'rwkv_r_k': rwkv_r_k,
        'rwkv_ln_w': rwkv_ln_w, 'rwkv_ln_b': rwkv_ln_b,
        'ffn_up': ffn_up, 'ffn_conv': ffn_conv, 'ffn_down': ffn_down,
    }

def second_block(x, meta_tokens, norm_mix_pre, norm_mix_post, norm_ffn_pre, norm_ffn_post,
              w_in, w_out, lru_conv_w, lru_conv_b, lru_gate_a_w, lru_gate_a_b,
              lru_gate_x_w, lru_gate_x_b, lru_lambda, fox_f_bias,
              rwkv_mu, rwkv_w0, rwkv_w_up, rwkv_a0, rwkv_a_up, rwkv_g_up,
              rwkv_v0, rwkv_v_down, rwkv_v_up, rwkv_k_k, rwkv_k_a, rwkv_r_k,
              rwkv_ln_w, rwkv_ln_b, ffn_up, ffn_conv, ffn_down):
    bsz = x.shape[0]
    meta = jnp.broadcast_to(meta_tokens.astype(x.dtype)[None], (bsz, N_META, D_MODEL))
    h = jnp.concatenate([meta, x], axis=1)
    v_first = None
    for l in range(DEPTH_2):
        p = rms_norm_2(h, norm_mix_pre[l]) @ w_in[l]
        pa = p[..., :A_COLS]
        pb = p[..., A_COLS:A_COLS + B_COLS]
        pc = p[..., A_COLS + B_COLS:]
        xa, ya = jnp.split(pa, 2, axis=-1)
        oa = rg_lru_group(xa, ya, lru_conv_w[l], lru_conv_b[l], lru_gate_a_w[l], lru_gate_a_b[l],
                          lru_gate_x_w[l], lru_gate_x_b[l], lru_lambda[l])
        ob = forgetting_attention_group(pb[..., :FOX_WIDTH], pb[..., FOX_WIDTH:2 * FOX_WIDTH],
                                        pb[..., 2 * FOX_WIDTH:3 * FOX_WIDTH], pb[..., 3 * FOX_WIDTH:],
                                        fox_f_bias[l])
        v_mix = None if l == 0 else (rwkv_v0[l - 1], rwkv_v_down[l - 1], rwkv_v_up[l - 1])
        oc, v_own = rwkv7_group(pc, rwkv_mu[l], rwkv_w0[l], rwkv_w_up[l], rwkv_a0[l], rwkv_a_up[l],
                                rwkv_g_up[l], rwkv_k_k[l], rwkv_k_a[l], rwkv_r_k[l],
                                rwkv_ln_w[l], rwkv_ln_b[l], v_first, v_mix)
        if l == 0:
            v_first = v_own
        mixed = jnp.concatenate([oa, ob, oc], axis=-1) @ w_out[l]
        h = h + rms_norm_2(mixed, norm_mix_post[l])
        f = causal_dwconv(rms_norm_2(h, norm_ffn_pre[l]) @ ffn_up[l], ffn_conv[l])
        gate, val = jnp.split(f, 2, axis=-1)
        f = (jax.nn.gelu(gate, approximate=True) * val) @ ffn_down[l]
        h = h + rms_norm_2(f, norm_ffn_post[l])
    return h[:, N_META:]


def setup_inputs(seed=0):
    out = dict(first_inputs(seed))
    for name, value in second_inputs(seed + 1).items():
        if name != "x":
            out[name + "_2"] = value
    return out


def reference(
    x, c, ctx, c_ctx, adaln_w, adaln_b, norm_g, w_out, ab_w_in, a_q_norm, a_k_norm, a_sink,
    b_q_norm, b_k_norm, b_lambda_q1, b_lambda_k1, b_lambda_q2, b_lambda_k2, b_subln, gla_w_in,
    gla_wa_f, gla_ba_f, gla_wa_b, gla_ba_b, gla_out_norm, meta_tokens_2, norm_mix_pre_2,
    norm_mix_post_2, norm_ffn_pre_2, norm_ffn_post_2, w_in_2, w_out_2, lru_conv_w_2,
    lru_conv_b_2, lru_gate_a_w_2, lru_gate_a_b_2, lru_gate_x_w_2, lru_gate_x_b_2, lru_lambda_2,
    fox_f_bias_2, rwkv_mu_2, rwkv_w0_2, rwkv_w_up_2, rwkv_a0_2, rwkv_a_up_2, rwkv_g_up_2,
    rwkv_v0_2, rwkv_v_down_2, rwkv_v_up_2, rwkv_k_k_2, rwkv_k_a_2, rwkv_r_k_2, rwkv_ln_w_2,
    rwkv_ln_b_2, ffn_up_2, ffn_conv_2, ffn_down_2,
):
    x = first_block(
        x, c, ctx, c_ctx, adaln_w, adaln_b, norm_g, w_out, ab_w_in, a_q_norm, a_k_norm, a_sink,
        b_q_norm, b_k_norm, b_lambda_q1, b_lambda_k1, b_lambda_q2, b_lambda_k2, b_subln,
        gla_w_in, gla_wa_f, gla_ba_f, gla_wa_b, gla_ba_b, gla_out_norm,
    )
    return second_block(
        x, meta_tokens_2, norm_mix_pre_2, norm_mix_post_2, norm_ffn_pre_2, norm_ffn_post_2,
        w_in_2, w_out_2, lru_conv_w_2, lru_conv_b_2, lru_gate_a_w_2, lru_gate_a_b_2,
        lru_gate_x_w_2, lru_gate_x_b_2, lru_lambda_2, fox_f_bias_2, rwkv_mu_2, rwkv_w0_2,
        rwkv_w_up_2, rwkv_a0_2, rwkv_a_up_2, rwkv_g_up_2, rwkv_v0_2, rwkv_v_down_2, rwkv_v_up_2,
        rwkv_k_k_2, rwkv_k_a_2, rwkv_r_k_2, rwkv_ln_w_2, rwkv_ln_b_2, ffn_up_2, ffn_conv_2,
        ffn_down_2,
    )


_drawn_inputs = setup_inputs


def setup_inputs(seed=0):
    import zlib

    import numpy as np

    out = dict(_drawn_inputs(seed))
    spreads = {}
    factors = {'a_q_norm': 8.0,
     'a_k_norm': 8.0,
     'a_sink': 8.0,
     'b_q_norm': 8.0,
     'b_k_norm': 8.0,
     'b_lambda_q1': 64.0,
     'b_lambda_k1': 6.013,
     'b_lambda_q2': 6.485,
     'b_lambda_k2': 3.486,
     'gla_ba_f': 5.694,
     'gla_ba_b': 5.385,
     'lru_gate_a_b_2': 46.626,
     'lru_gate_x_b_2': 32.414,
     'rwkv_w_up_2': 8.0,
     'rwkv_a0_2': 3.103,
     'rwkv_ln_w_2': 2.735,
     'rwkv_ln_b_2': 6.469,
     'b_subln': 3.022}
    for name, (base, spread) in spreads.items():
        noise = np.random.default_rng([zlib.crc32(name.encode()), seed]).standard_normal(out[name].shape)
        drawn = base * np.exp(spread * noise) if base else spread * noise
        out[name] = jnp.asarray(drawn.astype(out[name].dtype))
    for name, factor in factors.items():
        out[name] = (out[name] * factor).astype(out[name].dtype)
    return out
```

```python
from contextlib import ExitStack

import concourse.bass as bass
from concourse import mybir

ALU = mybir.AluOpType
ACT = mybir.ActivationFunctionType
F32 = mybir.dt.float32
AX = mybir.AxisListType

P = 128
D = 1024
KD = D // P
SEQ = 1024
CTX = 256
NT = SEQ // P
NC = CTX // P
ALLT = SEQ + CTX
EPS = 1e-6
NEG = -1e30
HD = 64

A_HEADS = 8
B_HEADS = 4
EVEN_IN = 3328
ODD_IN = 3104
LAMBDA_INIT = 0.8 - 0.6

META = 16
T2 = META + SEQ
D_FF = 2816
D_IN2 = 3080
TILES2 = [(0, META)] + [(META + P * t, P) for t in range(NT)]


class Chain:

    def __init__(self, eng, sem, start=0):
        self.eng, self.sem, self.base, self.k = eng, sem, start, 0

    def step(self, ins):
        ins.then_inc(self.sem, 1)
        self.k += 1

    def settle(self):
        self.eng.wait_ge(self.sem, self.base + self.k)

    def link(self, ins):
        self.step(ins)
        self.settle()


class Phase:

    def __init__(self, nc, tag):
        self.nc, self.tag, self.ctx, self.held = nc, tag, ExitStack(), []

    def __enter__(self):
        return self

    def __exit__(self, *what):
        self.ctx.close()
        self.nc.clear_and_free_semaphores(self.held)
        self.nc.all_engine_barrier()

    def sb(self, name, shape, dt=F32):
        return self.ctx.enter_context(self.nc.sbuf_tensor(f"{self.tag}_{name}", shape, dt))

    def ps(self, name, shape):
        return self.ctx.enter_context(self.nc.psum_tensor(f"{self.tag}_{name}", shape, F32))

    def sem(self, name):
        self.held.append(self.nc.alloc_semaphore(f"{self.tag}_{name}"))
        return self.held[-1]

    def sems(self, names):
        return [self.sem(n) for n in names.split()]


def rows(ap, n=P):
    return ap.partition_broadcast(n)


def modulation(nc, a, g):
    BLK = 512
    NB = 3 * D // BLK
    w_v = a["adaln_w"].rearrange("l (k p) (b n) -> p l k b n", p=P, n=BLK)
    with Phase(nc, "mod") as ph:
        w = [ph.sb(f"w{s}", [P, KD, BLK]) for s in range(2)]
        cond = ph.sb("cond", [P, 2, KD])
        act_c = ph.sb("act_c", [P, KD, 2])
        bias = ph.sb("bias", [P, 48])
        gain = ph.sb("gain", [P, 2, KD])
        grow = ph.sb("grow", [KD, 3, P])
        lam = ph.sb("lam", [P, 4, HD])
        lprod = ph.sb("lprod", [P, 2, HD])
        lsum = ph.sb("lsum", [P, 2])
        lexp = ph.sb("lexp", [P, 2])
        pm = [ph.ps(f"pm{s}", [P, 4, 2]) for s in range(2)]
        pg = ph.ps("pg", [KD, 3, P])
        small, zeroed, ident_ready, silu_ready, w0_in, w1_in, pm_ready, pm_free, mod_ready, g_t, g_c, g_out, lam_p, lam_e, dstep = ph.sems(
            "small zeroed ident_ready silu_ready w0_in w1_in pm_ready pm_free mod_ready g_t g_c g_out lam_p lam_e dstep")
        w_in = [w0_in, w1_in]
        with nc.Block() as block:
            @block.sync
            def _(sp):
                with nc.allow_non_contiguous_dma(reason="short vectors, feature-major"):
                    sp.dma_start(cond[:, 0, :], a["c"].rearrange("o (k p) -> p (o k)", p=P)).then_inc(small, 16)
                    sp.dma_start(cond[:, 1, :], a["c_ctx"].rearrange("(k p) -> p k", p=P)).then_inc(small, 16)
                    sp.dma_start(bias[:, :], a["adaln_b"].rearrange("l (j p) -> p (l j)", p=P)).then_inc(small, 16)
                    sp.dma_start(gain[:, :, :], a["norm_g"].rearrange("l (k p) -> p l k", p=P)).then_inc(small, 16)
                for j, name in enumerate(("b_lambda_q1", "b_lambda_k1", "b_lambda_q2", "b_lambda_k2")):
                    sp.dma_start(lam[:, j, :], rows(a[name][0, :])).then_inc(small, 16)
                for layer in range(2):
                    sp.dma_start(w[layer][:, :, :], w_v[:, layer, :, 0, :]).then_inc(w_in[layer], 16)
                with sp.Fori(1, NB, 1) as i:
                    for layer in range(2):
                        sp.wait_ge(pm_ready, i * 2 + layer - 1)
                        sp.dma_start(w[layer][:, :, :], w_v[:, layer, :, i, :]).then_inc(w_in[layer], 16)
                sp.wait_ge(g_c, 1)
                sp.dma_start(g.gate_dram.rearrange("r (k p) -> k r p", p=P), grow[:, :, :]).then_inc(g_out, 16)
                sp.wait_ge(g_out, 16)

            @block.gpsimd
            def _(pool):
                pool.memset(g.ident[:, :], 0.0).then_inc(zeroed, 1)
                pool.wait_ge(zeroed, 1)
                pool.affine_select(out=g.ident[:, :], in_=g.ident[:, :], compare_op=ALU.not_equal, fill=1.0, base=0,
                                   pattern=[[-1, P]], channel_multiplier=1).then_inc(ident_ready, 1)

            @block.scalar
            def _(act):
                act.wait_ge(small, 16 * 8)
                act.activation(act_c[:, :, :].rearrange("p k c -> p c k"), cond[:, :, :], ACT.Silu).then_inc(silu_ready, 1)
                act.wait_ge(lam_p, 1)
                act.activation(lexp[:, :], lsum[:, :], ACT.Exp).then_inc(lam_e, 1)

            @block.vector
            def _(dve):
                ch = Chain(dve, dstep)
                ch.link(dve.memset(g.epsc[:, :], EPS))
                dve.wait_ge(small, 16 * 8)
                ch.step(dve.tensor_tensor(lprod[:, 0, :], lam[:, 0, :], lam[:, 1, :], ALU.mult))
                ch.link(dve.tensor_tensor(lprod[:, 1, :], lam[:, 2, :], lam[:, 3, :], ALU.mult))
                dve.tensor_reduce(lsum[:, :], lprod[:, :, :], AX.X, ALU.add).then_inc(lam_p, 1)
                dve.wait_ge(lam_e, 1)
                ch.link(dve.tensor_tensor(g.neglam[:, :], lexp[:, 1:2], lexp[:, 0:1], ALU.subtract))
                ch.step(dve.tensor_scalar(g.neglam[:, :], g.neglam[:, :], -LAMBDA_INIT, None, ALU.add))
                dve.sem_inc(pm_free, 2)
                with dve.Fori(0, NB, 1) as i:
                    for layer in range(2):
                        dve.wait_ge(pm_ready, i * 2 + layer + 1)
                        dve.tensor_copy(g.mod[:, bass.ds(i * 4 + 24 * layer, 4), :], pm[layer][:, :, :]).then_inc(pm_free, 1)
                dve.wait_ge(pm_free, 2 + 2 * NB)
                for c in range(2):
                    ch.step(dve.tensor_tensor(g.mod[:, :, c], g.mod[:, :, c], bias[:, :], ALU.add))
                ch.settle()
                for layer in range(2):
                    for c in range(2):
                        ins = dve.scalar_tensor_tensor(g.gs[:, layer, c, :], g.mod[:, 24 * layer + 8:24 * layer + 16, c], 1.0,
                                                       gain[:, layer, :], ALU.add, ALU.mult)
                        if (layer, c) == (1, 1):
                            ins.then_inc(mod_ready, 1)
                dve.wait_ge(g_t, 1)
                dve.tensor_copy(grow[:, :, :], pg[:, :, :]).then_inc(g_c, 1)

            @block.tensor
            def _(pe):
                pe.wait_ge(silu_ready, 1)
                with pe.Fori(0, NB, 1) as i:
                    for layer in range(2):
                        pe.wait_ge(w_in[layer], i * 16 + 16)
                        pe.wait_ge(pm_free, i * 2 + layer + 1)
                        for j in range(4):
                            for k in range(KD):
                                mm = pe.matmul(pm[layer][:, j, :], w[layer][:, k, P * j:P * j + P], act_c[:, k, :],
                                               start=(k == 0), stop=(k == KD - 1))
                        mm.then_inc(pm_ready, 1)
                pe.wait_ge(mod_ready, 1)
                pe.wait_ge(ident_ready, 1)
                for r, (layer, c) in enumerate(((0, 0), (0, 1), (1, 0))):
                    mm = pe.transpose(pg[:, r, :], g.mod[:, 24 * layer + 16:24 * layer + 24, c], g.ident[:, :])
                mm.then_inc(g_t, 1)


def norm_turn(nc, g, tag, parts, load=None):
    with Phase(nc, tag) as ph:
        sq = ph.sb("sq", [P, D])
        xn = ph.sb("xn", [P, D])
        ss = ph.sb("ss", [P, 1])
        rt = ph.sb("rt", [P, 1])
        rs = ph.sb("rs", [P, 1])
        pt = ph.ps("pt", [P, 2, 4, P])
        loaded, squared, rooted, recip, scaled, turned, evac, evac2 = ph.sems("loaded squared rooted recip scaled turned evac evac2")
        with nc.Block() as block:
            n_load = 16 * len(load or [])

            @block.sync
            def _(sp):
                with nc.allow_non_contiguous_dma(reason="short vectors, feature-major"):
                    for dst, src in load or []:
                        sp.dma_start(dst, src).then_inc(loaded, 16)
                if load:
                    sp.wait_ge(loaded, n_load)

            def loops(eng, body):
                at = 0
                for part in parts:
                    if part[2] == 1:
                        body(0, at, part)
                    else:
                        with eng.Fori(0, part[2], 1) as i:
                            body(i, i + at, part)
                    at += part[2]

            @block.scalar
            def _(act):
                if load:
                    act.wait_ge(loaded, n_load)

                def body(i, n, part):
                    x, r, _, _, gain, shift = part
                    act.activation(sq[0:r, :], x[0:r, i, :], ACT.Square, accum_out=ss[0:r, :]).then_inc(squared, 1)
                    act.wait_ge(squared, n + 1)
                    act.activation(rt[0:r, :], ss[0:r, :], ACT.Sqrt, scale=1.0 / D, bias=g.epsc[0:r, :]).then_inc(rooted, 1)
                    act.wait_ge(turned, n + 1)
                    c0 = part[3]
                    for k in range(4):
                        ins = act.activation(g.hT[:, k, bass.ds(c0 + i * P, r)], pt[:, 0, k, 0:r], ACT.Identity,
                                             scale=gain[:, k:k + 1], bias=shift[:, k:k + 1] if shift is not None else 0.0)
                    ins.then_inc(evac, 1)
                loops(act, body)

            @block.vector
            def _(dve):
                if load:
                    dve.wait_ge(loaded, n_load)

                def body(i, n, part):
                    x, r, _, c0, gain, shift = part
                    dve.wait_ge(rooted, n + 1)
                    dve.reciprocal(rs[0:r, :], rt[0:r, :]).then_inc(recip, 1)
                    dve.wait_ge(recip, n + 1)
                    dve.tensor_scalar(xn[0:r, :], x[0:r, i, :], rs[0:r, :], None, ALU.mult).then_inc(scaled, 1)
                    dve.wait_ge(turned, n + 1)
                    for k in range(4, KD):
                        out, src = g.hT[:, k, bass.ds(c0 + i * P, r)], pt[:, 1, k - 4, 0:r]
                        if shift is None:
                            ins = dve.tensor_scalar(out, src, gain[:, k:k + 1], None, ALU.mult)
                        else:
                            ins = dve.tensor_scalar(out, src, gain[:, k:k + 1], shift[:, k:k + 1], ALU.mult, ALU.add)
                    ins.then_inc(evac2, 1)
                loops(dve, body)

            @block.tensor
            def _(pe):
                def body(i, n, part):
                    r = part[1]
                    pe.wait_ge(scaled, n + 1)
                    pe.wait_ge(rooted, n + 1)
                    for k in range(KD):
                        mm = pe.transpose(pt[:, k // 4, k % 4, 0:r], xn[0:r, P * k:P * k + P], g.ident[0:r, 0:r])
                    mm.then_inc(turned, 1)
                loops(pe, body)


def project_rows(nc, g, tag, tiles, w_dram, blk, nblk, dst):
    NBANK = 4
    n = len(tiles)
    w_v = w_dram.rearrange("(k p) (b n) -> p k b n", p=P, n=blk)
    with Phase(nc, tag) as ph:
        w = [ph.sb(f"w{s}", [P, KD, blk]) for s in range(2)]
        o = [ph.sb(f"o{s}", [P, blk]) for s in range(NBANK)]
        pb = [ph.ps(f"pb{s}", [P, 512]) for s in range(NBANK)]
        w_in = ph.sems("w_in0 w_in1")
        made = ph.sems("made0 made1 made2 made3")
        copied = ph.sems("copied0 copied1 copied2 copied3")
        stored = ph.sems("stored0 stored1 stored2 stored3")
        slots = [(s, t) for s in range(2) for t in range(n)]
        per = [sum(1 for q in range(2 * n) if q % NBANK == b) for b in range(NBANK)]
        with nc.Block() as block:
            @block.gpsimd
            def _(pool):
                for s in range(2):
                    pool.dma_start(w[s][:, :, :], w_v[:, :, s, :]).then_inc(w_in[s], 16)
                if nblk > 2:
                    with pool.Fori(1, nblk // 2, 1) as i:
                        for s in range(2):
                            q = s * n + n - 1
                            pool.wait_ge(made[q % NBANK], (i - 1) * per[q % NBANK] + q // NBANK + 1)
                            pool.dma_start(w[s][:, :, :], w_v[:, :, i * 2 + s, :]).then_inc(w_in[s], 16)

            @block.sync
            def _(sp):
                for b in range(NBANK):
                    sp.sem_inc(stored[b], 16)
                with sp.Fori(0, nblk // 2, 1) as i:
                    for q, (s, t) in enumerate(slots):
                        b = q % NBANK
                        c0, r = tiles[t]
                        sp.wait_ge(copied[b], i * per[b] + q // NBANK + 1)
                        sp.dma_start(dst[c0:c0 + r, bass.ds((i * 2 + s) * blk, blk)], o[b][0:r, :]).then_inc(stored[b], 16)
                for b in range(NBANK):
                    sp.wait_ge(stored[b], 16 + 16 * per[b] * (nblk // 2))

            def copies(eng, mine):
                with eng.Fori(0, nblk // 2, 1) as i:
                    for q, (s, t) in enumerate(slots):
                        b = q % NBANK
                        if b % 2 != mine:
                            continue
                        r = tiles[t][1]
                        eng.wait_ge(made[b], i * per[b] + q // NBANK + 1)
                        eng.wait_ge(stored[b], (i * per[b] + q // NBANK) * 16 + 16)
                        if mine:
                            eng.tensor_copy(o[b][0:r, :], pb[b][0:r, 0:blk]).then_inc(copied[b], 1)
                        else:
                            eng.activation(o[b][0:r, :], pb[b][0:r, 0:blk], ACT.Copy).then_inc(copied[b], 1)

            @block.scalar
            def _(act):
                copies(act, 0)

            @block.vector
            def _(dve):
                copies(dve, 1)

            @block.tensor
            def _(pe):
                with pe.Fori(0, nblk // 2, 1) as i:
                    for q, (s, t) in enumerate(slots):
                        b = q % NBANK
                        c0, r = tiles[t]
                        if t == 0:
                            pe.wait_ge(w_in[s], i * 16 + 16)
                        if q >= NBANK:
                            pe.wait_ge(copied[b], i * per[b] + q // NBANK)
                        else:
                            pe.wait_ge(stored[b], (i * per[b]) * 16 + 16)
                        for k in range(KD):
                            mm = pe.matmul(pb[b][0:r, 0:blk], g.hT[:, k, c0:c0 + r], w[s][:, k, :],
                                           start=(k == 0), stop=(k == KD - 1))
                        mm.then_inc(made[b], 1)


QK_HEADS = 26
V_B = 2304


def rotate_heads(nc, a, g, p0, KB, KA, va, vb):
    n_all = NT + NC
    with Phase(nc, "rot") as ph:
        rope = ph.sb("rope", [P, 2, n_all, HD])
        gain = ph.sb("gain", [P, 4, HD])
        qk = [ph.sb(f"qk{s}", [P, QK_HEADS, HD]) for s in range(2)]
        tmp = ph.sb("tmp", [P, QK_HEADS, HD])
        rot = ph.sb("rotated", [P, 28, HD])
        ss = ph.sb("ss", [P, QK_HEADS])
        rt = ph.sb("rt", [P, QK_HEADS])
        pt = ph.ps("pt", [P, 16, P])
        small, in0, in1, squared, summed, rooted, plain, rotated, turned, evac_a, evac_d, dstep, padded = ph.sems(
            "small in0 in1 squared summed rooted plain rotated turned evac_a evac_d dstep padded")
        qk_in = [in0, in1]
        spans = ((0, 8), (8, 10), (10, 18), (18, 26))
        with nc.Block() as block:
            @block.sync
            def _(sp):
                def load(s, i):
                    src = p0[bass.ds(i * P, P), :]
                    sp.dma_start(qk[s][:, 0:10, :], src[:, 0:640]).then_inc(qk_in[s], 16)
                    sp.dma_start(qk[s][:, 10:26, :], src[:, 1280:2304]).then_inc(qk_in[s], 16)

                for s in range(2):
                    load(s, s)
                sp.dma_start(rope[:, :, :, :], a["k_rope"].rearrange("c (t p) d -> p c t d", p=P)).then_inc(small, 16)
                for j, name in enumerate(("a_q_norm", "a_k_norm", "b_q_norm", "b_k_norm")):
                    sp.dma_start(gain[:, j, :], rows(a[name][0, :])).then_inc(small, 16)
                sp.dma_start(va[:, 1:, :], p0[:, 640:768].rearrange("(t p) d -> p t d", p=P)).then_inc(small, 16)
                sp.dma_start(vb[:, :, :], p0[:, V_B:V_B + 512].rearrange("(t p) d -> p t d", p=P)).then_inc(small, 16)
                with sp.Fori(1, n_all // 2, 1) as i:
                    for s in range(2):
                        sp.wait_ge(plain, i * 2 + s - 1)
                        load(s, i * 2 + s)
                sp.wait_ge(small, 16 * 7)

            @block.gpsimd
            def _(pool):
                pool.memset(va[:, 0, :], 0.0).then_inc(padded, 1)
                pool.memset(KA[:, :, 0:P], 0.0).then_inc(padded, 1)
                pool.wait_ge(padded, 2)

            @block.scalar
            def _(act):
                with act.Fori(0, n_all // 2, 1) as i:
                    for s in range(2):
                        n = i * 2 + s
                        act.wait_ge(qk_in[s], i * 32 + 32)
                        act.activation(tmp[:, :, :], qk[s][:, :, :], ACT.Square).then_inc(squared, 1)
                        act.wait_ge(summed, n + 1)
                        act.activation(rt[:, :], ss[:, :], ACT.Sqrt, scale=1.0 / HD, bias=g.epsc[:, :]).then_inc(rooted, 1)
                        act.wait_ge(turned, n + 1)
                        act.activation(g.hT[:, 0:4, bass.ds(n * P, P)], pt[:, 0:4, :], ACT.Copy)
                        act.activation(g.hT[:, 4:8, bass.ds(n * P, P)], pt[:, 4:8, :], ACT.Copy).then_inc(evac_a, 1)
                        act.wait_ge(evac_d, n + 1)

            @block.vector
            def _(dve):
                dve.wait_ge(small, 16 * 7)
                per = 5
                with dve.Fori(0, n_all // 2, 1) as i:
                    for s in range(2):
                        n = i * 2 + s
                        ch = Chain(dve, dstep, n * per)
                        dve.wait_ge(squared, n + 1)
                        dve.tensor_reduce(ss[:, :], tmp[:, :, :], AX.X, ALU.add).then_inc(summed, 1)
                        dve.wait_ge(rooted, n + 1)
                        ch.link(dve.reciprocal(rt[:, :], rt[:, :]))
                        ch.link(dve.tensor_tensor(qk[s][:, :, :], qk[s][:, :, :],
                                                  rt[:, :].unsqueeze(2).broadcast_to([P, QK_HEADS, HD]), ALU.mult))
                        for j, (h0, h1) in enumerate(spans):
                            ins = dve.tensor_tensor(qk[s][:, h0:h1, :], qk[s][:, h0:h1, :],
                                                    gain[:, j:j + 1, :].broadcast_to([P, h1 - h0, HD]), ALU.mult)
                        ch.link(ins)
                        pairs = qk[s][:, :, :].rearrange("p h (x y m) -> p h x y m", x=2, y=2)
                        out = tmp[:, :, :].rearrange("p h (x y m) -> p h x y m", x=2, y=2)
                        sin = rope[:, 1, n, :].rearrange("p (x y m) -> p x y m", x=2, y=2)
                        for y in range(2):
                            ins = dve.tensor_tensor(out[:, :, :, y, :], pairs[:, :, :, 1 - y, :],
                                                    sin[:, :, y, :].unsqueeze(1).broadcast_to([P, QK_HEADS, 2, 16]), ALU.mult)
                        ch.link(ins)
                        cos = rope[:, 0, n, :].unsqueeze(1).broadcast_to([P, QK_HEADS, HD])
                        ch.link(dve.tensor_tensor(qk[s][:, :, :], qk[s][:, :, :], cos, ALU.mult))
                        assert ch.k == per
                        dve.tensor_tensor(rot[:, 0:8, :], qk[s][:, 0:8, :], tmp[:, 0:8, :], ALU.add)
                        for half in range(2):
                            dve.tensor_tensor(rot[:, 8:12, :].rearrange("p (k r) d -> p k r d", r=2)[:, :, half, :],
                                              qk[s][:, 8:10, :], tmp[:, 8:10, :], ALU.add)
                        dve.tensor_tensor(rot[:, 12:28, :], qk[s][:, 10:26, :], tmp[:, 10:26, :], ALU.add).then_inc(rotated, 1)
                        dve.wait_ge(rotated, n + 1)
                        dve.sem_inc(plain, 1)
                        dve.wait_ge(turned, n + 1)
                        dve.tensor_copy(KA[:, :, bass.ds(n * P + P, P)], pt[:, 8:10, :])
                        dve.tensor_copy(KB[:, :, bass.ds(n * P, P)], pt[:, 12:16, :]).then_inc(evac_d, 1)

            @block.tensor
            def _(pe):
                with pe.Fori(0, n_all // 2, 1) as i:
                    for s in range(2):
                        n = i * 2 + s
                        pe.wait_ge(rotated, n + 1)
                        pe.wait_ge(rooted, n + 1)
                        for c, at in enumerate((0, 1, 2, 3, 8, 9, 4, 5, 6, 7, 12, 13, 14, 15)):
                            mm = pe.transpose(pt[:, at, :], rot[:, 2 * c:2 * c + 2, :].rearrange("p h d -> p (h d)"), g.ident[:, :])
                        mm.then_inc(turned, 1)


SCALE = HD ** -0.5


def window_attention(nc, a, g, KA, va, o_dram):
    NP = A_HEADS // 2
    W3 = 3 * P
    with Phase(nc, "wa") as ph:
        mask = ph.sb("mask", [P, NT, W3])
        sink = ph.sb("sink", [P, A_HEADS])
        qc = ph.sb("qc", [P, NP, P])
        kw = ph.sb("kw", [P, 2, W3])
        S = [ph.sb(f"S{e}", [P, W3 + CTX]) for e in range(2)]
        E = [ph.sb(f"E{e}", [P, W3 + CTX]) for e in range(2)]
        ET = [ph.sb(f"ET{e}", [P, 5, P]) for e in range(2)]
        mx = ph.sb("mx", [P, 2])
        nm = ph.sb("nm", [P, 2])
        l = ph.sb("l", [P, 2])
        es = ph.sb("es", [P, 2])
        r = ph.sb("r", [P, 2])
        oa = ph.sb("oa", [P, A_HEADS, HD])
        pS = [ph.ps(f"pS{e}", [P, 1024]) for e in range(2)]
        pw = [pS[e][:, 0:W3] for e in range(2)]
        pc = [pS[e][:, 512:512 + CTX] for e in range(2)]
        pT = [ph.ps(f"pT{e}", [P, 1024]) for e in range(2)]
        po = [pT[e][:, 5 * P:5 * P + NP * HD].rearrange("p (n d) -> p n d", d=HD) for e in range(2)]
        small, window, scores, s_ctx, negmax, expd, turned, et0, et1, pv, o_done, stored, dstep = ph.sems(
            "small window scores s_ctx negmax expd turned et0 et1 pv o_done stored dstep")
        et = [et0, et1]
        with nc.Block() as block:
            def loops(eng, body):
                with eng.Fori(0, NT, 1) as i:
                    body(i, i, True)
                with eng.Fori(0, NC, 1) as i:
                    body(i, i + NT, False)

            @block.sync
            def _(sp):
                sp.dma_start(mask[:, :, :], a["k_window"].rearrange("t p k -> p t k")).then_inc(small, 16)
                sp.dma_start(sink[:, :], rows(a["a_sink"][0, :])).then_inc(small, 16)
                sp.sem_inc(stored, 16)

                def body(i, t, win):
                    sp.wait_ge(o_done, t * NP + NP)
                    sp.dma_start(o_dram[bass.ds(t * P, P), 0:512], oa[:, :, :]).then_inc(stored, 16)
                loops(sp, body)
                sp.wait_ge(stored, 16 + 16 * (NT + NC))

            @block.gpsimd
            def _(pool):
                pool.sem_inc(scores, 1)

                def body(i, t, win):
                    pool.wait_ge(scores, t * NP + 1)
                    pool.tensor_copy(qc[:, :, :], g.hT[:, 0:NP, bass.ds(t * P, P)])
                    if win:
                        ins = pool.tensor_copy(kw[:, :, :], KA[:, :, bass.ds(t * P, W3)])
                    else:
                        ins = pool.tensor_copy(kw[:, :, 0:P], KA[:, :, 0:P])
                    ins.then_inc(window, 1)
                loops(pool, body)

            @block.scalar
            def _(act):
                act.wait_ge(small, 32)

                def body(i, t, win):
                    w0 = 0 if win else W3
                    for n in range(NP):
                        m = t * NP + n
                        act.wait_ge(scores, m + 2)
                        for e in range(2):
                            ins = act.activation(S[e][:, W3:], pc[e], ACT.Copy, scale=SCALE)
                        ins.then_inc(s_ctx, 1)
                        act.wait_ge(negmax, m + 1)
                        for e in range(2):
                            act.activation(E[e][:, w0:], S[e][:, w0:], ACT.Exp, bias=nm[:, e:e + 1], accum_out=l[:, e:e + 1])
                            ins = act.activation(es[:, e:e + 1], sink[:, 2 * n + e:2 * n + e + 1], ACT.Exp, bias=nm[:, e:e + 1])
                        ins.then_inc(expd, 1)
                        act.wait_ge(turned, m + 1)
                        if win:
                            ins = act.activation(ET[1][:, :, :], pT[1][:, 0:5 * P], ACT.Copy)
                        else:
                            ins = act.activation(ET[1][:, 3:5, :], pT[1][:, W3:5 * P], ACT.Copy)
                        ins.then_inc(et[1], 1)
                loops(act, body)

            @block.vector
            def _(dve):
                dve.wait_ge(small, 32)
                per = 3 * NP

                def body(i, t, win):
                    w0 = 0 if win else W3
                    ch = Chain(dve, dstep, t * per)
                    for n in range(NP):
                        m = t * NP + n
                        dve.wait_ge(scores, m + 2)
                        if win:
                            for e in range(2):
                                ins = dve.scalar_tensor_tensor(S[e][:, 0:W3], pw[e], SCALE, mask[:, i, :], ALU.mult, ALU.add)
                            ch.link(ins)
                        else:
                            ch.link(dve.memset(mx[:, :], 0.0))
                        dve.wait_ge(s_ctx, m + 1)
                        for e in range(2):
                            ins = dve.tensor_reduce(mx[:, e:e + 1], S[e][:, w0:], AX.X, ALU.max)
                        ch.link(ins)
                        for e in range(2):
                            ins = dve.tensor_scalar(nm[:, e:e + 1], mx[:, e:e + 1], sink[:, 2 * n + e:2 * n + e + 1], -1.0, ALU.max, ALU.mult)
                        ins.then_inc(negmax, 1)
                        dve.wait_ge(expd, m + 1)
                        ch.link(dve.tensor_tensor(l[:, :], l[:, :], es[:, :], ALU.add))
                        dve.reciprocal(r[:, :], l[:, :])
                        dve.wait_ge(turned, m + 1)
                        if win:
                            ins = dve.tensor_copy(ET[0][:, :, :], pT[0][:, 0:5 * P])
                        else:
                            ins = dve.tensor_copy(ET[0][:, 3:5, :], pT[0][:, W3:5 * P])
                        ins.then_inc(et[0], 1)
                        dve.wait_ge(et[0], m + 1)
                        dve.wait_ge(pv, m + 1)
                        if n == 0:
                            dve.wait_ge(stored, t * 16 + 16)
                        for e in range(2):
                            h = 2 * n + e
                            ins = dve.tensor_scalar(oa[:, h, :], po[e][:, n, :], r[:, e:e + 1], None, ALU.mult)
                        ins.then_inc(o_done, 1)
                    assert ch.k == per
                loops(dve, body)

            @block.tensor
            def _(pe):
                def body(i, t, win):
                    pe.wait_ge(window, t + 1)
                    k0 = 0 if win else 3
                    for n in range(NP):
                        m = t * NP + n
                        kv = n // 2
                        for e in range(2):
                            half = slice(64 * e, 64 * e + 64)
                            if win:
                                pe.matmul(pw[e], qc[half, n, :], kw[half, kv, :], start=True, stop=True)
                            mm = pe.matmul(pc[e], qc[half, n, :], KA[half, kv, P + SEQ:P + ALLT], start=True, stop=True)
                        mm.then_inc(scores, 1)
                        pe.wait_ge(expd, m + 1)
                        for e in range(2):
                            for k in range(k0, 5):
                                mm = pe.transpose(pT[e][:, P * k:P * k + P], E[e][:, P * k:P * k + P], g.ident[:, :])
                        mm.then_inc(turned, 1)
                        for e in range(2):
                            h = 2 * n + e
                            pe.wait_ge(et[e], m + 1)
                            for k in range(k0, 5):
                                v = va[:, bass.ds(i + k, 1), :] if k < 3 else va[:, NT + 1 + k - 3:NT + 2 + k - 3, :]
                                mm = pe.matmul(po[e][:, n, :], ET[e][:, k, :], v[:, 0, HD * kv:HD * kv + HD], start=(k == k0), stop=(k == 4))
                        mm.then_inc(pv, 1)
                loops(pe, body)


def differential_attention(nc, a, g, KB, vb, o_dram):
    with Phase(nc, "da") as ph:
        qc = ph.sb("qc", [P, B_HEADS, P])
        E = [ph.sb(f"E{m}", [P, ALLT]) for m in range(2)]
        ET = ph.sb("ET", [P, 10, P])
        mx = ph.sb("mx", [P, 2])
        nm = ph.sb("nm", [P, 2])
        l = ph.sb("l", [P, 2])
        r = ph.sb("r", [P, 2])
        ob = ph.sb("ob", [P, B_HEADS, P])
        pS = [ph.ps(f"pS{m}", [P, 1536]) for m in range(2)]
        pT = ph.ps("pT", [P, 4, P])
        po = ph.ps("po", [P, B_HEADS, P])
        qcopied, sc0, sc1, top0, top1, neg0, neg1, ex0, ex1, weights, turned, evac, pv, o_done, stored, dstep = ph.sems(
            "qcopied sc0 sc1 top0 top1 neg0 neg1 ex0 ex1 weights turned evac pv o_done stored dstep")
        sc, top, neg, ex = [sc0, sc1], [top0, top1], [neg0, neg1], [ex0, ex1]
        H = B_HEADS

        def groups(full):
            return [(0, 4), (4, 8), (8, 10)] if full else [(8, 10)]

        def group_count(t, h, full):
            return (t * H + h) * 3 if full else NT * H * 3 + (t - NT) * H + h

        with nc.Block() as block:
            def loops(eng, body):
                with eng.Fori(0, NT, 1) as i:
                    body(i, True)
                with eng.Fori(NT, NT + NC, 1) as i:
                    body(i, False)

            @block.sync
            def _(sp):
                sp.sem_inc(stored, 16)

                def body(t, full):
                    sp.wait_ge(o_done, t * H + H)
                    sp.dma_start(o_dram[bass.ds(t * P, P), 512:1024], ob[:, :, :]).then_inc(stored, 16)
                loops(sp, body)
                sp.wait_ge(stored, 16 + 16 * (NT + NC))

            @block.gpsimd
            def _(pool):
                pool.sem_inc(sc[1], 1)

                def body(t, full):
                    pool.wait_ge(sc[1], t * H + 1)
                    pool.tensor_copy(qc[:, :, :], g.hT[:, 4:8, bass.ds(t * P, P)]).then_inc(qcopied, 1)
                loops(pool, body)

            @block.scalar
            def _(act):
                def body(t, full):
                    k0 = 0 if full else SEQ

                    def exps(h):
                        for m in range(2):
                            act.wait_ge(neg[m], t * H + h + 1)
                            act.activation(E[m][:, k0:], pS[m][:, k0:ALLT], ACT.Exp, scale=SCALE,
                                           bias=nm[:, m:m + 1], accum_out=l[:, m:m + 1]).then_inc(ex[m], 1)

                    exps(0)
                    for h in range(H):
                        for j, (a0, a1) in enumerate(groups(full)):
                            act.wait_ge(turned, group_count(t, h, full) + j + 1)
                            act.activation(ET[:, a0:a1, :], pT[:, 0:a1 - a0, :], ACT.Copy).then_inc(evac, 1)
                        if h + 1 < H:
                            exps(h + 1)
                loops(act, body)

            @block.vector
            def _(dve):
                per = 2 * H

                def body(t, full):
                    k0 = 0 if full else SEQ
                    ch = Chain(dve, dstep, t * per)

                    def maxima(h):
                        n = t * H + h
                        for m in range(2):
                            dve.wait_ge(sc[m], n + 1 + m)
                            dve.tensor_reduce(mx[:, m:m + 1], pS[m][:, k0:ALLT], AX.X, ALU.max).then_inc(top[m], 1)
                            dve.wait_ge(top[m], n + 1)
                            dve.tensor_scalar(nm[:, m:m + 1], mx[:, m:m + 1], -SCALE, None, ALU.mult).then_inc(neg[m], 1)

                    maxima(0)
                    for h in range(H):
                        n = t * H + h
                        for m in range(2):
                            dve.wait_ge(ex[m], n + 1)
                        ch.link(dve.reciprocal(r[:, :], l[:, :]))
                        dve.tensor_tensor(r[:, 1:2], r[:, 1:2], g.neglam[:, :], ALU.mult)
                        ch.link(dve.tensor_scalar(E[0][:, k0:], E[0][:, k0:], r[:, 0:1], None, ALU.mult))
                        dve.scalar_tensor_tensor(E[0][:, k0:], E[1][:, k0:], r[:, 1:2], E[0][:, k0:], ALU.mult, ALU.add).then_inc(weights, 1)
                        if h + 1 < H:
                            dve.wait_ge(weights, n + 1)
                            maxima(h + 1)
                        dve.wait_ge(pv, n + 1)
                        if h == 0:
                            dve.wait_ge(stored, t * 16 + 16)
                        dve.tensor_copy(ob[:, h, :], po[:, h, :]).then_inc(o_done, 1)
                    assert ch.k == per
                loops(dve, body)

            @block.tensor
            def _(pe):
                def body(t, full):
                    pe.wait_ge(qcopied, t + 1)

                    def scores(h):
                        for m in range(2):
                            half = slice(64 * m, 64 * m + 64)
                            if h:
                                pe.wait_ge(ex[m], t * H + h)
                            for c0, c1 in [(0, 512), (512, 1024), (1024, 1280)] if full else [(SEQ, ALLT)]:
                                mm = pe.matmul(pS[m][:, c0:c1], qc[half, h, :], KB[half, h, c0:c1], start=True, stop=True)
                            mm.then_inc(sc[m], 1)

                    scores(0)
                    for h in range(H):
                        n = t * H + h
                        if h + 1 < H:
                            scores(h + 1)
                        pe.wait_ge(weights, n + 1)
                        gs = groups(full)

                        def values(j):
                            for k in range(*gs[j]):
                                mm = pe.matmul(po[:, h, :], ET[:, k, :], vb[:, k, P * h:P * h + P], start=(k == gs[0][0]), stop=(k == 9))
                            return mm

                        for j, (a0, a1) in enumerate(gs):
                            for k in range(a0, a1):
                                mm = pe.transpose(pT[:, k - a0, :], E[0][:, P * k:P * k + P], g.ident[:, :])
                            mm.then_inc(turned, 1)
                            if j:
                                values(j - 1)
                            pe.wait_ge(evac, group_count(t, h, full) + j + 1)
                        values(len(gs) - 1).then_inc(pv, 1)
                loops(pe, body)


def merge_even(nc, a, g, p0, o_dram):
    n_all = NT + NC
    with Phase(nc, "me") as ph:
        o = [ph.sb(f"o{s}", [P, 8, P]) for s in range(2)]
        gt = [ph.sb(f"gt{s}", [P, 8, P]) for s in range(2)]
        sub = ph.sb("sub", [P, P])
        sq = ph.sb("sq", [P, B_HEADS, P])
        ss = ph.sb("ss", [P, B_HEADS])
        pt = ph.ps("pt", [P, 2, 4, P])
        small, in0, in1, squared, summed, rooted, gated, merged, turned, ev, evd, dstep = ph.sems(
            "small in0 in1 squared summed rooted gated merged turned ev evd dstep")
        o_in = [in0, in1]
        with nc.Block() as block:
            @block.sync
            def _(sp):
                sp.dma_start(sub[:, :], rows(a["b_subln"][0, :])).then_inc(small, 16)

                def load(s, t):
                    sp.dma_start(o[s][:, :, :], o_dram[bass.ds(t * P, P), :]).then_inc(o_in[s], 16)
                    sp.dma_start(gt[s][:, 0:4, :], p0[bass.ds(t * P, P), 768:1280]).then_inc(o_in[s], 16)
                    sp.dma_start(gt[s][:, 4:8, :], p0[bass.ds(t * P, P), 2816:3328]).then_inc(o_in[s], 16)
                for s in range(2):
                    load(s, s)
                with sp.Fori(1, n_all // 2, 1) as i:
                    for s in range(2):
                        sp.wait_ge(turned, i * 2 + s - 1)
                        load(s, i * 2 + s)

            @block.scalar
            def _(act):
                with act.Fori(0, n_all // 2, 1) as i:
                    for s in range(2):
                        n = i * 2 + s
                        act.wait_ge(o_in[s], i * 48 + 48)
                        act.activation(sq[:, :, :], o[s][:, 4:8, :], ACT.Square).then_inc(squared, 1)
                        act.activation(gt[s][:, :, :], gt[s][:, :, :], ACT.Silu).then_inc(gated, 1)
                        act.wait_ge(summed, n + 1)
                        act.activation(ss[:, :], ss[:, :], ACT.Sqrt, scale=1.0 / P, bias=g.epsc[:, :]).then_inc(rooted, 1)
                        act.wait_ge(turned, n + 1)
                        act.activation(g.hT[:, 0:4, bass.ds(n * P, P)], pt[:, 0, :, :], ACT.Copy).then_inc(ev, 1)

            @block.vector
            def _(dve):
                dve.wait_ge(small, 16)
                dve.wait_ge(o_in[0], 48)
                per = 3
                with dve.Fori(0, n_all // 2, 1) as i:
                    for s in range(2):
                        n = i * 2 + s
                        ch = Chain(dve, dstep, n * per)
                        dve.wait_ge(squared, n + 1)
                        dve.tensor_reduce(ss[:, :], sq[:, :, :], AX.X, ALU.add).then_inc(summed, 1)
                        dve.wait_ge(rooted, n + 1)
                        ch.link(dve.reciprocal(ss[:, :], ss[:, :]))
                        ch.link(dve.scalar_tensor_tensor(o[s][:, 4:8, :], o[s][:, 4:8, :], 1.0 - LAMBDA_INIT,
                                                         ss[:, :].unsqueeze(2).broadcast_to([P, B_HEADS, P]), ALU.mult, ALU.mult))
                        ch.link(dve.tensor_tensor(o[s][:, 4:8, :], o[s][:, 4:8, :],
                                                  sub[:, :].unsqueeze(1).broadcast_to([P, B_HEADS, P]), ALU.mult))
                        assert ch.k == per
                        dve.wait_ge(gated, n + 1)
                        dve.tensor_tensor(o[s][:, :, :], o[s][:, :, :], gt[s][:, :, :], ALU.mult).then_inc(merged, 1)
                        dve.wait_ge(turned, n + 1)
                        dve.tensor_copy(g.hT[:, 4:8, bass.ds(n * P, P)], pt[:, 1, :, :]).then_inc(evd, 1)

            @block.tensor
            def _(pe):
                with pe.Fori(0, n_all // 2, 1) as i:
                    for s in range(2):
                        n = i * 2 + s
                        pe.wait_ge(merged, n + 1)
                        pe.wait_ge(rooted, n + 1)
                        for k in range(KD):
                            mm = pe.transpose(pt[:, k // 4, k % 4, :], o[s][:, k, :], g.ident[:, :])
                        mm.then_inc(turned, 1)


def project_out(nc, g, tag, parts, w_dram):
    BLK = 256
    NBLK = D // BLK
    tiles = [(x, t, c0 + P * t, gi) for gi, (x, n, c0, _) in enumerate(parts) for t in range(n)]
    n = len(tiles)
    w_v = w_dram.rearrange("(k p) (b n) -> p k b n", p=P, n=BLK)
    with Phase(nc, tag) as ph:
        gate = ph.sb("gate", [P, len(parts), D])
        w = [ph.sb(f"w{s}", [P, KD, BLK]) for s in range(2)]
        tmp = [ph.sb(f"tmp{b}", [P, BLK]) for b in range(4)]
        pb = [ph.ps(f"pb{b}", [P, 512]) for b in range(4)]
        small, in0, in1, made, scaled, added = ph.sems("small in0 in1 made scaled added")
        w_in = [in0, in1]
        with nc.Block() as block:
            @block.sync
            def _(sp):
                for j, part in enumerate(parts):
                    sp.dma_start(gate[:, j, :], rows(g.gate_dram[part[3], :])).then_inc(small, 16)
                for s in range(2):
                    sp.dma_start(w[s][:, :, :], w_v[:, :, s, :]).then_inc(w_in[s], 16)
                with sp.Fori(1, NBLK // 2, 1) as i:
                    for s in range(2):
                        sp.wait_ge(made, (i * 2 + s - 1) * n)
                        sp.dma_start(w[s][:, :, :], w_v[:, :, i * 2 + s, :]).then_inc(w_in[s], 16)

            @block.vector
            def _(dve):
                dve.wait_ge(small, 16 * len(parts))
                dve.sem_inc(scaled, 4)
                with dve.Fori(0, NBLK // 2, 1) as i:
                    for s in range(2):
                        cols = bass.ds((i * 2 + s) * BLK, BLK)
                        for q, (x, t, _, gi) in enumerate(tiles):
                            b = (s * n + q) % 4
                            m = i * 2 * n + s * n + q
                            dve.wait_ge(made, m + 1)
                            dve.tensor_tensor(tmp[b][:, :], pb[b][:, 0:BLK], gate[:, gi, cols], ALU.mult).then_inc(scaled, 1)
                            dve.wait_ge(scaled, m + 5)
                            dve.tensor_tensor(x[:, t, cols], x[:, t, cols], tmp[b][:, :], ALU.add)

            @block.tensor
            def _(pe):
                with pe.Fori(0, NBLK // 2, 1) as i:
                    for s in range(2):
                        pe.wait_ge(w_in[s], i * 16 + 16)
                        for q, (_, _, c0, _) in enumerate(tiles):
                            b = (s * n + q) % 4
                            m = i * 2 * n + s * n + q
                            pe.wait_ge(scaled, m + 1)
                            for k in range(KD):
                                mm = pe.matmul(pb[b][:, 0:BLK], g.hT[:, k, c0:c0 + P], w[s][:, k, :],
                                               start=(k == 0), stop=(k == KD - 1))
                            mm.then_inc(made, 1)


G_HEADS = 4
G_DK = 128
G_DV = 256
G_RANK = 16
G_TAU = 16.0
GK = G_HEADS * G_DK
GV = G_HEADS * G_DV


def log_decays(nc, a, g, p1, la, dec):
    n_all = NT + NC
    with Phase(nc, "ld") as ph:
        wa = ph.sb("wa", [2 * G_RANK, 2, GK])
        ba = ph.sb("ba", [P, 2, GK])
        chunk_of = ph.sb("chunk_of", [P, 2])
        r = ph.sb("r", [P, n_all, 2 * G_RANK])
        rc = ph.sb("rc", [P, 2 * G_RANK])
        rT = ph.sb("rT", [2 * G_RANK, P])
        z = ph.sb("z", [P, 2 * GK])
        e = ph.sb("e", [P, 2 * GK])
        pr = ph.ps("pr", [2 * G_RANK, P])
        pz = ph.ps("pz", [P, 2, GK])
        pd = ph.ps("pd", [P, 2, G_HEADS, 2])
        small, zeroed, placed, turned, copied, logits, biased, absed, logged, made, summed, decayed = ph.sems(
            "small zeroed placed turned copied logits biased absed logged made summed decayed")
        with nc.Block() as block:
            @block.sync
            def _(sp):
                sp.wait_ge(zeroed, 1)
                sp.dma_start(wa[0:G_RANK, 0, :], a["gla_wa_f"][0, :, :]).then_inc(small, 16)
                sp.dma_start(wa[G_RANK:2 * G_RANK, 1, :], a["gla_wa_b"][0, :, :]).then_inc(small, 16)
                sp.dma_start(ba[:, 0, :], rows(a["gla_ba_f"][0, :])).then_inc(small, 16)
                sp.dma_start(ba[:, 1, :], rows(a["gla_ba_b"][0, :])).then_inc(small, 16)
                sp.dma_start(chunk_of[:, :], a["k_chunk_of"][:, :]).then_inc(small, 16)
                sp.dma_start(r[:, :, :], p1[:, 3072:3104].rearrange("(t p) d -> p t d", p=P)).then_inc(small, 16)

            @block.scalar
            def _(act):
                with act.Fori(0, n_all, 1) as t:
                    act.wait_ge(biased, t + 1)
                    act.activation(e[:, :], z[:, :], ACT.Abs).then_inc(absed, 1)
                    act.wait_ge(absed, t * 2 + 1)
                    act.activation(e[:, :], e[:, :], ACT.Exp, scale=-1.0).then_inc(absed, 1)
                    act.wait_ge(absed, t * 2 + 2)
                    act.activation(e[:, :], e[:, :], ACT.Ln, bias=1.0).then_inc(logged, 1)
                    act.wait_ge(summed, t + 1)
                    act.activation(dec[:, bass.ds(t, 1), :], pd[:, :, :, :], ACT.Exp).then_inc(decayed, 1)

            @block.vector
            def _(dve):
                dve.memset(wa[:, :, :], 0.0).then_inc(zeroed, 1)
                dve.wait_ge(small, 16 * 6)
                with dve.Fori(0, n_all, 1) as t:
                    dve.tensor_copy(rc[:, :], r[:, t, :]).then_inc(placed, 1)
                    dve.wait_ge(turned, t + 1)
                    dve.tensor_copy(rT[:, :], pr[:, :]).then_inc(copied, 1)
                    dve.wait_ge(logits, t + 1)
                    dve.tensor_tensor(z[:, :], pz[:, :, :], ba[:, :, :], ALU.add).then_inc(biased, 1)
                    dve.wait_ge(logged, t + 1)
                    dve.scalar_tensor_tensor(z[:, :], z[:, :], 0.0, e[:, :], ALU.min, ALU.subtract).then_inc(made, 1)
                    dve.wait_ge(made, t * 2 + 1)
                    dve.tensor_scalar(la[:, t, :], z[:, :], 1.0 / G_TAU, None, ALU.mult)
                    dve.tensor_scalar(e[:, :], z[:, :], 1.0 / G_TAU, None, ALU.mult).then_inc(made, 1)

            @block.tensor
            def _(pe):
                pe.wait_ge(small, 16 * 6)
                with pe.Fori(0, n_all, 1) as t:
                    pe.wait_ge(placed, t + 1)
                    pe.transpose(pr[:, :], rc[:, :], g.ident[:, :]).then_inc(turned, 1)
                    pe.wait_ge(copied, t + 1)
                    for d in range(2):
                        mm = pe.matmul(pz[:, d, :], rT[:, :], wa[:, d, :], start=True, stop=True)
                    mm.then_inc(logits, 1)
                    pe.wait_ge(made, t * 2 + 2)
                    for d in range(2):
                        for h in range(G_HEADS):
                            mm = pe.matmul(pd[:, d, h, :], e[:, GK * d + G_DK * h:GK * d + G_DK * h + G_DK], chunk_of[:, :],
                                           start=True, stop=True)
                    mm.then_inc(summed, 1)


def linear_attention(nc, a, g, p1, la, dec, O):
    with Phase(nc, "la") as ph:
        masks = ph.sb("masks", [P, 5, P])
        qkv = [ph.sb(f"qkv{d}", [P, 2 * GK + GV]) for d in range(2)]
        eb = ph.sb("eb", [P, GK])
        en = ph.sb("en", [P, GK])
        er = ph.sb("er", [P, GK])
        qd = ph.sb("qd", [P, GK])
        kd = ph.sb("kd", [P, GK])
        ke = ph.sb("ke", [P, GK])
        qdT = ph.sb("qdT", [P, G_HEADS, P])
        kdT = ph.sb("kdT", [P, G_HEADS, P])
        at = ph.sb("at", [P, G_HEADS, P])
        S = [ph.sb(f"S{d}", [P, G_HEADS, G_DV]) for d in range(2)]
        pA = ph.ps("pA", [P, 512])
        pB = ph.ps("pB", [P, 512])
        pq = ph.ps("pq", [P, G_HEADS, P])
        pk = ph.ps("pk", [P, G_HEADS, P])
        po = ph.ps("po", [P, G_HEADS, G_DV])
        pd = ph.ps("pd", [P, G_HEADS, G_DV])
        small, in0, in1, cum, expd, prod, kept, turned, qT_done, kT_done, att, masked, outer, sread, upd, added, zeroed = ph.sems(
            "small in0 in1 cum expd prod kept turned qT_done kT_done att masked outer sread upd added zeroed")
        qkv_in = [in0, in1]
        upto, after = (0, 1), (4, 3)

        def run(eng, unit):
            for j in range(NC):
                for d in range(2):
                    unit(d, 2 * j + d, None, NT + (j if d == 0 else NC - 1 - j), j)
            with eng.Fori(0, NT, 1) as i:
                for d in range(2):
                    unit(d, i * 2 + d + 2 * NC, i * 2 + d, i if d == 0 else i * -1 + NT - 1, i + NC)

        with nc.Block() as block:
            @block.sync
            def _(sp):
                sp.dma_start(masks[:, :, :], a["k_masks"].rearrange("m p k -> p m k")).then_inc(small, 16)

                def unit(d, n, u, tile, j):
                    if u is not None or j > 0:
                        sp.wait_ge(outer, n * 2 - 2)
                    if u is None:
                        src = p1[tile * P:tile * P + P, :]
                        sp.dma_start(qkv[d][:, GK:], src[:, GK:2 * GK + GV]).then_inc(qkv_in[d], 16)
                    else:
                        src = p1[bass.ds(tile * P, P), :]
                        sp.dma_start(qkv[d][:, :], src[:, 0:2 * GK + GV]).then_inc(qkv_in[d], 16)
                run(sp, unit)

            @block.gpsimd
            def _(pool):
                for d in range(2):
                    pool.memset(S[d][:, :, :], 0.0).then_inc(zeroed, 1)
                pool.memset(O[:, :, :], 0.0).then_inc(zeroed, 1)

                def unit(d, n, u, tile, j):
                    pool.wait_ge(qkv_in[d], j * 16 + 16)
                    pool.wait_ge(expd, n + 1)
                    pool.tensor_tensor(ke[:, :], qkv[d][:, GK:2 * GK], er[:, :], ALU.mult).then_inc(kept, 1)
                run(pool, unit)

            @block.scalar
            def _(act):
                def unit(d, n, u, tile, j):
                    act.wait_ge(cum, n + 1)
                    if u is not None:
                        act.activation(eb[:, :], pA[:, :], ACT.Exp)
                        act.activation(en[:, :], pA[:, :], ACT.Exp, scale=-1.0)
                    act.activation(er[:, :], pB[:, :], ACT.Exp).then_inc(expd, 1)
                    if u is not None:
                        act.wait_ge(turned, u + 1)
                        act.activation(qdT[:, :, :], pq[:, :, :], ACT.Copy).then_inc(qT_done, 1)
                run(act, unit)

            @block.vector
            def _(dve):
                dve.wait_ge(small, 16)
                dve.wait_ge(zeroed, 3)
                dve.sem_inc(added, 1)

                def unit(d, n, u, tile, j):
                    if u is not None:
                        dve.wait_ge(qkv_in[d], j * 16 + 16)
                        dve.wait_ge(expd, n + 1)
                        dve.scalar_tensor_tensor(qd[:, :], qkv[d][:, 0:GK], G_DK ** -0.5, eb[:, :], ALU.mult, ALU.mult)
                        dve.tensor_tensor(kd[:, :], qkv[d][:, GK:2 * GK], en[:, :], ALU.mult).then_inc(prod, 1)
                        dve.wait_ge(turned, u + 1)
                        dve.tensor_copy(kdT[:, :, :], pk[:, :, :]).then_inc(kT_done, 1)
                        dve.wait_ge(att, u + 1)
                        dve.tensor_tensor(at[:, :, :], pA[:, :].rearrange("p (h t) -> p h t", t=P),
                                          masks[:, upto[d], :].unsqueeze(1).broadcast_to([P, G_HEADS, P]), ALU.mult).then_inc(masked, 1)
                    for half, c in enumerate((0, 1) if d == 0 else (1, 0)):
                        dve.wait_ge(outer, n * 2 + half + 1)
                        if u is not None:
                            dve.wait_ge(sread, u * 2 + half + 1)
                        if u is not None or n or half:
                            dve.wait_ge(upd, n * 2 + half)
                        for h in range(G_HEADS):
                            ins = dve.scalar_tensor_tensor(S[d][:, h, :], S[d][:, h, :], dec[:, tile, 8 * d + 2 * h + c:8 * d + 2 * h + c + 1],
                                                           pd[:, h, :], ALU.mult, ALU.add)
                        ins.then_inc(upd, 1)
                    if u is not None:
                        dve.wait_ge(added, u + 1)
                        dve.tensor_tensor(O[:, tile, :], O[:, tile, :], po[:, :, :].rearrange("p h e -> p (h e)"), ALU.add).then_inc(added, 1)
                run(dve, unit)

            @block.tensor
            def _(pe):
                pe.wait_ge(small, 16)
                pe.wait_ge(zeroed, 3)

                def unit(d, n, u, tile, j):
                    la_d = la[:, bass.ds(tile, 1), GK * d:GK * d + GK]
                    if u is not None:
                        pe.matmul(pA[:, :], masks[:, upto[d], :], la_d, start=True, stop=True)
                    pe.matmul(pB[:, :], masks[:, after[d], :], la_d, start=True, stop=True).then_inc(cum, 1)
                    if u is not None:
                        pe.wait_ge(prod, u + 1)
                        for h in range(G_HEADS):
                            pe.transpose(pq[:, h, :], qd[:, G_DK * h:G_DK * h + G_DK], g.ident[:, :])
                        for h in range(G_HEADS):
                            mm = pe.transpose(pk[:, h, :], kd[:, G_DK * h:G_DK * h + G_DK], g.ident[:, :])
                        mm.then_inc(turned, 1)
                    pe.wait_ge(kept, n + 1)
                    if u is None:
                        pe.wait_ge(qkv_in[d], j * 16 + 16)
                    order = (0, 1) if d == 0 else (1, 0)

                    def outers(c):
                        toks = slice(64 * c, 64 * c + 64)
                        for h in range(G_HEADS):
                            mm = pe.matmul(pd[:, h, :], ke[toks, G_DK * h:G_DK * h + G_DK],
                                           qkv[d][toks, 2 * GK + G_DV * h:2 * GK + G_DV * h + G_DV], start=True, stop=True)
                        mm.then_inc(outer, 1)

                    def from_state(c):
                        toks = slice(64 * c, 64 * c + 64)
                        for h in range(G_HEADS):
                            mm = pe.matmul(po[toks, h, :], qdT[:, h, toks], S[d][:, h, :], start=False, stop=(c == order[1]),
                                           skip_group_check=True)
                        mm.then_inc(sread, 1)

                    if u is not None or n:
                        pe.wait_ge(upd, n * 2)
                    outers(order[0])
                    if u is not None:
                        pe.wait_ge(qT_done, u + 1)
                        pe.wait_ge(kT_done, u + 1)
                        for h in range(G_HEADS):
                            mm = pe.matmul(pA[:, P * h:P * h + P], kdT[:, h, :], qdT[:, h, :], start=True, stop=True)
                        mm.then_inc(att, 1)
                        pe.wait_ge(masked, u + 1)
                        pe.wait_ge(added, u + 1)
                        for h in range(G_HEADS):
                            pe.matmul(po[:, h, :], at[:, h, :], qkv[d][:, 2 * GK + G_DV * h:2 * GK + G_DV * h + G_DV],
                                      start=(h % 2 == 0), stop=False, skip_group_check=True)
                        from_state(order[0])
                    pe.wait_ge(upd, n * 2 + 1)
                    if u is not None:
                        from_state(order[1])
                    outers(order[1])
                run(pe, unit)


def merge_odd(nc, a, g, p1, O):
    with Phase(nc, "mo") as ph:
        gt = [ph.sb(f"gt{s}", [P, G_HEADS, G_DV]) for s in range(2)]
        gain = ph.sb("gain", [P, G_DV])
        sq = ph.sb("sq", [P, G_HEADS, G_DV])
        on = ph.sb("on", [P, G_HEADS, G_DV])
        ss = ph.sb("ss", [P, G_HEADS])
        pt = ph.ps("pt", [P, 2, 4, P])
        small, in0, in1, squared, summed, rooted, gated, merged, turned, ev, evd, dstep = ph.sems(
            "small in0 in1 squared summed rooted gated merged turned ev evd dstep")
        g_in = [in0, in1]
        with nc.Block() as block:
            @block.sync
            def _(sp):
                sp.dma_start(gain[:, :], rows(a["gla_out_norm"][0, :])).then_inc(small, 16)

                def load(s, t):
                    sp.dma_start(gt[s][:, :, :], p1[bass.ds(t * P, P), 2048:3072]).then_inc(g_in[s], 16)
                for s in range(2):
                    load(s, s)
                with sp.Fori(1, NT // 2, 1) as i:
                    for s in range(2):
                        sp.wait_ge(turned, i * 2 + s - 1)
                        load(s, i * 2 + s)

            @block.scalar
            def _(act):
                with act.Fori(0, NT // 2, 1) as i:
                    for s in range(2):
                        n = i * 2 + s
                        act.activation(sq[:, :, :], O[:, n, :], ACT.Square).then_inc(squared, 1)
                        act.wait_ge(g_in[s], i * 16 + 16)
                        act.activation(gt[s][:, :, :], gt[s][:, :, :], ACT.Silu).then_inc(gated, 1)
                        act.wait_ge(summed, n + 1)
                        act.activation(ss[:, :], ss[:, :], ACT.Sqrt, scale=1.0 / G_DV, bias=g.epsc[:, :]).then_inc(rooted, 1)
                        act.wait_ge(turned, n + 1)
                        act.activation(g.hT[:, 0:4, bass.ds(n * P, P)], pt[:, 0, :, :], ACT.Copy).then_inc(ev, 1)

            @block.vector
            def _(dve):
                dve.wait_ge(small, 16)
                per = 3
                with dve.Fori(0, NT // 2, 1) as i:
                    for s in range(2):
                        n = i * 2 + s
                        ch = Chain(dve, dstep, n * per)
                        dve.wait_ge(squared, n + 1)
                        dve.tensor_reduce(ss[:, :], sq[:, :, :], AX.X, ALU.add).then_inc(summed, 1)
                        dve.wait_ge(rooted, n + 1)
                        ch.link(dve.reciprocal(ss[:, :], ss[:, :]))
                        ch.link(dve.tensor_tensor(on[:, :, :], O[:, n, :].rearrange("p (h e) -> p h e", e=G_DV),
                                                  ss[:, :].unsqueeze(2).broadcast_to([P, G_HEADS, G_DV]), ALU.mult))
                        ch.link(dve.tensor_tensor(on[:, :, :], on[:, :, :], gain[:, :].unsqueeze(1).broadcast_to([P, G_HEADS, G_DV]), ALU.mult))
                        assert ch.k == per
                        dve.wait_ge(gated, n + 1)
                        dve.tensor_tensor(on[:, :, :], on[:, :, :], gt[s][:, :, :], ALU.mult).then_inc(merged, 1)
                        dve.wait_ge(turned, n + 1)
                        dve.tensor_copy(g.hT[:, 4:8, bass.ds(n * P, P)], pt[:, 1, :, :]).then_inc(evd, 1)

            @block.tensor
            def _(pe):
                with pe.Fori(0, NT // 2, 1) as i:
                    for s in range(2):
                        n = i * 2 + s
                        pe.wait_ge(merged, n + 1)
                        pe.wait_ge(rooted, n + 1)
                        flat = on[:, :, :].rearrange("p h e -> p (h e)")
                        for k in range(KD):
                            mm = pe.transpose(pt[:, k // 4, k % 4, :], flat[:, P * k:P * k + P], g.ident[:, :])
                        mm.then_inc(turned, 1)


NCUT = [(0, 512), (512, 1024), (1024, T2)]


def project_cols(nc, g, tag, w_dram, c_from, nblk, dst, narrow=None):
    BLK = 256
    w_v = w_dram.rearrange("(k p) n -> p k n", p=P)
    with Phase(nc, tag) as ph:
        w = [ph.sb(f"w{s}", [P, KD, BLK]) for s in range(2)]
        o = [ph.sb(f"o{b}", [P, T2]) for b in range(2)]
        wn = ph.sb("wn", [P, KD, 8])
        on = ph.sb("on", [8, T2])
        pb = [ph.ps(f"pb{b}", [P, 1536]) for b in range(2)]
        in0, in1, in_n, made0, made1, made_n, copied0, copied1, copied_n, st0, st1, st_n = ph.sems(
            "in0 in1 in_n made0 made1 made_n copied0 copied1 copied_n st0 st1 st_n")
        w_in, made, copied, stored = [in0, in1], [made0, made1], [copied0, copied1], [st0, st1]
        with nc.Block() as block:
            @block.gpsimd
            def _(pool):
                def load(s, blk):
                    pool.dma_start(w[s][:, :, :], w_v[:, :, bass.ds(c_from + blk * BLK, BLK)]).then_inc(w_in[s], 16)
                for s in range(2):
                    load(s, s)
                if narrow:
                    pool.dma_start(wn[:, :, :], w_v[:, :, narrow[0]:narrow[0] + narrow[1]]).then_inc(in_n, 16)
                with pool.Fori(1, nblk // 2, 1) as i:
                    for s in range(2):
                        pool.wait_ge(made[1], i * 2 + s - 1)
                        load(s, i * 2 + s)

            @block.sync
            def _(sp):
                for b in range(2):
                    sp.sem_inc(stored[b], 16)
                with sp.Fori(0, nblk // 2, 1) as i:
                    for s in range(2):
                        for b in range(2):
                            m = i * 2 + s
                            sp.wait_ge(copied[b], m + 1)
                            sp.dma_start(dst[bass.ds(m * BLK + b * P, P), :], o[b][:, :]).then_inc(stored[b], 16)
                if narrow:
                    sp.wait_ge(copied_n, 1)
                    sp.dma_start(narrow[2], on[0:narrow[1], :]).then_inc(st_n, 16)
                    sp.wait_ge(st_n, 16)
                for b in range(2):
                    sp.wait_ge(stored[b], 16 + 16 * nblk)

            @block.scalar
            def _(act):
                with act.Fori(0, nblk // 2, 1) as i:
                    for s in range(2):
                        m = i * 2 + s
                        act.wait_ge(made[0], m + 1)
                        act.wait_ge(stored[0], m * 16 + 16)
                        act.activation(o[0][:, :], pb[0][:, 0:T2], ACT.Copy).then_inc(copied[0], 1)
                if narrow:
                    act.wait_ge(made_n, 1)
                    act.activation(on[0:narrow[1], :], pb[0][0:narrow[1], 0:T2], ACT.Copy).then_inc(copied_n, 1)

            @block.vector
            def _(dve):
                with dve.Fori(0, nblk // 2, 1) as i:
                    for s in range(2):
                        m = i * 2 + s
                        dve.wait_ge(made[1], m + 1)
                        dve.wait_ge(stored[1], m * 16 + 16)
                        dve.tensor_copy(o[1][:, :], pb[1][:, 0:T2]).then_inc(copied[1], 1)

            @block.tensor
            def _(pe):
                with pe.Fori(0, nblk // 2, 1) as i:
                    for s in range(2):
                        m = i * 2 + s
                        pe.wait_ge(w_in[s], i * 16 + 16)
                        for b in range(2):
                            pe.wait_ge(stored[b], m * 16 + 16)
                            for c0, c1 in NCUT:
                                for k in range(KD):
                                    mm = pe.matmul(pb[b][:, c0:c1], w[s][:, k, P * b:P * b + P], g.hT[:, k, c0:c1],
                                                   start=(k == 0), stop=(k == KD - 1))
                            mm.then_inc(made[b], 1)
                if narrow:
                    pe.wait_ge(in_n, 16)
                    pe.wait_ge(copied[0], nblk)
                    for c0, c1 in NCUT:
                        for k in range(KD):
                            mm = pe.matmul(pb[0][0:narrow[1], c0:c1], wn[:, k, 0:narrow[1]], g.hT[:, k, c0:c1],
                                           start=(k == 0), stop=(k == KD - 1))
                    mm.then_inc(made_n, 1)


LRU = 256
NL = LRU // P
CONV_A = 4
LRU_C = 8.0


def linear_recurrence(nc, a, g, pT):
    with Phase(nc, "lr") as ph:
        x = ph.sb("x", [P, NL, CONV_A - 1 + T2])
        y = ph.sb("y", [P, NL, T2])
        cw = ph.sb("cw", [P, NL, CONV_A])
        vec = ph.sb("vec", [P, 4, NL])
        sp_ = ph.sb("sp", [P, 3, NL])
        gw = ph.sb("gw", [P, 2, NL, P])
        u = ph.sb("u", [P, NL, T2])
        r = ph.sb("r", [P, NL, T2])
        gi = ph.sb("gi", [P, NL, T2])
        th = ph.sb("th", [P, NL, T2])
        pr = ph.ps("pr", [P, 1536])
        pi = ph.ps("pi", [P, 1536])
        small, zeroed, conv, gates, sig, lam_e, lam_l, decayed, tanhed, ratio, rooted, gelued, dstep = ph.sems(
            "small zeroed conv gates sig lam_e lam_l decayed tanhed ratio rooted gelued dstep")
        with nc.Block() as block:
            @block.sync
            def _(sp):
                sp.wait_ge(zeroed, 2)
                with nc.allow_non_contiguous_dma(reason="short vectors, feature-major"):
                    for c in range(NL):
                        sp.dma_start(cw[:, c, :], a["lru_conv_w_2"][0, :, P * c:P * c + P].rearrange("t p -> p t")).then_inc(small, 16)
                    for j, name in enumerate(("lru_conv_b_2", "lru_gate_a_b_2", "lru_gate_x_b_2", "lru_lambda_2")):
                        sp.dma_start(vec[:, j, :], a[name][0, :].rearrange("(c p) -> p c", p=P)).then_inc(small, 16)
                for j, name in enumerate(("lru_gate_a_w_2", "lru_gate_x_w_2")):
                    for h in range(4):
                        half = slice(64 * (h % 2), 64 * (h % 2) + 64)
                        sp.dma_start(gw[half, j, h // 2, half], a[name][0, h, :, :]).then_inc(small, 16)
                sp.dma_start(x[:, :, CONV_A - 1:], pT[0:LRU, :].rearrange("(c p) t -> p c t", p=P)).then_inc(small, 16)
                sp.dma_start(y[:, :, :], pT[LRU:2 * LRU, :].rearrange("(c p) t -> p c t", p=P)).then_inc(small, 16)
                sp.wait_ge(small, 16 * 16)

            @block.gpsimd
            def _(pool):
                pool.memset(x[:, :, 0:CONV_A - 1], 0.0).then_inc(zeroed, 1)
                pool.memset(gw[:, :, :, :], 0.0).then_inc(zeroed, 1)

            @block.scalar
            def _(act):
                act.wait_ge(small, 16 * 16)
                act.activation(sp_[:, 0, :], vec[:, 3, :], ACT.Abs).then_inc(lam_e, 1)
                act.wait_ge(lam_e, 1)
                act.activation(sp_[:, 1, :], sp_[:, 0, :], ACT.Exp, scale=-1.0).then_inc(lam_e, 1)
                act.wait_ge(lam_e, 2)
                act.activation(sp_[:, 2, :], sp_[:, 1, :], ACT.Ln, bias=1.0).then_inc(lam_l, 1)
                for c in range(NL):
                    act.wait_ge(gates, c + 1)
                    act.activation(r[:, c, :], pr[:, 0:T2], ACT.Sigmoid, bias=vec[:, 1, c:c + 1])
                    act.activation(gi[:, c, :], pi[:, 0:T2], ACT.Sigmoid, bias=vec[:, 2, c:c + 1]).then_inc(sig, 1)
                act.wait_ge(decayed, 1)
                act.activation(th[:, :, :], r[:, :, :], ACT.Tanh).then_inc(tanhed, 1)
                act.activation(r[:, :, :], r[:, :, :], ACT.Exp).then_inc(tanhed, 1)
                act.wait_ge(ratio, 1)
                act.activation(th[:, :, :], th[:, :, :], ACT.Sqrt).then_inc(rooted, 1)
                act.activation(y[:, :, :], y[:, :, :], ACT.Gelu_apprx_tanh).then_inc(gelued, 1)

            @block.vector
            def _(dve):
                ch = Chain(dve, dstep)
                dve.wait_ge(small, 16 * 16)
                dve.wait_ge(zeroed, 2)
                for c in range(NL):
                    ch.link(dve.tensor_scalar(u[:, c, :], x[:, c, 0:T2], cw[:, c, 0:1], vec[:, 0, c:c + 1], ALU.mult, ALU.add))
                    for j in range(1, CONV_A):
                        ins = dve.scalar_tensor_tensor(u[:, c, :], x[:, c, j:j + T2], cw[:, c, j:j + 1], u[:, c, :], ALU.mult, ALU.add)
                        if j < CONV_A - 1:
                            ch.link(ins)
                    ins.then_inc(conv, 1)
                dve.wait_ge(lam_l, 1)
                ch.link(dve.tensor_scalar(sp_[:, 0, :], vec[:, 3, :], -1.0, 0.0, ALU.mult, ALU.max))
                ch.link(dve.tensor_tensor(sp_[:, 0, :], sp_[:, 0, :], sp_[:, 2, :], ALU.add))
                ch.link(dve.tensor_scalar(sp_[:, 0, :], sp_[:, 0, :], -LRU_C, None, ALU.mult))
                dve.wait_ge(sig, NL)
                for c in range(NL):
                    ins = dve.tensor_scalar(r[:, c, :], r[:, c, :], sp_[:, 0, c:c + 1], None, ALU.mult)
                ins.then_inc(decayed, 1)
                ch.link(dve.tensor_tensor(gi[:, :, :], gi[:, :, :], u[:, :, :], ALU.mult))
                dve.wait_ge(tanhed, 1)
                ch.link(dve.tensor_scalar(u[:, :, :], th[:, :, :], -1.0, 1.0, ALU.mult, ALU.add))
                ch.link(dve.reciprocal(u[:, :, :], u[:, :, :]))
                dve.scalar_tensor_tensor(th[:, :, :], th[:, :, :], -2.0, u[:, :, :], ALU.mult, ALU.mult).then_inc(ratio, 1)
                dve.wait_ge(rooted, 1)
                ch.link(dve.tensor_tensor(gi[:, :, :], gi[:, :, :], th[:, :, :], ALU.mult))
                dve.wait_ge(tanhed, 2)
                for c in range(NL):
                    ins = dve.tensor_tensor_scan(u[:, c, :], r[:, c, :], gi[:, c, :], 0.0, ALU.mult, ALU.add)
                ch.link(ins)
                dve.wait_ge(gelued, 1)
                ch.link(dve.tensor_tensor(g.hT[:, 0:NL, 0:T2], u[:, :, :], y[:, :, :], ALU.mult))

            @block.tensor
            def _(pe):
                pe.wait_ge(small, 16 * 16)
                for c in range(NL):
                    pe.wait_ge(conv, c + 1)
                    if c:
                        pe.wait_ge(sig, c)
                    for j, ps in enumerate((pr, pi)):
                        for c0, c1 in NCUT:
                            mm = pe.matmul(ps[:, c0:c1], gw[:, j, c, :], u[:, c, c0:c1], start=True, stop=True)
                    mm.then_inc(gates, 1)


FOX_HEADS = 8
AUG = HD + 2


def forget_sums(nc, a, g, fT, cum_dram):
    with Phase(nc, "fs") as ph:
        f = ph.sb("f", [FOX_HEADS, T2])
        e = ph.sb("e", [FOX_HEADS, T2])
        one = ph.sb("one", [FOX_HEADS, T2])
        bias = ph.sb("bias", [FOX_HEADS, 1])
        small, absed, logged, summed, stored, dstep = ph.sems("small absed logged summed stored dstep")
        with nc.Block() as block:
            @block.sync
            def _(sp):
                sp.dma_start(f[:, :], fT).then_inc(small, 16)
                with nc.allow_non_contiguous_dma(reason="a short vector"):
                    sp.dma_start(bias[:, :], a["fox_f_bias_2"].rearrange("o h -> h o")).then_inc(small, 16)
                sp.wait_ge(summed, 1)
                sp.dma_start(cum_dram[0, :, :], f[:, :]).then_inc(stored, 16)
                sp.dma_start(cum_dram[1, :, :], e[:, :]).then_inc(stored, 16)
                sp.wait_ge(stored, 32)

            @block.scalar
            def _(act):
                act.wait_ge(small, 32)
                act.activation(e[:, :], f[:, :], ACT.Abs, bias=bias[:, :]).then_inc(absed, 1)
                act.wait_ge(absed, 1)
                act.activation(e[:, :], e[:, :], ACT.Exp, scale=-1.0).then_inc(absed, 1)
                act.wait_ge(absed, 2)
                act.activation(e[:, :], e[:, :], ACT.Ln, bias=1.0).then_inc(logged, 1)

            @block.vector
            def _(dve):
                ch = Chain(dve, dstep)
                dve.wait_ge(small, 32)
                ch.step(dve.memset(one[:, :], 1.0))
                dve.wait_ge(absed, 1)
                ch.link(dve.tensor_scalar(f[:, :], f[:, :], bias[:, :], 0.0, ALU.add, ALU.min))
                dve.wait_ge(logged, 1)
                ch.link(dve.tensor_tensor(f[:, :], f[:, :], e[:, :], ALU.subtract))
                ch.link(dve.tensor_tensor_scan(e[:, :], one[:, :], f[:, :], 0.0, ALU.mult, ALU.add))
                ch.link(dve.tensor_scalar(f[:, :], e[:, :], 1.0 / SCALE, None, ALU.mult))
                dve.tensor_scalar(e[:, :], f[:, :], -1.0, None, ALU.mult).then_inc(summed, 1)


def forgetting_attention(nc, a, g, pT, pv, cum):
    NT2 = len(TILES2)
    with Phase(nc, "fx") as ph:
        q = [ph.sb(f"q{s}", [AUG, T2]) for s in range(2)]
        k = [ph.sb(f"k{s}", [AUG, T2]) for s in range(2)]
        vs = [ph.sb(f"v{s}", [P, NT2, HD]) for s in range(2)]
        causal = ph.sb("causal", [P, P])
        E = [ph.sb(f"E{b}", [P, T2]) for b in range(2)]
        ET = ph.sb("ET", [P, NT2, P])
        mx = ph.sb("mx", [P, 2])
        nm = ph.sb("nm", [P, 2])
        l = ph.sb("l", [P, 2])
        r = ph.sb("r", [P, 2])
        pS = [ph.ps(f"pS{b}", [P, 1536]) for b in range(2)]
        pT_ = ph.ps("pT", [P, 4, P])
        po = ph.ps("po", [P, 512])
        small, ones, in0, in1, scores, topped, negmax, expd, weights, turned, evac, values_in, o_done, dstep = ph.sems(
            "small ones in0 in1 scores topped negmax expd weights turned evac values_in o_done dstep")
        qk_in = [in0, in1]
        seq = [(s, j) for s in range(2) for j in range(NT2)]
        NS = len(seq)

        def groups(j):
            return [(a0, min(a0 + 4, j + 1)) for a0 in range(0, j + 1, 4)]

        def groups_before(n):
            return sum(len(groups(seq[m][1])) for m in range(n))

        per_round = groups_before(NS)
        with nc.Block() as block:
            @block.sync
            def _(sp):
                sp.wait_ge(ones, 6)
                def load(s, h):
                    sp.dma_start(q[s][0:HD, :], pT[bass.ds(512 + h * HD, HD), :]).then_inc(qk_in[s], 16)
                    sp.dma_start(k[s][0:HD, :], pT[bass.ds(1024 + h * HD, HD), :]).then_inc(qk_in[s], 16)
                    sp.dma_start(q[s][HD:HD + 1, :], cum[0, bass.ds(h, 1), :]).then_inc(qk_in[s], 16)
                    sp.dma_start(k[s][HD + 1:HD + 2, :], cum[1, bass.ds(h, 1), :]).then_inc(qk_in[s], 16)
                    sp.dma_start(vs[s][0:META, 0, :], pv[0:META, bass.ds(h * HD, HD)]).then_inc(qk_in[s], 16)
                    sp.dma_start(vs[s][:, 1:, :], pv[META:T2, bass.ds(h * HD, HD)].rearrange("(t p) d -> p t d", p=P)).then_inc(qk_in[s], 16)
                for s in range(2):
                    load(s, s)
                sp.dma_start(causal[:, :], a["k_causal"]).then_inc(small, 16)
                with sp.Fori(1, FOX_HEADS // 2, 1) as i:
                    for s in range(2):
                        sp.wait_ge(values_in, (i - 1) * NS + NT2 * (s + 1))
                        load(s, i * 2 + s)

            @block.gpsimd
            def _(pool):
                first = [(E[s][:, 0:META], 0.0) for s in range(2)] + [(x[s][HD:HD + 2, :], 1.0) for s in range(2) for x in (q, k)]
                for m, (cells, value) in enumerate(first):
                    if m:
                        pool.wait_ge(ones, m)
                    pool.memset(cells, value).then_inc(ones, 1)

            @block.scalar
            def _(act):
                act.wait_ge(ones, 6)
                with act.Fori(0, FOX_HEADS // 2, 1) as i:
                    def exps(n):
                        s, j = seq[n]
                        b, (c0, rr) = n % 2, TILES2[j]
                        act.wait_ge(negmax, i * NS + n + 1)
                        act.activation(E[b][0:rr, 0:c0 + rr], pS[b][0:rr, 0:c0 + rr], ACT.Exp, scale=SCALE,
                                       bias=nm[0:rr, b:b + 1], accum_out=l[0:rr, b:b + 1]).then_inc(expd, 1)
                    exps(0)
                    for n, (s, j) in enumerate(seq):
                        if n + 1 < NS:
                            exps(n + 1)
                        rr = TILES2[j][1]
                        for gi, (a0, a1) in enumerate(groups(j)):
                            act.wait_ge(turned, i * per_round + groups_before(n) + gi + 1)
                            if a0 == 0:
                                ins = act.activation(ET[0:META, 0, 0:rr], pT_[0:META, 0, 0:rr], ACT.Copy)
                            b0 = max(a0, 1)
                            if a1 > b0:
                                ins = act.activation(ET[:, b0:a1, 0:rr], pT_[:, b0 - a0:a1 - a0, 0:rr], ACT.Copy)
                            ins.then_inc(evac, 1)

            @block.vector
            def _(dve):
                dve.wait_ge(small, 16)
                with dve.Fori(0, FOX_HEADS // 2, 1) as i:
                    ch = Chain(dve, dstep, i * 2 * NS)

                    def maxima(n):
                        s, j = seq[n]
                        b, (c0, rr) = n % 2, TILES2[j]
                        dve.wait_ge(scores, i * NS + n + 1)
                        ch.link(dve.tensor_tensor(pS[b][0:rr, c0:c0 + rr], pS[b][0:rr, c0:c0 + rr], causal[0:rr, 0:rr], ALU.add))
                        dve.tensor_reduce(mx[0:rr, b:b + 1], pS[b][0:rr, 0:c0 + rr], AX.X, ALU.max).then_inc(topped, 1)
                        dve.wait_ge(topped, i * NS + n + 1)
                        dve.tensor_scalar(nm[0:rr, b:b + 1], mx[0:rr, b:b + 1], -SCALE, None, ALU.mult).then_inc(negmax, 1)

                    maxima(0)
                    for n, (s, j) in enumerate(seq):
                        b, (c0, rr) = n % 2, TILES2[j]
                        dve.wait_ge(expd, i * NS + n + 1)
                        ch.link(dve.reciprocal(r[0:rr, b:b + 1], l[0:rr, b:b + 1]))
                        dve.tensor_scalar(E[b][0:rr, 0:c0 + rr], E[b][0:rr, 0:c0 + rr], r[0:rr, b:b + 1], None, ALU.mult).then_inc(weights, 1)
                        if n + 1 < NS:
                            maxima(n + 1)
                        dve.wait_ge(values_in, i * NS + n + 1)
                        half = slice(64 * s, 64 * s + 64)
                        dve.tensor_copy(g.hT[half, bass.ds(i + 2, 1), c0:c0 + rr], po[half, 0:rr]).then_inc(o_done, 1)
                    assert ch.k == 2 * NS

            @block.tensor
            def _(pe):
                pe.wait_ge(small, 16)
                with pe.Fori(0, FOX_HEADS // 2, 1) as i:
                    def scores_of(n):
                        s, j = seq[n]
                        b, (c0, rr) = n % 2, TILES2[j]
                        if j == 0:
                            pe.wait_ge(qk_in[s], i * 96 + 96)
                        if n >= 2:
                            pe.wait_ge(expd, i * NS + n - 1)
                        for k0, k1 in NCUT:
                            k1 = min(k1, c0 + rr)
                            if k0 < k1:
                                mm = pe.matmul(pS[b][0:rr, k0:k1], q[s][:, c0:c0 + rr], k[s][:, k0:k1], start=True, stop=True)
                        mm.then_inc(scores, 1)

                    scores_of(0)
                    for n, (s, j) in enumerate(seq):
                        b, (c0, rr) = n % 2, TILES2[j]
                        if n + 1 < NS:
                            scores_of(n + 1)
                        pe.wait_ge(weights, i * NS + n + 1)
                        te = P if j == 0 else rr
                        gs = groups(j)
                        half = slice(64 * s, 64 * s + 64)

                        def values(gi):
                            for t in range(*gs[gi]):
                                kr = TILES2[t][1]
                                mm = pe.matmul(po[half, 0:rr], vs[s][0:kr, t, :], ET[0:kr, t, 0:rr], start=(t == 0), stop=(t == j))
                            return mm

                        for gi, (a0, a1) in enumerate(gs):
                            for t in range(a0, a1):
                                k0, kr = TILES2[t]
                                mm = pe.transpose(pT_[0:kr, t - a0, 0:te], E[b][0:te, k0:k0 + kr], g.ident[0:te, 0:te])
                            mm.then_inc(turned, 1)
                            if gi:
                                values(gi - 1)
                            pe.wait_ge(evac, i * per_round + groups_before(n) + gi + 1)
                        values(len(gs) - 1).then_inc(values_in, 1)


RW = 256
RW_HEADS = 4
TP = P * len(TILES2)
PADT = TP - T2
R_, K_, V_, KK_, LW_, A_, G_ = (2 * j for j in range(7))
GN_EPS = 64e-5


def delta_inputs(nc, a, g, pT, F):
    with Phase(nc, "di") as ph:
        p = ph.sb("p", [P, 8, 1 + T2])
        d = ph.sb("d", [P, T2])
        kx = ph.sb("kx", [P, 2, T2])
        mu = ph.sb("mu", [P, 8])
        vec = ph.sb("vec", [P, 5, 2])
        up = ph.sb("up", [P, RW])
        gup = ph.sb("gup", [P, RW])
        pw = ph.ps("pw", [P, 1536])
        pa = ph.ps("pa", [P, 1536])
        small, padded, shifted, lora, gated, w_made, a_made, g_made, w_sig, a_sig, g_copied, dstep = ph.sems(
            "small padded shifted lora gated w_made a_made g_made w_sig a_sig g_copied dstep")
        with nc.Block() as block:
            @block.sync
            def _(sp):
                sp.dma_start(p[:, :, 1:], pT[2056:3080, :].rearrange("(c p) t -> p c t", p=P)).then_inc(small, 16)
                with nc.allow_non_contiguous_dma(reason="short vectors, feature-major"):
                    sp.dma_start(mu[:, :], a["rwkv_mu_2"][0, :].rearrange("(c p) -> p c", p=P)).then_inc(small, 16)
                    for j, name in enumerate(("rwkv_w0_2", "rwkv_a0_2", "rwkv_k_k_2", "rwkv_k_a_2")):
                        sp.dma_start(vec[:, j, :], a[name][0, :].rearrange("(c p) -> p c", p=P)).then_inc(small, 16)
                sp.dma_start(up[0:64, :], a["rwkv_w_up_2"][0, :, :]).then_inc(small, 16)
                sp.dma_start(up[64:P, :], a["rwkv_a_up_2"][0, :, :]).then_inc(small, 16)
                sp.dma_start(gup[:, :], a["rwkv_g_up_2"][0, :, :]).then_inc(small, 16)

            @block.gpsimd
            def _(pool):
                pool.memset(F[:, :, 0:PADT], 0.0).then_inc(padded, 1)
                pool.memset(p[:, :, 0:1], 0.0).then_inc(padded, 1)

            @block.scalar
            def _(act):
                act.wait_ge(small, 16 * 9)
                act.wait_ge(shifted, 1)
                act.activation(p[0:64, 6, 1:], p[0:64, 6, 1:], ACT.Tanh).then_inc(lora, 1)
                act.wait_ge(shifted, 2)
                act.activation(p[:, 7, 1:], p[:, 7, 1:], ACT.Sigmoid).then_inc(gated, 1)
                for c in range(2):
                    act.wait_ge(w_made, c + 1)
                    act.activation(F[:, LW_ + c, PADT:], pw[:, 0:T2], ACT.Sigmoid, bias=vec[:, 0, c:c + 1]).then_inc(w_sig, 1)
                    act.wait_ge(a_made, c + 1)
                    act.activation(F[:, A_ + c, PADT:], pa[:, 0:T2], ACT.Sigmoid, bias=vec[:, 1, c:c + 1]).then_inc(a_sig, 1)
                for c in range(2):
                    act.wait_ge(g_made, c + 1)
                    act.activation(F[:, G_ + c, PADT:], (pw, pa)[c][:, 0:T2], ACT.Copy).then_inc(g_copied, 1)

            @block.vector
            def _(dve):
                ch = Chain(dve, dstep)
                dve.wait_ge(small, 16 * 9)
                dve.wait_ge(padded, 2)
                for c in (6, 7, 2, 3, 0, 1, 4, 5):
                    dst = {6: p[:, 6, 1:], 7: p[:, 7, 1:], 2: kx[:, 0, :], 3: kx[:, 1, :], 0: F[:, R_, PADT:],
                           1: F[:, R_ + 1, PADT:], 4: F[:, V_, PADT:], 5: F[:, V_ + 1, PADT:]}[c]
                    ch.link(dve.tensor_tensor(d[:, :], p[:, c, 0:T2], p[:, c, 1:], ALU.subtract))
                    ins = dve.scalar_tensor_tensor(dst, d[:, :], mu[:, c:c + 1], p[:, c, 1:], ALU.mult, ALU.add)
                    if c >= 6:
                        ins.then_inc(shifted, 1)
                        dve.wait_ge(shifted, c - 5)
                    else:
                        ch.link(ins)
                for c in range(2):
                    dve.tensor_scalar(F[:, KK_ + c, PADT:], kx[:, c, :], vec[:, 2, c:c + 1], None, ALU.mult)
                ch.link(dve.tensor_scalar(vec[:, 4, :], vec[:, 3, :], -1.0, 1.0, ALU.mult, ALU.add))
                for c in range(2):
                    dve.wait_ge(w_sig, c + 1)
                    dve.tensor_scalar(F[:, LW_ + c, PADT:], F[:, LW_ + c, PADT:], -(2.718281828459045 ** -0.5), None, ALU.mult)
                    dve.wait_ge(a_sig, c + 1)
                    ch.link(dve.tensor_scalar(d[:, :], F[:, A_ + c, PADT:], vec[:, 3, c:c + 1], vec[:, 4, c:c + 1], ALU.mult, ALU.add))
                    ch.link(dve.tensor_tensor(F[:, K_ + c, PADT:], kx[:, c, :], d[:, :], ALU.mult))

            @block.tensor
            def _(pe):
                pe.wait_ge(lora, 1)
                for c in range(2):
                    cols = slice(P * c, P * c + P)
                    if c:
                        pe.wait_ge(w_sig, c)
                    for c0, c1 in NCUT:
                        mm = pe.matmul(pw[:, c0:c1], up[0:64, cols], p[0:64, 6, 1 + c0:1 + c1], start=True, stop=True)
                    mm.then_inc(w_made, 1)
                    if c:
                        pe.wait_ge(a_sig, c)
                    for c0, c1 in NCUT:
                        mm = pe.matmul(pa[:, c0:c1], up[64:P, cols], p[64:P, 6, 1 + c0:1 + c1], start=True, stop=True)
                    mm.then_inc(a_made, 1)
                pe.wait_ge(gated, 1)
                for c in range(2):
                    pe.wait_ge((w_sig, a_sig)[c], 2)
                    for c0, c1 in NCUT:
                        mm = pe.matmul((pw, pa)[c][:, c0:c1], gup[:, P * c:P * c + P], p[:, 7, 1 + c0:1 + c1], start=True, stop=True)
                    mm.then_inc(g_made, 1)


def delta_rule(nc, a, g, F):
    NTP = len(TILES2)
    H = RW_HEADS
    with Phase(nc, "dr") as ph:
        masks = ph.sb("masks", [P, 2, P])
        levels = ph.sb("levels", [P, 6, P])
        chunk_of = ph.sb("chunk_of", [P, 2])
        rk_row = ph.sb("rk_row", [P, RW])
        lnw = ph.sb("lnw", [P, RW])
        lnb = ph.sb("lnb", [P, RW])
        gneps = ph.sb("gneps", [P, 1])
        Fc = ph.sb("Fc", [P, 14, P])
        T = ph.sb("T", [P, 7, RW])
        Vc = ph.sb("Vc", [P, 2, RW])
        Uc = ph.sb("Uc", [P, 2, RW])
        eb = ph.sb("eb", [P, 3, RW])
        dec = ph.sb("dec", [64, H, 2])
        sq = ph.sb("sq", [P, RW])
        n4 = ph.sb("n4", [P, 4])
        hat = ph.sb("hat", [P, 4, RW])
        hatT = ph.sb("hatT", [64, 4, H, P])
        AT = ph.sb("AT", [P, 4, H, P])
        Lm = ph.sb("Lm", [P, 2, H, P])
        X = ph.sb("X", [P, H, P])
        XT = ph.sb("XT", [P, H, P])
        Y = ph.sb("Y", [P, H, P])
        P1T = ph.sb("P1T", [64, H, P])
        W = ph.sb("W", [P, RW])
        P2 = ph.sb("P2", [P, RW])
        S = ph.sb("S", [64, RW])
        d = ph.sb("d", [P, RW])
        bo = ph.sb("bo", [P, RW])
        s4 = ph.sb("s4", [P, 4])
        v4 = ph.sb("v4", [P, 4])
        bsum = ph.sb("bsum", [P, 4])
        b = [ph.ps(f"b{j}", [P, 512]) for j in range(8)]
        (small, zeroed, copied, turned, ev_a, ev_d, cum, expd, sqd, rooted, hats, hat_t, hT_a, hT_d, att, masked,
         lvl, x0, x0_t, X_ev, y_made, y_ev, z_made, xs, pre, pre_a, pre_d, p2m, p2e, u_made, u_done, ds_made, s_done,
         bonus, o_made, osq, oroot, vsum, vroot, out_done, out_t, mixed, dstep) = ph.sems(
            "small zeroed copied turned ev_a ev_d cum expd sqd rooted hats hat_t hT_a hT_d att masked "
            "lvl x0 x0_t X_ev y_made y_ev z_made xs pre pre_a pre_d p2m p2e u_made u_done ds_made s_done "
            "bonus o_made osq oroot vsum vroot out_done out_t mixed dstep")

        def heads(ap):
            return ap.rearrange("p (h d) -> p h d", h=H)

        def wide(ap4, n=64):
            return ap4.unsqueeze(2).broadcast_to([P, 4, n])

        with nc.Block() as block:
            @block.sync
            def _(sp):
                sp.dma_start(masks[:, :, :], a["k_masks"][0:4:3, :, :].rearrange("m p k -> p m k")).then_inc(small, 16)
                sp.dma_start(levels[:, :, :], a["k_levels"].rearrange("m p k -> p m k")).then_inc(small, 16)
                sp.dma_start(chunk_of[:, :], a["k_chunk_of"]).then_inc(small, 16)
                sp.dma_start(rk_row[:, :], rows(a["rwkv_r_k_2"].rearrange("o h d -> (o h d)"))).then_inc(small, 16)
                sp.dma_start(lnw[:, :], rows(a["rwkv_ln_w_2"][0, :])).then_inc(small, 16)
                sp.dma_start(lnb[:, :], rows(a["rwkv_ln_b_2"][0, :])).then_inc(small, 16)

            @block.gpsimd
            def _(pool):
                pool.wait_ge(small, 16 * 6)
                for m, (cells, value) in enumerate(((Vc[:, :, :], 0.0), (Uc[:, :, :], 0.0), (S[:, :], 0.0), (gneps[:, :], GN_EPS))):
                    if m:
                        pool.wait_ge(zeroed, m)
                    pool.memset(cells, value).then_inc(zeroed, 1)
                pool.sem_inc(turned, 1)
                with pool.Fori(0, NTP, 1) as i:
                    pool.wait_ge(turned, i + 1)
                    pool.tensor_copy(Fc[:, :, :], F[:, :, bass.ds(i * P, P)]).then_inc(copied, 1)
                    pool.wait_ge(copied, i + 1)
                    pool.wait_ge(ev_a, i + 1)
                    pool.tensor_tensor(bo[:, :], T[:, 0, :], T[:, 1, :], ALU.mult).then_inc(bonus, 1)
                    pool.wait_ge(bonus, i * 2 + 1)
                    pool.tensor_tensor(bo[:, :], bo[:, :], rk_row[:, :], ALU.mult).then_inc(bonus, 1)
                    pool.wait_ge(bonus, i * 2 + 2)
                    pool.wait_ge(masked, i + 1)
                    for n in range(5):
                        if n >= 2:
                            pool.wait_ge(y_made, i * 5 + n - 1)
                            pool.wait_ge(lvl, i * 5 + n - 1)
                        pool.tensor_tensor(Lm[:, n % 2, :, :], AT[:, 0, :, :], levels[:, n + 1, :].unsqueeze(1).broadcast_to([P, H, P]),
                                           ALU.mult).then_inc(lvl, 1)
                    pool.wait_ge(lvl, i * 5 + 5)

            @block.scalar
            def _(act):
                act.wait_ge(zeroed, 4)
                with act.Fori(0, NTP, 1) as i:
                    act.wait_ge(turned, i + 2)
                    act.activation(T[:, 0:2, :], b[0][:, :], ACT.Copy)
                    act.activation(T[:, 2:4, :], b[1][:, :], ACT.Copy)
                    for c in range(2):
                        toks = slice(64 * c, 64 * c + 64)
                        ins = act.activation(Vc[toks, c, :], b[1][toks, 0:RW], ACT.Copy)
                    ins.then_inc(ev_a, 1)
                    act.wait_ge(sqd, i + 1)
                    act.activation(n4[:, :], n4[:, :], ACT.Sqrt).then_inc(rooted, 1)
                    act.wait_ge(cum, i + 1)
                    act.activation(eb[:, 0, :], b[4][:, 0:RW], ACT.Exp)
                    act.activation(eb[:, 1, :], b[4][:, 0:RW], ACT.Exp, scale=-1.0)
                    act.activation(eb[:, 2, :], b[4][:, RW:], ACT.Exp)
                    act.activation(dec[:, :, :], b[5][0:64, 0:8], ACT.Exp).then_inc(expd, 1)
                    act.wait_ge(hat_t, i + 1)
                    act.activation(hatT[:, 0, :, :], b[0][0:64, :], ACT.Copy)
                    act.activation(hatT[:, 1, :, :], b[1][0:64, :], ACT.Copy).then_inc(hT_a, 1)
                    act.wait_ge(x0_t, i + 1)
                    act.activation(X[:, :, :], b[4][:, :], ACT.Copy).then_inc(X_ev, 1)
                    for n in range(5):
                        act.wait_ge(y_made, i * 5 + n + 1)
                        act.activation(Y[:, :, :], b[5][:, :], ACT.Copy).then_inc(y_ev, 1)
                    act.wait_ge(pre, i + 1)
                    act.activation(P1T[:, :, :], b[0][0:64, :], ACT.Copy).then_inc(pre_a, 1)
                    act.wait_ge(p2m, i + 1)
                    act.activation(P2[:, :], b[2][:, 0:RW], ACT.Copy).then_inc(p2e, 1)
                    act.wait_ge(osq, i + 1)
                    act.activation(sq[:, :], d[:, :], ACT.Square).then_inc(oroot, 1)
                    act.wait_ge(vsum, i + 1)
                    act.activation(v4[:, :], v4[:, :], ACT.Sqrt, scale=1.0 / 64, bias=gneps[:, :]).then_inc(vroot, 1)
                    act.wait_ge(out_t, i + 1)
                    act.activation(g.hT[:, 6:8, bass.ds(i * P, P)], b[7][:, 0:RW].rearrange("p (c t) -> p c t", c=2), ACT.Copy).then_inc(mixed, 1)

            @block.vector
            def _(dve):
                dve.wait_ge(small, 16 * 6)
                dve.wait_ge(zeroed, 4)
                per = 18
                with dve.Fori(0, NTP, 1) as i:
                    ch = Chain(dve, dstep, i * per)
                    dve.wait_ge(turned, i + 2)
                    dve.tensor_copy(T[:, 4:6, :], b[2][:, :])
                    dve.tensor_copy(T[:, 6, :], b[3][:, 0:RW]).then_inc(ev_d, 1)
                    dve.wait_ge(ev_a, i + 1)
                    ch.link(dve.tensor_tensor(d[:, :], T[:, 3, :], T[:, 3, :], ALU.mult))
                    dve.tensor_reduce(n4[:, :], heads(d[:, :]), AX.X, ALU.add).then_inc(sqd, 1)
                    dve.wait_ge(rooted, i + 1)
                    ch.link(dve.tensor_scalar(n4[:, :], n4[:, :], 1e-12, None, ALU.max))
                    ch.link(dve.reciprocal(n4[:, :], n4[:, :]))
                    dve.wait_ge(ev_d, i + 1)
                    ch.link(dve.tensor_tensor(heads(T[:, 3, :]), heads(T[:, 3, :]), wide(n4[:, :]), ALU.mult))
                    ch.link(dve.scalar_tensor_tensor(d[:, :], T[:, 3, :], -1.0, T[:, 5, :], ALU.mult, ALU.mult))
                    dve.wait_ge(expd, i + 1)
                    dve.tensor_tensor(hat[:, 0, :], T[:, 3, :], eb[:, 2, :], ALU.mult)
                    dve.tensor_tensor(hat[:, 1, :], T[:, 0, :], eb[:, 0, :], ALU.mult)
                    dve.tensor_tensor(hat[:, 2, :], T[:, 1, :], eb[:, 1, :], ALU.mult)
                    dve.tensor_tensor(hat[:, 3, :], d[:, :], eb[:, 1, :], ALU.mult).then_inc(hats, 1)
                    dve.wait_ge(hat_t, i + 1)
                    dve.tensor_copy(hatT[:, 2, :, :], b[2][0:64, :])
                    dve.tensor_copy(hatT[:, 3, :, :], b[3][0:64, :]).then_inc(hT_d, 1)
                    dve.wait_ge(att, i + 1)
                    for j, m in enumerate((1, 1, 0, 0)):
                        ins = dve.tensor_tensor(AT[:, j, :, :], b[4 + j][:, :].rearrange("p (h t) -> p h t", h=H),
                                                masks[:, m, :].unsqueeze(1).broadcast_to([P, H, P]), ALU.mult)
                    ins.then_inc(masked, 1)
                    dve.wait_ge(masked, i + 1)
                    ch.link(dve.tensor_tensor(XT[:, :, :], AT[:, 0, :, :], levels[:, 0, :].unsqueeze(1).broadcast_to([P, H, P]), ALU.mult))
                    dve.tensor_tensor(XT[:, :, :], XT[:, :, :], g.ident[:, :].unsqueeze(1).broadcast_to([P, H, P]), ALU.add).then_inc(x0, 1)
                    for n in range(5):
                        dve.wait_ge(z_made, i * 5 + n + 1)
                        if n == 0:
                            dve.wait_ge(X_ev, i + 1)
                            dve.wait_ge(x0, i + 1)
                        else:
                            dve.wait_ge(xs, i * 5 + n)
                        if n < 4:
                            dve.tensor_tensor(X[:, :, :], X[:, :, :], b[6][:, :].rearrange("p (h t) -> p h t", h=H), ALU.add)
                        dve.tensor_tensor(XT[:, :, :], XT[:, :, :], b[7][:, :].rearrange("p (h t) -> p h t", h=H), ALU.add).then_inc(xs, 1)
                    dve.wait_ge(pre, i + 1)
                    dve.tensor_copy(W[:, :], b[1][:, 0:RW]).then_inc(pre_d, 1)
                    dve.wait_ge(p2e, i + 1)
                    for c in range(2):
                        toks = slice(64 * c, 64 * c + 64)
                        dve.wait_ge(u_made, i * 2 + c + 1)
                        dve.tensor_tensor(Uc[toks, c, :], b[3][toks, 0:RW], P2[toks, :], ALU.add).then_inc(u_done, 1)
                        dve.wait_ge(ds_made, i * 2 + c + 1)
                        ch.link(dve.tensor_tensor(S[:, :], S[:, :], b[5 + c][0:64, 0:RW], ALU.add))
                        dve.tensor_tensor(heads(S[:, :]), heads(S[:, :]), dec[:, :, c:c + 1].broadcast_to([64, H, 64]), ALU.mult).then_inc(s_done, 1)
                        dve.wait_ge(s_done, i * 2 + c + 1)
                    dve.wait_ge(o_made, i + 1)
                    o = heads(b[4][:, 0:RW])
                    ch.link(dve.tensor_reduce(s4[:, :], o, AX.X, ALU.add))
                    ch.link(dve.tensor_scalar(s4[:, :], s4[:, :], 1.0 / 64, None, ALU.mult))
                    dve.tensor_tensor(heads(d[:, :]), o, wide(s4[:, :]), ALU.subtract).then_inc(osq, 1)
                    dve.wait_ge(oroot, i + 1)
                    dve.tensor_reduce(v4[:, :], heads(sq[:, :]), AX.X, ALU.add).then_inc(vsum, 1)
                    dve.wait_ge(bonus, i * 2 + 2)
                    ch.link(dve.tensor_reduce(bsum[:, :], heads(bo[:, :]), AX.X, ALU.add))
                    ch.link(dve.tensor_tensor(heads(sq[:, :]), heads(T[:, 2, :]), wide(bsum[:, :]), ALU.mult))
                    dve.wait_ge(vroot, i + 1)
                    ch.link(dve.reciprocal(v4[:, :], v4[:, :]))
                    ch.link(dve.tensor_tensor(heads(d[:, :]), heads(d[:, :]), wide(v4[:, :]), ALU.mult))
                    ch.link(dve.tensor_tensor(d[:, :], d[:, :], lnw[:, :], ALU.mult))
                    ch.link(dve.tensor_tensor(d[:, :], d[:, :], lnb[:, :], ALU.add))
                    ch.link(dve.tensor_tensor(d[:, :], d[:, :], sq[:, :], ALU.add))
                    dve.tensor_tensor(d[:, :], d[:, :], T[:, 6, :], ALU.mult).then_inc(out_done, 1)
                    assert ch.k <= per, ch.k
                    for _ in range(per - ch.k):
                        dve.sem_inc(dstep, 1)

            @block.tensor
            def _(pe):
                pe.wait_ge(small, 16 * 6)
                pe.wait_ge(zeroed, 4)
                with pe.Fori(0, NTP, 1) as i:
                    pe.wait_ge(copied, i + 1)
                    for c in range(14):
                        mm = pe.transpose(b[c // 4][:, P * (c % 4):P * (c % 4) + P], Fc[:, c, :], g.ident[:, :])
                    mm.then_inc(turned, 1)
                    pe.wait_ge(ev_d, i + 1)
                    pe.matmul(b[4][:, 0:RW], masks[:, 0, :], T[:, 4, :], start=True, stop=True)
                    pe.matmul(b[4][:, RW:], masks[:, 1, :], T[:, 4, :], start=True, stop=True)
                    for h in range(H):
                        mm = pe.matmul(b[5][0:64, 2 * h:2 * h + 2], T[:, 4, 64 * h:64 * h + 64], chunk_of[:, :], start=True, stop=True)
                    mm.then_inc(cum, 1)
                    pe.wait_ge(hats, i + 1)
                    for j in range(4):
                        for h in range(H):
                            mm = pe.matmul(b[j][0:64, P * h:P * h + P], hat[:, j, 64 * h:64 * h + 64], g.ident[:, :],
                                           start=True, stop=True, is_transpose=(j + h > 0))
                    mm.then_inc(hat_t, 1)
                    pe.wait_ge(hT_a, i + 1)
                    pe.wait_ge(hT_d, i + 1)
                    for j, (l, r) in enumerate(((3, 0), (2, 0), (2, 1), (3, 1))):
                        for h in range(H):
                            mm = pe.matmul(b[4 + j][:, P * h:P * h + P], hatT[:, l, h, :], hatT[:, r, h, :], start=True, stop=True)
                    mm.then_inc(att, 1)
                    pe.wait_ge(x0, i + 1)
                    for h in range(H):
                        mm = pe.transpose(b[4][:, P * h:P * h + P], XT[:, h, :], g.ident[:, :])
                    mm.then_inc(x0_t, 1)
                    for n in range(5):
                        if n == 0:
                            pe.wait_ge(X_ev, i + 1)
                        else:
                            pe.wait_ge(xs, i * 5 + n)
                        pe.wait_ge(lvl, i * 5 + n + 1)
                        for h in range(H):
                            mm = pe.matmul(b[5][:, P * h:P * h + P], Lm[:, n % 2, h, :], X[:, h, :], start=True, stop=True)
                        mm.then_inc(y_made, 1)
                        pe.wait_ge(y_ev, i * 5 + n + 1)
                        if n < 4:
                            for h in range(H):
                                pe.matmul(b[6][:, P * h:P * h + P], XT[:, h, :], Y[:, h, :], start=True, stop=True)
                        for h in range(H):
                            mm = pe.matmul(b[7][:, P * h:P * h + P], Y[:, h, :], XT[:, h, :], start=True, stop=True)
                        mm.then_inc(z_made, 1)
                    pe.wait_ge(xs, i * 5 + 5)
                    for h in range(H):
                        pe.matmul(b[0][0:64, P * h:P * h + P], hat[:, 0, 64 * h:64 * h + 64], XT[:, h, :], start=True, stop=True)
                    for h in range(H):
                        mm = pe.matmul(b[1][:, 64 * h:64 * h + 64], AT[:, 1, h, :], T[:, 2, 64 * h:64 * h + 64], start=True, stop=True)
                    mm.then_inc(pre, 1)
                    for h in range(H):
                        pe.matmul(b[4][:, 64 * h:64 * h + 64], AT[:, 2, h, :], T[:, 2, 64 * h:64 * h + 64],
                                  start=(h == 0), stop=False, skip_group_check=True)
                    pe.wait_ge(pre_d, i + 1)
                    for h in range(H):
                        mm = pe.matmul(b[2][:, 64 * h:64 * h + 64], XT[:, h, :], W[:, 64 * h:64 * h + 64], start=True, stop=True)
                    mm.then_inc(p2m, 1)
                    pe.wait_ge(pre_a, i + 1)
                    for c in range(2):
                        toks = slice(64 * c, 64 * c + 64)
                        if c:
                            pe.wait_ge(s_done, i * 2 + c)
                        for h in range(H):
                            mm = pe.matmul(b[3][:, 64 * h:64 * h + 64], P1T[:, h, :], S[:, 64 * h:64 * h + 64], start=True, stop=True)
                        mm.then_inc(u_made, 1)
                        for h in range(H):
                            pe.matmul(b[4][toks, 64 * h:64 * h + 64], hatT[:, 1, h, toks], S[:, 64 * h:64 * h + 64],
                                      start=False, stop=False, skip_group_check=True)
                        for h in range(H):
                            pe.matmul(b[5 + c][0:64, 64 * h:64 * h + 64], hat[:, 2, 64 * h:64 * h + 64], Vc[:, c, 64 * h:64 * h + 64],
                                      start=(h == 0), stop=False, skip_group_check=True)
                        pe.wait_ge(u_done, i * 2 + c + 1)
                        for h in range(H):
                            mm = pe.matmul(b[5 + c][0:64, 64 * h:64 * h + 64], hat[:, 3, 64 * h:64 * h + 64], Uc[:, c, 64 * h:64 * h + 64],
                                           start=False, stop=True, skip_group_check=True)
                        mm.then_inc(ds_made, 1)
                        for h in range(H):
                            mm = pe.matmul(b[4][:, 64 * h:64 * h + 64], AT[:, 3, h, :], Uc[:, c, 64 * h:64 * h + 64],
                                           start=False, stop=(c == 1), skip_group_check=True)
                    mm.then_inc(o_made, 1)
                    pe.wait_ge(out_done, i + 1)
                    for c in range(2):
                        mm = pe.transpose(b[7][:, P * c:P * c + P], d[:, P * c:P * c + P], g.ident[:, :])
                    mm.then_inc(out_t, 1)
                    pe.wait_ge(mixed, i + 1)


def mix_out(nc, a, g):
    with Phase(nc, "xo") as ph:
        w = ph.sb("w", [P, KD, D])
        gain = ph.sb("gain", [P, D])
        hc = [ph.sb(f"hc{s}", [P, KD, P]) for s in range(2)]
        sq = ph.sb("sq", [P, D])
        y = ph.sb("y", [P, D])
        ss = ph.sb("ss", [P, 2])
        po = [ph.ps(f"po{s}", [P, 1024]) for s in range(2)]
        small, w_in, placed, made, squared, rooted, recips, normed, added = ph.sems(
            "small w_in placed made squared rooted recips normed added")

        def run(eng, tile):
            tile(0, 0, META, g.m[:, 0, :], 0)
            with eng.Fori(0, NT // 2, 1) as i:
                for s in range(2):
                    t = i * 2 + s
                    tile(t + 1, (s + 1) % 2, P, g.x[:, t, :], t * P + META)

        with nc.Block() as block:
            @block.sync
            def _(sp):
                sp.dma_start(w[:, :, :], a["w_out_2"][0, :, :].rearrange("(k p) n -> p k n", p=P)).then_inc(w_in, 16)
                sp.dma_start(gain[:, :], rows(a["norm_mix_post_2"][0, :])).then_inc(small, 16)

            @block.gpsimd
            def _(pool):
                def tile(n, s, r, x, c0):
                    if not isinstance(n, int):
                        pool.wait_ge(made, n)
                    pool.tensor_copy(hc[s][:, 0:6, 0:r], g.hT[:, 0:6, bass.ds(c0, r)])
                    pool.tensor_copy(hc[s][:, 6:8, 0:r], g.hT[:, 6:8, bass.ds(c0 + PADT, r)]).then_inc(placed, 1)
                    pool.wait_ge(placed, n + 1)
                run(pool, tile)

            @block.scalar
            def _(act):
                def tile(n, s, r, x, c0):
                    act.wait_ge(made, n + 1)
                    act.activation(sq[0:r, :], po[s][0:r, :], ACT.Square, accum_out=ss[0:r, s:s + 1]).then_inc(squared, 1)
                    act.wait_ge(squared, n + 1)
                    act.activation(ss[0:r, s:s + 1], ss[0:r, s:s + 1], ACT.Sqrt, scale=1.0 / D, bias=g.epsc[0:r, :]).then_inc(rooted, 1)
                run(act, tile)

            @block.vector
            def _(dve):
                dve.wait_ge(small, 16)

                def tile(n, s, r, x, c0):
                    dve.wait_ge(rooted, n + 1)
                    dve.reciprocal(ss[0:r, s:s + 1], ss[0:r, s:s + 1]).then_inc(recips, 1)
                    dve.wait_ge(recips, n + 1)
                    dve.scalar_tensor_tensor(y[0:r, :], po[s][0:r, :], ss[0:r, s:s + 1], gain[0:r, :], ALU.mult, ALU.mult).then_inc(normed, 1)
                    dve.wait_ge(normed, n + 1)
                    dve.tensor_tensor(x, x, y[0:r, :], ALU.add).then_inc(added, 1)
                run(dve, tile)

            @block.tensor
            def _(pe):
                pe.wait_ge(w_in, 16)

                def tile(n, s, r, x, c0):
                    pe.wait_ge(placed, n + 1)
                    for j in range(2):
                        for k in range(KD):
                            mm = pe.matmul(po[s][0:r, 512 * j:512 * j + 512], hc[s][:, k, 0:r], w[:, k, 512 * j:512 * j + 512],
                                           start=(k == 0), stop=(k == KD - 1))
                    mm.then_inc(made, 1)
                    if not isinstance(n, int):
                        pe.wait_ge(normed, n)
                run(pe, tile)


NF = D_FF // P
CONV_F = 3


def ffn_up(nc, a, g, fT):
    w_v = a["ffn_up_2"][0, :, :].rearrange("(k p) n -> p k n", p=P)
    with Phase(nc, "fu") as ph:
        w = [[ph.sb(f"w{s}{e}", [P, KD, P]) for e in range(2)] for s in range(2)]
        cw = ph.sb("cw", [P, 2 * NF, CONV_F])
        f = [ph.sb(f"f{e}", [P, T2]) for e in range(2)]
        pf = [ph.ps(f"pf{e}", [P, 1536]) for e in range(2)]
        small, in0, in1, made0, made1, read0, read1, conv, gelued, dstep = ph.sems(
            "small in0 in1 made0 made1 read0 read1 conv gelued dstep")
        w_in, made, read = [in0, in1], [made0, made1], [read0, read1]
        with nc.Block() as block:
            @block.sync
            def _(sp):
                def load(s, j):
                    for e in range(2):
                        sp.dma_start(w[s][e][:, :, :], w_v[:, :, bass.ds(j * P + D_FF * e, P)]).then_inc(w_in[s], 16)
                for s in range(2):
                    load(s, s)
                with nc.allow_non_contiguous_dma(reason="the taps, feature-major"):
                    for t in range(CONV_F):
                        sp.dma_start(cw[:, :, t], a["ffn_conv_2"][0, t, :].rearrange("(j p) -> p j", p=P)).then_inc(small, 16)
                with sp.Fori(1, NF // 2, 1) as i:
                    for s in range(2):
                        sp.wait_ge(made[1], i * 2 + s - 1)
                        load(s, i * 2 + s)

            @block.scalar
            def _(act):
                with act.Fori(0, NF, 1) as j:
                    act.wait_ge(conv, j + 1)
                    act.activation(f[0][:, :], f[0][:, :], ACT.Gelu_apprx_tanh).then_inc(gelued, 1)

            @block.vector
            def _(dve):
                dve.wait_ge(small, 16 * CONV_F)
                for e in range(2):
                    dve.sem_inc(read[e], 1)
                per = 6
                with dve.Fori(0, NF, 1) as j:
                    ch = Chain(dve, dstep, j * per)
                    for e in range(2):
                        dve.wait_ge(made[e], j + 1)
                        taps = [cw[:, bass.ds(j + NF * e, 1), t].rearrange("p a -> p a") for t in range(CONV_F)]
                        ch.link(dve.tensor_scalar(f[e][:, :], pf[e][:, 0:T2], taps[2], None, ALU.mult))
                        ch.link(dve.scalar_tensor_tensor(f[e][:, 1:], pf[e][:, 0:T2 - 1], taps[1], f[e][:, 1:], ALU.mult, ALU.add))
                        dve.scalar_tensor_tensor(f[e][:, 2:], pf[e][:, 0:T2 - 2], taps[0], f[e][:, 2:], ALU.mult, ALU.add).then_inc(read[e], 1)
                        if e == 0:
                            dve.wait_ge(read[0], j + 2)
                            dve.sem_inc(conv, 1)
                    dve.wait_ge(read[1], j + 2)
                    dve.wait_ge(gelued, j + 1)
                    ch.step(dve.tensor_tensor(fT[:, j, :], f[0][:, :], f[1][:, :], ALU.mult))
                    ch.settle()
                    assert ch.k <= per
                    for _ in range(per - ch.k):
                        dve.sem_inc(dstep, 1)

            @block.tensor
            def _(pe):
                with pe.Fori(0, NF // 2, 1) as i:
                    for s in range(2):
                        pe.wait_ge(w_in[s], i * 32 + 32)
                        for e in range(2):
                            pe.wait_ge(read[e], i * 2 + s + 1)
                            for c0, c1 in NCUT:
                                for k in range(KD):
                                    mm = pe.matmul(pf[e][:, c0:c1], w[s][e][:, k, :], g.hT[:, k, c0:c1], start=(k == 0), stop=(k == KD - 1))
                            mm.then_inc(made[e], 1)


def ffn_down(nc, a, g, fT):
    w_v = a["ffn_down_2"][0, :, :].rearrange("(k p) n -> p k n", p=P)
    with Phase(nc, "fd") as ph:
        w = [ph.sb(f"w{s}", [P, NF, P]) for s in range(2)]
        pf = [ph.ps(f"pf{s}", [P, 1024]) for s in range(2)]
        in0, in1, made, copied, copied_d = ph.sems("in0 in1 made copied copied_d")
        w_in = [in0, in1]
        with nc.Block() as block:
            @block.sync
            def _(sp):
                def load(s, j):
                    sp.dma_start(w[s][:, :, :], w_v[:, :, bass.ds(j * P, P)]).then_inc(w_in[s], 16)
                for s in range(2):
                    load(s, s)
                with sp.Fori(1, KD // 2, 1) as i:
                    for s in range(2):
                        sp.wait_ge(made, i * 2 + s - 1)
                        load(s, i * 2 + s)

            @block.scalar
            def _(act):
                act.sem_inc(copied, 2)
                with act.Fori(0, KD // 2, 1) as i:
                    for s in range(2):
                        m = i * 2 + s
                        act.wait_ge(made, m + 1)
                        act.activation(g.hT[:, bass.ds(m, 1), 0:SEQ], pf[s][:, :], ACT.Copy).then_inc(copied, 1)

            @block.tensor
            def _(pe):
                with pe.Fori(0, KD // 2, 1) as i:
                    for s in range(2):
                        m = i * 2 + s
                        pe.wait_ge(w_in[s], i * 16 + 16)
                        pe.wait_ge(copied, m + 1)
                        for c in range(2):
                            for k in range(NF):
                                mm = pe.matmul(pf[s][:, 512 * c:512 * c + 512], w[s][:, k, :],
                                               fT[:, k, META + 512 * c:META + 512 * c + 512], start=(k == 0), stop=(k == NF - 1))
                        mm.then_inc(made, 1)


def finish(nc, a, g, out):
    out_v = out.rearrange("o (t p) d -> (o t) p d", p=P)
    with Phase(nc, "fi") as ph:
        gain = ph.sb("gain", [P, D])
        hc = [ph.sb(f"hc{s}", [P, KD, P]) for s in range(2)]
        sq = ph.sb("sq", [P, D])
        y = ph.sb("y", [P, D])
        ss = ph.sb("ss", [P, 2])
        po = [ph.ps(f"po{s}", [P, 1024]) for s in range(2)]
        small, placed, turned, squared, rooted, recips, normed, added, stored = ph.sems(
            "small placed turned squared rooted recips normed added stored")

        def run(eng, tile):
            with eng.Fori(0, NT // 2, 1) as i:
                for s in range(2):
                    tile(i * 2 + s, s)

        with nc.Block() as block:
            @block.sync
            def _(sp):
                sp.dma_start(gain[:, :], rows(a["norm_ffn_post_2"][0, :])).then_inc(small, 16)

                def tile(n, s):
                    sp.wait_ge(added, n + 1)
                    sp.dma_start(out_v[bass.ds(n, 1), :, :].rearrange("a p d -> p (a d)"), g.x[:, n, :]).then_inc(stored, 16)
                run(sp, tile)
                sp.wait_ge(stored, 16 * NT)

            @block.gpsimd
            def _(pool):
                pool.sem_inc(turned, 2)

                def tile(n, s):
                    pool.wait_ge(turned, n + 1)
                    pool.tensor_copy(hc[s][:, :, :], g.hT[:, :, bass.ds(n * P, P)]).then_inc(placed, 1)
                    pool.wait_ge(placed, n + 1)
                run(pool, tile)

            @block.scalar
            def _(act):
                def tile(n, s):
                    act.wait_ge(turned, n + 3)
                    act.activation(sq[:, :], po[s][:, :], ACT.Square, accum_out=ss[:, s:s + 1]).then_inc(squared, 1)
                    act.wait_ge(squared, n + 1)
                    act.activation(ss[:, s:s + 1], ss[:, s:s + 1], ACT.Sqrt, scale=1.0 / D, bias=g.epsc[:, :]).then_inc(rooted, 1)
                run(act, tile)

            @block.vector
            def _(dve):
                dve.wait_ge(small, 16)
                dve.sem_inc(normed, 2)

                def tile(n, s):
                    dve.wait_ge(rooted, n + 1)
                    dve.reciprocal(ss[:, s:s + 1], ss[:, s:s + 1]).then_inc(recips, 1)
                    dve.wait_ge(recips, n + 1)
                    dve.scalar_tensor_tensor(y[:, :], po[s][:, :], ss[:, s:s + 1], gain[:, :], ALU.mult, ALU.mult).then_inc(normed, 1)
                    dve.wait_ge(normed, n + 3)
                    dve.tensor_tensor(g.x[:, n, :], g.x[:, n, :], y[:, :], ALU.add).then_inc(added, 1)
                run(dve, tile)

            @block.tensor
            def _(pe):
                def tile(n, s):
                    pe.wait_ge(placed, n + 1)
                    pe.wait_ge(normed, n + 1)
                    for k in range(KD):
                        mm = pe.transpose(po[s][:, P * k:P * k + P], hc[s][:, k, :], g.ident[:, :])
                    mm.then_inc(turned, 1)
                run(pe, tile)


class Held:
    pass


def program(nc, a, out, scratch, stop=99):
    g = Held()
    with ExitStack() as ctx:
        def sb(name, shape):
            return ctx.enter_context(nc.sbuf_tensor(name, shape, F32))

        g.ident = sb("ident", [P, P])
        g.epsc = sb("epsc", [P, 1])
        g.mod = sb("mod", [P, 48, 2])
        g.gs = sb("gs", [P, 2, 2, KD])
        g.neglam = sb("neglam", [P, 1])
        g.x = sb("x", [P, NT, D])
        g.hT = sb("hT", [P, KD, ALLT])
        g.gate_dram = scratch("gate_d", (3, D))
        with ExitStack() as first:
            g.c = first.enter_context(nc.sbuf_tensor("c", [P, NC, D], F32))
            modulation(nc, a, g)
            p0 = scratch("p0", (ALLT, EVEN_IN))
            tiles1 = [(P * t, P) for t in range(NT + NC)]

            def shift(layer, c):
                return g.mod[:, 24 * layer:24 * layer + 8, c]

            parts = [(g.x, P, NT, 0, g.gs[:, 0, 0, :], shift(0, 0)), (g.c, P, NC, SEQ, g.gs[:, 0, 1, :], shift(0, 1))]
            norm_turn(nc, g, "n0", parts, [(g.x[:, :, :], a["x"].rearrange("o (t p) d -> p (o t) d", p=P)),
                                           (g.c[:, :, :], a["ctx"].rearrange("o (t p) d -> p (o t) d", p=P))])
            project_rows(nc, g, "p0", tiles1, a["ab_w_in"][0, :, :], 416, 8, p0)
            if stop <= 0:
                return
            o0 = scratch("o0", (ALLT, D))
            with ExitStack() as inner:
                def isb(name, shape):
                    return inner.enter_context(nc.sbuf_tensor(name, shape, F32))
                KB = isb("KB", [P, 4, ALLT])
                KA = isb("KA", [P, 2, P + ALLT])
                va = isb("va", [P, 1 + NT + NC, P])
                vb = isb("vb", [P, NT + NC, 512])
                rotate_heads(nc, a, g, p0, KB, KA, va, vb)
                window_attention(nc, a, g, KA, va, o0)
                differential_attention(nc, a, g, KB, vb, o0)
            merge_even(nc, a, g, p0, o0)
            project_out(nc, g, "w0", [(g.x, NT, 0, 0), (g.c, NC, SEQ, 1)], a["w_out"][0, :, :])
            norm_turn(nc, g, "n1", [(g.x, P, NT, 0, g.gs[:, 1, 0, :], shift(1, 0)), (g.c, P, NC, SEQ, g.gs[:, 1, 1, :], shift(1, 1))])
            p1 = scratch("p1", (ALLT, ODD_IN))
            project_rows(nc, g, "p1", tiles1, a["gla_w_in"][0, :, :], ODD_IN // 8, 8, p1)
            if stop <= 1:
                return
        with ExitStack() as inner:
            la = g.hT[:, :, :].rearrange("p k t -> p (k t)").rearrange("p (t c) -> p t c", c=2 * GK)
            dec = inner.enter_context(nc.sbuf_tensor("dec", [P, NT + NC, 16], F32))
            O = inner.enter_context(nc.sbuf_tensor("O", [P, NT, GV], F32))
            log_decays(nc, a, g, p1, la, dec)
            linear_attention(nc, a, g, p1, la, dec, O)
            merge_odd(nc, a, g, p1, O)
        project_out(nc, g, "w1", [(g.x, NT, 0, 2)], a["w_out"][1, :, :])
        if stop <= 2:
            xd = scratch("xd", (SEQ, D))
            with Phase(nc, "dump") as ph:
                s = ph.sem("s")
                with nc.Block() as block:
                    @block.sync
                    def _(sp):
                        sp.dma_start(xd.rearrange("(t p) d -> p t d", p=P), g.x[:, :, :]).then_inc(s, 16)
                        sp.wait_ge(s, 16)
            return
        pT = scratch("pT", (D_IN2, T2))
        pv = scratch("pv", (T2, 512))
        cum = scratch("cum", (2, FOX_HEADS, T2))
        g.m = ctx.enter_context(nc.sbuf_tensor("m", [META, 1, D], F32))
        g.pre = ctx.enter_context(nc.sbuf_tensor("pre", [P, 2, KD], F32))
        pre_loads = [(g.m[:, 0, :], a["meta_tokens_2"])] + [
            (g.pre[:, j, :], a[name][0, :].rearrange("(k p) -> p k", p=P))
            for j, name in enumerate(("norm_mix_pre_2", "norm_ffn_pre_2"))]
        w2 = a["w_in_2"][0, :, :]

        def parts2(j):
            return [(g.m, META, 1, 0, g.pre[:, j, :], None), (g.x, P, NT, META, g.pre[:, j, :], None)]

        norm_turn(nc, g, "n2", parts2(0), pre_loads)
        project_cols(nc, g, "ca", w2, 0, 6, pT, (2048, 8, pT[2048:2056, :]))
        project_cols(nc, g, "cc", w2, 2056, 4, pT[2056:3080, :])
        project_rows(nc, g, "cv", TILES2, w2[:, 1536:2048], 256, 2, pv)
        linear_recurrence(nc, a, g, pT)
        forget_sums(nc, a, g, pT[2048:2056, :], cum)
        forgetting_attention(nc, a, g, pT, pv, cum)
        if stop <= 3:
            xd = scratch("hTd", (P, KD, T2))
            with Phase(nc, "dump") as ph:
                s = ph.sem("s")
                with nc.Block() as block:
                    @block.sync
                    def _(sp):
                        sp.dma_start(xd, g.hT[:, :, 0:T2]).then_inc(s, 16)
                        sp.wait_ge(s, 16)
            return
        with ExitStack() as inner:
            F = inner.enter_context(nc.sbuf_tensor("F", [P, 14, TP], F32))
            delta_inputs(nc, a, g, pT, F)
            delta_rule(nc, a, g, F)
        mix_out(nc, a, g)
        norm_turn(nc, g, "n3", parts2(1))
        with ExitStack() as inner:
            fT = inner.enter_context(nc.sbuf_tensor("fT", [P, NF, T2], F32))
            ffn_up(nc, a, g, fT)
            ffn_down(nc, a, g, fT)
        finish(nc, a, g, out)


DEBUG = False
STOP = 99


def shape_constants():
    import numpy as np

    grid_w, m = 64, 16
    inv = 10000.0 ** (-np.arange(m, dtype=np.float32) / m)
    rope = np.zeros((2, ALLT, HD), np.float32)
    rope[0] = 1.0
    pos = np.arange(SEQ)
    for half, p in enumerate((pos // grid_w, pos % grid_w)):
        ang = p.astype(np.float32)[:, None] * inv[None, :].astype(np.float32)
        for quarter, sign in ((0, -1.0), (1, 1.0)):
            cols = slice(32 * half + 16 * quarter, 32 * half + 16 * quarter + 16)
            rope[0, :SEQ, cols] = np.cos(ang)
            rope[1, :SEQ, cols] = sign * np.sin(ang)
    q, k = np.arange(P)[:, None], np.arange(3 * P)[None, :] - P
    near = np.abs(q - k) <= P
    window = np.zeros((NT, P, 3 * P), np.float32)
    for t in range(NT):
        inside = (t * P + k >= 0) & (t * P + k < SEQ)
        window[t] = np.where(near & inside, 0.0, NEG)
    i, j = np.arange(P)[:, None], np.arange(P)[None, :]
    same = i // 64 == j // 64
    masks = np.stack([same & (i <= j), same & (i >= j), same, same & (i < j), same & (i > j)]).astype(np.float32)
    levels = np.zeros((6, P, P), np.float32)
    for n in range(6):
        b = 1 << n
        levels[n] = (i // (2 * b) == j // (2 * b)) & ((j // b) % 2 == 1) & ((i // b) % 2 == 0)
    causal = np.where(j <= i, 0.0, NEG).astype(np.float32)
    chunk_of = (np.arange(P)[:, None] // 64 == np.arange(2)[None, :]).astype(np.float32)
    return {"k_rope": rope, "k_window": window, "k_masks": masks, "k_levels": levels, "k_causal": causal,
            "k_chunk_of": chunk_of}


def kernel(**inputs):
    import numpy as np
    import concourse.bacc as bacc
    from concourse.bass_utils import run_bass_kernel_spmd as run

    nc = bacc.Bacc("TRN2", target_bir_lowering=False, num_devices=1)
    arrays, args = {}, {}
    unused = ("rwkv_v0_2", "rwkv_v_down_2", "rwkv_v_up_2")
    for name, value in {**inputs, **shape_constants()}.items():
        if name in unused:
            continue
        v = np.ascontiguousarray(value)
        arrays["in_" + name] = v
        args[name] = nc.dram_tensor("in_" + name, v.shape, mybir.dt.from_np(v.dtype), kind="ExternalInput").ap()
    out = nc.dram_tensor("out_0", (1, SEQ, D), F32, kind="ExternalOutput").ap()

    def scratch(name, shape):
        if DEBUG:
            return nc.dram_tensor("out_" + name, shape, F32, kind="ExternalOutput").ap()
        return nc.dram_tensor(name, shape, F32).ap()

    program(nc, args, out, scratch, STOP)
    r = run(nc, [arrays], core_ids=[0])
    return r.results[0]["out_0"]
```

```python
from contextlib import ExitStack

import concourse.bass as bass
from concourse import mybir

ALU = mybir.AluOpType
ACT = mybir.ActivationFunctionType
F32 = mybir.dt.float32
F32R = mybir.dt.float32r
AX = mybir.AxisListType

P = 128
D = 1024
KD = D // P
SEQ = 1024
CTX = 256
NT = SEQ // P
NC = CTX // P
ALLT = SEQ + CTX
EPS = 1e-6
NEG = -1e30
HD = 64

A_HEADS = 8
B_HEADS = 4
EVEN_IN = 3328
ODD_IN = 3104
LAMBDA_INIT = 0.8 - 0.6

META = 16
T2 = META + SEQ
D_FF = 2816
D_IN2 = 3080
TILES2 = [(0, META)] + [(META + P * t, P) for t in range(NT)]


class Chain:

    def __init__(self, eng, sem, start=0):
        self.eng, self.sem, self.base, self.k = eng, sem, start, 0

    def step(self, ins):
        ins.then_inc(self.sem, 1)
        self.k += 1

    def settle(self):
        self.eng.wait_ge(self.sem, self.base + self.k)

    def link(self, ins):
        self.step(ins)
        self.settle()


class Phase:

    def __init__(self, nc, tag):
        self.nc, self.tag, self.ctx, self.held = nc, tag, ExitStack(), []

    def __enter__(self):
        return self

    def __exit__(self, *what):
        self.ctx.close()
        self.nc.clear_and_free_semaphores(self.held)
        self.nc.all_engine_barrier()

    def sb(self, name, shape, dt=F32):
        return self.ctx.enter_context(self.nc.sbuf_tensor(f"{self.tag}_{name}", shape, dt))

    def pair(self, name, shape):
        return pair(self.nc, self.ctx, f"{self.tag}_{name}", shape)

    def ps(self, name, shape):
        return self.ctx.enter_context(self.nc.psum_tensor(f"{self.tag}_{name}", shape, F32))

    def sem(self, name):
        self.held.append(self.nc.alloc_semaphore(f"{self.tag}_{name}"))
        return self.held[-1]

    def sems(self, names):
        return [self.sem(n) for n in names.split()]


def rows(ap, n=P):
    return ap.partition_broadcast(n)


def pair(nc, ctx, name, shape):
    return [ctx.enter_context(nc.sbuf_tensor(f"{name}_{part}", shape, F32R)) for part in ("hi", "lo")]


def lo_part(eng, lo, x, hi):
    return eng.tensor_tensor(lo, x, hi.bitcast(F32), ALU.subtract)


def product(pe, out, left, right, start, stop):
    pe.matmul(out, left[0], right[0], start=start, stop=False)
    pe.matmul(out, left[0], right[1], start=False, stop=False)
    return pe.matmul(out, left[1], right[0], start=False, stop=stop)


class Weights:

    def __init__(self, ph, kd, blk):
        self.half = kd // 2
        self.raw = [ph.sb(f"raw{h}", [P, self.half, blk]) for h in range(2)]
        self.slots = [ph.pair(f"w{s}", [P, kd, blk]) for s in range(2)]
        self.raw_in = ph.sems("raw_in0 raw_in1")
        self.hi_done = ph.sems("hi_done0 hi_done1")
        self.lo_done = ph.sems("lo_done0 lo_done1")

    def load(self, eng, b, src):
        for h in range(2):
            if not (isinstance(b, int) and b == 0):
                eng.wait_ge(self.lo_done[h], b)
            eng.dma_start(self.raw[h][:, :, :], src(self.half * h, self.half * h + self.half)).then_inc(self.raw_in[h], 16)

    def make_hi(self, eng, b, s):
        for h in range(2):
            eng.wait_ge(self.raw_in[h], b * 16 + 16)
            eng.activation(self.slots[s][0][:, self.half * h:self.half * h + self.half, :], self.raw[h][:, :, :],
                           ACT.Copy).then_inc(self.hi_done[h], 1)

    def make_lo(self, eng, b, s):
        for h in range(2):
            ks = slice(self.half * h, self.half * h + self.half)
            eng.wait_ge(self.hi_done[h], b + 1)
            lo_part(eng, self.slots[s][1][:, ks, :], self.raw[h][:, :, :],
                    self.slots[s][0][:, ks, :]).then_inc(self.lo_done[h], 1)

    def ready(self, pe, b):
        for h in range(2):
            pe.wait_ge(self.lo_done[h], b + 1)

    def cut(self, s, k, c0, c1):
        return [w[:, k, c0:c1] for w in self.slots[s]]


def in_pairs(eng, n, step):
    for s in range(2):
        step(0, s, s == 0, n == 2 and s == 1)
    if n > 4:
        with eng.Fori(1, n // 2 - 1, 1) as i:
            for s in range(2):
                step(i, s, False, False)
    if n > 2:
        for s in range(2):
            step(n // 2 - 1, s, False, s == 1)


def in_turn(eng, parts, ahead, behind):
    at, last = 0, None
    for part in parts:
        count = part[0]
        for t in range(min(count, 2)):
            now = (at + t, (at + t) % 2, part, t)
            ahead(*now)
            if last:
                behind(*last)
            last = now
        if count > 2:
            with eng.Fori(1, count // 2, 1) as i:
                for s in range(2):
                    t = i * 2 + s
                    ahead(t + at, (at + s) % 2, part, t)
                    behind(t + (at - 1), (at + s + 1) % 2, part, t - 1)
            last = (at + count - 1, (at + count - 1) % 2, part, count - 1)
        at += count
    behind(*last)


def modulation(nc, a, g):
    BLK = 512
    NB = 6 * D // BLK
    RING = 4
    w_v = a["adaln_w"].rearrange("l (k p) (b n) -> p k l b n", p=P, n=BLK)
    with Phase(nc, "mod") as ph:
        w = [ph.sb(f"w{s}", [P, KD, BLK]) for s in range(RING)]
        cond = ph.sb("cond", [P, 2, KD])
        act_c = ph.sb("act_c", [P, KD, 2])
        bias = ph.sb("bias", [2, 2, 3, D])
        gain = ph.sb("gain", [2, 2, D])
        mod = ph.sb("mod", [2, 2, 3, D])
        lam = ph.sb("lam", [P, 4, HD])
        lprod = ph.sb("lprod", [P, 2, HD])
        lsum = ph.sb("lsum", [P, 2])
        lexp = ph.sb("lexp", [P, 2])
        pm = [ph.ps(f"pm{s}", [P, BLK]) for s in range(RING)]
        small, zeroed, silu_ready, made, added, mod_ready, g_out, lam_p, lam_e, dstep = ph.sems(
            "small zeroed silu_ready made added mod_ready g_out lam_p lam_e dstep")
        w_in = ph.sems("w_in0 w_in1 w_in2 w_in3")
        with nc.Block() as block:
            def load(eng, mine):
                for b in range(NB):
                    if b % 2 == mine:
                        if b >= RING:
                            eng.wait_ge(made, b - RING + 1)
                        eng.dma_start(w[b % RING][:, :, :], w_v[:, :, b // 6, b % 6, :]).then_inc(w_in[b % RING], 16)

            @block.sync
            def _(sp):
                with nc.allow_non_contiguous_dma(reason="short vectors, feature-major"):
                    sp.dma_start(cond[:, 0, :], a["c"].rearrange("o (k p) -> p (o k)", p=P)).then_inc(small, 16)
                    sp.dma_start(cond[:, 1, :], a["c_ctx"].rearrange("(k p) -> p k", p=P)).then_inc(small, 16)
                sp.dma_start(bias[:, :, :, :].rearrange("c l j d -> c (l j d)"),
                             a["adaln_b"].rearrange("l n -> (l n)").partition_broadcast(2)).then_inc(small, 16)
                sp.dma_start(gain[:, :, :].rearrange("c l d -> c (l d)"),
                             a["norm_g"].rearrange("l d -> (l d)").partition_broadcast(2)).then_inc(small, 16)
                for j, name in enumerate(("b_lambda_q1", "b_lambda_k1", "b_lambda_q2", "b_lambda_k2")):
                    sp.dma_start(lam[:, j, :], rows(a[name][0, :])).then_inc(small, 16)
                load(sp, 0)
                sp.wait_ge(mod_ready, 1)
                sp.dma_start(g.mod_dram.rearrange("c l j d -> c (l j d)"),
                             mod[:, :, :, :].rearrange("c l j d -> c (l j d)")).then_inc(g_out, 16)
                sp.wait_ge(g_out, 16)

            @block.gpsimd
            def _(pool):
                pool.memset(g.ident[:, :], 0.0).then_inc(zeroed, 1)
                pool.wait_ge(zeroed, 1)
                pool.affine_select(out=g.ident[:, :], in_=g.ident[:, :], compare_op=ALU.not_equal, fill=1.0, base=0,
                                   pattern=[[-1, P]], channel_multiplier=1)

            @block.scalar
            def _(act):
                act.wait_ge(small, 16 * 8)
                act.activation(act_c[:, :, :].rearrange("p k c -> p c k"), cond[:, :, :], ACT.Silu).then_inc(silu_ready, 1)
                load(act, 1)
                act.wait_ge(lam_p, 1)
                act.activation(lexp[:, :], lsum[:, :], ACT.Exp).then_inc(lam_e, 1)

            @block.vector
            def _(dve):
                ch = Chain(dve, dstep)
                ch.link(dve.memset(g.epsc[:, :], EPS))
                dve.wait_ge(small, 16 * 8)
                ch.step(dve.tensor_tensor(lprod[:, 0, :], lam[:, 0, :], lam[:, 1, :], ALU.mult))
                ch.link(dve.tensor_tensor(lprod[:, 1, :], lam[:, 2, :], lam[:, 3, :], ALU.mult))
                dve.tensor_reduce(lsum[:, :], lprod[:, :, :], AX.X, ALU.add).then_inc(lam_p, 1)
                flat = [t[:, :, :, :].rearrange("c l j d -> c (l j d)") for t in (mod, bias)]
                for b in range(NB):
                    cols = slice(b * BLK, b * BLK + BLK)
                    dve.wait_ge(made, b + 1)
                    dve.tensor_tensor(flat[0][:, cols], pm[b % RING][0:2, :], flat[1][:, cols], ALU.add).then_inc(added, 1)
                dve.wait_ge(added, NB)
                dve.scalar_tensor_tensor(mod[:, :, 1, :], mod[:, :, 1, :], 1.0, gain[:, :, :], ALU.add, ALU.mult).then_inc(mod_ready, 1)
                dve.wait_ge(lam_e, 1)
                ch.link(dve.tensor_tensor(g.neglam[:, :], lexp[:, 1:2], lexp[:, 0:1], ALU.subtract))
                ch.step(dve.tensor_scalar(g.neglam[:, :], g.neglam[:, :], -LAMBDA_INIT, None, ALU.add))

            @block.tensor
            def _(pe):
                pe.wait_ge(silu_ready, 1)
                for b in range(NB):
                    pe.wait_ge(w_in[b % RING], (b // RING) * 16 + 16)
                    if b >= RING:
                        pe.wait_ge(added, b - RING + 1)
                    for k in range(KD):
                        mm = pe.matmul(pm[b % RING][0:2, :], act_c[:, k, :], w[b % RING][:, k, :],
                                       start=(k == 0), stop=(k == KD - 1))
                    mm.then_inc(made, 1)


def norm_turn(nc, g, tag, hT, parts, load=(), spill=None):
    with Phase(nc, tag) as ph:
        affine = {}
        for part in parts:
            if part[6] not in affine:
                affine[part[6]] = [(ph.sb(f"{name}{part[6]}", [P, D]), src)
                                   for name, src in zip(("gain", "shift"), part[4:6]) if src is not None]
        fetched = [(dst[:, :], rows(src)) for both in affine.values() for dst, src in both]
        shifted = parts[0][5] is not None
        sq = ph.sb("sq", [P, D])
        xn = [ph.sb(f"xn{s}", [P, D]) for s in range(2)]
        ss = ph.sb("ss", [P, 2])
        rs = ph.sb("rs", [P, 2])
        pt = [ph.ps(f"pt{s}", [P, KD, P]) for s in range(2)]
        loaded, squared, rooted, recip, normed, scaled, turned, hi_done, lo_done, spilled = ph.sems(
            "loaded squared rooted recip normed scaled turned hi_done lo_done spilled")
        if not shifted:
            scaled = normed
        with nc.Block() as block:
            n_load = 16 * (len(load) + len(fetched))

            @block.sync
            def _(sp):
                for dst, src in list(load) + fetched:
                    sp.dma_start(dst, src).then_inc(loaded, 16)
                if spill:
                    sp.dma_start(spill[0], spill[1]).then_inc(spilled, 16)
                    sp.wait_ge(spilled, 16)

            @block.scalar
            def _(act):
                act.wait_ge(loaded, n_load)

                def root(n, s, part, t):
                    x, r = part[1], part[2]
                    act.activation(sq[0:r, :], x[0:r, t, :], ACT.Square, accum_out=ss[0:r, s:s + 1]).then_inc(squared, 1)
                    act.wait_ge(squared, n + 1)
                    act.activation(ss[0:r, s:s + 1], ss[0:r, s:s + 1], ACT.Sqrt, scale=1.0 / D, bias=g.epsc[0:r, :]).then_inc(rooted, 1)

                def high(n, s, part, t):
                    r, c0 = part[2], part[3]
                    act.wait_ge(turned, n + 1)
                    act.activation(hT[0][:, :, bass.ds(c0 + t * P, r)], pt[s][:, :, 0:r], ACT.Copy).then_inc(hi_done, 1)
                in_turn(act, parts, root, high)

            @block.vector
            def _(dve):
                dve.wait_ge(loaded, n_load)

                def norm(n, s, part, t):
                    x, r = part[1], part[2]
                    dve.wait_ge(rooted, n + 1)
                    dve.reciprocal(rs[0:r, s:s + 1], ss[0:r, s:s + 1]).then_inc(recip, 1)
                    dve.wait_ge(recip, n + 1)
                    dve.scalar_tensor_tensor(xn[s][0:r, :], x[0:r, t, :], rs[0:r, s:s + 1], affine[part[6]][0][0][0:r, :],
                                             ALU.mult, ALU.mult).then_inc(normed, 1)

                def low(n, s, part, t):
                    r, c0 = part[2], part[3]
                    dve.wait_ge(hi_done, n + 1)
                    cols = bass.ds(c0 + t * P, r)
                    lo_part(dve, hT[1][:, :, cols], pt[s][:, :, 0:r], hT[0][:, :, cols]).then_inc(lo_done, 1)
                in_turn(dve, parts, norm, low)

            @block.gpsimd
            def _(pool):
                if not shifted:
                    return
                pool.wait_ge(loaded, n_load)

                def shift(n, s, part, t):
                    r = part[2]
                    pool.wait_ge(normed, n + 1)
                    pool.tensor_tensor(xn[s][0:r, :], xn[s][0:r, :], affine[part[6]][1][0][0:r, :], ALU.add).then_inc(scaled, 1)
                in_turn(pool, parts, shift, lambda *tile: None)

            @block.tensor
            def _(pe):
                def turn(n, s, part, t):
                    r = part[2]
                    pe.wait_ge(scaled, n + 1)
                    if not (isinstance(n, int) and n < 2):
                        pe.wait_ge(lo_done, n - 1)
                    for k in range(KD):
                        mm = pe.transpose(pt[s][:, k, 0:r], xn[s][0:r, P * k:P * k + P], g.ident[0:r, 0:r])
                    mm.then_inc(turned, 1)
                in_turn(pe, parts, turn, lambda *tile: None)


def project_rows(nc, hT, tag, tiles, w_dram, blk, nblk, dst):
    NBANK = 4
    n = len(tiles)
    w_v = w_dram.rearrange("(k p) (b n) -> p k b n", p=P, n=blk)
    with Phase(nc, tag) as ph:
        w = Weights(ph, KD, blk)
        o = [ph.sb(f"o{s}", [P, blk]) for s in range(NBANK)]
        pb = [ph.ps(f"pb{s}", [P, 512]) for s in range(NBANK)]
        made = ph.sems("made0 made1 made2 made3")
        copied = ph.sems("copied0 copied1 copied2 copied3")
        stored = ph.sems("stored0 stored1 stored2 stored3")
        slots = [(s, t) for s in range(2) for t in range(n)]
        per = [sum(1 for q in range(2 * n) if q % NBANK == b) for b in range(NBANK)]
        with nc.Block() as block:
            @block.gpsimd
            def _(pool):
                def load(b):
                    w.load(pool, b, lambda k0, k1: w_v[:, k0:k1, b, :])
                load(0)
                with pool.Fori(1, nblk, 1) as b:
                    load(b)

            @block.sync
            def _(sp):
                for b in range(NBANK):
                    sp.sem_inc(stored[b], 16)
                with sp.Fori(0, nblk // 2, 1) as i:
                    for q, (s, t) in enumerate(slots):
                        b = q % NBANK
                        c0, r = tiles[t]
                        sp.wait_ge(copied[b], i * per[b] + q // NBANK + 1)
                        sp.dma_start(dst[c0:c0 + r, bass.ds((i * 2 + s) * blk, blk)], o[b][0:r, :]).then_inc(stored[b], 16)
                for b in range(NBANK):
                    sp.wait_ge(stored[b], 16 + 16 * per[b] * (nblk // 2))

            def copies(eng, mine, i, s):
                for q in range(s * n, s * n + n):
                    b = q % NBANK
                    if b % 2 != mine:
                        continue
                    r = tiles[q - s * n][1]
                    eng.wait_ge(made[b], i * per[b] + q // NBANK + 1)
                    eng.wait_ge(stored[b], (i * per[b] + q // NBANK) * 16 + 16)
                    if mine:
                        eng.tensor_copy(o[b][0:r, :], pb[b][0:r, 0:blk]).then_inc(copied[b], 1)
                    else:
                        eng.activation(o[b][0:r, :], pb[b][0:r, 0:blk], ACT.Copy).then_inc(copied[b], 1)

            def slot_free(eng, i, s, first):
                if not first:
                    q = (s * n - 1) % (2 * n)
                    eng.wait_ge(made[q % NBANK], (i if s else i - 1) * per[q % NBANK] + q // NBANK + 1)

            @block.scalar
            def _(act):
                w.make_hi(act, 0, 0)

                def step(i, s, first, last):
                    if not last:
                        slot_free(act, i, s, first)
                        w.make_hi(act, i * 2 + s + 1, 1 - s)
                    copies(act, 0, i, s)
                in_pairs(act, nblk, step)

            @block.vector
            def _(dve):
                w.make_lo(dve, 0, 0)

                def step(i, s, first, last):
                    if not last:
                        w.make_lo(dve, i * 2 + s + 1, 1 - s)
                    copies(dve, 1, i, s)
                in_pairs(dve, nblk, step)

            @block.tensor
            def _(pe):
                with pe.Fori(0, nblk // 2, 1) as i:
                    for q, (s, t) in enumerate(slots):
                        b = q % NBANK
                        c0, r = tiles[t]
                        if t == 0:
                            w.ready(pe, i * 2 + s)
                        if q >= NBANK:
                            pe.wait_ge(copied[b], i * per[b] + q // NBANK)
                        else:
                            pe.wait_ge(stored[b], (i * per[b]) * 16 + 16)
                        for k in range(KD):
                            mm = product(pe, pb[b][0:r, 0:blk], [h[:, k, c0:c0 + r] for h in hT], w.cut(s, k, 0, blk),
                                         k == 0, k == KD - 1)
                        mm.then_inc(made[b], 1)


QK_HEADS = 26
V_B = 2304


def rotate_heads(nc, a, g, p0, KB, KA, va, vb):
    n_all = NT + NC
    with Phase(nc, "rot") as ph:
        rope = ph.sb("rope", [P, 2, n_all, HD])
        gain = ph.sb("gain", [P, 4, HD])
        qk = [ph.sb(f"qk{s}", [P, QK_HEADS, HD]) for s in range(2)]
        tmp = ph.sb("tmp", [P, QK_HEADS, HD])
        rot = ph.sb("rotated", [P, 28, HD])
        ss = ph.sb("ss", [P, QK_HEADS])
        rt = ph.sb("rt", [P, QK_HEADS])
        pt = ph.ps("pt", [P, 16, P])
        small, in0, in1, squared, summed, rooted, plain, rotated, turned, evac_a, evac_d, dstep, padded = ph.sems(
            "small in0 in1 squared summed rooted plain rotated turned evac_a evac_d dstep padded")
        qk_in = [in0, in1]
        spans = ((0, 8), (8, 10), (10, 18), (18, 26))
        with nc.Block() as block:
            @block.sync
            def _(sp):
                def load(s, i):
                    src = p0[bass.ds(i * P, P), :]
                    sp.dma_start(qk[s][:, 0:10, :], src[:, 0:640]).then_inc(qk_in[s], 16)
                    sp.dma_start(qk[s][:, 10:26, :], src[:, 1280:2304]).then_inc(qk_in[s], 16)

                for s in range(2):
                    load(s, s)
                sp.dma_start(rope[:, :, :, :], a["k_rope"].rearrange("c (t p) d -> p c t d", p=P)).then_inc(small, 16)
                for j, name in enumerate(("a_q_norm", "a_k_norm", "b_q_norm", "b_k_norm")):
                    sp.dma_start(gain[:, j, :], rows(a[name][0, :])).then_inc(small, 16)
                sp.dma_start(va[:, 1:, :], p0[:, 640:768].rearrange("(t p) d -> p t d", p=P)).then_inc(small, 16)
                sp.dma_start(vb[:, :, :], p0[:, V_B:V_B + 512].rearrange("(t p) d -> p t d", p=P)).then_inc(small, 16)
                with sp.Fori(1, n_all // 2, 1) as i:
                    for s in range(2):
                        sp.wait_ge(plain, i * 2 + s - 1)
                        load(s, i * 2 + s)
                sp.wait_ge(small, 16 * 7)

            @block.gpsimd
            def _(pool):
                pool.memset(va[:, 0, :], 0.0).then_inc(padded, 1)
                pool.memset(KA[:, :, 0:P], 0.0).then_inc(padded, 1)
                pool.wait_ge(padded, 2)

            @block.scalar
            def _(act):
                with act.Fori(0, n_all // 2, 1) as i:
                    for s in range(2):
                        n = i * 2 + s
                        act.wait_ge(qk_in[s], i * 32 + 32)
                        act.activation(tmp[:, :, :], qk[s][:, :, :], ACT.Square).then_inc(squared, 1)
                        act.wait_ge(summed, n + 1)
                        act.activation(rt[:, :], ss[:, :], ACT.Sqrt, scale=1.0 / HD, bias=g.epsc[:, :]).then_inc(rooted, 1)
                        act.wait_ge(turned, n + 1)
                        act.activation(g.hT[:, 0:4, bass.ds(n * P, P)], pt[:, 0:4, :], ACT.Copy)
                        act.activation(g.hT[:, 4:8, bass.ds(n * P, P)], pt[:, 4:8, :], ACT.Copy).then_inc(evac_a, 1)
                        act.wait_ge(evac_d, n + 1)

            @block.vector
            def _(dve):
                dve.wait_ge(small, 16 * 7)
                per = 5
                with dve.Fori(0, n_all // 2, 1) as i:
                    for s in range(2):
                        n = i * 2 + s
                        ch = Chain(dve, dstep, n * per)
                        dve.wait_ge(squared, n + 1)
                        dve.tensor_reduce(ss[:, :], tmp[:, :, :], AX.X, ALU.add).then_inc(summed, 1)
                        dve.wait_ge(rooted, n + 1)
                        ch.link(dve.reciprocal(rt[:, :], rt[:, :]))
                        ch.link(dve.tensor_tensor(qk[s][:, :, :], qk[s][:, :, :],
                                                  rt[:, :].unsqueeze(2).broadcast_to([P, QK_HEADS, HD]), ALU.mult))
                        for j, (h0, h1) in enumerate(spans):
                            ins = dve.tensor_tensor(qk[s][:, h0:h1, :], qk[s][:, h0:h1, :],
                                                    gain[:, j:j + 1, :].broadcast_to([P, h1 - h0, HD]), ALU.mult)
                        ch.link(ins)
                        pairs = qk[s][:, :, :].rearrange("p h (x y m) -> p h x y m", x=2, y=2)
                        out = tmp[:, :, :].rearrange("p h (x y m) -> p h x y m", x=2, y=2)
                        sin = rope[:, 1, n, :].rearrange("p (x y m) -> p x y m", x=2, y=2)
                        for y in range(2):
                            ins = dve.tensor_tensor(out[:, :, :, y, :], pairs[:, :, :, 1 - y, :],
                                                    sin[:, :, y, :].unsqueeze(1).broadcast_to([P, QK_HEADS, 2, 16]), ALU.mult)
                        ch.link(ins)
                        cos = rope[:, 0, n, :].unsqueeze(1).broadcast_to([P, QK_HEADS, HD])
                        ch.link(dve.tensor_tensor(qk[s][:, :, :], qk[s][:, :, :], cos, ALU.mult))
                        assert ch.k == per
                        dve.tensor_tensor(rot[:, 0:8, :], qk[s][:, 0:8, :], tmp[:, 0:8, :], ALU.add)
                        for half in range(2):
                            dve.tensor_tensor(rot[:, 8:12, :].rearrange("p (k r) d -> p k r d", r=2)[:, :, half, :],
                                              qk[s][:, 8:10, :], tmp[:, 8:10, :], ALU.add)
                        dve.tensor_tensor(rot[:, 12:28, :], qk[s][:, 10:26, :], tmp[:, 10:26, :], ALU.add).then_inc(rotated, 1)
                        dve.wait_ge(rotated, n + 1)
                        dve.sem_inc(plain, 1)
                        dve.wait_ge(turned, n + 1)
                        dve.tensor_copy(KA[:, :, bass.ds(n * P + P, P)], pt[:, 8:10, :])
                        dve.tensor_copy(KB[:, :, bass.ds(n * P, P)], pt[:, 12:16, :]).then_inc(evac_d, 1)

            @block.tensor
            def _(pe):
                with pe.Fori(0, n_all // 2, 1) as i:
                    for s in range(2):
                        n = i * 2 + s
                        pe.wait_ge(rotated, n + 1)
                        pe.wait_ge(rooted, n + 1)
                        for c, at in enumerate((0, 1, 2, 3, 8, 9, 4, 5, 6, 7, 12, 13, 14, 15)):
                            mm = pe.transpose(pt[:, at, :], rot[:, 2 * c:2 * c + 2, :].rearrange("p h d -> p (h d)"), g.ident[:, :])
                        mm.then_inc(turned, 1)


SCALE = HD ** -0.5


def window_attention(nc, a, g, KA, va, o_dram):
    NP = A_HEADS // 2
    NS = 2 * NP
    W3 = 3 * P
    with Phase(nc, "wa") as ph:
        mask = ph.sb("mask", [P, NT, W3])
        sink = ph.sb("sink", [P, A_HEADS])
        qc = [ph.sb(f"qc{s}", [P, NP, P]) for s in range(2)]
        kw = [ph.sb(f"kw{s}", [P, 2, W3]) for s in range(2)]
        S = [ph.sb(f"S{e}", [P, W3 + CTX]) for e in range(2)]
        E = [ph.sb(f"E{e}", [P, W3 + CTX]) for e in range(2)]
        ET = [ph.sb(f"ET{e}", [P, 5, P]) for e in range(2)]
        mx = ph.sb("mx", [P, 2])
        nm = ph.sb("nm", [P, 2])
        l = ph.sb("l", [P, 2])
        es = ph.sb("es", [P, 2])
        r = ph.sb("r", [P, 2])
        oa = [ph.sb(f"oa{s}", [P, A_HEADS, HD]) for s in range(2)]
        pS = [ph.ps(f"pS{e}", [P, 1024]) for e in range(2)]
        pw = [pS[e][:, 0:W3] for e in range(2)]
        pc = [pS[e][:, 512:512 + CTX] for e in range(2)]
        pT = [ph.ps(f"pT{e}", [P, 1024]) for e in range(2)]
        po = [pT[e][:, 5 * P:5 * P + NP * HD].rearrange("p (n d) -> p n d", d=HD) for e in range(2)]
        small, window, scores, s_ctx, negmax, expd, summed, turned, et0, et1, pv, o_done, st0, st1, dstep = ph.sems(
            "small window scores s_ctx negmax expd summed turned et0 et1 pv o_done st0 st1 dstep")
        et, stored = [et0, et1], [st0, st1]
        with nc.Block() as block:
            def loops(eng, body):
                with eng.Fori(0, NT // 2, 1) as i:
                    body(i * 2, i, True)
                body(NT, NT // 2, False)

            @block.sync
            def _(sp):
                sp.dma_start(mask[:, :, :], a["k_window"].rearrange("t p k -> p t k")).then_inc(small, 16)
                sp.dma_start(sink[:, :], rows(a["a_sink"][0, :])).then_inc(small, 16)
                for s in range(2):
                    sp.sem_inc(stored[s], 16)

                def body(t, i, win):
                    for s in range(2):
                        sp.wait_ge(o_done, i * NS + NP * (s + 1))
                        sp.dma_start(o_dram[bass.ds((t + s) * P, P), 0:512], oa[s][:, :, :]).then_inc(stored[s], 16)
                loops(sp, body)
                for s in range(2):
                    sp.wait_ge(stored[s], 16 + 16 * (NT + NC) // 2)

            @block.gpsimd
            def _(pool):
                pool.sem_inc(scores, NS)

                def body(t, i, win):
                    for s in range(2):
                        pool.wait_ge(scores, i * NS + NP * (s + 1))
                        pool.tensor_copy(qc[s][:, :, :], g.hT[:, 0:NP, bass.ds((t + s) * P, P)])
                        if win:
                            ins = pool.tensor_copy(kw[s][:, :, :], KA[:, :, bass.ds((t + s) * P, W3)])
                        else:
                            ins = pool.tensor_copy(kw[s][:, :, 0:P], KA[:, :, 0:P])
                        ins.then_inc(window, 1)
                loops(pool, body)

            @block.scalar
            def _(act):
                act.wait_ge(small, 32)

                def body(t, i, win):
                    w0 = 0 if win else W3

                    def context_scores(n):
                        act.wait_ge(scores, i * NS + NS + n + 1)
                        if n:
                            act.wait_ge(expd, i * NS + n)
                        for e in range(2):
                            ins = act.activation(S[e][:, W3:], pc[e], ACT.Copy, scale=SCALE)
                        ins.then_inc(s_ctx, 1)

                    def exps(n):
                        act.wait_ge(negmax, i * NS + n + 1)
                        for e in range(2):
                            act.activation(E[e][:, w0:], S[e][:, w0:], ACT.Exp, bias=nm[:, e:e + 1], accum_out=l[:, e:e + 1])
                            ins = act.activation(es[:, e:e + 1], sink[:, 2 * (n % NP) + e:2 * (n % NP) + e + 1], ACT.Exp, bias=nm[:, e:e + 1])
                        ins.then_inc(expd, 1)

                    context_scores(0)
                    exps(0)
                    for n in range(NS):
                        if n + 1 < NS:
                            context_scores(n + 1)
                        act.wait_ge(turned, i * NS + n + 1)
                        k0 = 0 if win else 3
                        act.activation(ET[1][:, k0:5, :], pT[1][:, P * k0:5 * P], ACT.Copy).then_inc(et[1], 1)
                        if n + 1 < NS:
                            act.wait_ge(summed, i * NS + n + 1)
                            exps(n + 1)
                loops(act, body)

            @block.vector
            def _(dve):
                dve.wait_ge(small, 32)
                per = 3 * NS

                def body(t, i, win):
                    w0 = 0 if win else W3
                    ch = Chain(dve, dstep, i * per)

                    def window_scores(n):
                        dve.wait_ge(scores, i * NS + NS + n + 1)
                        if win:
                            for e in range(2):
                                ins = dve.scalar_tensor_tensor(S[e][:, 0:W3], pw[e], SCALE, mask[:, t + n // NP, :], ALU.mult, ALU.add)
                            ch.link(ins)
                        else:
                            ch.link(dve.memset(mx[:, :], 0.0))

                    def maxima(n):
                        dve.wait_ge(s_ctx, i * NS + n + 1)
                        for e in range(2):
                            ins = dve.tensor_reduce(mx[:, e:e + 1], S[e][:, w0:], AX.X, ALU.max)
                        ch.link(ins)
                        for e in range(2):
                            ins = dve.tensor_scalar(nm[:, e:e + 1], mx[:, e:e + 1], sink[:, 2 * (n % NP) + e:2 * (n % NP) + e + 1], -1.0, ALU.max, ALU.mult)
                        ins.then_inc(negmax, 1)

                    window_scores(0)
                    maxima(0)
                    for n in range(NS):
                        m = i * NS + n
                        dve.wait_ge(expd, m + 1)
                        ch.link(dve.tensor_tensor(l[:, :], l[:, :], es[:, :], ALU.add))
                        dve.reciprocal(r[:, :], l[:, :]).then_inc(summed, 1)
                        if n + 1 < NS:
                            window_scores(n + 1)
                        dve.wait_ge(turned, m + 1)
                        k0 = 0 if win else 3
                        dve.tensor_copy(ET[0][:, k0:5, :], pT[0][:, P * k0:5 * P]).then_inc(et[0], 1)
                        if n + 1 < NS:
                            maxima(n + 1)
                        dve.wait_ge(summed, m + 1)
                        dve.wait_ge(pv, m + 1)
                        if n % NP == 0:
                            dve.wait_ge(stored[n // NP], i * 16 + 16)
                        for e in range(2):
                            h = 2 * (n % NP) + e
                            ins = dve.tensor_scalar(oa[n // NP][:, h, :], po[e][:, n % NP, :], r[:, e:e + 1], None, ALU.mult)
                        ins.then_inc(o_done, 1)
                    assert ch.k == per
                loops(dve, body)

            @block.tensor
            def _(pe):
                def body(t, i, win):
                    k0 = 0 if win else 3

                    def scores_of(n):
                        kv = n % NP // 2
                        if n % NP == 0:
                            pe.wait_ge(window, t + n // NP + 1)
                        if n:
                            pe.wait_ge(negmax, i * NS + n)
                        for e in range(2):
                            half = slice(64 * e, 64 * e + 64)
                            if win:
                                pe.matmul(pw[e], qc[n // NP][half, n % NP, :], kw[n // NP][half, kv, :], start=True, stop=True)
                            mm = pe.matmul(pc[e], qc[n // NP][half, n % NP, :], KA[half, kv, P + SEQ:P + ALLT], start=True, stop=True)
                        mm.then_inc(scores, 1)

                    scores_of(0)
                    for n in range(NS):
                        m = i * NS + n
                        kv = n % NP // 2
                        if n + 1 < NS:
                            scores_of(n + 1)
                        pe.wait_ge(expd, m + 1)
                        if n:
                            pe.wait_ge(o_done, m)
                        for e in range(2):
                            for k in range(k0, 5):
                                mm = pe.transpose(pT[e][:, P * k:P * k + P], E[e][:, P * k:P * k + P], g.ident[:, :])
                        mm.then_inc(turned, 1)
                        for e in range(2):
                            pe.wait_ge(et[e], m + 1)
                            for k in range(k0, 5):
                                v = va[:, bass.ds(t + n // NP + k, 1), :] if k < 3 else va[:, NT + 1 + k - 3:NT + 2 + k - 3, :]
                                mm = pe.matmul(po[e][:, n % NP, :], ET[e][:, k, :], v[:, 0, HD * kv:HD * kv + HD], start=(k == k0), stop=(k == 4))
                        mm.then_inc(pv, 1)
                loops(pe, body)


def differential_attention(nc, a, g, KB, vb, o_dram):
    with Phase(nc, "da") as ph:
        qc = [ph.sb(f"qc{s}", [P, B_HEADS, P]) for s in range(2)]
        E = [ph.sb(f"E{m}", [P, ALLT]) for m in range(2)]
        ET = ph.sb("ET", [P, 10, P])
        mx = ph.sb("mx", [P, 2])
        nm = ph.sb("nm", [P, 2])
        l = ph.sb("l", [P, 2])
        r = ph.sb("r", [P, 2])
        ob = [ph.sb(f"ob{s}", [P, B_HEADS, P]) for s in range(2)]
        pS = [ph.ps(f"pS{m}", [P, 1536]) for m in range(2)]
        pT = ph.ps("pT", [P, 4, P])
        po = ph.ps("po", [P, B_HEADS, P])
        qcopied, sc0, sc1, top0, top1, neg0, neg1, ex0, ex1, weights, turned, evac, pv, o_done, st0, st1, dstep = ph.sems(
            "qcopied sc0 sc1 top0 top1 neg0 neg1 ex0 ex1 weights turned evac pv o_done st0 st1 dstep")
        stored = [st0, st1]
        sc, top, neg, ex = [sc0, sc1], [top0, top1], [neg0, neg1], [ex0, ex1]
        H = B_HEADS
        NS = 2 * H

        def groups(full):
            return [(0, 4), (4, 8), (8, 10)] if full else [(8, 10)]

        def group_count(i, n, full):
            return (i * NS + n) * 3 if full else NT * H * 3 + n

        with nc.Block() as block:
            def loops(eng, body):
                with eng.Fori(0, NT // 2, 1) as i:
                    body(i * 2, i, True)
                body(NT, NT // 2, False)

            @block.sync
            def _(sp):
                for s in range(2):
                    sp.sem_inc(stored[s], 16)

                def body(t, i, full):
                    for s in range(2):
                        sp.wait_ge(o_done, i * NS + H * (s + 1))
                        sp.dma_start(o_dram[bass.ds((t + s) * P, P), 512:1024], ob[s][:, :, :]).then_inc(stored[s], 16)
                loops(sp, body)
                for s in range(2):
                    sp.wait_ge(stored[s], 16 + 16 * (NT + NC) // 2)

            @block.gpsimd
            def _(pool):
                pool.sem_inc(sc[1], NS)

                def body(t, i, full):
                    for s in range(2):
                        pool.wait_ge(sc[1], i * NS + H * (s + 1))
                        pool.tensor_copy(qc[s][:, :, :], g.hT[:, 4:8, bass.ds((t + s) * P, P)]).then_inc(qcopied, 1)
                loops(pool, body)

            @block.scalar
            def _(act):
                def body(t, i, full):
                    k0 = 0 if full else SEQ

                    def exps(h):
                        for m in range(2):
                            act.wait_ge(neg[m], i * NS + h + 1)
                            act.activation(E[m][:, k0:], pS[m][:, k0:ALLT], ACT.Exp, scale=SCALE,
                                           bias=nm[:, m:m + 1], accum_out=l[:, m:m + 1]).then_inc(ex[m], 1)

                    exps(0)
                    for h in range(NS):
                        for j, (a0, a1) in enumerate(groups(full)):
                            act.wait_ge(turned, group_count(i, h, full) + j + 1)
                            act.activation(ET[:, a0:a1, :], pT[:, 0:a1 - a0, :], ACT.Copy).then_inc(evac, 1)
                        if h + 1 < NS:
                            exps(h + 1)
                loops(act, body)

            @block.vector
            def _(dve):
                per = 2 * NS

                def body(t, i, full):
                    k0 = 0 if full else SEQ
                    ch = Chain(dve, dstep, i * per)

                    def maxima(h):
                        n = i * NS + h
                        for m in range(2):
                            dve.wait_ge(sc[m], n + 1 + NS * m)
                            dve.tensor_reduce(mx[:, m:m + 1], pS[m][:, k0:ALLT], AX.X, ALU.max).then_inc(top[m], 1)
                            dve.wait_ge(top[m], n + 1)
                            dve.tensor_scalar(nm[:, m:m + 1], mx[:, m:m + 1], -SCALE, None, ALU.mult).then_inc(neg[m], 1)

                    maxima(0)
                    for h in range(NS):
                        n = i * NS + h
                        for m in range(2):
                            dve.wait_ge(ex[m], n + 1)
                        ch.link(dve.reciprocal(r[:, :], l[:, :]))
                        dve.tensor_tensor(r[:, 1:2], r[:, 1:2], g.neglam[:, :], ALU.mult)
                        ch.link(dve.tensor_scalar(E[0][:, k0:], E[0][:, k0:], r[:, 0:1], None, ALU.mult))
                        dve.scalar_tensor_tensor(E[0][:, k0:], E[1][:, k0:], r[:, 1:2], E[0][:, k0:], ALU.mult, ALU.add).then_inc(weights, 1)
                        if h + 1 < NS:
                            dve.wait_ge(weights, n + 1)
                            maxima(h + 1)
                        dve.wait_ge(pv, n + 1)
                        if h % H == 0:
                            dve.wait_ge(stored[h // H], i * 16 + 16)
                        dve.tensor_copy(ob[h // H][:, h % H, :], po[:, h % H, :]).then_inc(o_done, 1)
                    assert ch.k == per
                loops(dve, body)

            @block.tensor
            def _(pe):
                def body(t, i, full):
                    def scores(h):
                        if h % H == 0:
                            pe.wait_ge(qcopied, t + h // H + 1)
                        for m in range(2):
                            half = slice(64 * m, 64 * m + 64)
                            if h:
                                pe.wait_ge(ex[m], i * NS + h)
                            for c0, c1 in [(0, 512), (512, 1024), (1024, 1280)] if full else [(SEQ, ALLT)]:
                                mm = pe.matmul(pS[m][:, c0:c1], qc[h // H][half, h % H, :], KB[half, h % H, c0:c1], start=True, stop=True)
                            mm.then_inc(sc[m], 1)

                    scores(0)
                    for h in range(NS):
                        n = i * NS + h
                        if h + 1 < NS:
                            scores(h + 1)
                        pe.wait_ge(weights, n + 1)
                        gs = groups(full)

                        def values(j):
                            for k in range(*gs[j]):
                                hh = h % H
                                mm = pe.matmul(po[:, hh, :], ET[:, k, :], vb[:, k, P * hh:P * hh + P], start=(k == gs[0][0]), stop=(k == 9))
                            return mm

                        for j, (a0, a1) in enumerate(gs):
                            for k in range(a0, a1):
                                mm = pe.transpose(pT[:, k - a0, :], E[0][:, P * k:P * k + P], g.ident[:, :])
                            mm.then_inc(turned, 1)
                            if j:
                                values(j - 1)
                            pe.wait_ge(evac, group_count(i, h, full) + j + 1)
                        values(len(gs) - 1).then_inc(pv, 1)
                loops(pe, body)


def merge_even(nc, a, g, hT, p0, o_dram):
    n_all = NT + NC
    parts = [(n_all,)]
    with Phase(nc, "me") as ph:
        o = [ph.sb(f"o{s}", [P, 8, P]) for s in range(2)]
        gt = [ph.sb(f"gt{s}", [P, 8, P]) for s in range(2)]
        sub = ph.sb("sub", [P, P])
        sq = ph.sb("sq", [P, B_HEADS, P])
        ss = ph.sb("ss", [P, 2, B_HEADS])
        pt = [ph.ps(f"pt{s}", [P, KD, P]) for s in range(2)]
        small, in0, in1, squared, summed, rooted, normed, gated, merged, turned, hi_done, lo_done, dstep = ph.sems(
            "small in0 in1 squared summed rooted normed gated merged turned hi_done lo_done dstep")
        o_in = [in0, in1]
        with nc.Block() as block:
            @block.sync
            def _(sp):
                sp.dma_start(sub[:, :], rows(a["b_subln"][0, :])).then_inc(small, 16)

                def load(s, t):
                    sp.dma_start(o[s][:, :, :], o_dram[bass.ds(t * P, P), :]).then_inc(o_in[s], 16)
                    sp.dma_start(gt[s][:, 0:4, :], p0[bass.ds(t * P, P), 768:1280]).then_inc(o_in[s], 16)
                    sp.dma_start(gt[s][:, 4:8, :], p0[bass.ds(t * P, P), 2816:3328]).then_inc(o_in[s], 16)
                for s in range(2):
                    load(s, s)
                with sp.Fori(1, n_all // 2, 1) as i:
                    for s in range(2):
                        sp.wait_ge(turned, i * 2 + s - 1)
                        load(s, i * 2 + s)

            @block.scalar
            def _(act):
                def gate(n, s, part, t):
                    act.wait_ge(o_in[s], (t - s) * 24 + 48)
                    act.activation(sq[:, :, :], o[s][:, 4:8, :], ACT.Square).then_inc(squared, 1)
                    act.activation(gt[s][:, :, :], gt[s][:, :, :], ACT.Silu).then_inc(gated, 1)
                    act.wait_ge(summed, n + 1)
                    act.activation(ss[:, s, :], ss[:, s, :], ACT.Sqrt, scale=1.0 / P, bias=g.epsc[:, :]).then_inc(rooted, 1)

                def high(n, s, part, t):
                    act.wait_ge(turned, n + 1)
                    act.activation(hT[0][:, :, bass.ds(t * P, P)], pt[s][:, :, :], ACT.Copy).then_inc(hi_done, 1)
                in_turn(act, parts, gate, high)

            @block.vector
            def _(dve):
                dve.wait_ge(small, 16)
                per = 2

                def norm(n, s, part, t):
                    ch = Chain(dve, dstep, n * per)
                    dve.wait_ge(squared, n + 1)
                    dve.tensor_reduce(ss[:, s, :], sq[:, :, :], AX.X, ALU.add).then_inc(summed, 1)
                    dve.wait_ge(rooted, n + 1)
                    ch.link(dve.reciprocal(ss[:, s, :], ss[:, s, :]))
                    ch.link(dve.scalar_tensor_tensor(o[s][:, 4:8, :], o[s][:, 4:8, :], 1.0 - LAMBDA_INIT,
                                                     ss[:, s, :].unsqueeze(2).broadcast_to([P, B_HEADS, P]), ALU.mult, ALU.mult))
                    assert ch.k == per
                    dve.tensor_tensor(o[s][:, 4:8, :], o[s][:, 4:8, :],
                                      sub[:, :].unsqueeze(1).broadcast_to([P, B_HEADS, P]), ALU.mult).then_inc(normed, 1)

                def low(n, s, part, t):
                    cols = bass.ds(t * P, P)
                    dve.wait_ge(hi_done, n + 1)
                    lo_part(dve, hT[1][:, :, cols], pt[s][:, :, :], hT[0][:, :, cols]).then_inc(lo_done, 1)
                in_turn(dve, parts, norm, low)

            @block.gpsimd
            def _(pool):
                def merge(n, s, part, t):
                    pool.wait_ge(normed, n + 1)
                    pool.wait_ge(gated, n + 1)
                    pool.tensor_tensor(o[s][:, :, :], o[s][:, :, :], gt[s][:, :, :], ALU.mult).then_inc(merged, 1)
                in_turn(pool, parts, merge, lambda *tile: None)

            @block.tensor
            def _(pe):
                def turn(n, s, part, t):
                    pe.wait_ge(merged, n + 1)
                    if not (isinstance(n, int) and n < 2):
                        pe.wait_ge(lo_done, n - 1)
                    for k in range(KD):
                        mm = pe.transpose(pt[s][:, k, :], o[s][:, k, :], g.ident[:, :])
                    mm.then_inc(turned, 1)
                in_turn(pe, parts, turn, lambda *tile: None)


def project_out(nc, g, tag, hT, parts, w_dram):
    BLK = 256
    NBLK = D // BLK
    tiles = [(x, t, c0 + P * t, gi) for gi, (x, n, c0, _) in enumerate(parts) for t in range(n)]
    n = len(tiles)
    w_v = w_dram.rearrange("(k p) (b n) -> p k b n", p=P, n=BLK)
    with Phase(nc, tag) as ph:
        gate = ph.sb("gate", [P, len(parts), D])
        w = Weights(ph, KD, BLK)
        tmp = [ph.sb(f"tmp{b}", [P, BLK]) for b in range(4)]
        pb = [ph.ps(f"pb{b}", [P, 512]) for b in range(4)]
        small, made, scaled, added = ph.sems("small made scaled added")
        with nc.Block() as block:
            @block.sync
            def _(sp):
                def load(b):
                    w.load(sp, b, lambda k0, k1: w_v[:, k0:k1, b, :])
                load(0)
                for j, part in enumerate(parts):
                    sp.dma_start(gate[:, j, :], rows(part[3])).then_inc(small, 16)
                with sp.Fori(1, NBLK, 1) as b:
                    load(b)

            @block.scalar
            def _(act):
                w.make_hi(act, 0, 0)

                def step(i, s, first, last):
                    if not last:
                        if not first:
                            act.wait_ge(made, (i * 2 + s) * n)
                        w.make_hi(act, i * 2 + s + 1, 1 - s)
                in_pairs(act, NBLK, step)

            @block.vector
            def _(dve):
                w.make_lo(dve, 0, 0)
                dve.wait_ge(small, 16 * len(parts))
                dve.sem_inc(scaled, 4)

                def step(i, s, first, last):
                    if not last:
                        w.make_lo(dve, i * 2 + s + 1, 1 - s)
                    cols = bass.ds((i * 2 + s) * BLK, BLK)
                    for q, (x, t, _, gi) in enumerate(tiles):
                        b = (s * n + q) % 4
                        m = i * 2 * n + s * n + q
                        dve.wait_ge(made, m + 1)
                        dve.tensor_tensor(tmp[b][:, :], pb[b][:, 0:BLK], gate[:, gi, cols], ALU.mult).then_inc(scaled, 1)
                        dve.wait_ge(scaled, m + 5)
                        dve.tensor_tensor(x[:, t, cols], x[:, t, cols], tmp[b][:, :], ALU.add)
                in_pairs(dve, NBLK, step)

            @block.tensor
            def _(pe):
                with pe.Fori(0, NBLK // 2, 1) as i:
                    for s in range(2):
                        w.ready(pe, i * 2 + s)
                        for q, (_, _, c0, _) in enumerate(tiles):
                            b = (s * n + q) % 4
                            m = i * 2 * n + s * n + q
                            pe.wait_ge(scaled, m + 1)
                            for k in range(KD):
                                mm = product(pe, pb[b][:, 0:BLK], [h[:, k, c0:c0 + P] for h in hT], w.cut(s, k, 0, BLK),
                                             k == 0, k == KD - 1)
                            mm.then_inc(made, 1)


G_HEADS = 4
G_DK = 128
G_DV = 256
G_RANK = 16
G_TAU = 16.0
GK = G_HEADS * G_DK
GV = G_HEADS * G_DV


def log_decays(nc, a, g, p1, la, dec):
    n_all = NT + NC
    with Phase(nc, "ld") as ph:
        wa = ph.sb("wa", [2 * G_RANK, 2, GK])
        ba = ph.sb("ba", [P, 2, GK])
        chunk_of = ph.sb("chunk_of", [P, 2])
        r = ph.sb("r", [P, n_all, 2 * G_RANK])
        rc = ph.sb("rc", [P, 2 * G_RANK])
        rT = ph.sb("rT", [2 * G_RANK, P])
        z = ph.sb("z", [P, 2 * GK])
        e = ph.sb("e", [P, 2 * GK])
        pr = ph.ps("pr", [2 * G_RANK, P])
        pz = ph.ps("pz", [P, 2, GK])
        pd = ph.ps("pd", [P, 2, G_HEADS, 2])
        small, zeroed, placed, turned, copied, logits, biased, absed, logged, made, summed, decayed = ph.sems(
            "small zeroed placed turned copied logits biased absed logged made summed decayed")
        with nc.Block() as block:
            @block.sync
            def _(sp):
                sp.wait_ge(zeroed, 1)
                sp.dma_start(wa[0:G_RANK, 0, :], a["gla_wa_f"][0, :, :]).then_inc(small, 16)
                sp.dma_start(wa[G_RANK:2 * G_RANK, 1, :], a["gla_wa_b"][0, :, :]).then_inc(small, 16)
                sp.dma_start(ba[:, 0, :], rows(a["gla_ba_f"][0, :])).then_inc(small, 16)
                sp.dma_start(ba[:, 1, :], rows(a["gla_ba_b"][0, :])).then_inc(small, 16)
                sp.dma_start(chunk_of[:, :], a["k_chunk_of"][:, :]).then_inc(small, 16)
                sp.dma_start(r[:, :, :], p1[:, 3072:3104].rearrange("(t p) d -> p t d", p=P)).then_inc(small, 16)

            @block.scalar
            def _(act):
                with act.Fori(0, n_all, 1) as t:
                    act.wait_ge(biased, t + 1)
                    act.activation(e[:, :], z[:, :], ACT.Abs).then_inc(absed, 1)
                    act.wait_ge(absed, t * 2 + 1)
                    act.activation(e[:, :], e[:, :], ACT.Exp, scale=-1.0).then_inc(absed, 1)
                    act.wait_ge(absed, t * 2 + 2)
                    act.activation(e[:, :], e[:, :], ACT.Ln, bias=1.0).then_inc(logged, 1)
                    act.wait_ge(summed, t + 1)
                    act.activation(dec[:, bass.ds(t, 1), :], pd[:, :, :, :], ACT.Exp).then_inc(decayed, 1)

            @block.vector
            def _(dve):
                dve.memset(wa[:, :, :], 0.0).then_inc(zeroed, 1)
                dve.wait_ge(small, 16 * 6)
                with dve.Fori(0, n_all, 1) as t:
                    dve.tensor_copy(rc[:, :], r[:, t, :]).then_inc(placed, 1)
                    dve.wait_ge(turned, t + 1)
                    dve.tensor_copy(rT[:, :], pr[:, :]).then_inc(copied, 1)
                    dve.wait_ge(logits, t + 1)
                    dve.tensor_tensor(z[:, :], pz[:, :, :], ba[:, :, :], ALU.add).then_inc(biased, 1)
                    dve.wait_ge(logged, t + 1)
                    dve.scalar_tensor_tensor(z[:, :], z[:, :], 0.0, e[:, :], ALU.min, ALU.subtract).then_inc(made, 1)
                    dve.wait_ge(made, t * 2 + 1)
                    dve.tensor_scalar(la[:, t, :], z[:, :], 1.0 / G_TAU, None, ALU.mult)
                    dve.tensor_scalar(e[:, :], z[:, :], 1.0 / G_TAU, None, ALU.mult).then_inc(made, 1)

            @block.tensor
            def _(pe):
                pe.wait_ge(small, 16 * 6)
                with pe.Fori(0, n_all, 1) as t:
                    pe.wait_ge(placed, t + 1)
                    pe.transpose(pr[:, :], rc[:, :], g.ident[:, :]).then_inc(turned, 1)
                    pe.wait_ge(copied, t + 1)
                    for d in range(2):
                        mm = pe.matmul(pz[:, d, :], rT[:, :], wa[:, d, :], start=True, stop=True)
                    mm.then_inc(logits, 1)
                    pe.wait_ge(made, t * 2 + 2)
                    for d in range(2):
                        for h in range(G_HEADS):
                            mm = pe.matmul(pd[:, d, h, :], e[:, GK * d + G_DK * h:GK * d + G_DK * h + G_DK], chunk_of[:, :],
                                           start=True, stop=True)
                    mm.then_inc(summed, 1)


def linear_attention(nc, a, g, p1, la, dec, O):
    with Phase(nc, "la") as ph:
        masks = ph.sb("masks", [P, 5, P])
        qkv = [ph.sb(f"qkv{d}", [P, 2 * GK + GV]) for d in range(2)]
        eb = ph.sb("eb", [P, GK])
        en = ph.sb("en", [P, GK])
        er = ph.sb("er", [P, GK])
        qd = ph.sb("qd", [P, GK])
        kd = ph.sb("kd", [P, GK])
        ke = ph.sb("ke", [P, GK])
        qdT = ph.sb("qdT", [P, G_HEADS, P])
        kdT = ph.sb("kdT", [P, G_HEADS, P])
        at = ph.sb("at", [P, G_HEADS, P])
        S = [ph.sb(f"S{d}", [P, G_HEADS, G_DV]) for d in range(2)]
        pA = ph.ps("pA", [P, 512])
        pB = ph.ps("pB", [P, 512])
        pq = ph.ps("pq", [P, G_HEADS, P])
        pk = ph.ps("pk", [P, G_HEADS, P])
        po = ph.ps("po", [P, G_HEADS, G_DV])
        pd = ph.ps("pd", [P, G_HEADS, G_DV])
        small, in0, in1, cum, expd, prod, kept, turned, qT_done, kT_done, att, masked, outer, sread, upd, added, zeroed = ph.sems(
            "small in0 in1 cum expd prod kept turned qT_done kT_done att masked outer sread upd added zeroed")
        qkv_in = [in0, in1]
        upto, after = (0, 1), (4, 3)

        def run(eng, unit):
            for j in range(NC):
                for d in range(2):
                    unit(d, 2 * j + d, None, NT + (j if d == 0 else NC - 1 - j), j)
            with eng.Fori(0, NT, 1) as i:
                for d in range(2):
                    unit(d, i * 2 + d + 2 * NC, i * 2 + d, i if d == 0 else i * -1 + NT - 1, i + NC)

        with nc.Block() as block:
            @block.sync
            def _(sp):
                sp.dma_start(masks[:, :, :], a["k_masks"].rearrange("m p k -> p m k")).then_inc(small, 16)

                def unit(d, n, u, tile, j):
                    if u is not None or j > 0:
                        sp.wait_ge(outer, n * 2 - 2)
                    if u is None:
                        src = p1[tile * P:tile * P + P, :]
                        sp.dma_start(qkv[d][:, GK:], src[:, GK:2 * GK + GV]).then_inc(qkv_in[d], 16)
                    else:
                        src = p1[bass.ds(tile * P, P), :]
                        sp.dma_start(qkv[d][:, :], src[:, 0:2 * GK + GV]).then_inc(qkv_in[d], 16)
                run(sp, unit)

            @block.gpsimd
            def _(pool):
                for d in range(2):
                    pool.memset(S[d][:, :, :], 0.0).then_inc(zeroed, 1)
                pool.memset(O[:, :, :], 0.0).then_inc(zeroed, 1)

                def unit(d, n, u, tile, j):
                    pool.wait_ge(qkv_in[d], j * 16 + 16)
                    pool.wait_ge(expd, n + 1)
                    pool.tensor_tensor(ke[:, :], qkv[d][:, GK:2 * GK], er[:, :], ALU.mult).then_inc(kept, 1)
                run(pool, unit)

            @block.scalar
            def _(act):
                def unit(d, n, u, tile, j):
                    act.wait_ge(cum, n + 1)
                    if u is not None:
                        act.activation(eb[:, :], pA[:, :], ACT.Exp)
                        act.activation(en[:, :], pA[:, :], ACT.Exp, scale=-1.0)
                    act.activation(er[:, :], pB[:, :], ACT.Exp).then_inc(expd, 1)
                    if u is not None:
                        act.wait_ge(turned, u + 1)
                        act.activation(qdT[:, :, :], pq[:, :, :], ACT.Copy).then_inc(qT_done, 1)
                run(act, unit)

            @block.vector
            def _(dve):
                dve.wait_ge(small, 16)
                dve.wait_ge(zeroed, 3)
                dve.sem_inc(added, 1)

                def unit(d, n, u, tile, j):
                    if u is not None:
                        dve.wait_ge(qkv_in[d], j * 16 + 16)
                        dve.wait_ge(expd, n + 1)
                        dve.scalar_tensor_tensor(qd[:, :], qkv[d][:, 0:GK], G_DK ** -0.5, eb[:, :], ALU.mult, ALU.mult)
                        dve.tensor_tensor(kd[:, :], qkv[d][:, GK:2 * GK], en[:, :], ALU.mult).then_inc(prod, 1)
                        dve.wait_ge(turned, u + 1)
                        dve.tensor_copy(kdT[:, :, :], pk[:, :, :]).then_inc(kT_done, 1)
                        dve.wait_ge(att, u + 1)
                        dve.tensor_tensor(at[:, :, :], pA[:, :].rearrange("p (h t) -> p h t", t=P),
                                          masks[:, upto[d], :].unsqueeze(1).broadcast_to([P, G_HEADS, P]), ALU.mult).then_inc(masked, 1)
                    for half, c in enumerate((0, 1) if d == 0 else (1, 0)):
                        dve.wait_ge(outer, n * 2 + half + 1)
                        if u is not None:
                            dve.wait_ge(sread, u * 2 + half + 1)
                        if u is not None or n or half:
                            dve.wait_ge(upd, n * 2 + half)
                        for h in range(G_HEADS):
                            ins = dve.scalar_tensor_tensor(S[d][:, h, :], S[d][:, h, :], dec[:, tile, 8 * d + 2 * h + c:8 * d + 2 * h + c + 1],
                                                           pd[:, h, :], ALU.mult, ALU.add)
                        ins.then_inc(upd, 1)
                    if u is not None:
                        dve.wait_ge(added, u + 1)
                        dve.tensor_tensor(O[:, tile, :], O[:, tile, :], po[:, :, :].rearrange("p h e -> p (h e)"), ALU.add).then_inc(added, 1)
                run(dve, unit)

            @block.tensor
            def _(pe):
                pe.wait_ge(small, 16)
                pe.wait_ge(zeroed, 3)

                def unit(d, n, u, tile, j):
                    la_d = la[:, bass.ds(tile, 1), GK * d:GK * d + GK]
                    if u is not None:
                        pe.matmul(pA[:, :], masks[:, upto[d], :], la_d, start=True, stop=True)
                    pe.matmul(pB[:, :], masks[:, after[d], :], la_d, start=True, stop=True).then_inc(cum, 1)
                    if u is not None:
                        pe.wait_ge(prod, u + 1)
                        for h in range(G_HEADS):
                            pe.transpose(pq[:, h, :], qd[:, G_DK * h:G_DK * h + G_DK], g.ident[:, :])
                        for h in range(G_HEADS):
                            mm = pe.transpose(pk[:, h, :], kd[:, G_DK * h:G_DK * h + G_DK], g.ident[:, :])
                        mm.then_inc(turned, 1)
                    pe.wait_ge(kept, n + 1)
                    if u is None:
                        pe.wait_ge(qkv_in[d], j * 16 + 16)
                    order = (0, 1) if d == 0 else (1, 0)

                    def outers(c):
                        toks = slice(64 * c, 64 * c + 64)
                        for h in range(G_HEADS):
                            mm = pe.matmul(pd[:, h, :], ke[toks, G_DK * h:G_DK * h + G_DK],
                                           qkv[d][toks, 2 * GK + G_DV * h:2 * GK + G_DV * h + G_DV], start=True, stop=True)
                        mm.then_inc(outer, 1)

                    def from_state(c):
                        toks = slice(64 * c, 64 * c + 64)
                        for h in range(G_HEADS):
                            mm = pe.matmul(po[toks, h, :], qdT[:, h, toks], S[d][:, h, :], start=False, stop=(c == order[1]),
                                           skip_group_check=True)
                        mm.then_inc(sread, 1)

                    if u is not None or n:
                        pe.wait_ge(upd, n * 2)
                    outers(order[0])
                    if u is not None:
                        pe.wait_ge(qT_done, u + 1)
                        pe.wait_ge(kT_done, u + 1)
                        for h in range(G_HEADS):
                            mm = pe.matmul(pA[:, P * h:P * h + P], kdT[:, h, :], qdT[:, h, :], start=True, stop=True)
                        mm.then_inc(att, 1)
                        pe.wait_ge(masked, u + 1)
                        pe.wait_ge(added, u + 1)
                        for h in range(G_HEADS):
                            pe.matmul(po[:, h, :], at[:, h, :], qkv[d][:, 2 * GK + G_DV * h:2 * GK + G_DV * h + G_DV],
                                      start=(h % 2 == 0), stop=False, skip_group_check=True)
                        from_state(order[0])
                    pe.wait_ge(upd, n * 2 + 1)
                    if u is not None:
                        from_state(order[1])
                    outers(order[1])
                run(pe, unit)


def merge_odd(nc, a, g, hT, p1, O):
    parts = [(NT,)]
    with Phase(nc, "mo") as ph:
        gt = [ph.sb(f"gt{s}", [P, G_HEADS, G_DV]) for s in range(2)]
        gain = ph.sb("gain", [P, G_DV])
        sq = ph.sb("sq", [P, G_HEADS, G_DV])
        on = [ph.sb(f"on{s}", [P, G_HEADS, G_DV]) for s in range(2)]
        ss = ph.sb("ss", [P, 2, G_HEADS])
        pt = [ph.ps(f"pt{s}", [P, KD, P]) for s in range(2)]
        small, in0, in1, squared, summed, rooted, normed, gated, merged, turned, hi_done, lo_done, dstep = ph.sems(
            "small in0 in1 squared summed rooted normed gated merged turned hi_done lo_done dstep")
        g_in = [in0, in1]
        with nc.Block() as block:
            @block.sync
            def _(sp):
                sp.dma_start(gain[:, :], rows(a["gla_out_norm"][0, :])).then_inc(small, 16)

                def load(s, t):
                    sp.dma_start(gt[s][:, :, :], p1[bass.ds(t * P, P), 2048:3072]).then_inc(g_in[s], 16)
                for s in range(2):
                    load(s, s)
                with sp.Fori(1, NT // 2, 1) as i:
                    for s in range(2):
                        sp.wait_ge(merged, i * 2 + s - 1)
                        load(s, i * 2 + s)

            @block.scalar
            def _(act):
                def gate(n, s, part, t):
                    act.activation(sq[:, :, :], O[:, bass.ds(t, 1), :].rearrange("p a (h e) -> p (a h) e", e=G_DV), ACT.Square).then_inc(squared, 1)
                    act.wait_ge(g_in[s], (t - s) * 8 + 16)
                    act.activation(gt[s][:, :, :], gt[s][:, :, :], ACT.Silu).then_inc(gated, 1)
                    act.wait_ge(summed, n + 1)
                    act.activation(ss[:, s, :], ss[:, s, :], ACT.Sqrt, scale=1.0 / G_DV, bias=g.epsc[:, :]).then_inc(rooted, 1)

                def high(n, s, part, t):
                    act.wait_ge(turned, n + 1)
                    act.activation(hT[0][:, :, bass.ds(t * P, P)], pt[s][:, :, :], ACT.Copy).then_inc(hi_done, 1)
                in_turn(act, parts, gate, high)

            @block.vector
            def _(dve):
                dve.wait_ge(small, 16)
                per = 2

                def norm(n, s, part, t):
                    ch = Chain(dve, dstep, n * per)
                    dve.wait_ge(squared, n + 1)
                    dve.tensor_reduce(ss[:, s, :], sq[:, :, :], AX.X, ALU.add).then_inc(summed, 1)
                    dve.wait_ge(rooted, n + 1)
                    ch.link(dve.reciprocal(ss[:, s, :], ss[:, s, :]))
                    ch.link(dve.tensor_tensor(on[s][:, :, :], O[:, bass.ds(t, 1), :].rearrange("p a (h e) -> p (a h) e", e=G_DV),
                                              ss[:, s, :].unsqueeze(2).broadcast_to([P, G_HEADS, G_DV]), ALU.mult))
                    assert ch.k == per
                    dve.tensor_tensor(on[s][:, :, :], on[s][:, :, :],
                                      gain[:, :].unsqueeze(1).broadcast_to([P, G_HEADS, G_DV]), ALU.mult).then_inc(normed, 1)

                def low(n, s, part, t):
                    cols = bass.ds(t * P, P)
                    dve.wait_ge(hi_done, n + 1)
                    lo_part(dve, hT[1][:, :, cols], pt[s][:, :, :], hT[0][:, :, cols]).then_inc(lo_done, 1)
                in_turn(dve, parts, norm, low)

            @block.gpsimd
            def _(pool):
                def merge(n, s, part, t):
                    pool.wait_ge(normed, n + 1)
                    pool.wait_ge(gated, n + 1)
                    pool.tensor_tensor(on[s][:, :, :], on[s][:, :, :], gt[s][:, :, :], ALU.mult).then_inc(merged, 1)
                in_turn(pool, parts, merge, lambda *tile: None)

            @block.tensor
            def _(pe):
                def turn(n, s, part, t):
                    pe.wait_ge(merged, n + 1)
                    if not (isinstance(n, int) and n < 2):
                        pe.wait_ge(lo_done, n - 1)
                    flat = on[s][:, :, :].rearrange("p h e -> p (h e)")
                    for k in range(KD):
                        mm = pe.transpose(pt[s][:, k, :], flat[:, P * k:P * k + P], g.ident[:, :])
                    mm.then_inc(turned, 1)
                in_turn(pe, parts, turn, lambda *tile: None)


NCUT = [(0, 512), (512, 1024), (1024, T2)]


def project_cols(nc, hT, tag, w_dram, c_from, nblk, dst, narrow=None):
    BLK = 256
    w_v = w_dram.rearrange("(k p) n -> p k n", p=P)
    with Phase(nc, tag) as ph:
        w = Weights(ph, KD, BLK)
        o = [ph.sb(f"o{b}", [P, T2]) for b in range(2)]
        wn_raw = ph.sb("wn_raw", [P, KD, 8])
        wn = ph.pair("wn", [P, KD, 8])
        on = ph.sb("on", [8, T2])
        pb = [ph.ps(f"pb{b}", [P, 1536]) for b in range(2)]
        in_n, hi_n, lo_n, made_n, copied_n, st_n = ph.sems("in_n hi_n lo_n made_n copied_n st_n")
        made, copied, stored = ph.sems("made0 made1"), ph.sems("copied0 copied1"), ph.sems("stored0 stored1")
        with nc.Block() as block:
            @block.gpsimd
            def _(pool):
                def load(b):
                    w.load(pool, b, lambda k0, k1: w_v[:, k0:k1, bass.ds(c_from + b * BLK, BLK)])
                load(0)
                if narrow:
                    with nc.allow_non_contiguous_dma(reason="eight columns of the weights"):
                        pool.dma_start(wn_raw[:, :, :], w_v[:, :, narrow[0]:narrow[0] + narrow[1]]).then_inc(in_n, 16)
                with pool.Fori(1, nblk, 1) as b:
                    load(b)

            @block.sync
            def _(sp):
                for b in range(2):
                    sp.sem_inc(stored[b], 16)
                with sp.Fori(0, nblk // 2, 1) as i:
                    for s in range(2):
                        for b in range(2):
                            m = i * 2 + s
                            sp.wait_ge(copied[b], m + 1)
                            sp.dma_start(dst[bass.ds(m * BLK + b * P, P), :], o[b][:, :]).then_inc(stored[b], 16)
                if narrow:
                    sp.wait_ge(copied_n, 1)
                    sp.dma_start(narrow[2], on[0:narrow[1], :]).then_inc(st_n, 16)
                    sp.wait_ge(st_n, 16)
                for b in range(2):
                    sp.wait_ge(stored[b], 16 + 16 * nblk)

            @block.scalar
            def _(act):
                w.make_hi(act, 0, 0)
                if narrow:
                    act.wait_ge(in_n, 16)
                    act.activation(wn[0][:, :, :], wn_raw[:, :, :], ACT.Copy).then_inc(hi_n, 1)

                def step(i, s, first, last):
                    m = i * 2 + s
                    if not last:
                        if not first:
                            act.wait_ge(made[1], m)
                        w.make_hi(act, m + 1, 1 - s)
                    act.wait_ge(made[0], m + 1)
                    act.wait_ge(stored[0], m * 16 + 16)
                    act.activation(o[0][:, :], pb[0][:, 0:T2], ACT.Copy).then_inc(copied[0], 1)
                in_pairs(act, nblk, step)
                if narrow:
                    act.wait_ge(made_n, 1)
                    act.activation(on[0:narrow[1], :], pb[0][0:narrow[1], 0:T2], ACT.Copy).then_inc(copied_n, 1)

            @block.vector
            def _(dve):
                w.make_lo(dve, 0, 0)
                if narrow:
                    dve.wait_ge(hi_n, 1)
                    lo_part(dve, wn[1][:, :, :], wn_raw[:, :, :], wn[0][:, :, :]).then_inc(lo_n, 1)

                def step(i, s, first, last):
                    m = i * 2 + s
                    if not last:
                        w.make_lo(dve, m + 1, 1 - s)
                    dve.wait_ge(made[1], m + 1)
                    dve.wait_ge(stored[1], m * 16 + 16)
                    dve.tensor_copy(o[1][:, :], pb[1][:, 0:T2]).then_inc(copied[1], 1)
                in_pairs(dve, nblk, step)

            @block.tensor
            def _(pe):
                with pe.Fori(0, nblk // 2, 1) as i:
                    for s in range(2):
                        m = i * 2 + s
                        w.ready(pe, m)
                        for b in range(2):
                            pe.wait_ge(stored[b], m * 16 + 16)
                            for c0, c1 in NCUT:
                                for k in range(KD):
                                    mm = product(pe, pb[b][:, c0:c1], w.cut(s, k, P * b, P * b + P),
                                                 [h[:, k, c0:c1] for h in hT], k == 0, k == KD - 1)
                            mm.then_inc(made[b], 1)
                if narrow:
                    pe.wait_ge(lo_n, 1)
                    pe.wait_ge(copied[0], nblk)
                    for c0, c1 in NCUT:
                        for k in range(KD):
                            mm = product(pe, pb[0][0:narrow[1], c0:c1], [h[:, k, 0:narrow[1]] for h in wn],
                                         [h[:, k, c0:c1] for h in hT], k == 0, k == KD - 1)
                    mm.then_inc(made_n, 1)


LRU = 256
NL = LRU // P
CONV_A = 4
LRU_C = 8.0


def linear_recurrence(nc, a, g, pT):
    with Phase(nc, "lr") as ph:
        x = ph.sb("x", [P, NL, CONV_A - 1 + T2])
        y = ph.sb("y", [P, NL, T2])
        cw = ph.sb("cw", [P, NL, CONV_A])
        vec = ph.sb("vec", [P, 4, NL])
        sp_ = ph.sb("sp", [P, 3, NL])
        gw = ph.sb("gw", [P, 2, NL, P])
        u = ph.sb("u", [P, NL, T2])
        r = ph.sb("r", [P, NL, T2])
        gi = ph.sb("gi", [P, NL, T2])
        th = ph.sb("th", [P, NL, T2])
        pr = ph.ps("pr", [P, 1536])
        pi = ph.ps("pi", [P, 1536])
        small, zeroed, conv, gates, sig, lam_e, lam_l, decayed, tanhed, ratio, rooted, gelued, dstep = ph.sems(
            "small zeroed conv gates sig lam_e lam_l decayed tanhed ratio rooted gelued dstep")
        with nc.Block() as block:
            @block.sync
            def _(sp):
                sp.wait_ge(zeroed, 2)
                with nc.allow_non_contiguous_dma(reason="short vectors, feature-major"):
                    for c in range(NL):
                        sp.dma_start(cw[:, c, :], a["lru_conv_w_2"][0, :, P * c:P * c + P].rearrange("t p -> p t")).then_inc(small, 16)
                    for j, name in enumerate(("lru_conv_b_2", "lru_gate_a_b_2", "lru_gate_x_b_2", "lru_lambda_2")):
                        sp.dma_start(vec[:, j, :], a[name][0, :].rearrange("(c p) -> p c", p=P)).then_inc(small, 16)
                for j, name in enumerate(("lru_gate_a_w_2", "lru_gate_x_w_2")):
                    for h in range(4):
                        half = slice(64 * (h % 2), 64 * (h % 2) + 64)
                        sp.dma_start(gw[half, j, h // 2, half], a[name][0, h, :, :]).then_inc(small, 16)
                sp.dma_start(x[:, :, CONV_A - 1:], pT[0:LRU, :].rearrange("(c p) t -> p c t", p=P)).then_inc(small, 16)
                sp.dma_start(y[:, :, :], pT[LRU:2 * LRU, :].rearrange("(c p) t -> p c t", p=P)).then_inc(small, 16)
                sp.wait_ge(small, 16 * 16)

            @block.gpsimd
            def _(pool):
                pool.memset(x[:, :, 0:CONV_A - 1], 0.0).then_inc(zeroed, 1)
                pool.memset(gw[:, :, :, :], 0.0).then_inc(zeroed, 1)

            @block.scalar
            def _(act):
                act.wait_ge(small, 16 * 16)
                act.activation(sp_[:, 0, :], vec[:, 3, :], ACT.Abs).then_inc(lam_e, 1)
                act.wait_ge(lam_e, 1)
                act.activation(sp_[:, 1, :], sp_[:, 0, :], ACT.Exp, scale=-1.0).then_inc(lam_e, 1)
                act.wait_ge(lam_e, 2)
                act.activation(sp_[:, 2, :], sp_[:, 1, :], ACT.Ln, bias=1.0).then_inc(lam_l, 1)
                for c in range(NL):
                    act.wait_ge(gates, c + 1)
                    act.activation(r[:, c, :], pr[:, 0:T2], ACT.Sigmoid, bias=vec[:, 1, c:c + 1])
                    act.activation(gi[:, c, :], pi[:, 0:T2], ACT.Sigmoid, bias=vec[:, 2, c:c + 1]).then_inc(sig, 1)
                act.wait_ge(decayed, 1)
                act.activation(th[:, :, :], r[:, :, :], ACT.Tanh).then_inc(tanhed, 1)
                act.activation(r[:, :, :], r[:, :, :], ACT.Exp).then_inc(tanhed, 1)
                act.wait_ge(ratio, 1)
                act.activation(th[:, :, :], th[:, :, :], ACT.Sqrt).then_inc(rooted, 1)
                act.activation(y[:, :, :], y[:, :, :], ACT.Gelu_apprx_tanh).then_inc(gelued, 1)

            @block.vector
            def _(dve):
                ch = Chain(dve, dstep)
                dve.wait_ge(small, 16 * 16)
                dve.wait_ge(zeroed, 2)
                for c in range(NL):
                    ch.link(dve.tensor_scalar(u[:, c, :], x[:, c, 0:T2], cw[:, c, 0:1], vec[:, 0, c:c + 1], ALU.mult, ALU.add))
                    for j in range(1, CONV_A):
                        ins = dve.scalar_tensor_tensor(u[:, c, :], x[:, c, j:j + T2], cw[:, c, j:j + 1], u[:, c, :], ALU.mult, ALU.add)
                        if j < CONV_A - 1:
                            ch.link(ins)
                    ins.then_inc(conv, 1)
                dve.wait_ge(lam_l, 1)
                ch.link(dve.tensor_scalar(sp_[:, 0, :], vec[:, 3, :], -1.0, 0.0, ALU.mult, ALU.max))
                ch.link(dve.tensor_tensor(sp_[:, 0, :], sp_[:, 0, :], sp_[:, 2, :], ALU.add))
                ch.link(dve.tensor_scalar(sp_[:, 0, :], sp_[:, 0, :], -LRU_C, None, ALU.mult))
                dve.wait_ge(sig, NL)
                for c in range(NL):
                    ins = dve.tensor_scalar(r[:, c, :], r[:, c, :], sp_[:, 0, c:c + 1], None, ALU.mult)
                ins.then_inc(decayed, 1)
                ch.link(dve.tensor_tensor(gi[:, :, :], gi[:, :, :], u[:, :, :], ALU.mult))
                dve.wait_ge(tanhed, 1)
                ch.link(dve.tensor_scalar(u[:, :, :], th[:, :, :], -1.0, 1.0, ALU.mult, ALU.add))
                ch.link(dve.reciprocal(u[:, :, :], u[:, :, :]))
                dve.scalar_tensor_tensor(th[:, :, :], th[:, :, :], -2.0, u[:, :, :], ALU.mult, ALU.mult).then_inc(ratio, 1)
                dve.wait_ge(rooted, 1)
                ch.link(dve.tensor_tensor(gi[:, :, :], gi[:, :, :], th[:, :, :], ALU.mult))
                dve.wait_ge(tanhed, 2)
                for c in range(NL):
                    ins = dve.tensor_tensor_scan(u[:, c, :], r[:, c, :], gi[:, c, :], 0.0, ALU.mult, ALU.add)
                ch.link(ins)
                dve.wait_ge(gelued, 1)
                ch.link(dve.tensor_tensor(g.hT[:, 0:NL, 0:T2], u[:, :, :], y[:, :, :], ALU.mult))

            @block.tensor
            def _(pe):
                pe.wait_ge(small, 16 * 16)
                for c in range(NL):
                    pe.wait_ge(conv, c + 1)
                    if c:
                        pe.wait_ge(sig, c)
                    for j, ps in enumerate((pr, pi)):
                        for c0, c1 in NCUT:
                            mm = pe.matmul(ps[:, c0:c1], gw[:, j, c, :], u[:, c, c0:c1], start=True, stop=True)
                    mm.then_inc(gates, 1)


FOX_HEADS = 8
AUG = HD + 2


def forget_sums(nc, a, g, fT, cum_dram):
    with Phase(nc, "fs") as ph:
        f = ph.sb("f", [FOX_HEADS, T2])
        e = ph.sb("e", [FOX_HEADS, T2])
        one = ph.sb("one", [FOX_HEADS, T2])
        bias = ph.sb("bias", [FOX_HEADS, 1])
        small, absed, logged, summed, stored, dstep = ph.sems("small absed logged summed stored dstep")
        with nc.Block() as block:
            @block.sync
            def _(sp):
                sp.dma_start(f[:, :], fT).then_inc(small, 16)
                with nc.allow_non_contiguous_dma(reason="a short vector"):
                    sp.dma_start(bias[:, :], a["fox_f_bias_2"].rearrange("o h -> h o")).then_inc(small, 16)
                sp.wait_ge(summed, 1)
                sp.dma_start(cum_dram[0, :, :], f[:, :]).then_inc(stored, 16)
                sp.dma_start(cum_dram[1, :, :], e[:, :]).then_inc(stored, 16)
                sp.wait_ge(stored, 32)

            @block.scalar
            def _(act):
                act.wait_ge(small, 32)
                act.activation(e[:, :], f[:, :], ACT.Abs, bias=bias[:, :]).then_inc(absed, 1)
                act.wait_ge(absed, 1)
                act.activation(e[:, :], e[:, :], ACT.Exp, scale=-1.0).then_inc(absed, 1)
                act.wait_ge(absed, 2)
                act.activation(e[:, :], e[:, :], ACT.Ln, bias=1.0).then_inc(logged, 1)

            @block.vector
            def _(dve):
                ch = Chain(dve, dstep)
                dve.wait_ge(small, 32)
                ch.step(dve.memset(one[:, :], 1.0))
                dve.wait_ge(absed, 1)
                ch.link(dve.tensor_scalar(f[:, :], f[:, :], bias[:, :], 0.0, ALU.add, ALU.min))
                dve.wait_ge(logged, 1)
                ch.link(dve.tensor_tensor(f[:, :], f[:, :], e[:, :], ALU.subtract))
                ch.link(dve.tensor_tensor_scan(e[:, :], one[:, :], f[:, :], 0.0, ALU.mult, ALU.add))
                ch.link(dve.tensor_scalar(f[:, :], e[:, :], 1.0 / SCALE, None, ALU.mult))
                dve.tensor_scalar(e[:, :], f[:, :], -1.0, None, ALU.mult).then_inc(summed, 1)


def forgetting_attention(nc, a, g, pT, pv, cum):
    NT2 = len(TILES2)
    with Phase(nc, "fx") as ph:
        q = [ph.sb(f"q{s}", [AUG, T2]) for s in range(2)]
        k = [ph.sb(f"k{s}", [AUG, T2]) for s in range(2)]
        vs = [ph.sb(f"v{s}", [P, NT2, HD]) for s in range(2)]
        causal = ph.sb("causal", [P, P])
        E = [ph.sb(f"E{b}", [P, T2]) for b in range(2)]
        ET = ph.sb("ET", [P, NT2, P])
        mx = ph.sb("mx", [P, 2])
        nm = ph.sb("nm", [P, 2])
        l = ph.sb("l", [P, 2])
        r = ph.sb("r", [P, 2])
        pS = [ph.ps(f"pS{b}", [P, 1536]) for b in range(2)]
        pT_ = ph.ps("pT", [P, 4, P])
        po = ph.ps("po", [P, 512])
        small, ones, in0, in1, scores, topped, negmax, expd, weights, turned, evac, values_in, o_done, dstep = ph.sems(
            "small ones in0 in1 scores topped negmax expd weights turned evac values_in o_done dstep")
        qk_in = [in0, in1]
        seq = [(s, j) for s in range(2) for j in range(NT2)]
        NS = len(seq)

        def groups(j):
            return [(a0, min(a0 + 4, j + 1)) for a0 in range(0, j + 1, 4)]

        def groups_before(n):
            return sum(len(groups(seq[m][1])) for m in range(n))

        per_round = groups_before(NS)
        with nc.Block() as block:
            @block.sync
            def _(sp):
                sp.wait_ge(ones, 6)
                def load(s, h):
                    sp.dma_start(q[s][0:HD, :], pT[bass.ds(512 + h * HD, HD), :]).then_inc(qk_in[s], 16)
                    sp.dma_start(k[s][0:HD, :], pT[bass.ds(1024 + h * HD, HD), :]).then_inc(qk_in[s], 16)
                    sp.dma_start(q[s][HD:HD + 1, :], cum[0, bass.ds(h, 1), :]).then_inc(qk_in[s], 16)
                    sp.dma_start(k[s][HD + 1:HD + 2, :], cum[1, bass.ds(h, 1), :]).then_inc(qk_in[s], 16)
                    sp.dma_start(vs[s][0:META, 0, :], pv[0:META, bass.ds(h * HD, HD)]).then_inc(qk_in[s], 16)
                    sp.dma_start(vs[s][:, 1:, :], pv[META:T2, bass.ds(h * HD, HD)].rearrange("(t p) d -> p t d", p=P)).then_inc(qk_in[s], 16)
                for s in range(2):
                    load(s, s)
                sp.dma_start(causal[:, :], a["k_causal"]).then_inc(small, 16)
                with sp.Fori(1, FOX_HEADS // 2, 1) as i:
                    for s in range(2):
                        sp.wait_ge(values_in, (i - 1) * NS + NT2 * (s + 1))
                        load(s, i * 2 + s)

            @block.gpsimd
            def _(pool):
                first = [(E[s][:, 0:META], 0.0) for s in range(2)] + [(x[s][HD:HD + 2, :], 1.0) for s in range(2) for x in (q, k)]
                for m, (cells, value) in enumerate(first):
                    if m:
                        pool.wait_ge(ones, m)
                    pool.memset(cells, value).then_inc(ones, 1)

            @block.scalar
            def _(act):
                act.wait_ge(ones, 6)
                with act.Fori(0, FOX_HEADS // 2, 1) as i:
                    def exps(n):
                        s, j = seq[n]
                        b, (c0, rr) = n % 2, TILES2[j]
                        act.wait_ge(negmax, i * NS + n + 1)
                        act.activation(E[b][0:rr, 0:c0 + rr], pS[b][0:rr, 0:c0 + rr], ACT.Exp, scale=SCALE,
                                       bias=nm[0:rr, b:b + 1], accum_out=l[0:rr, b:b + 1]).then_inc(expd, 1)
                    exps(0)
                    for n, (s, j) in enumerate(seq):
                        if n + 1 < NS:
                            exps(n + 1)
                        rr = TILES2[j][1]
                        for gi, (a0, a1) in enumerate(groups(j)):
                            act.wait_ge(turned, i * per_round + groups_before(n) + gi + 1)
                            if a0 == 0:
                                ins = act.activation(ET[0:META, 0, 0:rr], pT_[0:META, 0, 0:rr], ACT.Copy)
                            b0 = max(a0, 1)
                            if a1 > b0:
                                ins = act.activation(ET[:, b0:a1, 0:rr], pT_[:, b0 - a0:a1 - a0, 0:rr], ACT.Copy)
                            ins.then_inc(evac, 1)

            @block.vector
            def _(dve):
                dve.wait_ge(small, 16)
                with dve.Fori(0, FOX_HEADS // 2, 1) as i:
                    ch = Chain(dve, dstep, i * 2 * NS)

                    def maxima(n):
                        s, j = seq[n]
                        b, (c0, rr) = n % 2, TILES2[j]
                        dve.wait_ge(scores, i * NS + n + 1)
                        ch.link(dve.tensor_tensor(pS[b][0:rr, c0:c0 + rr], pS[b][0:rr, c0:c0 + rr], causal[0:rr, 0:rr], ALU.add))
                        dve.tensor_reduce(mx[0:rr, b:b + 1], pS[b][0:rr, 0:c0 + rr], AX.X, ALU.max).then_inc(topped, 1)
                        dve.wait_ge(topped, i * NS + n + 1)
                        dve.tensor_scalar(nm[0:rr, b:b + 1], mx[0:rr, b:b + 1], -SCALE, None, ALU.mult).then_inc(negmax, 1)

                    maxima(0)
                    for n, (s, j) in enumerate(seq):
                        b, (c0, rr) = n % 2, TILES2[j]
                        dve.wait_ge(expd, i * NS + n + 1)
                        ch.link(dve.reciprocal(r[0:rr, b:b + 1], l[0:rr, b:b + 1]))
                        dve.tensor_scalar(E[b][0:rr, 0:c0 + rr], E[b][0:rr, 0:c0 + rr], r[0:rr, b:b + 1], None, ALU.mult).then_inc(weights, 1)
                        if n + 1 < NS:
                            maxima(n + 1)
                        dve.wait_ge(values_in, i * NS + n + 1)
                        half = slice(64 * s, 64 * s + 64)
                        dve.tensor_copy(g.hT[half, bass.ds(i + 2, 1), c0:c0 + rr], po[half, 0:rr]).then_inc(o_done, 1)
                    assert ch.k == 2 * NS

            @block.tensor
            def _(pe):
                pe.wait_ge(small, 16)
                with pe.Fori(0, FOX_HEADS // 2, 1) as i:
                    def scores_of(n):
                        s, j = seq[n]
                        b, (c0, rr) = n % 2, TILES2[j]
                        if j == 0:
                            pe.wait_ge(qk_in[s], i * 96 + 96)
                        if n >= 2:
                            pe.wait_ge(expd, i * NS + n - 1)
                        for k0, k1 in NCUT:
                            k1 = min(k1, c0 + rr)
                            if k0 < k1:
                                mm = pe.matmul(pS[b][0:rr, k0:k1], q[s][:, c0:c0 + rr], k[s][:, k0:k1], start=True, stop=True)
                        mm.then_inc(scores, 1)

                    scores_of(0)
                    for n, (s, j) in enumerate(seq):
                        b, (c0, rr) = n % 2, TILES2[j]
                        if n + 1 < NS:
                            scores_of(n + 1)
                        pe.wait_ge(weights, i * NS + n + 1)
                        te = P if j == 0 else rr
                        gs = groups(j)
                        half = slice(64 * s, 64 * s + 64)

                        def values(gi):
                            for t in range(*gs[gi]):
                                kr = TILES2[t][1]
                                mm = pe.matmul(po[half, 0:rr], vs[s][0:kr, t, :], ET[0:kr, t, 0:rr], start=(t == 0), stop=(t == j))
                            return mm

                        for gi, (a0, a1) in enumerate(gs):
                            for t in range(a0, a1):
                                k0, kr = TILES2[t]
                                mm = pe.transpose(pT_[0:kr, t - a0, 0:te], E[b][0:te, k0:k0 + kr], g.ident[0:te, 0:te])
                            mm.then_inc(turned, 1)
                            if gi:
                                values(gi - 1)
                            pe.wait_ge(evac, i * per_round + groups_before(n) + gi + 1)
                        values(len(gs) - 1).then_inc(values_in, 1)


RW = 256
RW_HEADS = 4
TP = P * len(TILES2)
PADT = TP - T2
R_, K_, V_, KK_, LW_, A_, G_ = (2 * j for j in range(7))
GN_EPS = 64e-5


def delta_inputs(nc, a, g, pT, F):
    with Phase(nc, "di") as ph:
        p = ph.sb("p", [P, 8, 1 + T2])
        d = ph.sb("d", [P, T2])
        kx = ph.sb("kx", [P, 2, T2])
        mu = ph.sb("mu", [P, 8])
        vec = ph.sb("vec", [P, 5, 2])
        up = ph.sb("up", [P, RW])
        gup = ph.sb("gup", [P, RW])
        pw = ph.ps("pw", [P, 1536])
        pa = ph.ps("pa", [P, 1536])
        small, padded, shifted, lora, gated, w_made, a_made, g_made, w_sig, a_sig, g_copied, dstep = ph.sems(
            "small padded shifted lora gated w_made a_made g_made w_sig a_sig g_copied dstep")
        with nc.Block() as block:
            @block.sync
            def _(sp):
                sp.dma_start(p[:, :, 1:], pT[2056:3080, :].rearrange("(c p) t -> p c t", p=P)).then_inc(small, 16)
                with nc.allow_non_contiguous_dma(reason="short vectors, feature-major"):
                    sp.dma_start(mu[:, :], a["rwkv_mu_2"][0, :].rearrange("(c p) -> p c", p=P)).then_inc(small, 16)
                    for j, name in enumerate(("rwkv_w0_2", "rwkv_a0_2", "rwkv_k_k_2", "rwkv_k_a_2")):
                        sp.dma_start(vec[:, j, :], a[name][0, :].rearrange("(c p) -> p c", p=P)).then_inc(small, 16)
                sp.dma_start(up[0:64, :], a["rwkv_w_up_2"][0, :, :]).then_inc(small, 16)
                sp.dma_start(up[64:P, :], a["rwkv_a_up_2"][0, :, :]).then_inc(small, 16)
                sp.dma_start(gup[:, :], a["rwkv_g_up_2"][0, :, :]).then_inc(small, 16)

            @block.gpsimd
            def _(pool):
                pool.memset(F[:, :, 0:PADT], 0.0).then_inc(padded, 1)
                pool.memset(p[:, :, 0:1], 0.0).then_inc(padded, 1)

            @block.scalar
            def _(act):
                act.wait_ge(small, 16 * 9)
                act.wait_ge(shifted, 1)
                act.activation(p[0:64, 6, 1:], p[0:64, 6, 1:], ACT.Tanh).then_inc(lora, 1)
                act.wait_ge(shifted, 2)
                act.activation(p[:, 7, 1:], p[:, 7, 1:], ACT.Sigmoid).then_inc(gated, 1)
                for c in range(2):
                    act.wait_ge(w_made, c + 1)
                    act.activation(F[:, LW_ + c, PADT:], pw[:, 0:T2], ACT.Sigmoid, bias=vec[:, 0, c:c + 1]).then_inc(w_sig, 1)
                    act.wait_ge(a_made, c + 1)
                    act.activation(F[:, A_ + c, PADT:], pa[:, 0:T2], ACT.Sigmoid, bias=vec[:, 1, c:c + 1]).then_inc(a_sig, 1)
                for c in range(2):
                    act.wait_ge(g_made, c + 1)
                    act.activation(F[:, G_ + c, PADT:], (pw, pa)[c][:, 0:T2], ACT.Copy).then_inc(g_copied, 1)

            @block.vector
            def _(dve):
                ch = Chain(dve, dstep)
                dve.wait_ge(small, 16 * 9)
                dve.wait_ge(padded, 2)
                for c in (6, 7, 2, 3, 0, 1, 4, 5):
                    dst = {6: p[:, 6, 1:], 7: p[:, 7, 1:], 2: kx[:, 0, :], 3: kx[:, 1, :], 0: F[:, R_, PADT:],
                           1: F[:, R_ + 1, PADT:], 4: F[:, V_, PADT:], 5: F[:, V_ + 1, PADT:]}[c]
                    ch.link(dve.tensor_tensor(d[:, :], p[:, c, 0:T2], p[:, c, 1:], ALU.subtract))
                    ins = dve.scalar_tensor_tensor(dst, d[:, :], mu[:, c:c + 1], p[:, c, 1:], ALU.mult, ALU.add)
                    if c >= 6:
                        ins.then_inc(shifted, 1)
                        dve.wait_ge(shifted, c - 5)
                    else:
                        ch.link(ins)
                for c in range(2):
                    dve.tensor_scalar(F[:, KK_ + c, PADT:], kx[:, c, :], vec[:, 2, c:c + 1], None, ALU.mult)
                ch.link(dve.tensor_scalar(vec[:, 4, :], vec[:, 3, :], -1.0, 1.0, ALU.mult, ALU.add))
                for c in range(2):
                    dve.wait_ge(w_sig, c + 1)
                    dve.tensor_scalar(F[:, LW_ + c, PADT:], F[:, LW_ + c, PADT:], -(2.718281828459045 ** -0.5), None, ALU.mult)
                    dve.wait_ge(a_sig, c + 1)
                    ch.link(dve.tensor_scalar(d[:, :], F[:, A_ + c, PADT:], vec[:, 3, c:c + 1], vec[:, 4, c:c + 1], ALU.mult, ALU.add))
                    ch.link(dve.tensor_tensor(F[:, K_ + c, PADT:], kx[:, c, :], d[:, :], ALU.mult))

            @block.tensor
            def _(pe):
                pe.wait_ge(lora, 1)
                for c in range(2):
                    cols = slice(P * c, P * c + P)
                    if c:
                        pe.wait_ge(w_sig, c)
                    for c0, c1 in NCUT:
                        mm = pe.matmul(pw[:, c0:c1], up[0:64, cols], p[0:64, 6, 1 + c0:1 + c1], start=True, stop=True)
                    mm.then_inc(w_made, 1)
                    if c:
                        pe.wait_ge(a_sig, c)
                    for c0, c1 in NCUT:
                        mm = pe.matmul(pa[:, c0:c1], up[64:P, cols], p[64:P, 6, 1 + c0:1 + c1], start=True, stop=True)
                    mm.then_inc(a_made, 1)
                pe.wait_ge(gated, 1)
                for c in range(2):
                    pe.wait_ge((w_sig, a_sig)[c], 2)
                    for c0, c1 in NCUT:
                        mm = pe.matmul((pw, pa)[c][:, c0:c1], gup[:, P * c:P * c + P], p[:, 7, 1 + c0:1 + c1], start=True, stop=True)
                    mm.then_inc(g_made, 1)


def delta_rule(nc, a, g, F):
    NTP = len(TILES2)
    H = RW_HEADS
    with Phase(nc, "dr") as ph:
        masks = ph.sb("masks", [P, 2, P])
        levels = ph.sb("levels", [P, 6, P])
        chunk_of = ph.sb("chunk_of", [P, 2])
        rk_row = ph.sb("rk_row", [P, RW])
        lnw = ph.sb("lnw", [P, RW])
        lnb = ph.sb("lnb", [P, RW])
        gneps = ph.sb("gneps", [P, 1])
        Fc = ph.sb("Fc", [P, 14, P])
        T = ph.sb("T", [P, 7, RW])
        Vc = ph.sb("Vc", [P, 2, RW])
        Uc = ph.sb("Uc", [P, 2, RW])
        eb = ph.sb("eb", [P, 3, RW])
        dec = ph.sb("dec", [64, H, 2])
        sq = ph.sb("sq", [P, RW])
        n4 = ph.sb("n4", [P, 4])
        hat = ph.sb("hat", [P, 4, RW])
        hatT = ph.sb("hatT", [64, 4, H, P])
        AT = ph.sb("AT", [P, 4, H, P])
        Lm = ph.sb("Lm", [P, 2, H, P])
        X = ph.sb("X", [P, H, P])
        XT = ph.sb("XT", [P, H, P])
        Y = ph.sb("Y", [P, H, P])
        P1T = ph.sb("P1T", [64, H, P])
        W = ph.sb("W", [P, RW])
        P2 = ph.sb("P2", [P, RW])
        S = ph.sb("S", [64, RW])
        d = ph.sb("d", [P, RW])
        bo = ph.sb("bo", [P, RW])
        s4 = ph.sb("s4", [P, 4])
        v4 = ph.sb("v4", [P, 4])
        bsum = ph.sb("bsum", [P, 4])
        b = [ph.ps(f"b{j}", [P, 512]) for j in range(8)]
        (small, zeroed, copied, turned, ev_a, ev_d, cum, expd, sqd, rooted, hats, hat_t, hT_a, hT_d, att, masked,
         lvl, x0, x0_t, X_ev, y_made, y_ev, z_made, xs, pre, pre_a, pre_d, p2m, p2e, u_made, u_done, ds_made, s_done,
         bonus, o_made, osq, oroot, vsum, vroot, out_done, out_t, mixed, dstep) = ph.sems(
            "small zeroed copied turned ev_a ev_d cum expd sqd rooted hats hat_t hT_a hT_d att masked "
            "lvl x0 x0_t X_ev y_made y_ev z_made xs pre pre_a pre_d p2m p2e u_made u_done ds_made s_done "
            "bonus o_made osq oroot vsum vroot out_done out_t mixed dstep")

        def heads(ap):
            return ap.rearrange("p (h d) -> p h d", h=H)

        def wide(ap4, n=64):
            return ap4.unsqueeze(2).broadcast_to([P, 4, n])

        with nc.Block() as block:
            @block.sync
            def _(sp):
                sp.dma_start(masks[:, :, :], a["k_masks"][0:4:3, :, :].rearrange("m p k -> p m k")).then_inc(small, 16)
                sp.dma_start(levels[:, :, :], a["k_levels"].rearrange("m p k -> p m k")).then_inc(small, 16)
                sp.dma_start(chunk_of[:, :], a["k_chunk_of"]).then_inc(small, 16)
                sp.dma_start(rk_row[:, :], rows(a["rwkv_r_k_2"].rearrange("o h d -> (o h d)"))).then_inc(small, 16)
                sp.dma_start(lnw[:, :], rows(a["rwkv_ln_w_2"][0, :])).then_inc(small, 16)
                sp.dma_start(lnb[:, :], rows(a["rwkv_ln_b_2"][0, :])).then_inc(small, 16)

            @block.gpsimd
            def _(pool):
                pool.wait_ge(small, 16 * 6)
                for m, (cells, value) in enumerate(((Vc[:, :, :], 0.0), (Uc[:, :, :], 0.0), (S[:, :], 0.0), (gneps[:, :], GN_EPS))):
                    if m:
                        pool.wait_ge(zeroed, m)
                    pool.memset(cells, value).then_inc(zeroed, 1)
                pool.sem_inc(turned, 1)
                with pool.Fori(0, NTP, 1) as i:
                    pool.wait_ge(turned, i + 1)
                    pool.tensor_copy(Fc[:, :, :], F[:, :, bass.ds(i * P, P)]).then_inc(copied, 1)
                    pool.wait_ge(copied, i + 1)
                    pool.wait_ge(ev_a, i + 1)
                    pool.tensor_tensor(bo[:, :], T[:, 0, :], T[:, 1, :], ALU.mult).then_inc(bonus, 1)
                    pool.wait_ge(bonus, i * 2 + 1)
                    pool.tensor_tensor(bo[:, :], bo[:, :], rk_row[:, :], ALU.mult).then_inc(bonus, 1)
                    pool.wait_ge(bonus, i * 2 + 2)
                    pool.wait_ge(masked, i + 1)
                    for n in range(5):
                        if n >= 2:
                            pool.wait_ge(y_made, i * 5 + n - 1)
                            pool.wait_ge(lvl, i * 5 + n - 1)
                        pool.tensor_tensor(Lm[:, n % 2, :, :], AT[:, 0, :, :], levels[:, n + 1, :].unsqueeze(1).broadcast_to([P, H, P]),
                                           ALU.mult).then_inc(lvl, 1)
                    pool.wait_ge(lvl, i * 5 + 5)

            @block.scalar
            def _(act):
                act.wait_ge(zeroed, 4)
                with act.Fori(0, NTP, 1) as i:
                    act.wait_ge(turned, i + 2)
                    act.activation(T[:, 0:2, :], b[0][:, :], ACT.Copy)
                    act.activation(T[:, 2:4, :], b[1][:, :], ACT.Copy)
                    for c in range(2):
                        toks = slice(64 * c, 64 * c + 64)
                        ins = act.activation(Vc[toks, c, :], b[1][toks, 0:RW], ACT.Copy)
                    ins.then_inc(ev_a, 1)
                    act.wait_ge(sqd, i + 1)
                    act.activation(n4[:, :], n4[:, :], ACT.Sqrt).then_inc(rooted, 1)
                    act.wait_ge(cum, i + 1)
                    act.activation(eb[:, 0, :], b[4][:, 0:RW], ACT.Exp)
                    act.activation(eb[:, 1, :], b[4][:, 0:RW], ACT.Exp, scale=-1.0)
                    act.activation(eb[:, 2, :], b[4][:, RW:], ACT.Exp)
                    act.activation(dec[:, :, :], b[5][0:64, 0:8], ACT.Exp).then_inc(expd, 1)
                    act.wait_ge(hat_t, i + 1)
                    act.activation(hatT[:, 0, :, :], b[0][0:64, :], ACT.Copy)
                    act.activation(hatT[:, 1, :, :], b[1][0:64, :], ACT.Copy).then_inc(hT_a, 1)
                    act.wait_ge(x0_t, i + 1)
                    act.activation(X[:, :, :], b[4][:, :], ACT.Copy).then_inc(X_ev, 1)
                    for n in range(5):
                        act.wait_ge(y_made, i * 5 + n + 1)
                        act.activation(Y[:, :, :], b[5][:, :], ACT.Copy).then_inc(y_ev, 1)
                    act.wait_ge(pre, i + 1)
                    act.activation(P1T[:, :, :], b[0][0:64, :], ACT.Copy).then_inc(pre_a, 1)
                    act.wait_ge(p2m, i + 1)
                    act.activation(P2[:, :], b[2][:, 0:RW], ACT.Copy).then_inc(p2e, 1)
                    act.wait_ge(osq, i + 1)
                    act.activation(sq[:, :], d[:, :], ACT.Square).then_inc(oroot, 1)
                    act.wait_ge(vsum, i + 1)
                    act.activation(v4[:, :], v4[:, :], ACT.Sqrt, scale=1.0 / 64, bias=gneps[:, :]).then_inc(vroot, 1)
                    act.wait_ge(out_t, i + 1)
                    act.activation(g.hT[:, 6:8, bass.ds(i * P, P)], b[7][:, 0:RW].rearrange("p (c t) -> p c t", c=2), ACT.Copy).then_inc(mixed, 1)

            @block.vector
            def _(dve):
                dve.wait_ge(small, 16 * 6)
                dve.wait_ge(zeroed, 4)
                per = 18
                with dve.Fori(0, NTP, 1) as i:
                    ch = Chain(dve, dstep, i * per)
                    dve.wait_ge(turned, i + 2)
                    dve.tensor_copy(T[:, 4:6, :], b[2][:, :])
                    dve.tensor_copy(T[:, 6, :], b[3][:, 0:RW]).then_inc(ev_d, 1)
                    dve.wait_ge(ev_a, i + 1)
                    ch.link(dve.tensor_tensor(d[:, :], T[:, 3, :], T[:, 3, :], ALU.mult))
                    dve.tensor_reduce(n4[:, :], heads(d[:, :]), AX.X, ALU.add).then_inc(sqd, 1)
                    dve.wait_ge(rooted, i + 1)
                    ch.link(dve.tensor_scalar(n4[:, :], n4[:, :], 1e-12, None, ALU.max))
                    ch.link(dve.reciprocal(n4[:, :], n4[:, :]))
                    dve.wait_ge(ev_d, i + 1)
                    ch.link(dve.tensor_tensor(heads(T[:, 3, :]), heads(T[:, 3, :]), wide(n4[:, :]), ALU.mult))
                    ch.link(dve.scalar_tensor_tensor(d[:, :], T[:, 3, :], -1.0, T[:, 5, :], ALU.mult, ALU.mult))
                    dve.wait_ge(expd, i + 1)
                    dve.tensor_tensor(hat[:, 0, :], T[:, 3, :], eb[:, 2, :], ALU.mult)
                    dve.tensor_tensor(hat[:, 1, :], T[:, 0, :], eb[:, 0, :], ALU.mult)
                    dve.tensor_tensor(hat[:, 2, :], T[:, 1, :], eb[:, 1, :], ALU.mult)
                    dve.tensor_tensor(hat[:, 3, :], d[:, :], eb[:, 1, :], ALU.mult).then_inc(hats, 1)
                    dve.wait_ge(hat_t, i + 1)
                    dve.tensor_copy(hatT[:, 2, :, :], b[2][0:64, :])
                    dve.tensor_copy(hatT[:, 3, :, :], b[3][0:64, :]).then_inc(hT_d, 1)
                    dve.wait_ge(att, i + 1)
                    for j, m in enumerate((1, 1, 0, 0)):
                        ins = dve.tensor_tensor(AT[:, j, :, :], b[4 + j][:, :].rearrange("p (h t) -> p h t", h=H),
                                                masks[:, m, :].unsqueeze(1).broadcast_to([P, H, P]), ALU.mult)
                    ins.then_inc(masked, 1)
                    dve.wait_ge(masked, i + 1)
                    ch.link(dve.tensor_tensor(XT[:, :, :], AT[:, 0, :, :], levels[:, 0, :].unsqueeze(1).broadcast_to([P, H, P]), ALU.mult))
                    dve.tensor_tensor(XT[:, :, :], XT[:, :, :], g.ident[:, :].unsqueeze(1).broadcast_to([P, H, P]), ALU.add).then_inc(x0, 1)
                    for n in range(5):
                        dve.wait_ge(z_made, i * 5 + n + 1)
                        if n == 0:
                            dve.wait_ge(X_ev, i + 1)
                            dve.wait_ge(x0, i + 1)
                        else:
                            dve.wait_ge(xs, i * 5 + n)
                        if n < 4:
                            dve.tensor_tensor(X[:, :, :], X[:, :, :], b[6][:, :].rearrange("p (h t) -> p h t", h=H), ALU.add)
                        dve.tensor_tensor(XT[:, :, :], XT[:, :, :], b[7][:, :].rearrange("p (h t) -> p h t", h=H), ALU.add).then_inc(xs, 1)
                    dve.wait_ge(pre, i + 1)
                    dve.tensor_copy(W[:, :], b[1][:, 0:RW]).then_inc(pre_d, 1)
                    dve.wait_ge(p2e, i + 1)
                    for c in range(2):
                        toks = slice(64 * c, 64 * c + 64)
                        dve.wait_ge(u_made, i * 2 + c + 1)
                        dve.tensor_tensor(Uc[toks, c, :], b[3][toks, 0:RW], P2[toks, :], ALU.add).then_inc(u_done, 1)
                        dve.wait_ge(ds_made, i * 2 + c + 1)
                        ch.link(dve.tensor_tensor(S[:, :], S[:, :], b[5 + c][0:64, 0:RW], ALU.add))
                        dve.tensor_tensor(heads(S[:, :]), heads(S[:, :]), dec[:, :, c:c + 1].broadcast_to([64, H, 64]), ALU.mult).then_inc(s_done, 1)
                        dve.wait_ge(s_done, i * 2 + c + 1)
                    dve.wait_ge(o_made, i + 1)
                    o = heads(b[4][:, 0:RW])
                    ch.link(dve.tensor_reduce(s4[:, :], o, AX.X, ALU.add))
                    ch.link(dve.tensor_scalar(s4[:, :], s4[:, :], 1.0 / 64, None, ALU.mult))
                    dve.tensor_tensor(heads(d[:, :]), o, wide(s4[:, :]), ALU.subtract).then_inc(osq, 1)
                    dve.wait_ge(oroot, i + 1)
                    dve.tensor_reduce(v4[:, :], heads(sq[:, :]), AX.X, ALU.add).then_inc(vsum, 1)
                    dve.wait_ge(bonus, i * 2 + 2)
                    ch.link(dve.tensor_reduce(bsum[:, :], heads(bo[:, :]), AX.X, ALU.add))
                    ch.link(dve.tensor_tensor(heads(sq[:, :]), heads(T[:, 2, :]), wide(bsum[:, :]), ALU.mult))
                    dve.wait_ge(vroot, i + 1)
                    ch.link(dve.reciprocal(v4[:, :], v4[:, :]))
                    ch.link(dve.tensor_tensor(heads(d[:, :]), heads(d[:, :]), wide(v4[:, :]), ALU.mult))
                    ch.link(dve.tensor_tensor(d[:, :], d[:, :], lnw[:, :], ALU.mult))
                    ch.link(dve.tensor_tensor(d[:, :], d[:, :], lnb[:, :], ALU.add))
                    ch.link(dve.tensor_tensor(d[:, :], d[:, :], sq[:, :], ALU.add))
                    dve.tensor_tensor(d[:, :], d[:, :], T[:, 6, :], ALU.mult).then_inc(out_done, 1)
                    assert ch.k <= per, ch.k
                    for _ in range(per - ch.k):
                        dve.sem_inc(dstep, 1)

            @block.tensor
            def _(pe):
                pe.wait_ge(small, 16 * 6)
                pe.wait_ge(zeroed, 4)
                with pe.Fori(0, NTP, 1) as i:
                    pe.wait_ge(copied, i + 1)
                    for c in range(14):
                        mm = pe.transpose(b[c // 4][:, P * (c % 4):P * (c % 4) + P], Fc[:, c, :], g.ident[:, :])
                    mm.then_inc(turned, 1)
                    pe.wait_ge(ev_d, i + 1)
                    pe.matmul(b[4][:, 0:RW], masks[:, 0, :], T[:, 4, :], start=True, stop=True)
                    pe.matmul(b[4][:, RW:], masks[:, 1, :], T[:, 4, :], start=True, stop=True)
                    for h in range(H):
                        mm = pe.matmul(b[5][0:64, 2 * h:2 * h + 2], T[:, 4, 64 * h:64 * h + 64], chunk_of[:, :], start=True, stop=True)
                    mm.then_inc(cum, 1)
                    pe.wait_ge(hats, i + 1)
                    for j in range(4):
                        for h in range(H):
                            mm = pe.matmul(b[j][0:64, P * h:P * h + P], hat[:, j, 64 * h:64 * h + 64], g.ident[:, :],
                                           start=True, stop=True, is_transpose=(j + h > 0))
                    mm.then_inc(hat_t, 1)
                    pe.wait_ge(hT_a, i + 1)
                    pe.wait_ge(hT_d, i + 1)
                    for j, (l, r) in enumerate(((3, 0), (2, 0), (2, 1), (3, 1))):
                        for h in range(H):
                            mm = pe.matmul(b[4 + j][:, P * h:P * h + P], hatT[:, l, h, :], hatT[:, r, h, :], start=True, stop=True)
                    mm.then_inc(att, 1)
                    pe.wait_ge(x0, i + 1)
                    for h in range(H):
                        mm = pe.transpose(b[4][:, P * h:P * h + P], XT[:, h, :], g.ident[:, :])
                    mm.then_inc(x0_t, 1)
                    for n in range(5):
                        if n == 0:
                            pe.wait_ge(X_ev, i + 1)
                        else:
                            pe.wait_ge(xs, i * 5 + n)
                        pe.wait_ge(lvl, i * 5 + n + 1)
                        for h in range(H):
                            mm = pe.matmul(b[5][:, P * h:P * h + P], Lm[:, n % 2, h, :], X[:, h, :], start=True, stop=True)
                        mm.then_inc(y_made, 1)
                        pe.wait_ge(y_ev, i * 5 + n + 1)
                        if n < 4:
                            for h in range(H):
                                pe.matmul(b[6][:, P * h:P * h + P], XT[:, h, :], Y[:, h, :], start=True, stop=True)
                        for h in range(H):
                            mm = pe.matmul(b[7][:, P * h:P * h + P], Y[:, h, :], XT[:, h, :], start=True, stop=True)
                        mm.then_inc(z_made, 1)
                    pe.wait_ge(xs, i * 5 + 5)
                    for h in range(H):
                        pe.matmul(b[0][0:64, P * h:P * h + P], hat[:, 0, 64 * h:64 * h + 64], XT[:, h, :], start=True, stop=True)
                    for h in range(H):
                        mm = pe.matmul(b[1][:, 64 * h:64 * h + 64], AT[:, 1, h, :], T[:, 2, 64 * h:64 * h + 64], start=True, stop=True)
                    mm.then_inc(pre, 1)
                    for h in range(H):
                        pe.matmul(b[4][:, 64 * h:64 * h + 64], AT[:, 2, h, :], T[:, 2, 64 * h:64 * h + 64],
                                  start=(h == 0), stop=False, skip_group_check=True)
                    pe.wait_ge(pre_d, i + 1)
                    for h in range(H):
                        mm = pe.matmul(b[2][:, 64 * h:64 * h + 64], XT[:, h, :], W[:, 64 * h:64 * h + 64], start=True, stop=True)
                    mm.then_inc(p2m, 1)
                    pe.wait_ge(pre_a, i + 1)
                    for c in range(2):
                        toks = slice(64 * c, 64 * c + 64)
                        if c:
                            pe.wait_ge(s_done, i * 2 + c)
                        for h in range(H):
                            mm = pe.matmul(b[3][:, 64 * h:64 * h + 64], P1T[:, h, :], S[:, 64 * h:64 * h + 64], start=True, stop=True)
                        mm.then_inc(u_made, 1)
                        for h in range(H):
                            pe.matmul(b[4][toks, 64 * h:64 * h + 64], hatT[:, 1, h, toks], S[:, 64 * h:64 * h + 64],
                                      start=False, stop=False, skip_group_check=True)
                        for h in range(H):
                            pe.matmul(b[5 + c][0:64, 64 * h:64 * h + 64], hat[:, 2, 64 * h:64 * h + 64], Vc[:, c, 64 * h:64 * h + 64],
                                      start=(h == 0), stop=False, skip_group_check=True)
                        pe.wait_ge(u_done, i * 2 + c + 1)
                        for h in range(H):
                            mm = pe.matmul(b[5 + c][0:64, 64 * h:64 * h + 64], hat[:, 3, 64 * h:64 * h + 64], Uc[:, c, 64 * h:64 * h + 64],
                                           start=False, stop=True, skip_group_check=True)
                        mm.then_inc(ds_made, 1)
                        for h in range(H):
                            mm = pe.matmul(b[4][:, 64 * h:64 * h + 64], AT[:, 3, h, :], Uc[:, c, 64 * h:64 * h + 64],
                                           start=False, stop=(c == 1), skip_group_check=True)
                    mm.then_inc(o_made, 1)
                    pe.wait_ge(out_done, i + 1)
                    for c in range(2):
                        mm = pe.transpose(b[7][:, P * c:P * c + P], d[:, P * c:P * c + P], g.ident[:, :])
                    mm.then_inc(out_t, 1)
                    pe.wait_ge(mixed, i + 1)


def mix_out(nc, a, g):
    w_v = a["w_out_2"][0, :, :].rearrange("(k p) n -> p k n", p=P)
    with Phase(nc, "xo") as ph:
        w = ph.pair("w", [P, KD, D])
        raw = [ph.sb(f"raw{s}", [P, D]) for s in range(2)]
        gain = ph.sb("gain", [P, D])
        hc = [ph.pair(f"hc{s}", [P, KD, P]) for s in range(2)]
        sq = ph.sb("sq", [P, D])
        y = ph.sb("y", [P, D])
        ss = ph.sb("ss", [P, 2])
        po = [ph.ps(f"po{s}", [P, 1024]) for s in range(2)]
        small, raw0_in, raw1_in, w_hi, w_lo, placed, split, made, squared, rooted, recips, normed, added = ph.sems(
            "small raw0_in raw1_in w_hi w_lo placed split made squared rooted recips normed added")
        raw_in = [raw0_in, raw1_in]
        parts = [(1, META, 0, g.m), (NT, P, META, g.x)]

        with nc.Block() as block:
            @block.sync
            def _(sp):
                sp.dma_start(gain[:, :], rows(a["norm_mix_post_2"][0, :])).then_inc(small, 16)
                for k in range(KD):
                    if k >= 2:
                        sp.wait_ge(w_lo, k - 1)
                    sp.dma_start(raw[k % 2][:, :], w_v[:, k, :]).then_inc(raw_in[k % 2], 16)

            @block.gpsimd
            def _(pool):
                def place(n, s, part, t):
                    _, r, c0, _ = part
                    if not (isinstance(n, int) and n < 2):
                        pool.wait_ge(made, n - 1)
                    pool.tensor_copy(hc[s][0][:, 0:6, 0:r], g.hT[:, 0:6, bass.ds(t * P + c0, r)])
                    pool.tensor_copy(hc[s][0][:, 6:8, 0:r], g.hT[:, 6:8, bass.ds(t * P + (c0 + PADT), r)]).then_inc(placed, 1)
                in_turn(pool, parts, place, lambda *tile: None)

            @block.scalar
            def _(act):
                for k in range(KD):
                    act.wait_ge(raw_in[k % 2], k // 2 * 16 + 16)
                    act.activation(w[0][:, k, :], raw[k % 2][:, :], ACT.Copy).then_inc(w_hi, 1)

                def root(n, s, part, t):
                    r = part[1]
                    act.wait_ge(made, n + 1)
                    act.activation(sq[0:r, :], po[s][0:r, :], ACT.Square, accum_out=ss[0:r, s:s + 1]).then_inc(squared, 1)
                    act.wait_ge(squared, n + 1)
                    act.activation(ss[0:r, s:s + 1], ss[0:r, s:s + 1], ACT.Sqrt, scale=1.0 / D, bias=g.epsc[0:r, :]).then_inc(rooted, 1)
                in_turn(act, parts, root, lambda *tile: None)

            @block.vector
            def _(dve):
                for k in range(KD):
                    dve.wait_ge(w_hi, k + 1)
                    lo_part(dve, w[1][:, k, :], raw[k % 2][:, :], w[0][:, k, :]).then_inc(w_lo, 1)
                dve.wait_ge(small, 16)

                def low(n, s, part, t):
                    _, r, c0, _ = part
                    dve.wait_ge(placed, n + 1)
                    lo_part(dve, hc[s][1][:, 0:6, 0:r], g.hT[:, 0:6, bass.ds(t * P + c0, r)], hc[s][0][:, 0:6, 0:r])
                    lo_part(dve, hc[s][1][:, 6:8, 0:r], g.hT[:, 6:8, bass.ds(t * P + (c0 + PADT), r)],
                            hc[s][0][:, 6:8, 0:r]).then_inc(split, 1)

                def norm(n, s, part, t):
                    _, r, _, x = part
                    dve.wait_ge(rooted, n + 1)
                    dve.reciprocal(ss[0:r, s:s + 1], ss[0:r, s:s + 1]).then_inc(recips, 1)
                    dve.wait_ge(recips, n + 1)
                    dve.scalar_tensor_tensor(y[0:r, :], po[s][0:r, :], ss[0:r, s:s + 1], gain[0:r, :], ALU.mult, ALU.mult).then_inc(normed, 1)
                    dve.wait_ge(normed, n + 1)
                    dve.tensor_tensor(x[0:r, t, :], x[0:r, t, :], y[0:r, :], ALU.add).then_inc(added, 1)
                in_turn(dve, parts, low, norm)

            @block.tensor
            def _(pe):
                def multiply(n, s, part, t):
                    r = part[1]
                    pe.wait_ge(split, n + 1)
                    if not (isinstance(n, int) and n < 2):
                        pe.wait_ge(normed, n - 1)
                    for j in range(2):
                        cols = slice(512 * j, 512 * j + 512)
                        for k in range(KD):
                            if isinstance(n, int) and n == 0 and j == 0:
                                pe.wait_ge(w_lo, k + 1)
                            mm = product(pe, po[s][0:r, cols], [h[:, k, 0:r] for h in hc[s]],
                                         [h[:, k, cols] for h in w], k == 0, k == KD - 1)
                    mm.then_inc(made, 1)
                in_turn(pe, parts, multiply, lambda *tile: None)


NF = D_FF // P
CONV_F = 3


def ffn_up(nc, a, hT, fT):
    w_v = a["ffn_up_2"][0, :, :].rearrange("(k p) n -> p k n", p=P)
    with Phase(nc, "fu") as ph:
        w = Weights(ph, KD, P)
        cw = ph.sb("cw", [P, 2 * NF, CONV_F])
        f = [ph.sb(f"f{e}", [P, T2]) for e in range(2)]
        pf = [ph.ps(f"pf{e}", [P, 1536]) for e in range(2)]
        small, made0, made1, read0, read1, conv, gelued, dstep = ph.sems(
            "small made0 made1 read0 read1 conv gelued dstep")
        made, read = [made0, made1], [read0, read1]
        with nc.Block() as block:
            @block.sync
            def _(sp):
                def load(j, e):
                    w.load(sp, j * 2 + e, lambda k0, k1: w_v[:, k0:k1, bass.ds(j * P + D_FF * e, P)])
                load(0, 0)
                with nc.allow_non_contiguous_dma(reason="the taps, feature-major"):
                    for t in range(CONV_F):
                        sp.dma_start(cw[:, :, t], a["ffn_conv_2"][0, t, :].rearrange("(j p) -> p j", p=P)).then_inc(small, 16)
                load(0, 1)
                with sp.Fori(1, NF, 1) as j:
                    for e in range(2):
                        load(j, e)

            @block.scalar
            def _(act):
                w.make_hi(act, 0, 0)

                def step(j, e, first, last):
                    if not last:
                        if not first:
                            act.wait_ge(made[1 - e], j + e)
                        w.make_hi(act, j * 2 + e + 1, 1 - e)
                    if e == 1:
                        act.wait_ge(conv, j + 1)
                        act.activation(f[0][:, :], f[0][:, :], ACT.Gelu_apprx_tanh).then_inc(gelued, 1)
                in_pairs(act, 2 * NF, step)

            @block.vector
            def _(dve):
                w.make_lo(dve, 0, 0)
                dve.wait_ge(small, 16 * CONV_F)
                for e in range(2):
                    dve.sem_inc(read[e], 1)
                per = 5

                def step(j, e, first, last):
                    if not last:
                        w.make_lo(dve, j * 2 + e + 1, 1 - e)
                    ch = Chain(dve, dstep, j * per + 2 * e)
                    dve.wait_ge(made[e], j + 1)
                    taps = [cw[:, bass.ds(j + NF * e, 1), t].rearrange("p a -> p a") for t in range(CONV_F)]
                    ch.link(dve.tensor_scalar(f[e][:, :], pf[e][:, 0:T2], taps[2], None, ALU.mult))
                    ch.link(dve.scalar_tensor_tensor(f[e][:, 1:], pf[e][:, 0:T2 - 1], taps[1], f[e][:, 1:], ALU.mult, ALU.add))
                    dve.scalar_tensor_tensor(f[e][:, 2:], pf[e][:, 0:T2 - 2], taps[0], f[e][:, 2:], ALU.mult, ALU.add).then_inc(read[e], 1)
                    dve.wait_ge(read[e], j + 2)
                    if e == 0:
                        dve.sem_inc(conv, 1)
                    else:
                        dve.wait_ge(gelued, j + 1)
                        ch.link(dve.tensor_tensor(fT[:, bass.ds(j, 1), :].rearrange("p a t -> p (a t)"), f[0][:, :], f[1][:, :], ALU.mult))
                in_pairs(dve, 2 * NF, step)

            @block.tensor
            def _(pe):
                with pe.Fori(0, NF, 1) as j:
                    for e in range(2):
                        w.ready(pe, j * 2 + e)
                        pe.wait_ge(read[e], j + 1)
                        for c0, c1 in NCUT:
                            for k in range(KD):
                                mm = product(pe, pf[e][:, c0:c1], w.cut(e, k, 0, P), [h[:, k, c0:c1] for h in hT],
                                             k == 0, k == KD - 1)
                        mm.then_inc(made[e], 1)


def ffn_down(nc, a, g, fT, x_dram, out):
    HALF = SEQ // 2
    HT = HALF // P
    w_v = a["ffn_down_2"][0, :, :].rearrange("(k p) n -> p k n", p=P)
    x_v = x_dram.rearrange("(t p) d -> t p d", p=P)
    out_v = out.rearrange("o (t p) d -> (o t) p d", p=P)
    with Phase(nc, "fd") as ph:
        raw = [ph.sb(f"raw{s}", [P, D]) for s in range(2)]
        w = [ph.pair(f"w{s}", [P, D]) for s in range(2)]
        fs = [ph.pair(f"fs{s}", [P, HALF]) for s in range(2)]
        gain = ph.sb("gain", [P, D])
        x = [ph.sb(f"x{t}", [P, D]) for t in range(HT)]
        y = [ph.sb(f"y{t}", [P, D]) for t in range(HT)]
        sq = ph.sb("sq", [P, D])
        ss = ph.sb("ss", [P, HT])
        po = [ph.ps(f"po{t}", [P, D]) for t in range(HT)]
        small, raw0_in, raw1_in, hi_done, lo_done, used, made, taken_a, taken_d, squared, rooted, recips, normed, added = ph.sems(
            "small raw0_in raw1_in hi_done lo_done used made taken_a taken_d squared rooted recips normed added")
        x_in, out_done = ph.sems("x_in out_done")
        raw_in = [raw0_in, raw1_in]

        def chunks(eng, half, step, between=None):
            n0 = NF * half
            for s in range(2):
                step(n0 + s, s, s, s == 0, False)
            if between:
                between()
            with eng.Fori(1, NF // 2 - 1, 1) as i:
                for s in range(2):
                    step(i * 2 + (n0 + s), s, i * 2 + s, False, False)
            for s in range(2):
                step(n0 + NF - 2 + s, s, NF - 2 + s, False, s == 1)

        with nc.Block() as block:
            @block.sync
            def _(sp):
                sp.dma_start(gain[:, :], rows(a["norm_ffn_post_2"][0, :])).then_inc(small, 16)
                for half in range(2):
                    def load(n, s, k, first, last):
                        if not (isinstance(n, int) and n < 2):
                            sp.wait_ge(lo_done, n - 1)
                        src = w_v[:, bass.ds(k, 1), :].rearrange("p a n -> p (a n)")
                        sp.dma_start(raw[s][:, :], src).then_inc(raw_in[s], 16)
                    chunks(sp, half, load)

            @block.gpsimd
            def _(pool):
                for half in range(2):
                    for t in range(HT):
                        if half:
                            pool.wait_ge(out_done, 16 * HT)
                        pool.dma_start(x[t][:, :], x_v[HT * half + t, :, :]).then_inc(x_in, 16)
                    pool.wait_ge(x_in, 16 * HT * (half + 1))
                    for t in range(HT):
                        m = HT * half + t
                        pool.wait_ge(normed, m + 1)
                        pool.tensor_tensor(x[t][:, :], x[t][:, :], y[t][:, :], ALU.add).then_inc(added, 1)
                        pool.wait_ge(added, m + 1)
                        pool.dma_start(out_v[m, :, :], x[t][:, :]).then_inc(out_done, 16)
                pool.wait_ge(out_done, 32 * HT)

            @block.scalar
            def _(act):
                def high(n, s, k, first, last):
                    act.wait_ge(raw_in[s], (n - s) * 8 + 16)
                    if not (isinstance(n, int) and n < 2):
                        act.wait_ge(used, n - 1)
                    act.activation(w[s][0][:, :], raw[s][:, :], ACT.Copy)
                    act.activation(fs[s][0][:, :], fT[:, bass.ds(k, 1), META + HALF * half:META + HALF * half + HALF].rearrange("p a t -> p (a t)"),
                                   ACT.Copy).then_inc(hi_done, 1)

                def finish(half):
                    for t in range(HT):
                        m = HT * half + t
                        act.wait_ge(taken_d, (HT // 2) * half + t // 2 + 1) if t % 2 else act.wait_ge(taken_a, (HT // 2) * half + t // 2 + 1)
                        act.activation(sq[:, :], y[t][:, :], ACT.Square, accum_out=ss[:, t:t + 1]).then_inc(squared, 1)
                        act.wait_ge(squared, m + 1)
                        act.activation(ss[:, t:t + 1], ss[:, t:t + 1], ACT.Sqrt, scale=1.0 / D, bias=g.epsc[:, :]).then_inc(rooted, 1)

                for half in range(2):
                    chunks(act, half, high, (lambda: finish(0)) if half else None)
                    act.wait_ge(made, half + 1)
                    for t in range(0, HT, 2):
                        if half:
                            act.wait_ge(normed, HT)
                            act.wait_ge(added, HT)
                        act.activation(y[t][:, :], po[t][:, :], ACT.Copy).then_inc(taken_a, 1)
                finish(1)

            @block.vector
            def _(dve):
                def low(n, s, k, first, last):
                    dve.wait_ge(hi_done, n + 1)
                    lo_part(dve, w[s][1][:, :], raw[s][:, :], w[s][0][:, :])
                    lo_part(dve, fs[s][1][:, :], fT[:, bass.ds(k, 1), META + HALF * half:META + HALF * half + HALF].rearrange("p a t -> p (a t)"),
                            fs[s][0][:, :]).then_inc(lo_done, 1)

                def finish(half):
                    for t in range(HT):
                        m = HT * half + t
                        dve.wait_ge(rooted, m + 1)
                        dve.reciprocal(ss[:, t:t + 1], ss[:, t:t + 1]).then_inc(recips, 1)
                        dve.wait_ge(recips, m + 1)
                        dve.scalar_tensor_tensor(y[t][:, :], y[t][:, :], ss[:, t:t + 1], gain[:, :], ALU.mult, ALU.mult).then_inc(normed, 1)

                dve.wait_ge(small, 16)
                for half in range(2):
                    chunks(dve, half, low, (lambda: finish(0)) if half else None)
                    dve.wait_ge(made, half + 1)
                    for t in range(1, HT, 2):
                        if half:
                            dve.wait_ge(added, HT)
                        dve.tensor_copy(y[t][:, :], po[t][:, :]).then_inc(taken_d, 1)
                finish(1)

            @block.tensor
            def _(pe):
                for half in range(2):
                    def multiply(n, s, k, first, last):
                        pe.wait_ge(lo_done, n + 1)
                        for t in range(HT):
                            if half and first:
                                pe.wait_ge(taken_d if t % 2 else taken_a, t // 2 + 1)
                            for j in range(2):
                                cols = slice(512 * j, 512 * j + 512)
                                mm = product(pe, po[t][:, cols], [h[:, P * t:P * t + P] for h in fs[s]],
                                             [h[:, cols] for h in w[s]], first, last)
                        mm.then_inc(used, 1)
                        if last:
                            pe.wait_ge(used, n + 1)
                            pe.sem_inc(made, 1)
                    chunks(pe, half, multiply)


class Held:
    pass


def program(nc, a, out, scratch, stop=99):
    g = Held()
    with ExitStack() as ctx:
        def sb(name, shape, within=ctx, side=None):
            return within.enter_context(nc.sbuf_tensor(name, shape, F32, side=side))

        g.ident = sb("ident", [P, P])
        g.epsc = sb("epsc", [P, 1])
        g.neglam = sb("neglam", [P, 1])
        g.mod_dram = scratch("mod_d", (2, 2, 3, D))
        x_spill = scratch("x_spill", (SEQ, D))
        modulation(nc, a, g)
        resident = ExitStack()
        g.x = sb("x", [P, NT, D], resident, "right")
        first = ExitStack()
        g.c = sb("c", [P, NC, D], first, "right")
        tiles1 = [(P * t, P) for t in range(NT + NC)]

        def parts1(layer):
            return [(n, x, P, c0, g.mod_dram[cond, layer, 1, :], g.mod_dram[cond, layer, 0, :], cond)
                    for cond, (n, x, c0) in enumerate(((NT, g.x, 0), (NC, g.c, SEQ)))]

        p0 = scratch("p0", (ALLT, EVEN_IN))
        o0 = scratch("o0", (ALLT, D))
        p1 = scratch("p1", (ALLT, ODD_IN))
        with ExitStack() as inner:
            hT = pair(nc, inner, "h0", [P, KD, ALLT])
            norm_turn(nc, g, "n0", hT, parts1(0), [(g.x[:, :, :], a["x"].rearrange("o (t p) d -> p (o t) d", p=P)),
                                                   (g.c[:, :, :], a["ctx"].rearrange("o (t p) d -> p (o t) d", p=P))])
            project_rows(nc, hT, "p0", tiles1, a["ab_w_in"][0, :, :], 416, 8, p0)
        if stop <= 0:
            return
        with ExitStack() as inner:
            g.hT = sb("qT", [P, KD, ALLT], inner)
            KB = sb("KB", [P, 4, ALLT], inner)
            KA = sb("KA", [P, 2, P + ALLT], inner)
            va = sb("va", [P, 1 + NT + NC, P], inner)
            vb = sb("vb", [P, NT + NC, 512], inner)
            rotate_heads(nc, a, g, p0, KB, KA, va, vb)
            window_attention(nc, a, g, KA, va, o0)
            differential_attention(nc, a, g, KB, vb, o0)
        with ExitStack() as inner:
            hT = pair(nc, inner, "h1", [P, KD, ALLT])
            merge_even(nc, a, g, hT, p0, o0)
            project_out(nc, g, "w0", hT, [(g.x, NT, 0, g.mod_dram[0, 0, 2, :]), (g.c, NC, SEQ, g.mod_dram[1, 0, 2, :])],
                        a["w_out"][0, :, :])
            norm_turn(nc, g, "n1", hT, parts1(1))
            project_rows(nc, hT, "p1", tiles1, a["gla_w_in"][0, :, :], ODD_IN // 8, 8, p1)
        if stop <= 1:
            return
        first.close()
        with ExitStack() as inner:
            O = sb("O", [P, NT, GV], inner)
            with ExitStack() as scan:
                la = sb("la", [P, NT + NC, 2 * GK], scan)
                dec = sb("dec", [P, NT + NC, 16], scan)
                log_decays(nc, a, g, p1, la, dec)
                linear_attention(nc, a, g, p1, la, dec, O)
            hT = pair(nc, inner, "h2", [P, KD, SEQ])
            merge_odd(nc, a, g, hT, p1, O)
            project_out(nc, g, "w1", hT, [(g.x, NT, 0, g.mod_dram[0, 1, 2, :])], a["w_out"][1, :, :])
        if stop <= 2:
            return
        pT = scratch("pT", (D_IN2, T2))
        pv = scratch("pv", (T2, 512))
        cum = scratch("cum", (2, FOX_HEADS, T2))
        g.m = sb("m", [META, 1, D], resident, "right")
        w2 = a["w_in_2"][0, :, :]

        def parts2(name):
            return [(1, g.m, META, 0, a[name][0, :], None, 0), (NT, g.x, P, META, a[name][0, :], None, 0)]

        with ExitStack() as inner:
            hT = pair(nc, inner, "h3", [P, KD, T2])
            norm_turn(nc, g, "n2", hT, parts2("norm_mix_pre_2"), [(g.m[:, 0, :], a["meta_tokens_2"])])
            project_cols(nc, hT, "ca", w2, 0, 6, pT, (2048, 8, pT[2048:2056, :]))
            project_cols(nc, hT, "cc", w2, 2056, 4, pT[2056:3080, :])
            project_rows(nc, hT, "cv", TILES2, w2[:, 1536:2048], 256, 2, pv)
        with ExitStack() as inner:
            g.hT = sb("mixT", [P, KD, ALLT], inner)
            linear_recurrence(nc, a, g, pT)
            forget_sums(nc, a, g, pT[2048:2056, :], cum)
            forgetting_attention(nc, a, g, pT, pv, cum)
            if stop <= 3:
                return
            with ExitStack() as delta:
                F = sb("F", [P, 14, TP], delta)
                delta_inputs(nc, a, g, pT, F)
                delta_rule(nc, a, g, F)
            mix_out(nc, a, g)
        with ExitStack() as inner:
            fT = sb("fT", [P, NF, T2], inner)
            with ExitStack() as up:
                hT = pair(nc, up, "h4", [P, KD, T2])
                norm_turn(nc, g, "n3", hT, parts2("norm_ffn_pre_2"),
                          spill=(x_spill.rearrange("(t p) d -> p t d", p=P), g.x[:, :, :]))
                resident.close()
                ffn_up(nc, a, hT, fT)
            ffn_down(nc, a, g, fT, x_spill, out)


DEBUG = False
STOP = 99


def shape_constants():
    import numpy as np

    grid_w, m = 64, 16
    inv = 10000.0 ** (-np.arange(m, dtype=np.float32) / m)
    rope = np.zeros((2, ALLT, HD), np.float32)
    rope[0] = 1.0
    pos = np.arange(SEQ)
    for half, p in enumerate((pos // grid_w, pos % grid_w)):
        ang = p.astype(np.float32)[:, None] * inv[None, :].astype(np.float32)
        for quarter, sign in ((0, -1.0), (1, 1.0)):
            cols = slice(32 * half + 16 * quarter, 32 * half + 16 * quarter + 16)
            rope[0, :SEQ, cols] = np.cos(ang)
            rope[1, :SEQ, cols] = sign * np.sin(ang)
    q, k = np.arange(P)[:, None], np.arange(3 * P)[None, :] - P
    near = np.abs(q - k) <= P
    window = np.zeros((NT, P, 3 * P), np.float32)
    for t in range(NT):
        inside = (t * P + k >= 0) & (t * P + k < SEQ)
        window[t] = np.where(near & inside, 0.0, NEG)
    i, j = np.arange(P)[:, None], np.arange(P)[None, :]
    same = i // 64 == j // 64
    masks = np.stack([same & (i <= j), same & (i >= j), same, same & (i < j), same & (i > j)]).astype(np.float32)
    levels = np.zeros((6, P, P), np.float32)
    for n in range(6):
        b = 1 << n
        levels[n] = (i // (2 * b) == j // (2 * b)) & ((j // b) % 2 == 1) & ((i // b) % 2 == 0)
    causal = np.where(j <= i, 0.0, NEG).astype(np.float32)
    chunk_of = (np.arange(P)[:, None] // 64 == np.arange(2)[None, :]).astype(np.float32)
    return {"k_rope": rope, "k_window": window, "k_masks": masks, "k_levels": levels, "k_causal": causal,
            "k_chunk_of": chunk_of}


def kernel(**inputs):
    import numpy as np
    import concourse.bacc as bacc
    from concourse.bass_utils import run_bass_kernel_spmd as run

    nc = bacc.Bacc("TRN2", target_bir_lowering=False, num_devices=1)
    arrays, args = {}, {}
    unused = ("rwkv_v0_2", "rwkv_v_down_2", "rwkv_v_up_2")
    for name, value in {**inputs, **shape_constants()}.items():
        if name in unused:
            continue
        v = np.ascontiguousarray(value)
        arrays["in_" + name] = v
        args[name] = nc.dram_tensor("in_" + name, v.shape, mybir.dt.from_np(v.dtype), kind="ExternalInput").ap()
    out = nc.dram_tensor("out_0", (1, SEQ, D), F32, kind="ExternalOutput").ap()

    def scratch(name, shape):
        if DEBUG:
            return nc.dram_tensor("out_" + name, shape, F32, kind="ExternalOutput").ap()
        return nc.dram_tensor(name, shape, F32).ap()

    program(nc, args, out, scratch, STOP)
    r = run(nc, [arrays], core_ids=[0])
    return r.results[0]["out_0"]
```

```python
from contextlib import ExitStack

import concourse.bass as bass
from concourse import mybir

ALU = mybir.AluOpType
ACT = mybir.ActivationFunctionType
F32 = mybir.dt.float32
F32R = mybir.dt.float32r
AX = mybir.AxisListType

P = 128
D = 1024
KD = D // P
SEQ = 1024
CTX = 256
NT = SEQ // P
NC = CTX // P
ALLT = SEQ + CTX
EPS = 1e-6
NEG = -1e30
HD = 64

A_HEADS = 8
B_HEADS = 4
EVEN_IN = 3328
ODD_IN = 3104
LAMBDA_INIT = 0.8 - 0.6

META = 16
T2 = META + SEQ
D_FF = 2816
D_IN2 = 3080
TILES2 = [(0, META)] + [(META + P * t, P) for t in range(NT)]


class Chain:

    def __init__(self, eng, sem, start=0):
        self.eng, self.sem, self.base, self.k = eng, sem, start, 0

    def step(self, ins):
        ins.then_inc(self.sem, 1)
        self.k += 1

    def settle(self):
        self.eng.wait_ge(self.sem, self.base + self.k)

    def link(self, ins):
        self.step(ins)
        self.settle()


class Phase:

    def __init__(self, nc, tag):
        self.nc, self.tag, self.ctx, self.held = nc, tag, ExitStack(), []

    def __enter__(self):
        return self

    def __exit__(self, *what):
        self.ctx.close()
        self.nc.clear_and_free_semaphores(self.held)
        self.nc.all_engine_barrier()

    def sb(self, name, shape, dt=F32):
        return self.ctx.enter_context(self.nc.sbuf_tensor(f"{self.tag}_{name}", shape, dt))

    def pair(self, name, shape):
        return pair(self.nc, self.ctx, f"{self.tag}_{name}", shape)

    def ps(self, name, shape):
        return self.ctx.enter_context(self.nc.psum_tensor(f"{self.tag}_{name}", shape, F32))

    def sem(self, name):
        self.held.append(self.nc.alloc_semaphore(f"{self.tag}_{name}"))
        return self.held[-1]

    def sems(self, names):
        return [self.sem(n) for n in names.split()]


def rows(ap, n=P):
    return ap.partition_broadcast(n)


def pair(nc, ctx, name, shape):
    return [ctx.enter_context(nc.sbuf_tensor(f"{name}_{part}", shape, F32R)) for part in ("hi", "lo")]


def lo_part(eng, lo, x, hi):
    return eng.tensor_tensor(lo, x, hi.bitcast(F32), ALU.subtract)


def product(pe, out, left, right, start, stop):
    pe.matmul(out, left[0], right[0], start=start, stop=False)
    pe.matmul(out, left[0], right[1], start=False, stop=False)
    return pe.matmul(out, left[1], right[0], start=False, stop=stop)


class Weights:

    def __init__(self, ph, kd, blk):
        self.half = kd // 2
        self.raw = [ph.sb(f"raw{h}", [P, self.half, blk]) for h in range(2)]
        self.slots = [ph.pair(f"w{s}", [P, kd, blk]) for s in range(2)]
        self.raw_in = ph.sems("raw_in0 raw_in1")
        self.hi_done = ph.sems("hi_done0 hi_done1")
        self.lo_done = ph.sems("lo_done0 lo_done1")

    def load(self, eng, b, src):
        for h in range(2):
            if not (isinstance(b, int) and b == 0):
                eng.wait_ge(self.lo_done[h], b)
            eng.dma_start(self.raw[h][:, :, :], src(self.half * h, self.half * h + self.half)).then_inc(self.raw_in[h], 16)

    def make_hi(self, eng, b, s):
        for h in range(2):
            eng.wait_ge(self.raw_in[h], b * 16 + 16)
            eng.activation(self.slots[s][0][:, self.half * h:self.half * h + self.half, :], self.raw[h][:, :, :],
                           ACT.Copy).then_inc(self.hi_done[h], 1)

    def make_lo(self, eng, b, s):
        for h in range(2):
            ks = slice(self.half * h, self.half * h + self.half)
            eng.wait_ge(self.hi_done[h], b + 1)
            lo_part(eng, self.slots[s][1][:, ks, :], self.raw[h][:, :, :],
                    self.slots[s][0][:, ks, :]).then_inc(self.lo_done[h], 1)

    def ready(self, pe, b):
        for h in range(2):
            pe.wait_ge(self.lo_done[h], b + 1)

    def cut(self, s, k, c0, c1):
        return [w[:, k, c0:c1] for w in self.slots[s]]


def in_pairs(eng, n, step):
    for s in range(2):
        step(0, s, s == 0, n == 2 and s == 1)
    if n > 4:
        with eng.Fori(1, n // 2 - 1, 1) as i:
            for s in range(2):
                step(i, s, False, False)
    if n > 2:
        for s in range(2):
            step(n // 2 - 1, s, False, s == 1)


def in_turn(eng, parts, ahead, behind):
    at, last = 0, None
    for part in parts:
        count = part[0]
        for t in range(min(count, 2)):
            now = (at + t, (at + t) % 2, part, t)
            ahead(*now)
            if last:
                behind(*last)
            last = now
        if count > 2:
            with eng.Fori(1, count // 2, 1) as i:
                for s in range(2):
                    t = i * 2 + s
                    ahead(t + at, (at + s) % 2, part, t)
                    behind(t + (at - 1), (at + s + 1) % 2, part, t - 1)
            last = (at + count - 1, (at + count - 1) % 2, part, count - 1)
        at += count
    behind(*last)


def modulation(nc, a, g):
    BLK = 512
    NB = 6 * D // BLK
    RING = 4
    w_v = a["adaln_w"].rearrange("l (k p) (b n) -> p k l b n", p=P, n=BLK)
    with Phase(nc, "mod") as ph:
        w = [ph.sb(f"w{s}", [P, KD, BLK]) for s in range(RING)]
        cond = ph.sb("cond", [P, 2, KD])
        act_c = ph.sb("act_c", [P, KD, 2])
        bias = ph.sb("bias", [2, 2, 3, D])
        gain = ph.sb("gain", [2, 2, D])
        mod = ph.sb("mod", [2, 2, 3, D])
        lam = ph.sb("lam", [P, 4, HD])
        lprod = ph.sb("lprod", [P, 2, HD])
        lsum = ph.sb("lsum", [P, 2])
        lexp = ph.sb("lexp", [P, 2])
        pm = [ph.ps(f"pm{s}", [P, BLK]) for s in range(RING)]
        small, zeroed, silu_ready, made, added, mod_ready, g_out, lam_p, lam_e, dstep = ph.sems(
            "small zeroed silu_ready made added mod_ready g_out lam_p lam_e dstep")
        w_in = ph.sems("w_in0 w_in1 w_in2 w_in3")
        with nc.Block() as block:
            def load(eng, mine):
                for b in range(NB):
                    if b % 2 == mine:
                        if b >= RING:
                            eng.wait_ge(made, b - RING + 1)
                        eng.dma_start(w[b % RING][:, :, :], w_v[:, :, b // 6, b % 6, :]).then_inc(w_in[b % RING], 16)

            @block.sync
            def _(sp):
                with nc.allow_non_contiguous_dma(reason="short vectors, feature-major"):
                    sp.dma_start(cond[:, 0, :], a["c"].rearrange("o (k p) -> p (o k)", p=P)).then_inc(small, 16)
                    sp.dma_start(cond[:, 1, :], a["c_ctx"].rearrange("(k p) -> p k", p=P)).then_inc(small, 16)
                sp.dma_start(bias[:, :, :, :].rearrange("c l j d -> c (l j d)"),
                             a["adaln_b"].rearrange("l n -> (l n)").partition_broadcast(2)).then_inc(small, 16)
                sp.dma_start(gain[:, :, :].rearrange("c l d -> c (l d)"),
                             a["norm_g"].rearrange("l d -> (l d)").partition_broadcast(2)).then_inc(small, 16)
                for j, name in enumerate(("b_lambda_q1", "b_lambda_k1", "b_lambda_q2", "b_lambda_k2")):
                    sp.dma_start(lam[:, j, :], rows(a[name][0, :])).then_inc(small, 16)
                load(sp, 0)
                sp.wait_ge(mod_ready, 1)
                sp.dma_start(g.mod_dram.rearrange("c l j d -> c (l j d)"),
                             mod[:, :, :, :].rearrange("c l j d -> c (l j d)")).then_inc(g_out, 16)
                sp.wait_ge(g_out, 16)

            @block.gpsimd
            def _(pool):
                pool.memset(g.ident[:, :], 0.0).then_inc(zeroed, 1)
                pool.wait_ge(zeroed, 1)
                pool.affine_select(out=g.ident[:, :], in_=g.ident[:, :], compare_op=ALU.not_equal, fill=1.0, base=0,
                                   pattern=[[-1, P]], channel_multiplier=1)

            @block.scalar
            def _(act):
                act.wait_ge(small, 16 * 8)
                act.activation(act_c[:, :, :].rearrange("p k c -> p c k"), cond[:, :, :], ACT.Silu).then_inc(silu_ready, 1)
                load(act, 1)
                act.wait_ge(lam_p, 1)
                act.activation(lexp[:, :], lsum[:, :], ACT.Exp).then_inc(lam_e, 1)

            @block.vector
            def _(dve):
                ch = Chain(dve, dstep)
                ch.link(dve.memset(g.epsc[:, :], EPS))
                dve.wait_ge(small, 16 * 8)
                ch.step(dve.tensor_tensor(lprod[:, 0, :], lam[:, 0, :], lam[:, 1, :], ALU.mult))
                ch.link(dve.tensor_tensor(lprod[:, 1, :], lam[:, 2, :], lam[:, 3, :], ALU.mult))
                dve.tensor_reduce(lsum[:, :], lprod[:, :, :], AX.X, ALU.add).then_inc(lam_p, 1)
                flat = [t[:, :, :, :].rearrange("c l j d -> c (l j d)") for t in (mod, bias)]
                for b in range(NB):
                    cols = slice(b * BLK, b * BLK + BLK)
                    dve.wait_ge(made, b + 1)
                    dve.tensor_tensor(flat[0][:, cols], pm[b % RING][0:2, :], flat[1][:, cols], ALU.add).then_inc(added, 1)
                dve.wait_ge(added, NB)
                dve.scalar_tensor_tensor(mod[:, :, 1, :], mod[:, :, 1, :], 1.0, gain[:, :, :], ALU.add, ALU.mult).then_inc(mod_ready, 1)
                dve.wait_ge(lam_e, 1)
                ch.link(dve.tensor_tensor(g.neglam[:, :], lexp[:, 1:2], lexp[:, 0:1], ALU.subtract))
                ch.step(dve.tensor_scalar(g.neglam[:, :], g.neglam[:, :], -LAMBDA_INIT, None, ALU.add))

            @block.tensor
            def _(pe):
                pe.wait_ge(silu_ready, 1)
                for b in range(NB):
                    pe.wait_ge(w_in[b % RING], (b // RING) * 16 + 16)
                    if b >= RING:
                        pe.wait_ge(added, b - RING + 1)
                    for k in range(KD):
                        mm = pe.matmul(pm[b % RING][0:2, :], act_c[:, k, :], w[b % RING][:, k, :],
                                       start=(k == 0), stop=(k == KD - 1))
                    mm.then_inc(made, 1)


def norm_turn(nc, g, tag, hT, parts, load=(), spill=None):
    with Phase(nc, tag) as ph:
        affine = {}
        for part in parts:
            if part[6] not in affine:
                affine[part[6]] = [(ph.sb(f"{name}{part[6]}", [P, D]), src)
                                   for name, src in zip(("gain", "shift"), part[4:6]) if src is not None]
        fetched = [(dst[:, :], rows(src)) for both in affine.values() for dst, src in both]
        shifted = parts[0][5] is not None
        sq = ph.sb("sq", [P, D])
        xn = [ph.sb(f"xn{s}", [P, D]) for s in range(2)]
        ss = ph.sb("ss", [P, 2])
        rs = ph.sb("rs", [P, 2])
        pt = [ph.ps(f"pt{s}", [P, KD, P]) for s in range(2)]
        loaded, squared, rooted, recip, normed, scaled, turned, hi_done, lo_done, spilled = ph.sems(
            "loaded squared rooted recip normed scaled turned hi_done lo_done spilled")
        if not shifted:
            scaled = normed
        with nc.Block() as block:
            n_load = 16 * (len(load) + len(fetched))

            @block.sync
            def _(sp):
                for dst, src in list(load) + fetched:
                    sp.dma_start(dst, src).then_inc(loaded, 16)
                if spill:
                    sp.dma_start(spill[0], spill[1]).then_inc(spilled, 16)
                    sp.wait_ge(spilled, 16)

            @block.scalar
            def _(act):
                act.wait_ge(loaded, n_load)

                def root(n, s, part, t):
                    x, r = part[1], part[2]
                    act.activation(sq[0:r, :], x[0:r, t, :], ACT.Square, accum_out=ss[0:r, s:s + 1]).then_inc(squared, 1)
                    act.wait_ge(squared, n + 1)
                    act.activation(ss[0:r, s:s + 1], ss[0:r, s:s + 1], ACT.Sqrt, scale=1.0 / D, bias=g.epsc[0:r, :]).then_inc(rooted, 1)

                def high(n, s, part, t):
                    r, c0 = part[2], part[3]
                    act.wait_ge(turned, n + 1)
                    act.activation(hT[0][:, :, bass.ds(c0 + t * P, r)], pt[s][:, :, 0:r], ACT.Copy).then_inc(hi_done, 1)
                in_turn(act, parts, root, high)

            @block.vector
            def _(dve):
                dve.wait_ge(loaded, n_load)

                def norm(n, s, part, t):
                    x, r = part[1], part[2]
                    dve.wait_ge(rooted, n + 1)
                    dve.reciprocal(rs[0:r, s:s + 1], ss[0:r, s:s + 1]).then_inc(recip, 1)
                    dve.wait_ge(recip, n + 1)
                    dve.scalar_tensor_tensor(xn[s][0:r, :], x[0:r, t, :], rs[0:r, s:s + 1], affine[part[6]][0][0][0:r, :],
                                             ALU.mult, ALU.mult).then_inc(normed, 1)

                def low(n, s, part, t):
                    r, c0 = part[2], part[3]
                    dve.wait_ge(hi_done, n + 1)
                    cols = bass.ds(c0 + t * P, r)
                    lo_part(dve, hT[1][:, :, cols], pt[s][:, :, 0:r], hT[0][:, :, cols]).then_inc(lo_done, 1)
                in_turn(dve, parts, norm, low)

            @block.gpsimd
            def _(pool):
                if not shifted:
                    return
                pool.wait_ge(loaded, n_load)

                def shift(n, s, part, t):
                    r = part[2]
                    pool.wait_ge(normed, n + 1)
                    pool.tensor_tensor(xn[s][0:r, :], xn[s][0:r, :], affine[part[6]][1][0][0:r, :], ALU.add).then_inc(scaled, 1)
                in_turn(pool, parts, shift, lambda *tile: None)

            @block.tensor
            def _(pe):
                def turn(n, s, part, t):
                    r = part[2]
                    pe.wait_ge(scaled, n + 1)
                    if not (isinstance(n, int) and n < 2):
                        pe.wait_ge(lo_done, n - 1)
                    for k in range(KD):
                        mm = pe.transpose(pt[s][:, k, 0:r], xn[s][0:r, P * k:P * k + P], g.ident[0:r, 0:r])
                    mm.then_inc(turned, 1)
                in_turn(pe, parts, turn, lambda *tile: None)


def project_rows(nc, hT, tag, tiles, w_dram, blk, nblk, dst):
    NBANK = 4
    n = len(tiles)
    w_v = w_dram.rearrange("(k p) (b n) -> p k b n", p=P, n=blk)
    with Phase(nc, tag) as ph:
        w = Weights(ph, KD, blk)
        o = [ph.sb(f"o{s}", [P, blk]) for s in range(NBANK)]
        pb = [ph.ps(f"pb{s}", [P, 512]) for s in range(NBANK)]
        made = ph.sems("made0 made1 made2 made3")
        copied = ph.sems("copied0 copied1 copied2 copied3")
        stored = ph.sems("stored0 stored1 stored2 stored3")
        slots = [(s, t) for s in range(2) for t in range(n)]
        per = [sum(1 for q in range(2 * n) if q % NBANK == b) for b in range(NBANK)]
        with nc.Block() as block:
            @block.gpsimd
            def _(pool):
                def load(b):
                    w.load(pool, b, lambda k0, k1: w_v[:, k0:k1, b, :])
                load(0)
                with pool.Fori(1, nblk, 1) as b:
                    load(b)

            @block.sync
            def _(sp):
                for b in range(NBANK):
                    sp.sem_inc(stored[b], 16)
                with sp.Fori(0, nblk // 2, 1) as i:
                    for q, (s, t) in enumerate(slots):
                        b = q % NBANK
                        c0, r = tiles[t]
                        sp.wait_ge(copied[b], i * per[b] + q // NBANK + 1)
                        sp.dma_start(dst[c0:c0 + r, bass.ds((i * 2 + s) * blk, blk)], o[b][0:r, :]).then_inc(stored[b], 16)
                for b in range(NBANK):
                    sp.wait_ge(stored[b], 16 + 16 * per[b] * (nblk // 2))

            def copies(eng, mine, i, s):
                for q in range(s * n, s * n + n):
                    b = q % NBANK
                    if b % 2 != mine:
                        continue
                    r = tiles[q - s * n][1]
                    eng.wait_ge(made[b], i * per[b] + q // NBANK + 1)
                    eng.wait_ge(stored[b], (i * per[b] + q // NBANK) * 16 + 16)
                    if mine:
                        eng.tensor_copy(o[b][0:r, :], pb[b][0:r, 0:blk]).then_inc(copied[b], 1)
                    else:
                        eng.activation(o[b][0:r, :], pb[b][0:r, 0:blk], ACT.Copy).then_inc(copied[b], 1)

            def slot_free(eng, i, s, first):
                if not first:
                    q = (s * n - 1) % (2 * n)
                    eng.wait_ge(made[q % NBANK], (i if s else i - 1) * per[q % NBANK] + q // NBANK + 1)

            @block.scalar
            def _(act):
                w.make_hi(act, 0, 0)

                def step(i, s, first, last):
                    if not last:
                        slot_free(act, i, s, first)
                        w.make_hi(act, i * 2 + s + 1, 1 - s)
                    copies(act, 0, i, s)
                in_pairs(act, nblk, step)

            @block.vector
            def _(dve):
                w.make_lo(dve, 0, 0)

                def step(i, s, first, last):
                    if not last:
                        w.make_lo(dve, i * 2 + s + 1, 1 - s)
                    copies(dve, 1, i, s)
                in_pairs(dve, nblk, step)

            @block.tensor
            def _(pe):
                with pe.Fori(0, nblk // 2, 1) as i:
                    for q, (s, t) in enumerate(slots):
                        b = q % NBANK
                        c0, r = tiles[t]
                        if t == 0:
                            w.ready(pe, i * 2 + s)
                        if q >= NBANK:
                            pe.wait_ge(copied[b], i * per[b] + q // NBANK)
                        else:
                            pe.wait_ge(stored[b], (i * per[b]) * 16 + 16)
                        for k in range(KD):
                            mm = product(pe, pb[b][0:r, 0:blk], [h[:, k, c0:c0 + r] for h in hT], w.cut(s, k, 0, blk),
                                         k == 0, k == KD - 1)
                        mm.then_inc(made[b], 1)


QK_HEADS = 26
V_B = 2304


def rotate_heads(nc, a, g, p0, KB, KA, va, vb):
    n_all = NT + NC
    with Phase(nc, "rot") as ph:
        rope = ph.sb("rope", [P, 2, n_all, HD])
        gain = ph.sb("gain", [P, 4, HD])
        qk = [ph.sb(f"qk{s}", [P, QK_HEADS, HD]) for s in range(2)]
        sq = ph.sb("sq", [P, QK_HEADS, HD])
        tmp = [ph.sb(f"tmp{s}", [P, QK_HEADS, HD]) for s in range(2)]
        rot = [ph.sb(f"rotated{s}", [P, 28, HD]) for s in range(2)]
        ss = ph.sb("ss", [P, QK_HEADS])
        rt = ph.sb("rt", [P, QK_HEADS])
        pt = [ph.ps(f"pt{s}", [P, 16, P]) for s in range(2)]
        small, in0, in1, squared, summed, rooted, normed, cosined, sined, rotated, turned, evac, dstep, padded = ph.sems(
            "small in0 in1 squared summed rooted normed cosined sined rotated turned evac dstep padded")
        qk_in = [in0, in1]
        spans = ((0, 8), (8, 10), (10, 18), (18, 26))
        with nc.Block() as block:
            @block.sync
            def _(sp):
                def load(s, i):
                    src = p0[bass.ds(i * P, P), :]
                    sp.dma_start(qk[s][:, 0:10, :], src[:, 0:640]).then_inc(qk_in[s], 16)
                    sp.dma_start(qk[s][:, 10:26, :], src[:, 1280:2304]).then_inc(qk_in[s], 16)

                for s in range(2):
                    load(s, s)
                sp.dma_start(rope[:, :, :, :], a["k_rope"].rearrange("c (t p) d -> p c t d", p=P)).then_inc(small, 16)
                for j, name in enumerate(("a_q_norm", "a_k_norm", "b_q_norm", "b_k_norm")):
                    sp.dma_start(gain[:, j, :], rows(a[name][0, :])).then_inc(small, 16)
                sp.dma_start(va[:, 1:, :], p0[:, 640:768].rearrange("(t p) d -> p t d", p=P)).then_inc(small, 16)
                sp.dma_start(vb[:, :, :], p0[:, V_B:V_B + 512].rearrange("(t p) d -> p t d", p=P)).then_inc(small, 16)
                with sp.Fori(1, n_all // 2, 1) as i:
                    for s in range(2):
                        sp.wait_ge(cosined, i * 2 + s - 1)
                        sp.wait_ge(sined, i * 2 + s - 1)
                        load(s, i * 2 + s)
                sp.wait_ge(small, 16 * 7)

            @block.gpsimd
            def _(pool):
                pool.memset(va[:, 0, :], 0.0).then_inc(padded, 1)
                pool.memset(KA[:, :, 0:P], 0.0).then_inc(padded, 1)
                pool.wait_ge(padded, 2)
                pool.wait_ge(small, 16 * 7)

                def step(i, s, first, last):
                    n = i * 2 + s
                    pool.wait_ge(normed, n + 1)
                    if not (isinstance(i, int) and i == 0):
                        pool.wait_ge(rotated, n - 1)
                    pairs = qk[s][:, :, :].rearrange("p h (x y m) -> p h x y m", x=2, y=2)
                    out = tmp[s][:, :, :].rearrange("p h (x y m) -> p h x y m", x=2, y=2)
                    sin = rope[:, 1, bass.ds(n, 1), :].rearrange("p a (x y m) -> p (a x) y m", x=2, y=2)
                    for y in range(2):
                        ins = pool.tensor_tensor(out[:, :, :, y, :], pairs[:, :, :, 1 - y, :],
                                                 sin[:, :, y, :].unsqueeze(1).broadcast_to([P, QK_HEADS, 2, 16]), ALU.mult)
                    ins.then_inc(sined, 1)
                in_pairs(pool, n_all, step)

            @block.scalar
            def _(act):
                def square(i, s):
                    act.wait_ge(qk_in[s], i * 32 + 32)
                    act.activation(sq[:, :, :], qk[s][:, :, :], ACT.Square).then_inc(squared, 1)

                def copy_out(n, s):
                    act.wait_ge(turned, n + 1)
                    act.activation(g.hT[:, :, bass.ds(n * P, P)], pt[s][:, 0:8, :], ACT.Copy)
                    act.activation(KA[:, :, bass.ds(n * P + P, P)], pt[s][:, 8:10, :], ACT.Copy)
                    act.activation(KB[:, :, bass.ds(n * P, P)], pt[s][:, 12:16, :], ACT.Copy).then_inc(evac, 1)
                square(0, 0)

                def step(i, s, first, last):
                    n = i * 2 + s
                    act.wait_ge(summed, n + 1)
                    act.activation(rt[:, :], ss[:, :], ACT.Sqrt, scale=1.0 / HD, bias=g.epsc[:, :]).then_inc(rooted, 1)
                    if not last:
                        square(i + s, 1 - s)
                    if not (isinstance(i, int) and i == 0):
                        copy_out(n - 2, s)
                in_pairs(act, n_all, step)
                for s in range(2):
                    copy_out(n_all - 2 + s, s)

            @block.vector
            def _(dve):
                dve.wait_ge(small, 16 * 7)
                per = 2

                def total(n):
                    dve.wait_ge(squared, n + 1)
                    dve.tensor_reduce(ss[:, :], sq[:, :, :], AX.X, ALU.add).then_inc(summed, 1)

                def add(n, s):
                    dve.wait_ge(sined, n + 1)
                    dve.wait_ge(cosined, n + 1)
                    dve.tensor_tensor(rot[s][:, 0:8, :], rot[s][:, 0:8, :], tmp[s][:, 0:8, :], ALU.add)
                    for half in range(2):
                        keys = rot[s][:, 8:12, :].rearrange("p (k r) d -> p k r d", r=2)[:, :, half, :]
                        dve.tensor_tensor(keys, keys, tmp[s][:, 8:10, :], ALU.add)
                    dve.tensor_tensor(rot[s][:, 12:28, :], rot[s][:, 12:28, :], tmp[s][:, 10:26, :], ALU.add).then_inc(rotated, 1)
                total(0)

                def step(i, s, first, last):
                    n = i * 2 + s
                    ch = Chain(dve, dstep, n * per)
                    dve.wait_ge(rooted, n + 1)
                    ch.link(dve.reciprocal(rt[:, :], rt[:, :]))
                    ch.link(dve.tensor_tensor(qk[s][:, :, :], qk[s][:, :, :],
                                              rt[:, :].unsqueeze(2).broadcast_to([P, QK_HEADS, HD]), ALU.mult))
                    assert ch.k == per
                    for j, (h0, h1) in enumerate(spans):
                        ins = dve.tensor_tensor(qk[s][:, h0:h1, :], qk[s][:, h0:h1, :],
                                                gain[:, j:j + 1, :].broadcast_to([P, h1 - h0, HD]), ALU.mult)
                    ins.then_inc(normed, 1)
                    dve.wait_ge(normed, n + 1)
                    if not (isinstance(i, int) and i == 0):
                        dve.wait_ge(turned, n - 1)
                    cos = rope[:, 0, bass.ds(n, 1), :]
                    dve.tensor_tensor(rot[s][:, 0:8, :], qk[s][:, 0:8, :], cos.broadcast_to([P, 8, HD]), ALU.mult)
                    for half in range(2):
                        dve.tensor_tensor(rot[s][:, 8:12, :].rearrange("p (k r) d -> p k r d", r=2)[:, :, half, :],
                                          qk[s][:, 8:10, :], cos.broadcast_to([P, 2, HD]), ALU.mult)
                    dve.tensor_tensor(rot[s][:, 12:28, :], qk[s][:, 10:26, :], cos.broadcast_to([P, 16, HD]), ALU.mult).then_inc(cosined, 1)
                    if not first:
                        add(n - 1, 1 - s)
                    if not last:
                        total(n + 1)
                in_pairs(dve, n_all, step)
                add(n_all - 1, 1)

            @block.tensor
            def _(pe):
                def step(i, s, first, last):
                    n = i * 2 + s
                    pe.wait_ge(rotated, n + 1)
                    if not (isinstance(i, int) and i == 0):
                        pe.wait_ge(evac, n - 1)
                    for c, at in enumerate((0, 1, 2, 3, 8, 9, 4, 5, 6, 7, 12, 13, 14, 15)):
                        mm = pe.transpose(pt[s][:, at, :], rot[s][:, 2 * c:2 * c + 2, :].rearrange("p h d -> p (h d)"), g.ident[:, :])
                    mm.then_inc(turned, 1)
                in_pairs(pe, n_all, step)


SCALE = HD ** -0.5


def window_attention(nc, a, g, KA, va, o_dram):
    NP = A_HEADS // 2
    NS = 2 * NP
    W3 = 3 * P
    with Phase(nc, "wa") as ph:
        mask = ph.sb("mask", [P, NT, W3])
        sink = ph.sb("sink", [P, A_HEADS])
        qc = [ph.sb(f"qc{s}", [P, NP, P]) for s in range(2)]
        kw = [ph.sb(f"kw{s}", [P, 2, W3]) for s in range(2)]
        S = [ph.sb(f"S{e}", [P, W3 + CTX]) for e in range(2)]
        E = [ph.sb(f"E{e}", [P, W3 + CTX]) for e in range(2)]
        ET = [ph.sb(f"ET{e}", [P, 5, P]) for e in range(2)]
        mx = ph.sb("mx", [P, 2])
        nm = ph.sb("nm", [P, 2])
        l = ph.sb("l", [P, 2])
        es = ph.sb("es", [P, 2])
        r = ph.sb("r", [P, 2])
        oa = [ph.sb(f"oa{s}", [P, A_HEADS, HD]) for s in range(2)]
        pS = [ph.ps(f"pS{e}", [P, 1024]) for e in range(2)]
        pw = [pS[e][:, 0:W3] for e in range(2)]
        pc = [pS[e][:, 512:512 + CTX] for e in range(2)]
        pT = [ph.ps(f"pT{e}", [P, 1024]) for e in range(2)]
        po = [pT[e][:, 5 * P:5 * P + NP * HD].rearrange("p (n d) -> p n d", d=HD) for e in range(2)]
        small, window, scores, s_ctx, negmax, expd, summed, turned, et0, et1, pv, o_done, st0, st1, dstep = ph.sems(
            "small window scores s_ctx negmax expd summed turned et0 et1 pv o_done st0 st1 dstep")
        et, stored = [et0, et1], [st0, st1]
        with nc.Block() as block:
            def loops(eng, body):
                with eng.Fori(0, NT // 2, 1) as i:
                    body(i * 2, i, True)
                body(NT, NT // 2, False)

            @block.sync
            def _(sp):
                sp.dma_start(mask[:, :, :], a["k_window"].rearrange("t p k -> p t k")).then_inc(small, 16)
                sp.dma_start(sink[:, :], rows(a["a_sink"][0, :])).then_inc(small, 16)
                for s in range(2):
                    sp.sem_inc(stored[s], 16)

                def body(t, i, win):
                    for s in range(2):
                        sp.wait_ge(o_done, i * NS + NP * (s + 1))
                        sp.dma_start(o_dram[bass.ds((t + s) * P, P), 0:512], oa[s][:, :, :]).then_inc(stored[s], 16)
                loops(sp, body)
                for s in range(2):
                    sp.wait_ge(stored[s], 16 + 16 * (NT + NC) // 2)

            @block.gpsimd
            def _(pool):
                pool.sem_inc(scores, NS)

                def body(t, i, win):
                    for s in range(2):
                        pool.wait_ge(scores, i * NS + NP * (s + 1))
                        pool.tensor_copy(qc[s][:, :, :], g.hT[:, 0:NP, bass.ds((t + s) * P, P)])
                        if win:
                            ins = pool.tensor_copy(kw[s][:, :, :], KA[:, :, bass.ds((t + s) * P, W3)])
                        else:
                            ins = pool.tensor_copy(kw[s][:, :, 0:P], KA[:, :, 0:P])
                        ins.then_inc(window, 1)
                loops(pool, body)

            @block.scalar
            def _(act):
                act.wait_ge(small, 32)

                def body(t, i, win):
                    w0 = 0 if win else W3

                    def context_scores(n):
                        act.wait_ge(scores, i * NS + NS + n + 1)
                        if n:
                            act.wait_ge(expd, i * NS + n)
                        for e in range(2):
                            ins = act.activation(S[e][:, W3:], pc[e], ACT.Copy, scale=SCALE)
                        ins.then_inc(s_ctx, 1)

                    def exps(n):
                        act.wait_ge(negmax, i * NS + n + 1)
                        for e in range(2):
                            act.activation(E[e][:, w0:], S[e][:, w0:], ACT.Exp, bias=nm[:, e:e + 1], accum_out=l[:, e:e + 1])
                            ins = act.activation(es[:, e:e + 1], sink[:, 2 * (n % NP) + e:2 * (n % NP) + e + 1], ACT.Exp, bias=nm[:, e:e + 1])
                        ins.then_inc(expd, 1)

                    context_scores(0)
                    exps(0)
                    for n in range(NS):
                        if n + 1 < NS:
                            context_scores(n + 1)
                        act.wait_ge(turned, i * NS + n + 1)
                        k0 = 0 if win else 3
                        act.activation(ET[1][:, k0:5, :], pT[1][:, P * k0:5 * P], ACT.Copy).then_inc(et[1], 1)
                        if n + 1 < NS:
                            act.wait_ge(summed, i * NS + n + 1)
                            exps(n + 1)
                loops(act, body)

            @block.vector
            def _(dve):
                dve.wait_ge(small, 32)
                per = 3 * NS

                def body(t, i, win):
                    w0 = 0 if win else W3
                    ch = Chain(dve, dstep, i * per)

                    def window_scores(n):
                        dve.wait_ge(scores, i * NS + NS + n + 1)
                        if win:
                            for e in range(2):
                                ins = dve.scalar_tensor_tensor(S[e][:, 0:W3], pw[e], SCALE, mask[:, t + n // NP, :], ALU.mult, ALU.add)
                            ch.link(ins)
                        else:
                            ch.link(dve.memset(mx[:, :], 0.0))

                    def maxima(n):
                        dve.wait_ge(s_ctx, i * NS + n + 1)
                        for e in range(2):
                            ins = dve.tensor_reduce(mx[:, e:e + 1], S[e][:, w0:], AX.X, ALU.max)
                        ch.link(ins)
                        for e in range(2):
                            ins = dve.tensor_scalar(nm[:, e:e + 1], mx[:, e:e + 1], sink[:, 2 * (n % NP) + e:2 * (n % NP) + e + 1], -1.0, ALU.max, ALU.mult)
                        ins.then_inc(negmax, 1)

                    window_scores(0)
                    maxima(0)
                    for n in range(NS):
                        m = i * NS + n
                        dve.wait_ge(expd, m + 1)
                        ch.link(dve.tensor_tensor(l[:, :], l[:, :], es[:, :], ALU.add))
                        dve.reciprocal(r[:, :], l[:, :]).then_inc(summed, 1)
                        if n + 1 < NS:
                            window_scores(n + 1)
                        dve.wait_ge(turned, m + 1)
                        k0 = 0 if win else 3
                        dve.tensor_copy(ET[0][:, k0:5, :], pT[0][:, P * k0:5 * P]).then_inc(et[0], 1)
                        if n + 1 < NS:
                            maxima(n + 1)
                        dve.wait_ge(summed, m + 1)
                        dve.wait_ge(pv, m + 1)
                        if n % NP == 0:
                            dve.wait_ge(stored[n // NP], i * 16 + 16)
                        for e in range(2):
                            h = 2 * (n % NP) + e
                            ins = dve.tensor_scalar(oa[n // NP][:, h, :], po[e][:, n % NP, :], r[:, e:e + 1], None, ALU.mult)
                        ins.then_inc(o_done, 1)
                    assert ch.k == per
                loops(dve, body)

            @block.tensor
            def _(pe):
                def body(t, i, win):
                    k0 = 0 if win else 3

                    def scores_of(n):
                        kv = n % NP // 2
                        if n % NP == 0:
                            pe.wait_ge(window, t + n // NP + 1)
                        if n:
                            pe.wait_ge(negmax, i * NS + n)
                        for e in range(2):
                            half = slice(64 * e, 64 * e + 64)
                            if win:
                                pe.matmul(pw[e], qc[n // NP][half, n % NP, :], kw[n // NP][half, kv, :], start=True, stop=True)
                            mm = pe.matmul(pc[e], qc[n // NP][half, n % NP, :], KA[half, kv, P + SEQ:P + ALLT], start=True, stop=True)
                        mm.then_inc(scores, 1)

                    scores_of(0)
                    for n in range(NS):
                        m = i * NS + n
                        kv = n % NP // 2
                        if n + 1 < NS:
                            scores_of(n + 1)
                        pe.wait_ge(expd, m + 1)
                        if n:
                            pe.wait_ge(o_done, m)
                        for e in range(2):
                            for k in range(k0, 5):
                                mm = pe.transpose(pT[e][:, P * k:P * k + P], E[e][:, P * k:P * k + P], g.ident[:, :])
                        mm.then_inc(turned, 1)
                        for e in range(2):
                            pe.wait_ge(et[e], m + 1)
                            for k in range(k0, 5):
                                v = va[:, bass.ds(t + n // NP + k, 1), :] if k < 3 else va[:, NT + 1 + k - 3:NT + 2 + k - 3, :]
                                mm = pe.matmul(po[e][:, n % NP, :], ET[e][:, k, :], v[:, 0, HD * kv:HD * kv + HD], start=(k == k0), stop=(k == 4))
                        mm.then_inc(pv, 1)
                loops(pe, body)


def differential_attention(nc, a, g, KB, vb, o_dram):
    with Phase(nc, "da") as ph:
        qc = [ph.sb(f"qc{s}", [P, B_HEADS, P]) for s in range(2)]
        E = [ph.sb(f"E{m}", [P, ALLT]) for m in range(2)]
        ET = ph.sb("ET", [P, 10, P])
        mx = ph.sb("mx", [P, 2])
        nm = ph.sb("nm", [P, 2])
        l = ph.sb("l", [P, 2])
        r = ph.sb("r", [P, 2])
        ob = [ph.sb(f"ob{s}", [P, B_HEADS, P]) for s in range(2)]
        pS = [ph.ps(f"pS{m}", [P, 1536]) for m in range(2)]
        pT = ph.ps("pT", [P, 4, P])
        po = ph.ps("po", [P, B_HEADS, P])
        qcopied, sc0, sc1, top0, top1, neg0, neg1, ex0, ex1, weights, turned, evac, pv, o_done, st0, st1, dstep = ph.sems(
            "qcopied sc0 sc1 top0 top1 neg0 neg1 ex0 ex1 weights turned evac pv o_done st0 st1 dstep")
        stored = [st0, st1]
        sc, top, neg, ex = [sc0, sc1], [top0, top1], [neg0, neg1], [ex0, ex1]
        H = B_HEADS
        NS = 2 * H

        def groups(full):
            return [(0, 4), (4, 8), (8, 10)] if full else [(8, 10)]

        def group_count(i, n, full):
            return (i * NS + n) * 3 if full else NT * H * 3 + n

        with nc.Block() as block:
            def loops(eng, body):
                with eng.Fori(0, NT // 2, 1) as i:
                    body(i * 2, i, True)
                body(NT, NT // 2, False)

            @block.sync
            def _(sp):
                for s in range(2):
                    sp.sem_inc(stored[s], 16)

                def body(t, i, full):
                    for s in range(2):
                        sp.wait_ge(o_done, i * NS + H * (s + 1))
                        sp.dma_start(o_dram[bass.ds((t + s) * P, P), 512:1024], ob[s][:, :, :]).then_inc(stored[s], 16)
                loops(sp, body)
                for s in range(2):
                    sp.wait_ge(stored[s], 16 + 16 * (NT + NC) // 2)

            @block.gpsimd
            def _(pool):
                pool.sem_inc(sc[1], NS)

                def body(t, i, full):
                    for s in range(2):
                        pool.wait_ge(sc[1], i * NS + H * (s + 1))
                        pool.tensor_copy(qc[s][:, :, :], g.hT[:, 4:8, bass.ds((t + s) * P, P)]).then_inc(qcopied, 1)
                loops(pool, body)

            @block.scalar
            def _(act):
                def body(t, i, full):
                    k0 = 0 if full else SEQ

                    def exps(h):
                        for m in range(2):
                            act.wait_ge(neg[m], i * NS + h + 1)
                            act.activation(E[m][:, k0:], pS[m][:, k0:ALLT], ACT.Exp, scale=SCALE,
                                           bias=nm[:, m:m + 1], accum_out=l[:, m:m + 1]).then_inc(ex[m], 1)

                    exps(0)
                    for h in range(NS):
                        for j, (a0, a1) in enumerate(groups(full)):
                            act.wait_ge(turned, group_count(i, h, full) + j + 1)
                            act.activation(ET[:, a0:a1, :], pT[:, 0:a1 - a0, :], ACT.Copy).then_inc(evac, 1)
                        if h + 1 < NS:
                            exps(h + 1)
                loops(act, body)

            @block.vector
            def _(dve):
                per = 2 * NS

                def body(t, i, full):
                    k0 = 0 if full else SEQ
                    ch = Chain(dve, dstep, i * per)

                    def maxima(h):
                        n = i * NS + h
                        for m in range(2):
                            dve.wait_ge(sc[m], n + 1 + NS * m)
                            dve.tensor_reduce(mx[:, m:m + 1], pS[m][:, k0:ALLT], AX.X, ALU.max).then_inc(top[m], 1)
                            dve.wait_ge(top[m], n + 1)
                            dve.tensor_scalar(nm[:, m:m + 1], mx[:, m:m + 1], -SCALE, None, ALU.mult).then_inc(neg[m], 1)

                    maxima(0)
                    for h in range(NS):
                        n = i * NS + h
                        for m in range(2):
                            dve.wait_ge(ex[m], n + 1)
                        ch.link(dve.reciprocal(r[:, :], l[:, :]))
                        dve.tensor_tensor(r[:, 1:2], r[:, 1:2], g.neglam[:, :], ALU.mult)
                        ch.link(dve.tensor_scalar(E[0][:, k0:], E[0][:, k0:], r[:, 0:1], None, ALU.mult))
                        dve.scalar_tensor_tensor(E[0][:, k0:], E[1][:, k0:], r[:, 1:2], E[0][:, k0:], ALU.mult, ALU.add).then_inc(weights, 1)
                        if h + 1 < NS:
                            dve.wait_ge(weights, n + 1)
                            maxima(h + 1)
                        dve.wait_ge(pv, n + 1)
                        if h % H == 0:
                            dve.wait_ge(stored[h // H], i * 16 + 16)
                        dve.tensor_copy(ob[h // H][:, h % H, :], po[:, h % H, :]).then_inc(o_done, 1)
                    assert ch.k == per
                loops(dve, body)

            @block.tensor
            def _(pe):
                def body(t, i, full):
                    def scores(h):
                        if h % H == 0:
                            pe.wait_ge(qcopied, t + h // H + 1)
                        for m in range(2):
                            half = slice(64 * m, 64 * m + 64)
                            if h:
                                pe.wait_ge(ex[m], i * NS + h)
                            for c0, c1 in [(0, 512), (512, 1024), (1024, 1280)] if full else [(SEQ, ALLT)]:
                                mm = pe.matmul(pS[m][:, c0:c1], qc[h // H][half, h % H, :], KB[half, h % H, c0:c1], start=True, stop=True)
                            mm.then_inc(sc[m], 1)

                    scores(0)
                    for h in range(NS):
                        n = i * NS + h
                        if h + 1 < NS:
                            scores(h + 1)
                        pe.wait_ge(weights, n + 1)
                        gs = groups(full)

                        def values(j):
                            for k in range(*gs[j]):
                                hh = h % H
                                mm = pe.matmul(po[:, hh, :], ET[:, k, :], vb[:, k, P * hh:P * hh + P], start=(k == gs[0][0]), stop=(k == 9))
                            return mm

                        for j, (a0, a1) in enumerate(gs):
                            for k in range(a0, a1):
                                mm = pe.transpose(pT[:, k - a0, :], E[0][:, P * k:P * k + P], g.ident[:, :])
                            mm.then_inc(turned, 1)
                            if j:
                                values(j - 1)
                            pe.wait_ge(evac, group_count(i, h, full) + j + 1)
                        values(len(gs) - 1).then_inc(pv, 1)
                loops(pe, body)


def merge_even(nc, a, g, hT, p0, o_dram):
    n_all = NT + NC
    parts = [(n_all,)]
    with Phase(nc, "me") as ph:
        o = [ph.sb(f"o{s}", [P, 8, P]) for s in range(2)]
        gt = [ph.sb(f"gt{s}", [P, 8, P]) for s in range(2)]
        sub = ph.sb("sub", [P, P])
        sq = ph.sb("sq", [P, B_HEADS, P])
        ss = ph.sb("ss", [P, 2, B_HEADS])
        pt = [ph.ps(f"pt{s}", [P, KD, P]) for s in range(2)]
        small, in0, in1, squared, summed, rooted, normed, gated, merged, turned, hi_done, lo_done, dstep = ph.sems(
            "small in0 in1 squared summed rooted normed gated merged turned hi_done lo_done dstep")
        o_in = [in0, in1]
        with nc.Block() as block:
            @block.sync
            def _(sp):
                sp.dma_start(sub[:, :], rows(a["b_subln"][0, :])).then_inc(small, 16)

                def load(s, t):
                    sp.dma_start(o[s][:, :, :], o_dram[bass.ds(t * P, P), :]).then_inc(o_in[s], 16)
                    sp.dma_start(gt[s][:, 0:4, :], p0[bass.ds(t * P, P), 768:1280]).then_inc(o_in[s], 16)
                    sp.dma_start(gt[s][:, 4:8, :], p0[bass.ds(t * P, P), 2816:3328]).then_inc(o_in[s], 16)
                for s in range(2):
                    load(s, s)
                with sp.Fori(1, n_all // 2, 1) as i:
                    for s in range(2):
                        sp.wait_ge(turned, i * 2 + s - 1)
                        load(s, i * 2 + s)

            @block.scalar
            def _(act):
                def gate(n, s, part, t):
                    act.wait_ge(o_in[s], (t - s) * 24 + 48)
                    act.activation(sq[:, :, :], o[s][:, 4:8, :], ACT.Square).then_inc(squared, 1)
                    act.activation(gt[s][:, :, :], gt[s][:, :, :], ACT.Silu).then_inc(gated, 1)
                    act.wait_ge(summed, n + 1)
                    act.activation(ss[:, s, :], ss[:, s, :], ACT.Sqrt, scale=1.0 / P, bias=g.epsc[:, :]).then_inc(rooted, 1)

                def high(n, s, part, t):
                    act.wait_ge(turned, n + 1)
                    act.activation(hT[0][:, :, bass.ds(t * P, P)], pt[s][:, :, :], ACT.Copy).then_inc(hi_done, 1)
                in_turn(act, parts, gate, high)

            @block.vector
            def _(dve):
                dve.wait_ge(small, 16)
                per = 2

                def norm(n, s, part, t):
                    ch = Chain(dve, dstep, n * per)
                    dve.wait_ge(squared, n + 1)
                    dve.tensor_reduce(ss[:, s, :], sq[:, :, :], AX.X, ALU.add).then_inc(summed, 1)
                    dve.wait_ge(rooted, n + 1)
                    ch.link(dve.reciprocal(ss[:, s, :], ss[:, s, :]))
                    ch.link(dve.scalar_tensor_tensor(o[s][:, 4:8, :], o[s][:, 4:8, :], 1.0 - LAMBDA_INIT,
                                                     ss[:, s, :].unsqueeze(2).broadcast_to([P, B_HEADS, P]), ALU.mult, ALU.mult))
                    assert ch.k == per
                    dve.tensor_tensor(o[s][:, 4:8, :], o[s][:, 4:8, :],
                                      sub[:, :].unsqueeze(1).broadcast_to([P, B_HEADS, P]), ALU.mult).then_inc(normed, 1)

                def low(n, s, part, t):
                    cols = bass.ds(t * P, P)
                    dve.wait_ge(hi_done, n + 1)
                    lo_part(dve, hT[1][:, :, cols], pt[s][:, :, :], hT[0][:, :, cols]).then_inc(lo_done, 1)
                in_turn(dve, parts, norm, low)

            @block.gpsimd
            def _(pool):
                def merge(n, s, part, t):
                    pool.wait_ge(normed, n + 1)
                    pool.wait_ge(gated, n + 1)
                    pool.tensor_tensor(o[s][:, :, :], o[s][:, :, :], gt[s][:, :, :], ALU.mult).then_inc(merged, 1)
                in_turn(pool, parts, merge, lambda *tile: None)

            @block.tensor
            def _(pe):
                def turn(n, s, part, t):
                    pe.wait_ge(merged, n + 1)
                    if not (isinstance(n, int) and n < 2):
                        pe.wait_ge(lo_done, n - 1)
                    for k in range(KD):
                        mm = pe.transpose(pt[s][:, k, :], o[s][:, k, :], g.ident[:, :])
                    mm.then_inc(turned, 1)
                in_turn(pe, parts, turn, lambda *tile: None)


def project_out(nc, g, tag, hT, parts, w_dram):
    BLK = 256
    NBLK = D // BLK
    tiles = [(x, t, c0 + P * t, gi) for gi, (x, n, c0, _) in enumerate(parts) for t in range(n)]
    n = len(tiles)
    w_v = w_dram.rearrange("(k p) (b n) -> p k b n", p=P, n=BLK)
    with Phase(nc, tag) as ph:
        gate = ph.sb("gate", [P, len(parts), D])
        w = Weights(ph, KD, BLK)
        tmp = [ph.sb(f"tmp{b}", [P, BLK]) for b in range(4)]
        pb = [ph.ps(f"pb{b}", [P, 512]) for b in range(4)]
        small, made, scaled, added = ph.sems("small made scaled added")
        with nc.Block() as block:
            @block.sync
            def _(sp):
                def load(b):
                    w.load(sp, b, lambda k0, k1: w_v[:, k0:k1, b, :])
                load(0)
                for j, part in enumerate(parts):
                    sp.dma_start(gate[:, j, :], rows(part[3])).then_inc(small, 16)
                with sp.Fori(1, NBLK, 1) as b:
                    load(b)

            @block.scalar
            def _(act):
                w.make_hi(act, 0, 0)

                def step(i, s, first, last):
                    if not last:
                        if not first:
                            act.wait_ge(made, (i * 2 + s) * n)
                        w.make_hi(act, i * 2 + s + 1, 1 - s)
                in_pairs(act, NBLK, step)

            @block.vector
            def _(dve):
                w.make_lo(dve, 0, 0)
                dve.wait_ge(small, 16 * len(parts))
                dve.sem_inc(scaled, 4)

                def step(i, s, first, last):
                    if not last:
                        w.make_lo(dve, i * 2 + s + 1, 1 - s)
                    cols = bass.ds((i * 2 + s) * BLK, BLK)
                    for q, (x, t, _, gi) in enumerate(tiles):
                        b = (s * n + q) % 4
                        m = i * 2 * n + s * n + q
                        dve.wait_ge(made, m + 1)
                        dve.tensor_tensor(tmp[b][:, :], pb[b][:, 0:BLK], gate[:, gi, cols], ALU.mult).then_inc(scaled, 1)
                        dve.wait_ge(scaled, m + 5)
                        dve.tensor_tensor(x[:, t, cols], x[:, t, cols], tmp[b][:, :], ALU.add)
                in_pairs(dve, NBLK, step)

            @block.tensor
            def _(pe):
                with pe.Fori(0, NBLK // 2, 1) as i:
                    for s in range(2):
                        w.ready(pe, i * 2 + s)
                        for q, (_, _, c0, _) in enumerate(tiles):
                            b = (s * n + q) % 4
                            m = i * 2 * n + s * n + q
                            pe.wait_ge(scaled, m + 1)
                            for k in range(KD):
                                mm = product(pe, pb[b][:, 0:BLK], [h[:, k, c0:c0 + P] for h in hT], w.cut(s, k, 0, BLK),
                                             k == 0, k == KD - 1)
                            mm.then_inc(made, 1)


G_HEADS = 4
G_DK = 128
G_DV = 256
G_RANK = 16
G_TAU = 16.0
GK = G_HEADS * G_DK
GV = G_HEADS * G_DV


def log_decays(nc, a, g, p1, la, dec):
    n_all = NT + NC
    with Phase(nc, "ld") as ph:
        wa = ph.sb("wa", [2 * G_RANK, 2, GK])
        ba = ph.sb("ba", [P, 2, GK])
        chunk_of = ph.sb("chunk_of", [P, 2])
        r = ph.sb("r", [P, n_all, 2 * G_RANK])
        rc = [ph.sb(f"rc{s}", [P, 2 * G_RANK]) for s in range(2)]
        rT = [ph.sb(f"rT{s}", [2 * G_RANK, P]) for s in range(2)]
        e = [ph.sb(f"e{s}", [P, 2 * GK]) for s in range(2)]
        lc = [ph.sb(f"lc{s}", [P, 2 * GK]) for s in range(2)]
        pr = [ph.ps(f"pr{s}", [2 * G_RANK, P]) for s in range(2)]
        pz = [ph.ps(f"pz{s}", [P, 2, GK]) for s in range(2)]
        pd = [ph.ps(f"pd{s}", [P, 2, G_HEADS, 2]) for s in range(2)]
        small, zeroed, placed, turned, copied, logits, biased, absed, logged, least, made, summed, decayed = ph.sems(
            "small zeroed placed turned copied logits biased absed logged least made summed decayed")
        with nc.Block() as block:
            @block.sync
            def _(sp):
                sp.wait_ge(zeroed, 1)
                sp.dma_start(wa[0:G_RANK, 0, :], a["gla_wa_f"][0, :, :]).then_inc(small, 16)
                sp.dma_start(wa[G_RANK:2 * G_RANK, 1, :], a["gla_wa_b"][0, :, :]).then_inc(small, 16)
                sp.dma_start(ba[:, 0, :], rows(a["gla_ba_f"][0, :])).then_inc(small, 16)
                sp.dma_start(ba[:, 1, :], rows(a["gla_ba_b"][0, :])).then_inc(small, 16)
                sp.dma_start(chunk_of[:, :], a["k_chunk_of"][:, :]).then_inc(small, 16)
                sp.dma_start(r[:, :, :], p1[:, 3072:3104].rearrange("(t p) d -> p t d", p=P)).then_inc(small, 16)

            @block.scalar
            def _(act):
                def decay(i, s):
                    t = i * 2 + s
                    act.wait_ge(summed, t + 1)
                    act.activation(dec[:, bass.ds(t, 1), :], pd[s][:, :, :, :], ACT.Exp).then_inc(decayed, 1)

                def step(i, s, first, last):
                    if s:
                        return
                    for q in range(2):
                        t = i * 2 + q
                        act.wait_ge(biased, t + 1)
                        if not first:
                            act.wait_ge(least, t - 1)
                        act.activation(e[q][:, :], la[:, bass.ds(t, 1), :].rearrange("p a c -> p (a c)"), ACT.Abs).then_inc(absed, 1)
                        act.wait_ge(absed, t * 2 + 1)
                        act.activation(e[q][:, :], e[q][:, :], ACT.Exp, scale=-1.0).then_inc(absed, 1)
                    if not first:
                        for q in range(2):
                            decay(i - 1, q)
                    for q in range(2):
                        t = i * 2 + q
                        act.wait_ge(absed, t * 2 + 2)
                        act.activation(e[q][:, :], e[q][:, :], ACT.Ln, bias=1.0).then_inc(logged, 1)
                in_pairs(act, n_all, step)
                for q in range(2):
                    decay(n_all // 2 - 1, q)

            @block.vector
            def _(dve):
                dve.memset(wa[:, :, :], 0.0).then_inc(zeroed, 1)
                dve.wait_ge(small, 16 * 6)

                def place(t, s):
                    dve.tensor_copy(rc[s][:, :], r[:, bass.ds(t, 1), :].rearrange("p a c -> p (a c)")).then_inc(placed, 1)

                def front(t, s):
                    dve.wait_ge(turned, t + 1)
                    dve.tensor_copy(rT[s][:, :], pr[s][:, :]).then_inc(copied, 1)

                def logit(t, s):
                    dve.wait_ge(logits, t + 1)
                    dve.tensor_tensor(la[:, bass.ds(t, 1), :].rearrange("p a c -> p (a c)"), pz[s][:, :, :], ba[:, :, :], ALU.add).then_inc(biased, 1)

                def fronts(i):
                    for stage in (place, front, logit):
                        for q in range(2):
                            stage(i * 2 + q, q)
                fronts(0)

                def step(i, s, first, last):
                    if s:
                        return
                    if not isinstance(i, int) or i < n_all // 2 - 1:
                        fronts(i + 1)
                    for q in range(2):
                        t = i * 2 + q
                        z = la[:, bass.ds(t, 1), :].rearrange("p a c -> p (a c)")
                        dve.wait_ge(logged, t + 1)
                        dve.scalar_tensor_tensor(z, z, 0.0, e[q][:, :], ALU.min, ALU.subtract).then_inc(least, 1)
                        dve.wait_ge(least, t + 1)
                        if not first:
                            dve.wait_ge(summed, t - 1)
                        dve.tensor_scalar(lc[q][:, :], z, 1.0 / G_TAU, None, ALU.mult).then_inc(made, 1)
                        dve.wait_ge(made, t + 1)
                        dve.tensor_scalar(z, z, 1.0 / G_TAU, None, ALU.mult)
                in_pairs(dve, n_all, step)

            @block.tensor
            def _(pe):
                pe.wait_ge(small, 16 * 6)

                def fronts(i, first):
                    for q in range(2):
                        t = i * 2 + q
                        pe.wait_ge(placed, t + 1)
                        pe.transpose(pr[q][:, :], rc[q][:, :], g.ident[:, :]).then_inc(turned, 1)
                    for q in range(2):
                        t = i * 2 + q
                        pe.wait_ge(copied, t + 1)
                        if not first:
                            pe.wait_ge(biased, t - 1)
                        for d in range(2):
                            mm = pe.matmul(pz[q][:, d, :], rT[q][:, :], wa[:, d, :], start=True, stop=True)
                        mm.then_inc(logits, 1)
                fronts(0, True)

                def step(i, s, first, last):
                    if s:
                        return
                    if not isinstance(i, int) or i < n_all // 2 - 1:
                        fronts(i + 1, False)
                    for q in range(2):
                        t = i * 2 + q
                        pe.wait_ge(made, t + 1)
                        if not first:
                            pe.wait_ge(decayed, t - 1)
                        for d in range(2):
                            for h in range(G_HEADS):
                                mm = pe.matmul(pd[q][:, d, h, :], lc[q][:, GK * d + G_DK * h:GK * d + G_DK * h + G_DK], chunk_of[:, :],
                                               start=True, stop=True)
                        mm.then_inc(summed, 1)
                in_pairs(pe, n_all, step)


def linear_attention(nc, a, g, p1, la, dec, O):
    with Phase(nc, "la") as ph:
        masks = ph.sb("masks", [P, 5, P])
        qkv = [ph.sb(f"qkv{d}", [P, 2 * GK + GV]) for d in range(2)]
        eb = ph.sb("eb", [P, GK])
        en = ph.sb("en", [P, GK])
        er = ph.sb("er", [P, GK])
        qd = ph.sb("qd", [P, GK])
        kd = ph.sb("kd", [P, GK])
        ke = [ph.sb(f"ke{d}", [P, GK]) for d in range(2)]
        qdT = ph.sb("qdT", [P, G_HEADS, P])
        kdT = ph.sb("kdT", [P, G_HEADS, P])
        at = ph.sb("at", [P, G_HEADS, P])
        S = [ph.sb(f"S{d}", [P, G_HEADS, G_DV]) for d in range(2)]
        pA = ph.ps("pA", [P, 512])
        pB = ph.ps("pB", [P, 512])
        pq = ph.ps("pq", [P, G_HEADS, P])
        pk = ph.ps("pk", [P, G_HEADS, P])
        po = ph.ps("po", [P, G_HEADS, G_DV])
        pd = ph.ps("pd", [P, G_HEADS, G_DV])
        small, in0, in1, cum, expd, prod, kept, turned, qT_done, kT_done, att, masked, outer, sread, upd, added, zeroed = ph.sems(
            "small in0 in1 cum expd prod kept turned qT_done kT_done att masked outer sread upd added zeroed")
        qkv_in = [in0, in1]
        upto, after = (0, 1), (4, 3)

        def context_unit(j, d):
            return d, 2 * j + d, None, NT + (j if d == 0 else NC - 1 - j), j

        def x_unit(i, d):
            return d, i * 2 + d + 2 * NC, i * 2 + d, i if d == 0 else i * -1 + NT - 1, i + NC

        def run(eng, front, back):
            def step(unit, following):
                back(*unit, (lambda: front(*following)) if following else (lambda: None))

            short = [context_unit(j, d) for j in range(NC) for d in range(2)] + [x_unit(0, 0)]
            front(*short[0])
            for unit, following in zip(short, short[1:]):
                step(unit, following)
            with eng.Fori(0, NT - 1, 1) as i:
                step(x_unit(i, 0), x_unit(i, 1))
                step(x_unit(i, 1), x_unit(i + 1, 0))
            step(x_unit(NT - 1, 0), x_unit(NT - 1, 1))
            step(x_unit(NT - 1, 1), None)

        def alone(unit):
            return (lambda *which: None), (lambda d, n, u, tile, j, following: unit(d, n, u, tile, j))

        with nc.Block() as block:
            @block.sync
            def _(sp):
                sp.dma_start(masks[:, :, :], a["k_masks"].rearrange("m p k -> p m k")).then_inc(small, 16)

                def unit(d, n, u, tile, j):
                    if u is not None or j > 0:
                        sp.wait_ge(outer, n * 2 - 2)
                    if u is None:
                        src = p1[tile * P:tile * P + P, :]
                        sp.dma_start(qkv[d][:, GK:], src[:, GK:2 * GK + GV]).then_inc(qkv_in[d], 16)
                    else:
                        src = p1[bass.ds(tile * P, P), :]
                        sp.dma_start(qkv[d][:, :], src[:, 0:2 * GK + GV]).then_inc(qkv_in[d], 16)
                run(sp, *alone(unit))

            @block.gpsimd
            def _(pool):
                for d in range(2):
                    pool.memset(S[d][:, :, :], 0.0).then_inc(zeroed, 1)
                pool.memset(O[:, :, :], 0.0).then_inc(zeroed, 1)

                def unit(d, n, u, tile, j):
                    pool.wait_ge(qkv_in[d], j * 16 + 16)
                    pool.wait_ge(expd, n + 1)
                    pool.tensor_tensor(ke[d][:, :], qkv[d][:, GK:2 * GK], er[:, :], ALU.mult).then_inc(kept, 1)
                run(pool, *alone(unit))

            @block.scalar
            def _(act):
                def front(d, n, u, tile, j):
                    act.wait_ge(cum, n + 1)
                    if u is not None:
                        act.activation(eb[:, :], pA[:, :], ACT.Exp)
                        act.activation(en[:, :], pA[:, :], ACT.Exp, scale=-1.0)
                    act.activation(er[:, :], pB[:, :], ACT.Exp).then_inc(expd, 1)

                def back(d, n, u, tile, j, following):
                    if u is not None:
                        act.wait_ge(turned, u + 1)
                        act.activation(qdT[:, :, :], pq[:, :, :], ACT.Copy).then_inc(qT_done, 1)
                    following()
                run(act, front, back)

            @block.vector
            def _(dve):
                dve.wait_ge(small, 16)
                dve.wait_ge(zeroed, 3)
                dve.sem_inc(added, 1)

                def front(d, n, u, tile, j):
                    if u is not None:
                        dve.wait_ge(qkv_in[d], j * 16 + 16)
                        dve.wait_ge(expd, n + 1)
                        dve.scalar_tensor_tensor(qd[:, :], qkv[d][:, 0:GK], G_DK ** -0.5, eb[:, :], ALU.mult, ALU.mult)
                        dve.tensor_tensor(kd[:, :], qkv[d][:, GK:2 * GK], en[:, :], ALU.mult).then_inc(prod, 1)

                def back(d, n, u, tile, j, following):
                    if u is not None:
                        dve.wait_ge(turned, u + 1)
                        dve.tensor_copy(kdT[:, :, :], pk[:, :, :]).then_inc(kT_done, 1)
                        dve.wait_ge(att, u + 1)
                        dve.tensor_tensor(at[:, :, :], pA[:, :].rearrange("p (h t) -> p h t", t=P),
                                          masks[:, upto[d], :].unsqueeze(1).broadcast_to([P, G_HEADS, P]), ALU.mult).then_inc(masked, 1)
                    for half, c in enumerate((0, 1) if d == 0 else (1, 0)):
                        dve.wait_ge(outer, n * 2 + half + 1)
                        if u is not None:
                            dve.wait_ge(sread, u * 2 + half + 1)
                        if u is not None or n or half:
                            dve.wait_ge(upd, n * 2 + half)
                        for h in range(G_HEADS):
                            ins = dve.scalar_tensor_tensor(S[d][:, h, :], S[d][:, h, :], dec[:, tile, 8 * d + 2 * h + c:8 * d + 2 * h + c + 1],
                                                           pd[:, h, :], ALU.mult, ALU.add)
                        ins.then_inc(upd, 1)
                        if half == 0:
                            following()
                    if u is not None:
                        dve.wait_ge(added, u + 1)
                        dve.tensor_tensor(O[:, tile, :], O[:, tile, :], po[:, :, :].rearrange("p h e -> p (h e)"), ALU.add).then_inc(added, 1)
                run(dve, front, back)

            @block.tensor
            def _(pe):
                pe.wait_ge(small, 16)
                pe.wait_ge(zeroed, 3)

                def front(d, n, u, tile, j):
                    la_d = la[:, bass.ds(tile, 1), GK * d:GK * d + GK]
                    if u is not None:
                        pe.matmul(pA[:, :], masks[:, upto[d], :], la_d, start=True, stop=True)
                    pe.matmul(pB[:, :], masks[:, after[d], :], la_d, start=True, stop=True).then_inc(cum, 1)

                def back(d, n, u, tile, j, following):
                    if u is not None:
                        pe.wait_ge(prod, u + 1)
                        for h in range(G_HEADS):
                            pe.transpose(pq[:, h, :], qd[:, G_DK * h:G_DK * h + G_DK], g.ident[:, :])
                        for h in range(G_HEADS):
                            mm = pe.transpose(pk[:, h, :], kd[:, G_DK * h:G_DK * h + G_DK], g.ident[:, :])
                        mm.then_inc(turned, 1)
                    pe.wait_ge(kept, n + 1)
                    if u is None:
                        pe.wait_ge(qkv_in[d], j * 16 + 16)
                    order = (0, 1) if d == 0 else (1, 0)

                    def outers(c):
                        toks = slice(64 * c, 64 * c + 64)
                        for h in range(G_HEADS):
                            mm = pe.matmul(pd[:, h, :], ke[d][toks, G_DK * h:G_DK * h + G_DK],
                                           qkv[d][toks, 2 * GK + G_DV * h:2 * GK + G_DV * h + G_DV], start=True, stop=True)
                        mm.then_inc(outer, 1)

                    def from_state(c):
                        toks = slice(64 * c, 64 * c + 64)
                        for h in range(G_HEADS):
                            mm = pe.matmul(po[toks, h, :], qdT[:, h, toks], S[d][:, h, :], start=False, stop=(c == order[1]),
                                           skip_group_check=True)
                        mm.then_inc(sread, 1)

                    if u is not None or n:
                        pe.wait_ge(upd, n * 2)
                    outers(order[0])
                    if u is not None:
                        pe.wait_ge(qT_done, u + 1)
                        pe.wait_ge(kT_done, u + 1)
                        for h in range(G_HEADS):
                            mm = pe.matmul(pA[:, P * h:P * h + P], kdT[:, h, :], qdT[:, h, :], start=True, stop=True)
                        mm.then_inc(att, 1)
                        pe.wait_ge(masked, u + 1)
                        pe.wait_ge(added, u + 1)
                        for h in range(G_HEADS):
                            pe.matmul(po[:, h, :], at[:, h, :], qkv[d][:, 2 * GK + G_DV * h:2 * GK + G_DV * h + G_DV],
                                      start=(h % 2 == 0), stop=False, skip_group_check=True)
                        from_state(order[0])
                    following()
                    pe.wait_ge(upd, n * 2 + 1)
                    if u is not None:
                        from_state(order[1])
                    outers(order[1])
                run(pe, front, back)


def merge_odd(nc, a, g, hT, p1, O):
    parts = [(NT,)]
    with Phase(nc, "mo") as ph:
        gt = [ph.sb(f"gt{s}", [P, G_HEADS, G_DV]) for s in range(2)]
        gain = ph.sb("gain", [P, G_DV])
        sq = ph.sb("sq", [P, G_HEADS, G_DV])
        on = [ph.sb(f"on{s}", [P, G_HEADS, G_DV]) for s in range(2)]
        ss = ph.sb("ss", [P, 2, G_HEADS])
        pt = [ph.ps(f"pt{s}", [P, KD, P]) for s in range(2)]
        small, in0, in1, squared, summed, rooted, normed, gated, merged, turned, hi_done, lo_done, dstep = ph.sems(
            "small in0 in1 squared summed rooted normed gated merged turned hi_done lo_done dstep")
        g_in = [in0, in1]
        with nc.Block() as block:
            @block.sync
            def _(sp):
                sp.dma_start(gain[:, :], rows(a["gla_out_norm"][0, :])).then_inc(small, 16)

                def load(s, t):
                    sp.dma_start(gt[s][:, :, :], p1[bass.ds(t * P, P), 2048:3072]).then_inc(g_in[s], 16)
                for s in range(2):
                    load(s, s)
                with sp.Fori(1, NT // 2, 1) as i:
                    for s in range(2):
                        sp.wait_ge(merged, i * 2 + s - 1)
                        load(s, i * 2 + s)

            @block.scalar
            def _(act):
                def gate(n, s, part, t):
                    act.activation(sq[:, :, :], O[:, bass.ds(t, 1), :].rearrange("p a (h e) -> p (a h) e", e=G_DV), ACT.Square).then_inc(squared, 1)
                    act.wait_ge(g_in[s], (t - s) * 8 + 16)
                    act.activation(gt[s][:, :, :], gt[s][:, :, :], ACT.Silu).then_inc(gated, 1)
                    act.wait_ge(summed, n + 1)
                    act.activation(ss[:, s, :], ss[:, s, :], ACT.Sqrt, scale=1.0 / G_DV, bias=g.epsc[:, :]).then_inc(rooted, 1)

                def high(n, s, part, t):
                    act.wait_ge(turned, n + 1)
                    act.activation(hT[0][:, :, bass.ds(t * P, P)], pt[s][:, :, :], ACT.Copy).then_inc(hi_done, 1)
                in_turn(act, parts, gate, high)

            @block.vector
            def _(dve):
                dve.wait_ge(small, 16)
                per = 2

                def norm(n, s, part, t):
                    ch = Chain(dve, dstep, n * per)
                    dve.wait_ge(squared, n + 1)
                    dve.tensor_reduce(ss[:, s, :], sq[:, :, :], AX.X, ALU.add).then_inc(summed, 1)
                    dve.wait_ge(rooted, n + 1)
                    ch.link(dve.reciprocal(ss[:, s, :], ss[:, s, :]))
                    ch.link(dve.tensor_tensor(on[s][:, :, :], O[:, bass.ds(t, 1), :].rearrange("p a (h e) -> p (a h) e", e=G_DV),
                                              ss[:, s, :].unsqueeze(2).broadcast_to([P, G_HEADS, G_DV]), ALU.mult))
                    assert ch.k == per
                    dve.tensor_tensor(on[s][:, :, :], on[s][:, :, :],
                                      gain[:, :].unsqueeze(1).broadcast_to([P, G_HEADS, G_DV]), ALU.mult).then_inc(normed, 1)

                def low(n, s, part, t):
                    cols = bass.ds(t * P, P)
                    dve.wait_ge(hi_done, n + 1)
                    lo_part(dve, hT[1][:, :, cols], pt[s][:, :, :], hT[0][:, :, cols]).then_inc(lo_done, 1)
                in_turn(dve, parts, norm, low)

            @block.gpsimd
            def _(pool):
                def merge(n, s, part, t):
                    pool.wait_ge(normed, n + 1)
                    pool.wait_ge(gated, n + 1)
                    pool.tensor_tensor(on[s][:, :, :], on[s][:, :, :], gt[s][:, :, :], ALU.mult).then_inc(merged, 1)
                in_turn(pool, parts, merge, lambda *tile: None)

            @block.tensor
            def _(pe):
                def turn(n, s, part, t):
                    pe.wait_ge(merged, n + 1)
                    if not (isinstance(n, int) and n < 2):
                        pe.wait_ge(lo_done, n - 1)
                    flat = on[s][:, :, :].rearrange("p h e -> p (h e)")
                    for k in range(KD):
                        mm = pe.transpose(pt[s][:, k, :], flat[:, P * k:P * k + P], g.ident[:, :])
                    mm.then_inc(turned, 1)
                in_turn(pe, parts, turn, lambda *tile: None)


CUT = (T2 // 3 + 2) // 2 * 2
NCUT = [(0, 512), (512, 1024), (1024, T2)]
THIRDS = [(0, CUT), (CUT, 2 * CUT), (2 * CUT, T2)]


def project_cols(nc, hT, tag, w_dram, c_from, nblk, dst, narrow=None):
    BLK = 256
    w_v = w_dram.rearrange("(k p) n -> p k n", p=P)
    with Phase(nc, tag) as ph:
        w = Weights(ph, KD, BLK)
        o = [ph.sb(f"o{b}", [P, T2]) for b in range(2)]
        wn_raw = ph.sb("wn_raw", [P, KD, 8])
        wn = ph.pair("wn", [P, KD, 8])
        on = ph.sb("on", [8, T2])
        pb = [ph.ps(f"pb{b}", [P, 3, 512]) for b in range(2)]
        in_n, hi_n, lo_n, made_n, copied_n, st_n = ph.sems("in_n hi_n lo_n made_n copied_n st_n")
        made, copied, stored = ph.sems("made0 made1"), ph.sems("copied0 copied1"), ph.sems("stored0 stored1")

        def first_two(t):
            return t[:, 0:2 * CUT].rearrange("p (j t) -> p j t", j=2)

        with nc.Block() as block:
            @block.gpsimd
            def _(pool):
                def load(b):
                    w.load(pool, b, lambda k0, k1: w_v[:, k0:k1, bass.ds(c_from + b * BLK, BLK)])
                load(0)
                if narrow:
                    with nc.allow_non_contiguous_dma(reason="eight columns of the weights"):
                        pool.dma_start(wn_raw[:, :, :], w_v[:, :, narrow[0]:narrow[0] + narrow[1]]).then_inc(in_n, 16)
                with pool.Fori(1, nblk, 1) as b:
                    load(b)

            @block.sync
            def _(sp):
                for b in range(2):
                    sp.sem_inc(stored[b], 16)
                with sp.Fori(0, nblk // 2, 1) as i:
                    for s in range(2):
                        for b in range(2):
                            m = i * 2 + s
                            sp.wait_ge(copied[b], m + 1)
                            sp.dma_start(dst[bass.ds(m * BLK + b * P, P), :], o[b][:, :]).then_inc(stored[b], 16)
                if narrow:
                    sp.wait_ge(copied_n, 1)
                    sp.dma_start(narrow[2], on[0:narrow[1], :]).then_inc(st_n, 16)
                    sp.wait_ge(st_n, 16)
                for b in range(2):
                    sp.wait_ge(stored[b], 16 + 16 * nblk)

            @block.scalar
            def _(act):
                w.make_hi(act, 0, 0)
                if narrow:
                    act.wait_ge(in_n, 16)
                    act.activation(wn[0][:, :, :], wn_raw[:, :, :], ACT.Copy).then_inc(hi_n, 1)

                def step(i, s, first, last):
                    m = i * 2 + s
                    if not last:
                        if not first:
                            act.wait_ge(made[1], m)
                        w.make_hi(act, m + 1, 1 - s)
                    act.wait_ge(made[0], m + 1)
                    act.wait_ge(stored[0], m * 16 + 16)
                    act.activation(first_two(o[0]), pb[0][:, 0:2, 0:CUT], ACT.Copy)
                    act.activation(o[0][:, 2 * CUT:], pb[0][:, 2, 0:T2 - 2 * CUT], ACT.Copy).then_inc(copied[0], 1)
                in_pairs(act, nblk, step)
                if narrow:
                    act.wait_ge(made_n, 1)
                    act.activation(first_two(on), pb[0][0:narrow[1], 0:2, 0:CUT], ACT.Copy)
                    act.activation(on[:, 2 * CUT:], pb[0][0:narrow[1], 2, 0:T2 - 2 * CUT], ACT.Copy).then_inc(copied_n, 1)

            @block.vector
            def _(dve):
                w.make_lo(dve, 0, 0)
                if narrow:
                    dve.wait_ge(hi_n, 1)
                    lo_part(dve, wn[1][:, :, :], wn_raw[:, :, :], wn[0][:, :, :]).then_inc(lo_n, 1)

                def step(i, s, first, last):
                    m = i * 2 + s
                    if not last:
                        w.make_lo(dve, m + 1, 1 - s)
                    dve.wait_ge(made[1], m + 1)
                    dve.wait_ge(stored[1], m * 16 + 16)
                    dve.tensor_copy(first_two(o[1]), pb[1][:, 0:2, 0:CUT])
                    dve.tensor_copy(o[1][:, 2 * CUT:], pb[1][:, 2, 0:T2 - 2 * CUT]).then_inc(copied[1], 1)
                in_pairs(dve, nblk, step)

            @block.tensor
            def _(pe):
                with pe.Fori(0, nblk // 2, 1) as i:
                    for s in range(2):
                        m = i * 2 + s
                        w.ready(pe, m)
                        for b in range(2):
                            pe.wait_ge(stored[b], m * 16 + 16)
                            for j, (c0, c1) in enumerate(THIRDS):
                                for k in range(KD):
                                    mm = product(pe, pb[b][:, j, 0:c1 - c0], w.cut(s, k, P * b, P * b + P),
                                                 [h[:, k, c0:c1] for h in hT], k == 0, k == KD - 1)
                            mm.then_inc(made[b], 1)
                if narrow:
                    pe.wait_ge(lo_n, 1)
                    pe.wait_ge(copied[0], nblk)
                    for j, (c0, c1) in enumerate(THIRDS):
                        for k in range(KD):
                            mm = product(pe, pb[0][0:narrow[1], j, 0:c1 - c0], [h[:, k, 0:narrow[1]] for h in wn],
                                         [h[:, k, c0:c1] for h in hT], k == 0, k == KD - 1)
                    mm.then_inc(made_n, 1)


LRU = 256
NL = LRU // P
CONV_A = 4
LRU_C = 8.0


def linear_recurrence(nc, a, g, pT):
    with Phase(nc, "lr") as ph:
        x = ph.sb("x", [P, NL, CONV_A - 1 + T2])
        y = ph.sb("y", [P, NL, T2])
        cw = ph.sb("cw", [P, NL, CONV_A])
        vec = ph.sb("vec", [P, 4, NL])
        sp_ = ph.sb("sp", [P, 3, NL])
        gw = ph.sb("gw", [P, 2, NL, P])
        u = ph.sb("u", [P, NL, T2])
        r = ph.sb("r", [P, NL, T2])
        gi = ph.sb("gi", [P, NL, T2])
        th = ph.sb("th", [P, NL, T2])
        pr = ph.ps("pr", [P, 1536])
        pi = ph.ps("pi", [P, 1536])
        small, zeroed, conv, gates, sig, lam_e, lam_l, decayed, tanhed, ratio, rooted, gelued, dstep = ph.sems(
            "small zeroed conv gates sig lam_e lam_l decayed tanhed ratio rooted gelued dstep")
        with nc.Block() as block:
            @block.sync
            def _(sp):
                sp.wait_ge(zeroed, 2)
                with nc.allow_non_contiguous_dma(reason="short vectors, feature-major"):
                    for c in range(NL):
                        sp.dma_start(cw[:, c, :], a["lru_conv_w_2"][0, :, P * c:P * c + P].rearrange("t p -> p t")).then_inc(small, 16)
                    for j, name in enumerate(("lru_conv_b_2", "lru_gate_a_b_2", "lru_gate_x_b_2", "lru_lambda_2")):
                        sp.dma_start(vec[:, j, :], a[name][0, :].rearrange("(c p) -> p c", p=P)).then_inc(small, 16)
                for j, name in enumerate(("lru_gate_a_w_2", "lru_gate_x_w_2")):
                    for h in range(4):
                        half = slice(64 * (h % 2), 64 * (h % 2) + 64)
                        sp.dma_start(gw[half, j, h // 2, half], a[name][0, h, :, :]).then_inc(small, 16)
                sp.dma_start(x[:, :, CONV_A - 1:], pT[0:LRU, :].rearrange("(c p) t -> p c t", p=P)).then_inc(small, 16)
                sp.dma_start(y[:, :, :], pT[LRU:2 * LRU, :].rearrange("(c p) t -> p c t", p=P)).then_inc(small, 16)
                sp.wait_ge(small, 16 * 16)

            @block.gpsimd
            def _(pool):
                pool.memset(x[:, :, 0:CONV_A - 1], 0.0).then_inc(zeroed, 1)
                pool.memset(gw[:, :, :, :], 0.0).then_inc(zeroed, 1)

            @block.scalar
            def _(act):
                act.wait_ge(small, 16 * 16)
                act.activation(sp_[:, 0, :], vec[:, 3, :], ACT.Abs).then_inc(lam_e, 1)
                act.wait_ge(lam_e, 1)
                act.activation(sp_[:, 1, :], sp_[:, 0, :], ACT.Exp, scale=-1.0).then_inc(lam_e, 1)
                act.wait_ge(lam_e, 2)
                act.activation(sp_[:, 2, :], sp_[:, 1, :], ACT.Ln, bias=1.0).then_inc(lam_l, 1)
                for c in range(NL):
                    act.wait_ge(gates, c + 1)
                    act.activation(r[:, c, :], pr[:, 0:T2], ACT.Sigmoid, bias=vec[:, 1, c:c + 1])
                    act.activation(gi[:, c, :], pi[:, 0:T2], ACT.Sigmoid, bias=vec[:, 2, c:c + 1]).then_inc(sig, 1)
                act.wait_ge(decayed, 1)
                act.activation(th[:, :, :], r[:, :, :], ACT.Tanh).then_inc(tanhed, 1)
                act.activation(r[:, :, :], r[:, :, :], ACT.Exp).then_inc(tanhed, 1)
                act.wait_ge(ratio, 1)
                act.activation(th[:, :, :], th[:, :, :], ACT.Sqrt).then_inc(rooted, 1)
                act.activation(y[:, :, :], y[:, :, :], ACT.Gelu_apprx_tanh).then_inc(gelued, 1)

            @block.vector
            def _(dve):
                ch = Chain(dve, dstep)
                dve.wait_ge(small, 16 * 16)
                dve.wait_ge(zeroed, 2)
                for c in range(NL):
                    ch.link(dve.tensor_scalar(u[:, c, :], x[:, c, 0:T2], cw[:, c, 0:1], vec[:, 0, c:c + 1], ALU.mult, ALU.add))
                    for j in range(1, CONV_A):
                        ins = dve.scalar_tensor_tensor(u[:, c, :], x[:, c, j:j + T2], cw[:, c, j:j + 1], u[:, c, :], ALU.mult, ALU.add)
                        if j < CONV_A - 1:
                            ch.link(ins)
                    ins.then_inc(conv, 1)
                dve.wait_ge(lam_l, 1)
                ch.link(dve.tensor_scalar(sp_[:, 0, :], vec[:, 3, :], -1.0, 0.0, ALU.mult, ALU.max))
                ch.link(dve.tensor_tensor(sp_[:, 0, :], sp_[:, 0, :], sp_[:, 2, :], ALU.add))
                ch.link(dve.tensor_scalar(sp_[:, 0, :], sp_[:, 0, :], -LRU_C, None, ALU.mult))
                dve.wait_ge(sig, NL)
                for c in range(NL):
                    ins = dve.tensor_scalar(r[:, c, :], r[:, c, :], sp_[:, 0, c:c + 1], None, ALU.mult)
                ins.then_inc(decayed, 1)
                ch.link(dve.tensor_tensor(gi[:, :, :], gi[:, :, :], u[:, :, :], ALU.mult))
                dve.wait_ge(tanhed, 1)
                ch.link(dve.tensor_scalar(u[:, :, :], th[:, :, :], -1.0, 1.0, ALU.mult, ALU.add))
                ch.link(dve.reciprocal(u[:, :, :], u[:, :, :]))
                dve.scalar_tensor_tensor(th[:, :, :], th[:, :, :], -2.0, u[:, :, :], ALU.mult, ALU.mult).then_inc(ratio, 1)
                dve.wait_ge(rooted, 1)
                ch.link(dve.tensor_tensor(gi[:, :, :], gi[:, :, :], th[:, :, :], ALU.mult))
                dve.wait_ge(tanhed, 2)
                for c in range(NL):
                    ins = dve.tensor_tensor_scan(u[:, c, :], r[:, c, :], gi[:, c, :], 0.0, ALU.mult, ALU.add)
                ch.link(ins)
                dve.wait_ge(gelued, 1)
                ch.link(dve.tensor_tensor(g.hT[:, 0:NL, 0:T2], u[:, :, :], y[:, :, :], ALU.mult))

            @block.tensor
            def _(pe):
                pe.wait_ge(small, 16 * 16)
                for c in range(NL):
                    pe.wait_ge(conv, c + 1)
                    if c:
                        pe.wait_ge(sig, c)
                    for j, ps in enumerate((pr, pi)):
                        for c0, c1 in NCUT:
                            mm = pe.matmul(ps[:, c0:c1], gw[:, j, c, :], u[:, c, c0:c1], start=True, stop=True)
                    mm.then_inc(gates, 1)


FOX_HEADS = 8
AUG = HD + 2


def forget_sums(nc, a, g, fT, cum_dram):
    with Phase(nc, "fs") as ph:
        f = ph.sb("f", [FOX_HEADS, T2])
        e = ph.sb("e", [FOX_HEADS, T2])
        one = ph.sb("one", [FOX_HEADS, T2])
        bias = ph.sb("bias", [FOX_HEADS, 1])
        small, absed, logged, summed, stored, dstep = ph.sems("small absed logged summed stored dstep")
        with nc.Block() as block:
            @block.sync
            def _(sp):
                sp.dma_start(f[:, :], fT).then_inc(small, 16)
                with nc.allow_non_contiguous_dma(reason="a short vector"):
                    sp.dma_start(bias[:, :], a["fox_f_bias_2"].rearrange("o h -> h o")).then_inc(small, 16)
                sp.wait_ge(summed, 1)
                sp.dma_start(cum_dram[0, :, :], f[:, :]).then_inc(stored, 16)
                sp.dma_start(cum_dram[1, :, :], e[:, :]).then_inc(stored, 16)
                sp.wait_ge(stored, 32)

            @block.scalar
            def _(act):
                act.wait_ge(small, 32)
                act.activation(e[:, :], f[:, :], ACT.Abs, bias=bias[:, :]).then_inc(absed, 1)
                act.wait_ge(absed, 1)
                act.activation(e[:, :], e[:, :], ACT.Exp, scale=-1.0).then_inc(absed, 1)
                act.wait_ge(absed, 2)
                act.activation(e[:, :], e[:, :], ACT.Ln, bias=1.0).then_inc(logged, 1)

            @block.vector
            def _(dve):
                ch = Chain(dve, dstep)
                dve.wait_ge(small, 32)
                ch.step(dve.memset(one[:, :], 1.0))
                dve.wait_ge(absed, 1)
                ch.link(dve.tensor_scalar(f[:, :], f[:, :], bias[:, :], 0.0, ALU.add, ALU.min))
                dve.wait_ge(logged, 1)
                ch.link(dve.tensor_tensor(f[:, :], f[:, :], e[:, :], ALU.subtract))
                ch.link(dve.tensor_tensor_scan(e[:, :], one[:, :], f[:, :], 0.0, ALU.mult, ALU.add))
                ch.link(dve.tensor_scalar(f[:, :], e[:, :], 1.0 / SCALE, None, ALU.mult))
                dve.tensor_scalar(e[:, :], f[:, :], -1.0, None, ALU.mult).then_inc(summed, 1)


def forgetting_attention(nc, a, g, pT, pv, cum):
    NT2 = len(TILES2)
    with Phase(nc, "fx") as ph:
        q = [ph.sb(f"q{s}", [AUG, T2]) for s in range(2)]
        k = [ph.sb(f"k{s}", [AUG, T2]) for s in range(2)]
        vs = [ph.sb(f"v{s}", [P, NT2, HD]) for s in range(2)]
        causal = ph.sb("causal", [P, P])
        E = [ph.sb(f"E{b}", [P, T2]) for b in range(2)]
        ET = ph.sb("ET", [P, NT2, P])
        mx = ph.sb("mx", [P, 2])
        nm = ph.sb("nm", [P, 2])
        l = ph.sb("l", [P, 2])
        r = ph.sb("r", [P, 2])
        pS = [ph.ps(f"pS{b}", [P, 1536]) for b in range(2)]
        pT_ = ph.ps("pT", [P, 4, P])
        po = ph.ps("po", [P, 512])
        small, ones, in0, in1, scores, topped, negmax, expd, weights, turned, evac, values_in, o_done, dstep = ph.sems(
            "small ones in0 in1 scores topped negmax expd weights turned evac values_in o_done dstep")
        qk_in = [in0, in1]
        seq = [(s, j) for s in range(2) for j in range(NT2)]
        NS = len(seq)

        def groups(j):
            return [(a0, min(a0 + 4, j + 1)) for a0 in range(0, j + 1, 4)]

        def groups_before(n):
            return sum(len(groups(seq[m][1])) for m in range(n))

        per_round = groups_before(NS)
        with nc.Block() as block:
            @block.sync
            def _(sp):
                sp.wait_ge(ones, 6)
                def load(s, h):
                    sp.dma_start(q[s][0:HD, :], pT[bass.ds(512 + h * HD, HD), :]).then_inc(qk_in[s], 16)
                    sp.dma_start(k[s][0:HD, :], pT[bass.ds(1024 + h * HD, HD), :]).then_inc(qk_in[s], 16)
                    sp.dma_start(q[s][HD:HD + 1, :], cum[0, bass.ds(h, 1), :]).then_inc(qk_in[s], 16)
                    sp.dma_start(k[s][HD + 1:HD + 2, :], cum[1, bass.ds(h, 1), :]).then_inc(qk_in[s], 16)
                    sp.dma_start(vs[s][0:META, 0, :], pv[0:META, bass.ds(h * HD, HD)]).then_inc(qk_in[s], 16)
                    sp.dma_start(vs[s][:, 1:, :], pv[META:T2, bass.ds(h * HD, HD)].rearrange("(t p) d -> p t d", p=P)).then_inc(qk_in[s], 16)
                for s in range(2):
                    load(s, s)
                sp.dma_start(causal[:, :], a["k_causal"]).then_inc(small, 16)
                with sp.Fori(1, FOX_HEADS // 2, 1) as i:
                    for s in range(2):
                        sp.wait_ge(values_in, (i - 1) * NS + NT2 * (s + 1))
                        load(s, i * 2 + s)

            @block.gpsimd
            def _(pool):
                first = [(E[s][:, 0:META], 0.0) for s in range(2)] + [(x[s][HD:HD + 2, :], 1.0) for s in range(2) for x in (q, k)]
                for m, (cells, value) in enumerate(first):
                    if m:
                        pool.wait_ge(ones, m)
                    pool.memset(cells, value).then_inc(ones, 1)

            @block.scalar
            def _(act):
                act.wait_ge(ones, 6)
                with act.Fori(0, FOX_HEADS // 2, 1) as i:
                    def exps(n):
                        s, j = seq[n]
                        b, (c0, rr) = n % 2, TILES2[j]
                        act.wait_ge(negmax, i * NS + n + 1)
                        act.activation(E[b][0:rr, 0:c0 + rr], pS[b][0:rr, 0:c0 + rr], ACT.Exp, scale=SCALE,
                                       bias=nm[0:rr, b:b + 1], accum_out=l[0:rr, b:b + 1]).then_inc(expd, 1)
                    exps(0)
                    for n, (s, j) in enumerate(seq):
                        rr = TILES2[j][1]
                        for gi, (a0, a1) in enumerate(groups(j)):
                            act.wait_ge(turned, i * per_round + groups_before(n) + gi + 1)
                            if a0 == 0:
                                ins = act.activation(ET[0:META, 0, 0:rr], pT_[0:META, 0, 0:rr], ACT.Copy)
                            b0 = max(a0, 1)
                            if a1 > b0:
                                ins = act.activation(ET[:, b0:a1, 0:rr], pT_[:, b0 - a0:a1 - a0, 0:rr], ACT.Copy)
                            ins.then_inc(evac, 1)
                        if n + 1 < NS:
                            exps(n + 1)

            @block.vector
            def _(dve):
                dve.wait_ge(small, 16)
                with dve.Fori(0, FOX_HEADS // 2, 1) as i:
                    ch = Chain(dve, dstep, i * 2 * NS)

                    def maxima(n):
                        s, j = seq[n]
                        b, (c0, rr) = n % 2, TILES2[j]
                        dve.wait_ge(scores, i * NS + n + 1)
                        ch.link(dve.tensor_tensor(pS[b][0:rr, c0:c0 + rr], pS[b][0:rr, c0:c0 + rr], causal[0:rr, 0:rr], ALU.add))
                        dve.tensor_reduce(mx[0:rr, b:b + 1], pS[b][0:rr, 0:c0 + rr], AX.X, ALU.max).then_inc(topped, 1)
                        dve.wait_ge(topped, i * NS + n + 1)
                        dve.tensor_scalar(nm[0:rr, b:b + 1], mx[0:rr, b:b + 1], -SCALE, None, ALU.mult).then_inc(negmax, 1)

                    maxima(0)
                    for n, (s, j) in enumerate(seq):
                        b, (c0, rr) = n % 2, TILES2[j]
                        dve.wait_ge(expd, i * NS + n + 1)
                        ch.link(dve.reciprocal(r[0:rr, b:b + 1], l[0:rr, b:b + 1]))
                        dve.tensor_scalar(E[b][0:rr, 0:c0 + rr], E[b][0:rr, 0:c0 + rr], r[0:rr, b:b + 1], None, ALU.mult).then_inc(weights, 1)
                        if n + 1 < NS:
                            maxima(n + 1)
                        dve.wait_ge(values_in, i * NS + n + 1)
                        half = slice(64 * s, 64 * s + 64)
                        dve.tensor_copy(g.hT[half, bass.ds(i + 2, 1), c0:c0 + rr], po[half, 0:rr]).then_inc(o_done, 1)
                    assert ch.k == 2 * NS

            @block.tensor
            def _(pe):
                pe.wait_ge(small, 16)
                with pe.Fori(0, FOX_HEADS // 2, 1) as i:
                    def scores_of(n):
                        s, j = seq[n]
                        b, (c0, rr) = n % 2, TILES2[j]
                        if j == 0:
                            pe.wait_ge(qk_in[s], i * 96 + 96)
                        if n >= 2:
                            pe.wait_ge(expd, i * NS + n - 1)
                        for k0, k1 in NCUT:
                            k1 = min(k1, c0 + rr)
                            if k0 < k1:
                                mm = pe.matmul(pS[b][0:rr, k0:k1], q[s][:, c0:c0 + rr], k[s][:, k0:k1], start=True, stop=True)
                        mm.then_inc(scores, 1)

                    scores_of(0)
                    for n, (s, j) in enumerate(seq):
                        b, (c0, rr) = n % 2, TILES2[j]
                        if n + 1 < NS:
                            scores_of(n + 1)
                        pe.wait_ge(weights, i * NS + n + 1)
                        te = P if j == 0 else rr
                        gs = groups(j)
                        half = slice(64 * s, 64 * s + 64)

                        def values(gi):
                            for t in range(*gs[gi]):
                                kr = TILES2[t][1]
                                mm = pe.matmul(po[half, 0:rr], vs[s][0:kr, t, :], ET[0:kr, t, 0:rr], start=(t == 0), stop=(t == j))
                            return mm

                        for gi, (a0, a1) in enumerate(gs):
                            for t in range(a0, a1):
                                k0, kr = TILES2[t]
                                mm = pe.transpose(pT_[0:kr, t - a0, 0:te], E[b][0:te, k0:k0 + kr], g.ident[0:te, 0:te])
                            mm.then_inc(turned, 1)
                            if gi:
                                values(gi - 1)
                            pe.wait_ge(evac, i * per_round + groups_before(n) + gi + 1)
                        values(len(gs) - 1).then_inc(values_in, 1)


RW = 256
RW_HEADS = 4
TP = P * len(TILES2)
PADT = TP - T2
R_, K_, V_, KK_, LW_, A_, G_ = (2 * j for j in range(7))
GN_EPS = 64e-5


def delta_inputs(nc, a, g, pT, F):
    with Phase(nc, "di") as ph:
        p = ph.sb("p", [P, 8, 1 + T2])
        d = ph.sb("d", [P, T2])
        kx = ph.sb("kx", [P, 2, T2])
        mu = ph.sb("mu", [P, 8])
        vec = ph.sb("vec", [P, 5, 2])
        up = ph.sb("up", [P, RW])
        gup = ph.sb("gup", [P, RW])
        pw = ph.ps("pw", [P, 1536])
        pa = ph.ps("pa", [P, 1536])
        small, padded, shifted, lora, gated, w_made, a_made, g_made, w_sig, a_sig, g_copied, dstep = ph.sems(
            "small padded shifted lora gated w_made a_made g_made w_sig a_sig g_copied dstep")
        with nc.Block() as block:
            @block.sync
            def _(sp):
                sp.dma_start(p[:, :, 1:], pT[2056:3080, :].rearrange("(c p) t -> p c t", p=P)).then_inc(small, 16)
                with nc.allow_non_contiguous_dma(reason="short vectors, feature-major"):
                    sp.dma_start(mu[:, :], a["rwkv_mu_2"][0, :].rearrange("(c p) -> p c", p=P)).then_inc(small, 16)
                    for j, name in enumerate(("rwkv_w0_2", "rwkv_a0_2", "rwkv_k_k_2", "rwkv_k_a_2")):
                        sp.dma_start(vec[:, j, :], a[name][0, :].rearrange("(c p) -> p c", p=P)).then_inc(small, 16)
                sp.dma_start(up[0:64, :], a["rwkv_w_up_2"][0, :, :]).then_inc(small, 16)
                sp.dma_start(up[64:P, :], a["rwkv_a_up_2"][0, :, :]).then_inc(small, 16)
                sp.dma_start(gup[:, :], a["rwkv_g_up_2"][0, :, :]).then_inc(small, 16)

            @block.gpsimd
            def _(pool):
                pool.memset(F[:, :, 0:PADT], 0.0).then_inc(padded, 1)
                pool.memset(p[:, :, 0:1], 0.0).then_inc(padded, 1)

            @block.scalar
            def _(act):
                act.wait_ge(small, 16 * 9)
                act.wait_ge(shifted, 1)
                act.activation(p[0:64, 6, 1:], p[0:64, 6, 1:], ACT.Tanh).then_inc(lora, 1)
                act.wait_ge(shifted, 2)
                act.activation(p[:, 7, 1:], p[:, 7, 1:], ACT.Sigmoid).then_inc(gated, 1)
                for c in range(2):
                    act.wait_ge(w_made, c + 1)
                    act.activation(F[:, LW_ + c, PADT:], pw[:, 0:T2], ACT.Sigmoid, bias=vec[:, 0, c:c + 1]).then_inc(w_sig, 1)
                    act.wait_ge(a_made, c + 1)
                    act.activation(F[:, A_ + c, PADT:], pa[:, 0:T2], ACT.Sigmoid, bias=vec[:, 1, c:c + 1]).then_inc(a_sig, 1)
                for c in range(2):
                    act.wait_ge(g_made, c + 1)
                    act.activation(F[:, G_ + c, PADT:], (pw, pa)[c][:, 0:T2], ACT.Copy).then_inc(g_copied, 1)

            @block.vector
            def _(dve):
                ch = Chain(dve, dstep)
                dve.wait_ge(small, 16 * 9)
                dve.wait_ge(padded, 2)
                for c in (6, 7, 2, 3, 0, 1, 4, 5):
                    dst = {6: p[:, 6, 1:], 7: p[:, 7, 1:], 2: kx[:, 0, :], 3: kx[:, 1, :], 0: F[:, R_, PADT:],
                           1: F[:, R_ + 1, PADT:], 4: F[:, V_, PADT:], 5: F[:, V_ + 1, PADT:]}[c]
                    ch.link(dve.tensor_tensor(d[:, :], p[:, c, 0:T2], p[:, c, 1:], ALU.subtract))
                    ins = dve.scalar_tensor_tensor(dst, d[:, :], mu[:, c:c + 1], p[:, c, 1:], ALU.mult, ALU.add)
                    if c >= 6:
                        ins.then_inc(shifted, 1)
                        dve.wait_ge(shifted, c - 5)
                    else:
                        ch.link(ins)
                for c in range(2):
                    dve.tensor_scalar(F[:, KK_ + c, PADT:], kx[:, c, :], vec[:, 2, c:c + 1], None, ALU.mult)
                ch.link(dve.tensor_scalar(vec[:, 4, :], vec[:, 3, :], -1.0, 1.0, ALU.mult, ALU.add))
                for c in range(2):
                    dve.wait_ge(w_sig, c + 1)
                    dve.tensor_scalar(F[:, LW_ + c, PADT:], F[:, LW_ + c, PADT:], -(2.718281828459045 ** -0.5), None, ALU.mult)
                    dve.wait_ge(a_sig, c + 1)
                    ch.link(dve.tensor_scalar(d[:, :], F[:, A_ + c, PADT:], vec[:, 3, c:c + 1], vec[:, 4, c:c + 1], ALU.mult, ALU.add))
                    ch.link(dve.tensor_tensor(F[:, K_ + c, PADT:], kx[:, c, :], d[:, :], ALU.mult))

            @block.tensor
            def _(pe):
                pe.wait_ge(lora, 1)
                for c in range(2):
                    cols = slice(P * c, P * c + P)
                    if c:
                        pe.wait_ge(w_sig, c)
                    for c0, c1 in NCUT:
                        mm = pe.matmul(pw[:, c0:c1], up[0:64, cols], p[0:64, 6, 1 + c0:1 + c1], start=True, stop=True)
                    mm.then_inc(w_made, 1)
                    if c:
                        pe.wait_ge(a_sig, c)
                    for c0, c1 in NCUT:
                        mm = pe.matmul(pa[:, c0:c1], up[64:P, cols], p[64:P, 6, 1 + c0:1 + c1], start=True, stop=True)
                    mm.then_inc(a_made, 1)
                pe.wait_ge(gated, 1)
                for c in range(2):
                    pe.wait_ge((w_sig, a_sig)[c], 2)
                    for c0, c1 in NCUT:
                        mm = pe.matmul((pw, pa)[c][:, c0:c1], gup[:, P * c:P * c + P], p[:, 7, 1 + c0:1 + c1], start=True, stop=True)
                    mm.then_inc(g_made, 1)


def delta_rule(nc, a, g, F):
    NTP = len(TILES2)
    H = RW_HEADS
    LEVELS = 5
    with Phase(nc, "dr") as ph:
        masks = ph.sb("masks", [P, 2, P])
        levels = ph.sb("levels", [P, 6, P])
        chunk_of = ph.sb("chunk_of", [P, 2])
        rk_row = ph.sb("rk_row", [P, RW])
        lnw = ph.sb("lnw", [P, RW])
        lnb = ph.sb("lnb", [P, RW])
        gneps = ph.sb("gneps", [P, 1])
        Fc = ph.sb("Fc", [P, 14, P])
        T = ph.sb("T", [P, 6, RW])
        V = [ph.sb(f"V{s}", [P, RW]) for s in range(2)]
        G = [ph.sb(f"G{s}", [P, RW]) for s in range(2)]
        Vc = [ph.sb(f"Vc{s}", [P, 2, RW]) for s in range(2)]
        Uc = ph.sb("Uc", [P, 2, RW])
        eb = ph.sb("eb", [P, 3, RW])
        dec = [ph.sb(f"dec{s}", [64, H, 2]) for s in range(2)]
        n4 = ph.sb("n4", [P, 4])
        kd = ph.sb("kd", [P, RW])
        hat = [ph.sb(f"hat{s}", [P, 4, RW]) for s in range(2)]
        RT = [ph.sb(f"RT{s}", [64, H, P]) for s in range(2)]
        hatT = ph.sb("hatT", [64, 3, H, P])
        AT = [ph.sb(f"AT{s}", [P, 4, H, P]) for s in range(2)]
        bo = [ph.sb(f"bo{s}", [P, RW]) for s in range(2)]
        Lm = ph.sb("Lm", [P, 2, H, P])
        X = ph.sb("X", [P, H, P])
        XT = ph.sb("XT", [P, H, P])
        Y = ph.sb("Y", [P, H, P])
        P1T = ph.sb("P1T", [64, H, P])
        W = ph.sb("W", [P, RW])
        P2 = ph.sb("P2", [P, RW])
        S = ph.sb("S", [64, RW])
        d = ph.sb("d", [P, RW])
        sq = ph.sb("sq", [P, RW])
        s4 = ph.sb("s4", [P, 4])
        v4 = ph.sb("v4", [P, 4])
        bsum = ph.sb("bsum", [P, 4])
        b = [ph.ps(f"b{j}", [P, 512]) for j in range(8)]
        (small, zeroed, copied, turned, ev_a, ev_d, cum, expd, sqd, rooted, hats, hat_t, hT_a, hT_d, att, masked,
         lvl, x0, x0_t, X_ev, y_made, y_ev, z_made, xs, pre, pre_a, pre_d, p2m, p2e, u_made, u_done, ds_made, s_done,
         bonus, o_made, osq, oroot, vsum, vroot, out_done, out_t, mixed, step_a, step_c) = ph.sems(
            "small zeroed copied turned ev_a ev_d cum expd sqd rooted hats hat_t hT_a hT_d att masked "
            "lvl x0 x0_t X_ev y_made y_ev z_made xs pre pre_a pre_d p2m p2e u_made u_done ds_made s_done "
            "bonus o_made osq oroot vsum vroot out_done out_t mixed step_a step_c")

        def heads(ap):
            return ap.rearrange("p (h d) -> p h d", h=H)

        def wide(ap4, n=64):
            return ap4.unsqueeze(2).broadcast_to([P, 4, n])

        def by_head(ap):
            return ap.rearrange("p (h t) -> p h t", h=H)

        def in_order(eng, tile):
            with eng.Fori(0, NTP // 2 - 1, 1) as i:
                for s in range(2):
                    tile(i * 2 + s, s, 2)
            for n in range(NTP - 3, NTP):
                tile(n, n % 2, NTP - 1 - n)

        with nc.Block() as block:
            @block.sync
            def _(sp):
                sp.dma_start(masks[:, :, :], a["k_masks"][0:4:3, :, :].rearrange("m p k -> p m k")).then_inc(small, 16)
                sp.dma_start(levels[:, :, :], a["k_levels"].rearrange("m p k -> p m k")).then_inc(small, 16)
                sp.dma_start(chunk_of[:, :], a["k_chunk_of"]).then_inc(small, 16)
                sp.dma_start(rk_row[:, :], rows(a["rwkv_r_k_2"].rearrange("o h d -> (o h d)"))).then_inc(small, 16)
                sp.dma_start(lnw[:, :], rows(a["rwkv_ln_w_2"][0, :])).then_inc(small, 16)
                sp.dma_start(lnb[:, :], rows(a["rwkv_ln_b_2"][0, :])).then_inc(small, 16)

            @block.gpsimd
            def _(pool):
                pool.wait_ge(small, 16 * 6)
                cleared = ((Vc[0][:, :, :], 0.0), (Vc[1][:, :, :], 0.0), (Uc[:, :, :], 0.0), (S[:, :], 0.0), (gneps[:, :], GN_EPS))
                for m, (cells, value) in enumerate(cleared):
                    if m:
                        pool.wait_ge(zeroed, m)
                    pool.memset(cells, value).then_inc(zeroed, 1)
                pool.wait_ge(zeroed, 5)

                def place(n):
                    if not (isinstance(n, int) and n == 0):
                        pool.wait_ge(turned, n)
                    pool.tensor_copy(Fc[:, :, :], F[:, :, bass.ds(n * P, P)]).then_inc(copied, 1)
                    pool.wait_ge(copied, n + 1)

                def products(n, s):
                    pool.wait_ge(ev_a, n + 1)
                    pool.tensor_tensor(bo[s][:, :], T[:, 0, :], T[:, 1, :], ALU.mult).then_inc(bonus, 1)
                    pool.wait_ge(bonus, n * 2 + 1)
                    pool.tensor_tensor(bo[s][:, :], bo[s][:, :], rk_row[:, :], ALU.mult).then_inc(bonus, 1)
                    pool.wait_ge(bonus, n * 2 + 2)

                place(0)
                products(0, 0)
                place(1)

                def tile(n, s, more):
                    pool.wait_ge(x0, n + 1)
                    for m in range(LEVELS):
                        if m >= 2:
                            pool.wait_ge(y_made, n * LEVELS + m - 1)
                            pool.wait_ge(lvl, n * LEVELS + m - 1)
                        pool.tensor_tensor(Lm[:, m % 2, :, :], AT[s][:, 0, :, :], levels[:, m + 1, :].unsqueeze(1).broadcast_to([P, H, P]),
                                           ALU.mult).then_inc(lvl, 1)
                    pool.wait_ge(lvl, n * LEVELS + LEVELS)
                    if more:
                        products(n + 1, 1 - s)
                    if more > 1:
                        place(n + 2)
                in_order(pool, tile)

            @block.scalar
            def _(act):
                act.wait_ge(zeroed, 5)

                def take(n, s):
                    act.wait_ge(turned, n + 1)
                    act.activation(T[:, 0:2, :], b[0][:, :], ACT.Copy)
                    act.activation(V[s][:, :], b[1][:, 0:RW], ACT.Copy)
                    act.activation(T[:, 3, :], b[1][:, RW:], ACT.Copy)
                    for c in range(2):
                        toks = slice(64 * c, 64 * c + 64)
                        ins = act.activation(Vc[s][toks, c, :], b[1][toks, 0:RW], ACT.Copy)
                    ins.then_inc(ev_a, 1)

                def decays(n, s):
                    act.wait_ge(sqd, n + 1)
                    act.activation(n4[:, :], n4[:, :], ACT.Sqrt).then_inc(rooted, 1)
                    act.wait_ge(cum, n + 1)
                    act.activation(eb[:, 0, :], b[0][:, 0:RW], ACT.Exp)
                    act.activation(eb[:, 1, :], b[0][:, 0:RW], ACT.Exp, scale=-1.0)
                    act.activation(eb[:, 2, :], b[0][:, RW:], ACT.Exp)
                    act.activation(dec[s][:, :, :], b[1][0:64, 0:8], ACT.Exp).then_inc(expd, 1)

                def take_turned(n, s):
                    act.wait_ge(hat_t, n + 1)
                    act.activation(hatT[:, 0, :, :], b[0][0:64, :], ACT.Copy)
                    act.activation(RT[s][:, :, :], b[1][0:64, :], ACT.Copy).then_inc(hT_a, 1)

                pieces = (take, decays, take_turned)
                for piece in pieces:
                    piece(0, 0)

                def tile(n, s, more):
                    act.wait_ge(x0_t, n + 1)
                    act.activation(X[:, :, :], b[4][:, :], ACT.Copy).then_inc(X_ev, 1)
                    for m in range(LEVELS):
                        act.wait_ge(y_made, n * LEVELS + m + 1)
                        act.activation(Y[:, :, :], b[5][:, :], ACT.Copy).then_inc(y_ev, 1)
                        if more and m < len(pieces):
                            pieces[m](n + 1, 1 - s)
                    act.wait_ge(pre, n + 1)
                    act.activation(P1T[:, :, :], b[5][0:64, :], ACT.Copy).then_inc(pre_a, 1)
                    act.wait_ge(p2m, n + 1)
                    act.activation(P2[:, :], b[7][:, 0:RW], ACT.Copy).then_inc(p2e, 1)
                    act.wait_ge(osq, n + 1)
                    act.activation(sq[:, :], d[:, :], ACT.Square).then_inc(oroot, 1)
                    act.wait_ge(vsum, n + 1)
                    act.activation(v4[:, :], v4[:, :], ACT.Sqrt, scale=1.0 / 64, bias=gneps[:, :]).then_inc(vroot, 1)
                    act.wait_ge(out_t, n + 1)
                    act.activation(g.hT[:, 6:8, bass.ds(n * P, P)], b[6][:, 0:RW].rearrange("p (c t) -> p c t", c=2), ACT.Copy).then_inc(mixed, 1)
                in_order(act, tile)

            @block.vector
            def _(dve):
                dve.wait_ge(small, 16 * 6)
                dve.wait_ge(zeroed, 5)
                per_a, per_c = 5, 12

                def take(n, s):
                    dve.wait_ge(turned, n + 1)
                    dve.tensor_copy(T[:, 4:6, :], b[2][:, :])
                    dve.tensor_copy(G[s][:, :], b[3][:, 0:RW]).then_inc(ev_d, 1)
                    ch = Chain(dve, step_a, n * per_a)
                    dve.wait_ge(ev_a, n + 1)
                    ch.link(dve.tensor_tensor(kd[:, :], T[:, 3, :], T[:, 3, :], ALU.mult))
                    dve.tensor_reduce(n4[:, :], heads(kd[:, :]), AX.X, ALU.add).then_inc(sqd, 1)
                    assert ch.k == 1

                def scale(n, s):
                    ch = Chain(dve, step_a, n * per_a + 1)
                    dve.wait_ge(rooted, n + 1)
                    ch.link(dve.tensor_scalar(n4[:, :], n4[:, :], 1e-12, None, ALU.max))
                    ch.link(dve.reciprocal(n4[:, :], n4[:, :]))
                    dve.wait_ge(ev_d, n + 1)
                    ch.link(dve.tensor_tensor(heads(T[:, 3, :]), heads(T[:, 3, :]), wide(n4[:, :]), ALU.mult))
                    ch.link(dve.scalar_tensor_tensor(kd[:, :], T[:, 3, :], -1.0, T[:, 5, :], ALU.mult, ALU.mult))
                    assert ch.k + 1 == per_a
                    dve.wait_ge(expd, n + 1)
                    dve.tensor_tensor(hat[s][:, 0, :], T[:, 3, :], eb[:, 2, :], ALU.mult)
                    dve.tensor_tensor(hat[s][:, 1, :], T[:, 0, :], eb[:, 0, :], ALU.mult)
                    dve.tensor_tensor(hat[s][:, 2, :], T[:, 1, :], eb[:, 1, :], ALU.mult)
                    dve.tensor_tensor(hat[s][:, 3, :], kd[:, :], eb[:, 1, :], ALU.mult).then_inc(hats, 1)

                def take_turned(n, s):
                    dve.wait_ge(hat_t, n + 1)
                    dve.tensor_copy(hatT[:, 1, :, :], b[2][0:64, :])
                    dve.tensor_copy(hatT[:, 2, :, :], b[3][0:64, :]).then_inc(hT_d, 1)

                def mask(n, s):
                    dve.wait_ge(att, n + 1)
                    for j, m in enumerate((1, 1, 0, 0)):
                        ins = dve.tensor_tensor(AT[s][:, j, :, :], by_head(b[j][:, :]),
                                                masks[:, m, :].unsqueeze(1).broadcast_to([P, H, P]), ALU.mult)
                    ins.then_inc(masked, 1)

                pieces = (take, scale, take_turned, mask)
                for piece in pieces:
                    piece(0, 0)

                def tile(n, s, more):
                    ch = Chain(dve, step_c, n * per_c)
                    dve.wait_ge(masked, n + 1)
                    ch.link(dve.tensor_tensor(XT[:, :, :], AT[s][:, 0, :, :], levels[:, 0, :].unsqueeze(1).broadcast_to([P, H, P]), ALU.mult))
                    dve.tensor_tensor(XT[:, :, :], XT[:, :, :], g.ident[:, :].unsqueeze(1).broadcast_to([P, H, P]), ALU.add).then_inc(x0, 1)
                    for m in range(LEVELS):
                        dve.wait_ge(z_made, n * LEVELS + m + 1)
                        if m == 0:
                            dve.wait_ge(X_ev, n + 1)
                            dve.wait_ge(x0, n + 1)
                        else:
                            dve.wait_ge(xs, n * LEVELS + m)
                        if m < LEVELS - 1:
                            dve.tensor_tensor(X[:, :, :], X[:, :, :], by_head(b[6][:, :]), ALU.add)
                        dve.tensor_tensor(XT[:, :, :], XT[:, :, :], by_head(b[7][:, :]), ALU.add).then_inc(xs, 1)
                        if more and m < len(pieces):
                            pieces[m](n + 1, 1 - s)
                    dve.wait_ge(pre, n + 1)
                    dve.tensor_copy(W[:, :], b[6][:, 0:RW]).then_inc(pre_d, 1)
                    dve.wait_ge(p2e, n + 1)
                    for c in range(2):
                        toks = slice(64 * c, 64 * c + 64)
                        ds = b[5 + 2 * c][0:64, 0:RW]
                        dve.wait_ge(u_made, n * 2 + c + 1)
                        dve.tensor_tensor(Uc[toks, c, :], b[6][toks, 0:RW], P2[toks, :], ALU.add).then_inc(u_done, 1)
                        dve.wait_ge(ds_made, n * 2 + c + 1)
                        ch.link(dve.tensor_tensor(S[:, :], S[:, :], ds, ALU.add))
                        dve.tensor_tensor(heads(S[:, :]), heads(S[:, :]), dec[s][:, :, c:c + 1].broadcast_to([64, H, 64]), ALU.mult).then_inc(s_done, 1)
                        dve.wait_ge(s_done, n * 2 + c + 1)
                    dve.wait_ge(o_made, n + 1)
                    o = heads(b[4][:, 0:RW])
                    ch.link(dve.tensor_reduce(s4[:, :], o, AX.X, ALU.add))
                    ch.link(dve.tensor_scalar(s4[:, :], s4[:, :], 1.0 / 64, None, ALU.mult))
                    dve.tensor_tensor(heads(d[:, :]), o, wide(s4[:, :]), ALU.subtract).then_inc(osq, 1)
                    dve.wait_ge(oroot, n + 1)
                    dve.tensor_reduce(v4[:, :], heads(sq[:, :]), AX.X, ALU.add).then_inc(vsum, 1)
                    dve.wait_ge(bonus, n * 2 + 2)
                    ch.link(dve.tensor_reduce(bsum[:, :], heads(bo[s][:, :]), AX.X, ALU.add))
                    ch.link(dve.tensor_tensor(heads(sq[:, :]), heads(V[s][:, :]), wide(bsum[:, :]), ALU.mult))
                    dve.wait_ge(vroot, n + 1)
                    ch.link(dve.reciprocal(v4[:, :], v4[:, :]))
                    ch.link(dve.tensor_tensor(heads(d[:, :]), heads(d[:, :]), wide(v4[:, :]), ALU.mult))
                    ch.link(dve.tensor_tensor(d[:, :], d[:, :], lnw[:, :], ALU.mult))
                    ch.link(dve.tensor_tensor(d[:, :], d[:, :], lnb[:, :], ALU.add))
                    ch.link(dve.tensor_tensor(d[:, :], d[:, :], sq[:, :], ALU.add))
                    dve.tensor_tensor(d[:, :], d[:, :], G[s][:, :], ALU.mult).then_inc(out_done, 1)
                    assert ch.k == per_c, ch.k
                in_order(dve, tile)

            @block.tensor
            def _(pe):
                pe.wait_ge(small, 16 * 6)
                pe.wait_ge(zeroed, 5)

                def turn(n, s):
                    pe.wait_ge(copied, n + 1)
                    for c in range(14):
                        mm = pe.transpose(b[c // 4][:, P * (c % 4):P * (c % 4) + P], Fc[:, c, :], g.ident[:, :])
                    mm.then_inc(turned, 1)

                def sum_decays(n, s):
                    pe.wait_ge(ev_a, n + 1)
                    pe.wait_ge(ev_d, n + 1)
                    pe.matmul(b[0][:, 0:RW], masks[:, 0, :], T[:, 4, :], start=True, stop=True)
                    pe.matmul(b[0][:, RW:], masks[:, 1, :], T[:, 4, :], start=True, stop=True)
                    for h in range(H):
                        mm = pe.matmul(b[1][0:64, 2 * h:2 * h + 2], T[:, 4, 64 * h:64 * h + 64], chunk_of[:, :], start=True, stop=True)
                    mm.then_inc(cum, 1)

                def turn_hats(n, s):
                    pe.wait_ge(hats, n + 1)
                    for j in range(4):
                        for h in range(H):
                            mm = pe.matmul(b[j][0:64, P * h:P * h + P], hat[s][:, j, 64 * h:64 * h + 64], g.ident[:, :],
                                           start=True, stop=True, is_transpose=(j + h > 0))
                    mm.then_inc(hat_t, 1)

                def attend(n, s):
                    pe.wait_ge(hT_a, n + 1)
                    pe.wait_ge(hT_d, n + 1)
                    K, R, Kt, Bt = hatT[:, 0], RT[s], hatT[:, 1], hatT[:, 2]
                    for j, (left, right) in enumerate(((Bt, K), (Kt, K), (Kt, R), (Bt, R))):
                        for h in range(H):
                            mm = pe.matmul(b[j][:, P * h:P * h + P], left[:, h, :], right[:, h, :], start=True, stop=True)
                    mm.then_inc(att, 1)

                pieces = (turn, sum_decays, turn_hats, attend)
                for piece in pieces:
                    piece(0, 0)

                def tile(n, s, more):
                    pe.wait_ge(x0, n + 1)
                    for h in range(H):
                        mm = pe.transpose(b[4][:, P * h:P * h + P], XT[:, h, :], g.ident[:, :])
                    mm.then_inc(x0_t, 1)
                    for m in range(LEVELS):
                        if m == 0:
                            pe.wait_ge(X_ev, n + 1)
                        else:
                            pe.wait_ge(xs, n * LEVELS + m)
                        pe.wait_ge(lvl, n * LEVELS + m + 1)
                        for h in range(H):
                            mm = pe.matmul(b[5][:, P * h:P * h + P], Lm[:, m % 2, h, :], X[:, h, :], start=True, stop=True)
                        mm.then_inc(y_made, 1)
                        pe.wait_ge(y_ev, n * LEVELS + m + 1)
                        if m < LEVELS - 1:
                            for h in range(H):
                                pe.matmul(b[6][:, P * h:P * h + P], XT[:, h, :], Y[:, h, :], start=True, stop=True)
                        for h in range(H):
                            mm = pe.matmul(b[7][:, P * h:P * h + P], Y[:, h, :], XT[:, h, :], start=True, stop=True)
                        mm.then_inc(z_made, 1)
                        if more and m < len(pieces):
                            pieces[m](n + 1, 1 - s)
                    pe.wait_ge(xs, n * LEVELS + LEVELS)
                    for h in range(H):
                        pe.matmul(b[5][0:64, P * h:P * h + P], hat[s][:, 0, 64 * h:64 * h + 64], XT[:, h, :], start=True, stop=True)
                    for h in range(H):
                        mm = pe.matmul(b[6][:, 64 * h:64 * h + 64], AT[s][:, 1, h, :], V[s][:, 64 * h:64 * h + 64], start=True, stop=True)
                    mm.then_inc(pre, 1)
                    for h in range(H):
                        pe.matmul(b[4][:, 64 * h:64 * h + 64], AT[s][:, 2, h, :], V[s][:, 64 * h:64 * h + 64],
                                  start=(h == 0), stop=False, skip_group_check=True)
                    pe.wait_ge(pre_d, n + 1)
                    for h in range(H):
                        mm = pe.matmul(b[7][:, 64 * h:64 * h + 64], XT[:, h, :], W[:, 64 * h:64 * h + 64], start=True, stop=True)
                    mm.then_inc(p2m, 1)
                    pe.wait_ge(pre_a, n + 1)
                    for c in range(2):
                        toks = slice(64 * c, 64 * c + 64)
                        ds = b[5 + 2 * c]
                        if c:
                            pe.wait_ge(s_done, n * 2 + c)
                        for h in range(H):
                            mm = pe.matmul(b[6][:, 64 * h:64 * h + 64], P1T[:, h, :], S[:, 64 * h:64 * h + 64], start=True, stop=True)
                        mm.then_inc(u_made, 1)
                        for h in range(H):
                            pe.matmul(b[4][toks, 64 * h:64 * h + 64], RT[s][:, h, toks], S[:, 64 * h:64 * h + 64],
                                      start=False, stop=False, skip_group_check=True)
                        for h in range(H):
                            pe.matmul(ds[0:64, 64 * h:64 * h + 64], hat[s][:, 2, 64 * h:64 * h + 64], Vc[s][:, c, 64 * h:64 * h + 64],
                                      start=(h == 0), stop=False, skip_group_check=True)
                        pe.wait_ge(u_done, n * 2 + c + 1)
                        for h in range(H):
                            mm = pe.matmul(ds[0:64, 64 * h:64 * h + 64], hat[s][:, 3, 64 * h:64 * h + 64], Uc[:, c, 64 * h:64 * h + 64],
                                           start=False, stop=True, skip_group_check=True)
                        mm.then_inc(ds_made, 1)
                        for h in range(H):
                            mm = pe.matmul(b[4][:, 64 * h:64 * h + 64], AT[s][:, 3, h, :], Uc[:, c, 64 * h:64 * h + 64],
                                           start=False, stop=(c == 1), skip_group_check=True)
                    mm.then_inc(o_made, 1)
                    pe.wait_ge(out_done, n + 1)
                    for c in range(2):
                        mm = pe.transpose(b[6][:, P * c:P * c + P], d[:, P * c:P * c + P], g.ident[:, :])
                    mm.then_inc(out_t, 1)
                    pe.wait_ge(mixed, n + 1)
                in_order(pe, tile)


def mix_out(nc, a, g, x_dram):
    w_v = a["w_out_2"][0, :, :].rearrange("(k p) n -> p k n", p=P)
    with Phase(nc, "xo") as ph:
        w = ph.pair("w", [P, KD, D])
        raw = [ph.sb(f"raw{s}", [P, D]) for s in range(2)]
        gain = ph.sb("gain", [P, D])
        hc = [ph.pair(f"hc{s}", [P, KD, P]) for s in range(2)]
        sq = ph.sb("sq", [P, D])
        y = ph.sb("y", [P, D])
        ss = ph.sb("ss", [P, 2])
        po = [ph.ps(f"po{s}", [P, 1024]) for s in range(2)]
        small, raw0_in, raw1_in, w_hi, w_lo, placed, split, made, squared, rooted, recips, normed, added = ph.sems(
            "small raw0_in raw1_in w_hi w_lo placed split made squared rooted recips normed added")
        x_in = ph.sem("x_in")
        raw_in = [raw0_in, raw1_in]
        parts = [(1, META, 0, g.m), (NT, P, META, g.x)]

        with nc.Block() as block:
            @block.sync
            def _(sp):
                sp.dma_start(gain[:, :], rows(a["norm_mix_post_2"][0, :])).then_inc(small, 16)
                for k in range(KD):
                    if k >= 2:
                        sp.wait_ge(w_lo, k - 1)
                    sp.dma_start(raw[k % 2][:, :], w_v[:, k, :]).then_inc(raw_in[k % 2], 16)
                sp.dma_start(g.m[:, 0, :], a["meta_tokens_2"]).then_inc(x_in, 16)
                sp.dma_start(g.x[:, :, :], x_dram.rearrange("(t p) d -> p t d", p=P)).then_inc(x_in, 16)

            @block.gpsimd
            def _(pool):
                def place(n, s, part, t):
                    _, r, c0, _ = part
                    if not (isinstance(n, int) and n < 2):
                        pool.wait_ge(made, n - 1)
                    pool.tensor_copy(hc[s][0][:, 0:6, 0:r], g.hT[:, 0:6, bass.ds(t * P + c0, r)])
                    pool.tensor_copy(hc[s][0][:, 6:8, 0:r], g.hT[:, 6:8, bass.ds(t * P + (c0 + PADT), r)]).then_inc(placed, 1)
                in_turn(pool, parts, place, lambda *tile: None)

            @block.scalar
            def _(act):
                for k in range(KD):
                    act.wait_ge(raw_in[k % 2], k // 2 * 16 + 16)
                    act.activation(w[0][:, k, :], raw[k % 2][:, :], ACT.Copy).then_inc(w_hi, 1)

                def root(n, s, part, t):
                    r = part[1]
                    act.wait_ge(made, n + 1)
                    act.activation(sq[0:r, :], po[s][0:r, :], ACT.Square, accum_out=ss[0:r, s:s + 1]).then_inc(squared, 1)
                    act.wait_ge(squared, n + 1)
                    act.activation(ss[0:r, s:s + 1], ss[0:r, s:s + 1], ACT.Sqrt, scale=1.0 / D, bias=g.epsc[0:r, :]).then_inc(rooted, 1)
                in_turn(act, parts, root, lambda *tile: None)

            @block.vector
            def _(dve):
                for k in range(KD):
                    dve.wait_ge(w_hi, k + 1)
                    lo_part(dve, w[1][:, k, :], raw[k % 2][:, :], w[0][:, k, :]).then_inc(w_lo, 1)
                dve.wait_ge(small, 16)

                def low(n, s, part, t):
                    _, r, c0, _ = part
                    dve.wait_ge(placed, n + 1)
                    lo_part(dve, hc[s][1][:, 0:6, 0:r], g.hT[:, 0:6, bass.ds(t * P + c0, r)], hc[s][0][:, 0:6, 0:r])
                    lo_part(dve, hc[s][1][:, 6:8, 0:r], g.hT[:, 6:8, bass.ds(t * P + (c0 + PADT), r)],
                            hc[s][0][:, 6:8, 0:r]).then_inc(split, 1)

                def norm(n, s, part, t):
                    _, r, _, x = part
                    dve.wait_ge(rooted, n + 1)
                    dve.reciprocal(ss[0:r, s:s + 1], ss[0:r, s:s + 1]).then_inc(recips, 1)
                    dve.wait_ge(recips, n + 1)
                    dve.scalar_tensor_tensor(y[0:r, :], po[s][0:r, :], ss[0:r, s:s + 1], gain[0:r, :], ALU.mult, ALU.mult).then_inc(normed, 1)
                    dve.wait_ge(normed, n + 1)
                    if isinstance(n, int) and n == 0:
                        dve.wait_ge(x_in, 32)
                    dve.tensor_tensor(x[0:r, t, :], x[0:r, t, :], y[0:r, :], ALU.add).then_inc(added, 1)
                in_turn(dve, parts, low, norm)

            @block.tensor
            def _(pe):
                def multiply(n, s, part, t):
                    r = part[1]
                    pe.wait_ge(split, n + 1)
                    if not (isinstance(n, int) and n < 2):
                        pe.wait_ge(normed, n - 1)
                    for j in range(2):
                        cols = slice(512 * j, 512 * j + 512)
                        for k in range(KD):
                            if isinstance(n, int) and n == 0 and j == 0:
                                pe.wait_ge(w_lo, k + 1)
                            mm = product(pe, po[s][0:r, cols], [h[:, k, 0:r] for h in hc[s]],
                                         [h[:, k, cols] for h in w], k == 0, k == KD - 1)
                    mm.then_inc(made, 1)
                in_turn(pe, parts, multiply, lambda *tile: None)


NF = D_FF // P
CONV_F = 3
HALO = CONV_F - 1
THIRD = (T2 // 3 + 2) // 2 * 2


def ffn_up(nc, a, hT, fT):
    w_v = a["ffn_up_2"][0, :, :].rearrange("(k p) n -> p k n", p=P)

    def flat(t):
        return t[:, :, :].rearrange("p c t -> p (c t)")[:, 0:T2]

    with Phase(nc, "fu") as ph:
        w = Weights(ph, KD, P)
        cw = ph.sb("cw", [P, 2 * NF, CONV_F])
        f = [ph.sb(f"f{e}", [P, 3, THIRD]) for e in range(2)]
        pf = [ph.ps(f"pf{e}", [P, 3, 512]) for e in range(2)]
        small, made0, made1, read0, read1, conv, gelued, dstep = ph.sems(
            "small made0 made1 read0 read1 conv gelued dstep")
        made, read = [made0, made1], [read0, read1]
        with nc.Block() as block:
            @block.sync
            def _(sp):
                def load(j, e):
                    w.load(sp, j * 2 + e, lambda k0, k1: w_v[:, k0:k1, bass.ds(j * P + D_FF * e, P)])
                load(0, 0)
                with nc.allow_non_contiguous_dma(reason="the taps, feature-major"):
                    for t in range(CONV_F):
                        sp.dma_start(cw[:, :, t], a["ffn_conv_2"][0, t, :].rearrange("(j p) -> p j", p=P)).then_inc(small, 16)
                load(0, 1)
                with sp.Fori(1, NF, 1) as j:
                    for e in range(2):
                        load(j, e)

            @block.scalar
            def _(act):
                w.make_hi(act, 0, 0)

                def step(j, e, first, last):
                    if not last:
                        if not first:
                            act.wait_ge(made[1 - e], j + e)
                        w.make_hi(act, j * 2 + e + 1, 1 - e)
                    if e == 1:
                        act.wait_ge(conv, j + 1)
                        act.activation(f[0][:, :, :], f[0][:, :, :], ACT.Gelu_apprx_tanh).then_inc(gelued, 1)
                in_pairs(act, 2 * NF, step)

            @block.vector
            def _(dve):
                w.make_lo(dve, 0, 0)
                dve.wait_ge(small, 16 * CONV_F)
                for e in range(2):
                    dve.memset(pf[e][:, 0, 0:HALO], 0.0)
                    dve.memset(pf[e][:, 2, T2 - 2 * THIRD + HALO:THIRD + HALO], 0.0).then_inc(read[e], 1)
                per = 5

                def step(j, e, first, last):
                    if not last:
                        w.make_lo(dve, j * 2 + e + 1, 1 - e)
                    ch = Chain(dve, dstep, j * per + 2 * e)
                    dve.wait_ge(made[e], j + 1)
                    taps = [cw[:, bass.ds(j + NF * e, 1), t].rearrange("p a -> p a") for t in range(CONV_F)]
                    ch.link(dve.tensor_scalar(f[e][:, :, :], pf[e][:, :, 2:THIRD + 2], taps[2], None, ALU.mult))
                    ch.link(dve.scalar_tensor_tensor(f[e][:, :, :], pf[e][:, :, 1:THIRD + 1], taps[1], f[e][:, :, :], ALU.mult, ALU.add))
                    dve.scalar_tensor_tensor(f[e][:, :, :], pf[e][:, :, 0:THIRD], taps[0], f[e][:, :, :], ALU.mult, ALU.add).then_inc(read[e], 1)
                    dve.wait_ge(read[e], j + 2)
                    if e == 0:
                        dve.sem_inc(conv, 1)
                    else:
                        dve.wait_ge(gelued, j + 1)
                        ch.link(dve.tensor_tensor(fT[:, bass.ds(j, 1), :].rearrange("p a t -> p (a t)"), flat(f[0]), flat(f[1]), ALU.mult))
                in_pairs(dve, 2 * NF, step)

            @block.tensor
            def _(pe):
                with pe.Fori(0, NF, 1) as j:
                    for e in range(2):
                        w.ready(pe, j * 2 + e)
                        pe.wait_ge(read[e], j + 1)
                        for j3, (c0, c1) in enumerate(((0, THIRD), (THIRD - HALO, 2 * THIRD), (2 * THIRD - HALO, T2))):
                            at = 0 if j3 else HALO
                            for k in range(KD):
                                mm = product(pe, pf[e][:, j3, at:at + c1 - c0], w.cut(e, k, 0, P), [h[:, k, c0:c1] for h in hT],
                                             k == 0, k == KD - 1)
                        mm.then_inc(made[e], 1)


def ffn_down(nc, a, g, fT, x_dram, out):
    HALF = SEQ // 2
    HT = HALF // P
    w_v = a["ffn_down_2"][0, :, :].rearrange("(k p) n -> p k n", p=P)
    x_v = x_dram.rearrange("(t p) d -> t p d", p=P)
    out_v = out.rearrange("o (t p) d -> (o t) p d", p=P)
    with Phase(nc, "fd") as ph:
        raw = [ph.sb(f"raw{s}", [P, D]) for s in range(2)]
        w = [ph.pair(f"w{s}", [P, D]) for s in range(2)]
        fs = [ph.pair(f"fs{s}", [P, HALF]) for s in range(2)]
        gain = ph.sb("gain", [P, D])
        x = [ph.sb(f"x{t}", [P, D]) for t in range(HT)]
        y = [ph.sb(f"y{t}", [P, D]) for t in range(HT)]
        sq = ph.sb("sq", [P, D])
        ss = ph.sb("ss", [P, HT])
        po = [ph.ps(f"po{t}", [P, D]) for t in range(HT)]
        small, raw0_in, raw1_in, hi_done, lo_done, used, made, taken_a, taken_d, squared, rooted, recips, normed, added = ph.sems(
            "small raw0_in raw1_in hi_done lo_done used made taken_a taken_d squared rooted recips normed added")
        x_in, out_done = ph.sems("x_in out_done")
        raw_in = [raw0_in, raw1_in]

        def chunks(eng, half, step, between=None):
            n0 = NF * half
            for s in range(2):
                step(n0 + s, s, s, s == 0, False)
            if between:
                between()
            with eng.Fori(1, NF // 2 - 1, 1) as i:
                for s in range(2):
                    step(i * 2 + (n0 + s), s, i * 2 + s, False, False)
            for s in range(2):
                step(n0 + NF - 2 + s, s, NF - 2 + s, False, s == 1)

        with nc.Block() as block:
            @block.sync
            def _(sp):
                sp.dma_start(gain[:, :], rows(a["norm_ffn_post_2"][0, :])).then_inc(small, 16)
                for half in range(2):
                    def load(n, s, k, first, last):
                        if not (isinstance(n, int) and n < 2):
                            sp.wait_ge(lo_done, n - 1)
                        src = w_v[:, bass.ds(k, 1), :].rearrange("p a n -> p (a n)")
                        sp.dma_start(raw[s][:, :], src).then_inc(raw_in[s], 16)
                    chunks(sp, half, load)

            @block.gpsimd
            def _(pool):
                for half in range(2):
                    for t in range(HT):
                        if half:
                            pool.wait_ge(out_done, 16 * HT)
                        pool.dma_start(x[t][:, :], x_v[HT * half + t, :, :]).then_inc(x_in, 16)
                    pool.wait_ge(x_in, 16 * HT * (half + 1))
                    for t in range(HT):
                        m = HT * half + t
                        pool.wait_ge(normed, m + 1)
                        pool.tensor_tensor(x[t][:, :], x[t][:, :], y[t][:, :], ALU.add).then_inc(added, 1)
                        pool.wait_ge(added, m + 1)
                        pool.dma_start(out_v[m, :, :], x[t][:, :]).then_inc(out_done, 16)
                pool.wait_ge(out_done, 32 * HT)

            @block.scalar
            def _(act):
                def high(n, s, k, first, last):
                    act.wait_ge(raw_in[s], (n - s) * 8 + 16)
                    if not (isinstance(n, int) and n < 2):
                        act.wait_ge(used, n - 1)
                    act.activation(w[s][0][:, :], raw[s][:, :], ACT.Copy)
                    act.activation(fs[s][0][:, :], fT[:, bass.ds(k, 1), META + HALF * half:META + HALF * half + HALF].rearrange("p a t -> p (a t)"),
                                   ACT.Copy).then_inc(hi_done, 1)

                def finish(half):
                    for t in range(HT):
                        m = HT * half + t
                        act.wait_ge(taken_d, (HT // 2) * half + t // 2 + 1) if t % 2 else act.wait_ge(taken_a, (HT // 2) * half + t // 2 + 1)
                        act.activation(sq[:, :], y[t][:, :], ACT.Square, accum_out=ss[:, t:t + 1]).then_inc(squared, 1)
                        act.wait_ge(squared, m + 1)
                        act.activation(ss[:, t:t + 1], ss[:, t:t + 1], ACT.Sqrt, scale=1.0 / D, bias=g.epsc[:, :]).then_inc(rooted, 1)

                for half in range(2):
                    chunks(act, half, high, (lambda: finish(0)) if half else None)
                    act.wait_ge(made, half + 1)
                    for t in range(0, HT, 2):
                        if half:
                            act.wait_ge(normed, HT)
                            act.wait_ge(added, HT)
                        act.activation(y[t][:, :], po[t][:, :], ACT.Copy).then_inc(taken_a, 1)
                finish(1)

            @block.vector
            def _(dve):
                def low(n, s, k, first, last):
                    dve.wait_ge(hi_done, n + 1)
                    lo_part(dve, w[s][1][:, :], raw[s][:, :], w[s][0][:, :])
                    lo_part(dve, fs[s][1][:, :], fT[:, bass.ds(k, 1), META + HALF * half:META + HALF * half + HALF].rearrange("p a t -> p (a t)"),
                            fs[s][0][:, :]).then_inc(lo_done, 1)

                def finish(half):
                    for t in range(HT):
                        m = HT * half + t
                        dve.wait_ge(rooted, m + 1)
                        dve.reciprocal(ss[:, t:t + 1], ss[:, t:t + 1]).then_inc(recips, 1)
                        dve.wait_ge(recips, m + 1)
                        dve.scalar_tensor_tensor(y[t][:, :], y[t][:, :], ss[:, t:t + 1], gain[:, :], ALU.mult, ALU.mult).then_inc(normed, 1)

                dve.wait_ge(small, 16)
                for half in range(2):
                    chunks(dve, half, low, (lambda: finish(0)) if half else None)
                    dve.wait_ge(made, half + 1)
                    for t in range(1, HT, 2):
                        if half:
                            dve.wait_ge(added, HT)
                        dve.tensor_copy(y[t][:, :], po[t][:, :]).then_inc(taken_d, 1)
                finish(1)

            @block.tensor
            def _(pe):
                for half in range(2):
                    def multiply(n, s, k, first, last):
                        pe.wait_ge(lo_done, n + 1)
                        for t in range(HT):
                            if half and first:
                                pe.wait_ge(taken_d if t % 2 else taken_a, t // 2 + 1)
                            for j in range(2):
                                cols = slice(512 * j, 512 * j + 512)
                                mm = product(pe, po[t][:, cols], [h[:, P * t:P * t + P] for h in fs[s]],
                                             [h[:, cols] for h in w[s]], first, last)
                        mm.then_inc(used, 1)
                        if last:
                            pe.wait_ge(used, n + 1)
                            pe.sem_inc(made, 1)
                    chunks(pe, half, multiply)


class Held:
    pass


def program(nc, a, out, scratch, stop=99):
    g = Held()
    with ExitStack() as ctx:
        def sb(name, shape, within=ctx, side=None):
            return within.enter_context(nc.sbuf_tensor(name, shape, F32, side=side))

        g.ident = sb("ident", [P, P])
        g.epsc = sb("epsc", [P, 1])
        g.neglam = sb("neglam", [P, 1])
        g.mod_dram = scratch("mod_d", (2, 2, 3, D))
        x_mid = scratch("x_mid", (SEQ, D))
        x_spill = scratch("x_spill", (SEQ, D))
        modulation(nc, a, g)
        resident = ExitStack()
        g.x = sb("x", [P, NT, D], resident, "right")
        first = ExitStack()
        g.c = sb("c", [P, NC, D], first, "right")
        tiles1 = [(P * t, P) for t in range(NT + NC)]

        def parts1(layer):
            return [(n, x, P, c0, g.mod_dram[cond, layer, 1, :], g.mod_dram[cond, layer, 0, :], cond)
                    for cond, (n, x, c0) in enumerate(((NT, g.x, 0), (NC, g.c, SEQ)))]

        p0 = scratch("p0", (ALLT, EVEN_IN))
        o0 = scratch("o0", (ALLT, D))
        p1 = scratch("p1", (ALLT, ODD_IN))
        with ExitStack() as inner:
            hT = pair(nc, inner, "h0", [P, KD, ALLT])
            norm_turn(nc, g, "n0", hT, parts1(0), [(g.x[:, :, :], a["x"].rearrange("o (t p) d -> p (o t) d", p=P)),
                                                   (g.c[:, :, :], a["ctx"].rearrange("o (t p) d -> p (o t) d", p=P))])
            project_rows(nc, hT, "p0", tiles1, a["ab_w_in"][0, :, :], 416, 8, p0)
        if stop <= 0:
            return
        with ExitStack() as inner:
            g.hT = sb("qT", [P, KD, ALLT], inner)
            KB = sb("KB", [P, 4, ALLT], inner)
            KA = sb("KA", [P, 2, P + ALLT], inner)
            va = sb("va", [P, 1 + NT + NC, P], inner)
            vb = sb("vb", [P, NT + NC, 512], inner)
            rotate_heads(nc, a, g, p0, KB, KA, va, vb)
            window_attention(nc, a, g, KA, va, o0)
            differential_attention(nc, a, g, KB, vb, o0)
        with ExitStack() as inner:
            hT = pair(nc, inner, "h1", [P, KD, ALLT])
            merge_even(nc, a, g, hT, p0, o0)
            project_out(nc, g, "w0", hT, [(g.x, NT, 0, g.mod_dram[0, 0, 2, :]), (g.c, NC, SEQ, g.mod_dram[1, 0, 2, :])],
                        a["w_out"][0, :, :])
            norm_turn(nc, g, "n1", hT, parts1(1))
            project_rows(nc, hT, "p1", tiles1, a["gla_w_in"][0, :, :], ODD_IN // 8, 8, p1)
        if stop <= 1:
            return
        first.close()
        with ExitStack() as inner:
            O = sb("O", [P, NT, GV], inner)
            with ExitStack() as scan:
                la = sb("la", [P, NT + NC, 2 * GK], scan)
                dec = sb("dec", [P, NT + NC, 16], scan)
                log_decays(nc, a, g, p1, la, dec)
                linear_attention(nc, a, g, p1, la, dec, O)
            hT = pair(nc, inner, "h2", [P, KD, SEQ])
            merge_odd(nc, a, g, hT, p1, O)
            project_out(nc, g, "w1", hT, [(g.x, NT, 0, g.mod_dram[0, 1, 2, :])], a["w_out"][1, :, :])
        if stop <= 2:
            return
        pT = scratch("pT", (D_IN2, T2))
        pv = scratch("pv", (T2, 512))
        cum = scratch("cum", (2, FOX_HEADS, T2))
        g.m = sb("m", [META, 1, D], resident, "right")
        w2 = a["w_in_2"][0, :, :]

        def parts2(name):
            return [(1, g.m, META, 0, a[name][0, :], None, 0), (NT, g.x, P, META, a[name][0, :], None, 0)]

        with ExitStack() as inner:
            hT = pair(nc, inner, "h3", [P, KD, T2])
            norm_turn(nc, g, "n2", hT, parts2("norm_mix_pre_2"), [(g.m[:, 0, :], a["meta_tokens_2"])],
                      spill=(x_mid.rearrange("(t p) d -> p t d", p=P), g.x[:, :, :]))
            resident.close()
            project_cols(nc, hT, "ca", w2, 0, 6, pT, (2048, 8, pT[2048:2056, :]))
            project_cols(nc, hT, "cc", w2, 2056, 4, pT[2056:3080, :])
            project_rows(nc, hT, "cv", TILES2, w2[:, 1536:2048], 256, 2, pv)
        with ExitStack() as inner:
            g.hT = sb("mixT", [P, KD, ALLT], inner)
            linear_recurrence(nc, a, g, pT)
            forget_sums(nc, a, g, pT[2048:2056, :], cum)
            forgetting_attention(nc, a, g, pT, pv, cum)
            if stop <= 3:
                return
            with ExitStack() as delta:
                F = sb("F", [P, 14, TP], delta)
                delta_inputs(nc, a, g, pT, F)
                delta_rule(nc, a, g, F)
            g.x = sb("x_back", [P, NT, D], resident, "right")
            g.m = sb("m_back", [META, 1, D], resident, "right")
            mix_out(nc, a, g, x_mid)
        with ExitStack() as inner:
            fT = sb("fT", [P, NF, T2], inner)
            with ExitStack() as up:
                hT = pair(nc, up, "h4", [P, KD, T2])
                norm_turn(nc, g, "n3", hT, parts2("norm_ffn_pre_2"),
                          spill=(x_spill.rearrange("(t p) d -> p t d", p=P), g.x[:, :, :]))
                resident.close()
                ffn_up(nc, a, hT, fT)
            ffn_down(nc, a, g, fT, x_spill, out)


DEBUG = False
STOP = 99


def shape_constants():
    import numpy as np

    grid_w, m = 64, 16
    inv = 10000.0 ** (-np.arange(m, dtype=np.float32) / m)
    rope = np.zeros((2, ALLT, HD), np.float32)
    rope[0] = 1.0
    pos = np.arange(SEQ)
    for half, p in enumerate((pos // grid_w, pos % grid_w)):
        ang = p.astype(np.float32)[:, None] * inv[None, :].astype(np.float32)
        for quarter, sign in ((0, -1.0), (1, 1.0)):
            cols = slice(32 * half + 16 * quarter, 32 * half + 16 * quarter + 16)
            rope[0, :SEQ, cols] = np.cos(ang)
            rope[1, :SEQ, cols] = sign * np.sin(ang)
    q, k = np.arange(P)[:, None], np.arange(3 * P)[None, :] - P
    near = np.abs(q - k) <= P
    window = np.zeros((NT, P, 3 * P), np.float32)
    for t in range(NT):
        inside = (t * P + k >= 0) & (t * P + k < SEQ)
        window[t] = np.where(near & inside, 0.0, NEG)
    i, j = np.arange(P)[:, None], np.arange(P)[None, :]
    same = i // 64 == j // 64
    masks = np.stack([same & (i <= j), same & (i >= j), same, same & (i < j), same & (i > j)]).astype(np.float32)
    levels = np.zeros((6, P, P), np.float32)
    for n in range(6):
        b = 1 << n
        levels[n] = (i // (2 * b) == j // (2 * b)) & ((j // b) % 2 == 1) & ((i // b) % 2 == 0)
    causal = np.where(j <= i, 0.0, NEG).astype(np.float32)
    chunk_of = (np.arange(P)[:, None] // 64 == np.arange(2)[None, :]).astype(np.float32)
    return {"k_rope": rope, "k_window": window, "k_masks": masks, "k_levels": levels, "k_causal": causal,
            "k_chunk_of": chunk_of}


def kernel(**inputs):
    import numpy as np
    import concourse.bacc as bacc
    from concourse.bass_utils import run_bass_kernel_spmd as run

    nc = bacc.Bacc("TRN2", target_bir_lowering=False, num_devices=1)
    arrays, args = {}, {}
    unused = ("rwkv_v0_2", "rwkv_v_down_2", "rwkv_v_up_2")
    for name, value in {**inputs, **shape_constants()}.items():
        if name in unused:
            continue
        v = np.ascontiguousarray(value)
        arrays["in_" + name] = v
        args[name] = nc.dram_tensor("in_" + name, v.shape, mybir.dt.from_np(v.dtype), kind="ExternalInput").ap()
    out = nc.dram_tensor("out_0", (1, SEQ, D), F32, kind="ExternalOutput").ap()

    def scratch(name, shape):
        if DEBUG:
            return nc.dram_tensor("out_" + name, shape, F32, kind="ExternalOutput").ap()
        return nc.dram_tensor(name, shape, F32).ap()

    program(nc, args, out, scratch, STOP)
    r = run(nc, [arrays], core_ids=[0])
    return r.results[0]["out_0"]
```
